# Optimizing a Trainium2 kernel written in Bass

```python
import math
import jax, jax.numpy as jnp
from jax import lax
import numpy as np

D_MODEL = 1024
BATCH = 1
SEQ = 1024
DEPTH = 1
DEC_BATCH = 8
DEC_SEQ = 8
PAST_LEN = 4096
PAGE_SIZE = 128

A_HEADS = 6
A_HEAD_DIM = 64
A_WIDTH = A_HEADS * A_HEAD_DIM
DECAY_LORA = 64
ICLR_LORA = 64
GATE_LORA = 128
A_COLS = 3 * A_WIDTH + DECAY_LORA + ICLR_LORA + GATE_LORA
B_HEADS = 6
B_NOPE_DIM = 64
B_ROPE_DIM = 32
B_V_DIM = 64
B_WIDTH = B_HEADS * B_V_DIM
KV_RANK = 256
ROPE_BASE = 10000.0
B_COLS = B_HEADS * (B_NOPE_DIM + B_ROPE_DIM) + KV_RANK + B_ROPE_DIM
Q_BLOCK = 128
C_GROUPS = 4
C_GROUP_DIM = 64
C_WIDTH = C_GROUPS * C_GROUP_DIM
POOL_WINDOWS = (2, 4, 8, 16)
POOL_PREFIX = 15
IN_COLS = A_COLS + B_COLS + C_WIDTH
D_FF = 2816
CONV_WIDTH = 3
NORM_EPS = 1e-6
GN_EPS = A_HEAD_DIM * 1e-5

kernel_name = 'hymba_rwkv7_mla_pool_convglu_step'

def rmsnorm(x, g):
    xf = x.astype(jnp.float32)
    y = xf * lax.rsqrt(jnp.mean(xf * xf, axis=-1, keepdims=True) + NORM_EPS)
    return (y * g.astype(jnp.float32)).astype(x.dtype)

def rope_tables(pos):
    inv = ROPE_BASE ** (-jnp.arange(0, B_ROPE_DIM, 2, dtype=jnp.float32) / B_ROPE_DIM)
    ang = pos.astype(jnp.float32)[:, None] * inv[None, :]
    return jnp.cos(ang), jnp.sin(ang)

def apply_rope(x, cos, sin):
    xf = x.astype(jnp.float32)
    h = xf.shape[-1] // 2
    x1, x2 = xf[..., :h], xf[..., h:]
    return jnp.concatenate([x1 * cos - x2 * sin, x1 * sin + x2 * cos], axis=-1).astype(x.dtype)

def rwkv7_mix(pa, shift_prev, wkv_prev, p):
    Bn, T, _ = pa.shape
    prev = jnp.concatenate([shift_prev[:, None].astype(pa.dtype), pa[:, :-1]], axis=1)
    s = (pa + (prev - pa) * p['mu_shift']).astype(jnp.float32)
    o1, o2, o3 = A_WIDTH, 2 * A_WIDTH, 3 * A_WIDTH
    o4 = o3 + DECAY_LORA
    o5 = o4 + ICLR_LORA
    r, k, v = s[..., :o1], s[..., o1:o2], s[..., o2:o3]
    wd, ad, gd = s[..., o3:o4], s[..., o4:o5], s[..., o5:]
    w_log = -jax.nn.softplus(-(p['decay_w0'] + jnp.tanh(wd) @ p['decay_w2'])) - 0.5
    decay = jnp.exp(-jnp.exp(w_log))
    a = jax.nn.sigmoid(p['iclr_a0'] + ad @ p['iclr_a2'])
    g = jax.nn.sigmoid(gd) @ p['gate_g2']
    hd = lambda t: t.reshape(Bn, T, A_HEADS, A_HEAD_DIM)
    kk = hd(k * p['k_k'])
    kk = kk * lax.rsqrt(jnp.maximum(jnp.sum(kk * kk, axis=-1, keepdims=True), 1e-24))
    k = k * (1.0 + (a - 1.0) * p['k_a'])
    rh, kh, vh, wh, ah = hd(r), hd(k), hd(v), hd(decay), hd(a)
    xs = tuple(jnp.moveaxis(t, 1, 0) for t in (rh, wh, kh, vh, -kk, kk * ah))

    def step(S, inp):
        r_t, w_t, k_t, v_t, a_t, b_t = inp
        sa = jnp.einsum('bhij,bhj->bhi', S, a_t)
        S = S * w_t[:, :, None, :] + sa[..., None] * b_t[:, :, None, :] + v_t[..., None] * k_t[:, :, None, :]
        return S, jnp.einsum('bhij,bhj->bhi', S, r_t)

    S_T, ys = lax.scan(step, wkv_prev.astype(jnp.float32), xs)
    y = jnp.moveaxis(ys, 0, 1)
    mu = jnp.mean(y, axis=-1, keepdims=True)
    var = jnp.mean(jnp.square(y - mu), axis=-1, keepdims=True)
    y = ((y - mu) * lax.rsqrt(var + GN_EPS)).reshape(Bn, T, A_WIDTH) * p['lnx_w'] + p['lnx_b']
    bonus = (jnp.sum(rh * kh * p['r_k'], axis=-1, keepdims=True) * vh).reshape(Bn, T, A_WIDTH)
    out = (y + bonus) * g
    return out.astype(pa.dtype), pa[:, -1], S_T

def mla_mix(pb, pos, past, p):
    Bn, T, _ = pb.shape
    qn_end = B_HEADS * B_NOPE_DIM
    qr_end = qn_end + B_HEADS * B_ROPE_DIM
    c_end = qr_end + KV_RANK
    q_nope = pb[..., :qn_end].reshape(Bn, T, B_HEADS, B_NOPE_DIM)
    q_rope = pb[..., qn_end:qr_end].reshape(Bn, T, B_HEADS, B_ROPE_DIM)
    ckv = rmsnorm(pb[..., qr_end:c_end], p['kv_norm_g'])
    cos, sin = rope_tables(pos)
    q_rope = apply_rope(q_rope, cos[:, None], sin[:, None])
    kr = apply_rope(pb[..., c_end:], cos, sin)
    q_lat = jnp.einsum('bthd,chd->bthc', q_nope, p['w_uk'])
    scale = (B_NOPE_DIM + B_ROPE_DIM) ** -0.5
    f32 = jnp.float32
    if past is None:
        nb = T // Q_BLOCK
        blocks = lambda t: jnp.moveaxis(t.reshape((Bn, nb, Q_BLOCK) + t.shape[2:]), 1, 0)

        def attend(blk):
            ql, qr, qp = blk
            sc = (jnp.einsum('bqhc,bkc->bhqk', ql, ckv, preferred_element_type=f32)
                  + jnp.einsum('bqhr,bkr->bhqk', qr, kr, preferred_element_type=f32)) * scale
            sc = jnp.where(pos[None, :] <= qp[:, None], sc, -jnp.inf)
            pr = jax.nn.softmax(sc, axis=-1)
            return jnp.einsum('bhqk,bkc->bqhc', pr, ckv.astype(f32))

        o = lax.map(attend, (blocks(q_lat), blocks(q_rope), pos.reshape(nb, Q_BLOCK)))
        o_lat = jnp.moveaxis(o, 0, 1).reshape(Bn, T, B_HEADS, KV_RANK)
    else:
        ckv_past, kr_past = past
        L = ckv_past.shape[1]
        s_past = (jnp.einsum('bqhc,blc->bhql', q_lat, ckv_past, preferred_element_type=f32)
                  + jnp.einsum('bqhr,blr->bhql', q_rope, kr_past, preferred_element_type=f32)) * scale
        s_new = (jnp.einsum('bqhc,bkc->bhqk', q_lat, ckv, preferred_element_type=f32)
                 + jnp.einsum('bqhr,bkr->bhqk', q_rope, kr, preferred_element_type=f32)) * scale
        s_new = jnp.where(pos[None, :] <= pos[:, None], s_new, -jnp.inf)
        pr = jax.nn.softmax(jnp.concatenate([s_past, s_new], axis=-1), axis=-1)
        o_lat = (jnp.einsum('bhql,blc->bqhc', pr[..., :L], ckv_past.astype(f32))
                 + jnp.einsum('bhqk,bkc->bqhc', pr[..., L:], ckv.astype(f32)))
    out = jnp.einsum('bthc,chd->bthd', o_lat, p['w_uv']).reshape(Bn, T, B_WIDTH)
    return out.astype(pb.dtype), ckv, kr

def pool_mix(pc, pool_prev, pos, p):
    Bn, T, _ = pc.shape
    u = jnp.concatenate([pool_prev.astype(pc.dtype), pc], axis=1)
    uf = u.astype(jnp.float32)
    cs = jnp.concatenate([jnp.zeros((Bn, 1, C_WIDTH), jnp.float32), jnp.cumsum(uf, axis=1)], axis=1)
    end = cs[:, POOL_PREFIX + 1:]
    groups = []
    for gi, w in enumerate(POOL_WINDOWS):
        sl = slice(gi * C_GROUP_DIM, (gi + 1) * C_GROUP_DIM)
        start = cs[:, POOL_PREFIX + 1 - w:POOL_PREFIX + 1 - w + T, sl]
        cnt = jnp.minimum(pos + 1, w).astype(jnp.float32)[None, :, None]
        groups.append((end[..., sl] - start) / cnt - uf[:, POOL_PREFIX:, sl])
    d = jnp.stack(groups, axis=2)
    y = jnp.einsum('btgc,gcd->btgd', d, p['pool_w']).reshape(Bn, T, C_WIDTH) * p['pool_scale']
    return y.astype(pc.dtype), u[:, -POOL_PREFIX:]

def conv_ffn(xn, conv_prev, p):
    Bn, T, _ = xn.shape
    h = xn @ p['w_up']
    up, gate = h[..., :D_FF], h[..., D_FF:]
    gx = jnp.concatenate([conv_prev.astype(h.dtype), gate], axis=1)
    gc = p['conv_b'] + p['conv_w'][0] * gx[:, 0:T]
    for j in range(1, CONV_WIDTH):
        gc = gc + p['conv_w'][j] * gx[:, j:j + T]
    hh = jax.nn.silu(gc) * up
    return hh @ p['w_down'], gx[:, T:]

def decoder_layer(x, pos, shift_prev, wkv_prev, pool_prev, conv_prev, mla_past, p):
    xn = rmsnorm(x, p['g_mix'])
    proj = xn @ p['w_in']
    pa = proj[..., :A_COLS]
    pb = proj[..., A_COLS:A_COLS + B_COLS]
    pc = proj[..., A_COLS + B_COLS:]
    ya, shift_new, wkv_new = rwkv7_mix(pa, shift_prev, wkv_prev, p)
    yb, ckv_new, kr_new = mla_mix(pb, pos, mla_past, p)
    yc, pool_new = pool_mix(pc, pool_prev, pos, p)
    x = x + jnp.concatenate([ya, yb, yc], axis=-1) @ p['w_out']
    yf, conv_new = conv_ffn(rmsnorm(x, p['g_ffn']), conv_prev, p)
    x = x + yf
    return x, (ckv_new, kr_new, wkv_new, shift_new, pool_new, conv_new)

def stack_layers(outs, i):
    return jnp.stack([o[i] for o in outs], axis=0)

def setup_inputs(seed: int = 0) -> dict:
    key = jax.random.key(seed)
    ks = jax.random.split(key, 40)
    f32 = jnp.float32
    nrm = lambda k, shape, sc: jax.random.normal(k, shape, f32) * sc
    n_pages = PAST_LEN // PAGE_SIZE
    n_pool = (DEC_BATCH * n_pages * 5) // 4
    page_table = jax.random.permutation(ks[4], n_pool)[:DEC_BATCH * n_pages].reshape(DEC_BATCH, n_pages).astype(jnp.int32)
    return {
        'x_prompt': nrm(ks[0], (BATCH, SEQ, D_MODEL), 1.0),
        'x_sample': nrm(ks[1], (DEC_BATCH, DEC_SEQ, D_MODEL), 1.0),
        'cache_kv_latent': nrm(ks[2], (DEPTH, n_pool, PAGE_SIZE, KV_RANK), 1.0),
        'cache_k_rope': nrm(ks[3], (DEPTH, n_pool, PAGE_SIZE, B_ROPE_DIM), 1.0),
        'page_table': page_table,
        'state_wkv': nrm(ks[5], (DEPTH, DEC_BATCH, A_HEADS, A_HEAD_DIM, A_HEAD_DIM), 0.5),
        'state_shift': nrm(ks[6], (DEPTH, DEC_BATCH, A_COLS), 1.0),
        'state_pool': nrm(ks[7], (DEPTH, DEC_BATCH, POOL_PREFIX, C_WIDTH), 1.0),
        'state_conv': nrm(ks[8], (DEPTH, DEC_BATCH, CONV_WIDTH - 1, D_FF), 1.0),
        'norm_mix_g': 1.0 + nrm(ks[9], (DEPTH, D_MODEL), 0.05),
        'w_in': nrm(ks[10], (DEPTH, D_MODEL, IN_COLS), D_MODEL ** -0.5),
        'mu_shift': jax.random.uniform(ks[11], (DEPTH, A_COLS), f32),
        'decay_w0': -2.0 + nrm(ks[12], (DEPTH, A_WIDTH), 0.5),
        'decay_w2': nrm(ks[13], (DEPTH, DECAY_LORA, A_WIDTH), DECAY_LORA ** -0.5),
        'iclr_a0': nrm(ks[14], (DEPTH, A_WIDTH), 0.1),
        'iclr_a2': nrm(ks[15], (DEPTH, ICLR_LORA, A_WIDTH), ICLR_LORA ** -0.5),
        'gate_g2': nrm(ks[16], (DEPTH, GATE_LORA, A_WIDTH), GATE_LORA ** -0.5),
        'k_k': 0.85 + nrm(ks[17], (DEPTH, A_WIDTH), 0.05),
        'k_a': 1.0 + nrm(ks[18], (DEPTH, A_WIDTH), 0.05),
        'r_k': nrm(ks[19], (DEPTH, A_HEADS, A_HEAD_DIM), 0.1),
        'lnx_w': 1.0 + nrm(ks[20], (DEPTH, A_WIDTH), 0.05),
        'lnx_b': nrm(ks[21], (DEPTH, A_WIDTH), 0.02),
        'kv_norm_g': 1.0 + nrm(ks[22], (DEPTH, KV_RANK), 0.05),
        'w_uk': nrm(ks[23], (DEPTH, KV_RANK, B_HEADS, B_NOPE_DIM), KV_RANK ** -0.5),
        'w_uv': nrm(ks[24], (DEPTH, KV_RANK, B_HEADS, B_V_DIM), KV_RANK ** -0.5),
        'pool_w': nrm(ks[25], (DEPTH, C_GROUPS, C_GROUP_DIM, C_GROUP_DIM), C_GROUP_DIM ** -0.5),
        'pool_scale': 1.0 + nrm(ks[26], (DEPTH, C_WIDTH), 0.1),
        'w_out': nrm(ks[27], (DEPTH, D_MODEL, D_MODEL), D_MODEL ** -0.5),
        'norm_ffn_g': 1.0 + nrm(ks[28], (DEPTH, D_MODEL), 0.05),
        'w_up': nrm(ks[29], (DEPTH, D_MODEL, 2 * D_FF), D_MODEL ** -0.5),
        'conv_w': nrm(ks[30], (DEPTH, CONV_WIDTH, D_FF), CONV_WIDTH ** -0.5),
        'conv_b': nrm(ks[31], (DEPTH, D_FF), 0.02),
        'w_down': nrm(ks[32], (DEPTH, D_FF, D_MODEL), D_FF ** -0.5),
        'norm_final_g': 1.0 + nrm(ks[33], (D_MODEL,), 0.05),
    }

def reference(x_prompt, x_sample, cache_kv_latent, cache_k_rope, page_table, state_wkv, state_shift,
              state_pool, state_conv, norm_mix_g, w_in, mu_shift, decay_w0, decay_w2, iclr_a0, iclr_a2,
              gate_g2, k_k, k_a, r_k, lnx_w, lnx_b, kv_norm_g, w_uk, w_uv, pool_w, pool_scale, w_out,
              norm_ffn_g, w_up, conv_w, conv_b, w_down, norm_final_g):
    Bp, Tp, _ = x_prompt.shape
    Bs, Ts, _ = x_sample.shape
    past_len = page_table.shape[1] * PAGE_SIZE
    pos_p = jnp.arange(Tp, dtype=jnp.int32)
    pos_s = past_len + jnp.arange(Ts, dtype=jnp.int32)
    dt = x_prompt.dtype
    zero_shift = jnp.zeros((Bp, A_COLS), dt)
    zero_wkv = jnp.zeros((Bp, A_HEADS, A_HEAD_DIM, A_HEAD_DIM), jnp.float32)
    zero_pool = jnp.zeros((Bp, POOL_PREFIX, C_WIDTH), dt)
    zero_conv = jnp.zeros((Bp, CONV_WIDTH - 1, D_FF), dt)
    xp, xs = x_prompt, x_sample
    outs_p, outs_s = [], []
    for l in range(DEPTH):
        p = dict(g_mix=norm_mix_g[l], w_in=w_in[l], mu_shift=mu_shift[l], decay_w0=decay_w0[l],
                 decay_w2=decay_w2[l], iclr_a0=iclr_a0[l], iclr_a2=iclr_a2[l], gate_g2=gate_g2[l],
                 k_k=k_k[l], k_a=k_a[l], r_k=r_k[l], lnx_w=lnx_w[l], lnx_b=lnx_b[l],
                 kv_norm_g=kv_norm_g[l], w_uk=w_uk[l], w_uv=w_uv[l], pool_w=pool_w[l],
                 pool_scale=pool_scale[l], w_out=w_out[l], g_ffn=norm_ffn_g[l], w_up=w_up[l],
                 conv_w=conv_w[l], conv_b=conv_b[l], w_down=w_down[l])
        xp, st_p = decoder_layer(xp, pos_p, zero_shift, zero_wkv, zero_pool, zero_conv, None, p)
        ckv_past = cache_kv_latent[l][page_table].reshape(Bs, past_len, KV_RANK)
        kr_past = cache_k_rope[l][page_table].reshape(Bs, past_len, B_ROPE_DIM)
        xs, st_s = decoder_layer(xs, pos_s, state_shift[l], state_wkv[l], state_pool[l], state_conv[l],
                                 (ckv_past, kr_past), p)
        outs_p.append(st_p)
        outs_s.append(st_s)
    y_prompt = rmsnorm(xp, norm_final_g)
    y_sample = rmsnorm(xs, norm_final_g)
    return (y_prompt, y_sample,
            stack_layers(outs_p, 0), stack_layers(outs_p, 1), stack_layers(outs_p, 2),
            stack_layers(outs_p, 3), stack_layers(outs_p, 4), stack_layers(outs_p, 5),
            stack_layers(outs_s, 0), stack_layers(outs_s, 1), stack_layers(outs_s, 2),
            stack_layers(outs_s, 3), stack_layers(outs_s, 4), stack_layers(outs_s, 5))


_drawn_inputs = setup_inputs


def setup_inputs(seed=0):
    import zlib

    import numpy as np

    out = dict(_drawn_inputs(seed))
    spreads = {}
    factors = {'cache_kv_latent': 3.638,
     'cache_k_rope': 6.767,
     'k_k': 3.243,
     'lnx_w': 3.591,
     'lnx_b': 8.0,
     'conv_b': 6.088}
    for name, (base, spread) in spreads.items():
        noise = np.random.default_rng([zlib.crc32(name.encode()), seed]).standard_normal(out[name].shape)
        drawn = base * np.exp(spread * noise) if base else spread * noise
        out[name] = __import__('jax').numpy.asarray(drawn.astype(out[name].dtype))
    for name, factor in factors.items():
        out[name] = (out[name] * factor).astype(out[name].dtype)
    return out
```

```python
from contextlib import ExitStack

import numpy as np
import concourse.bass as bass
from concourse import mybir

ALU = mybir.AluOpType
ACT = mybir.ActivationFunctionType
AX_X = mybir.AxisListType.X
F32 = mybir.dt.float32
F32R = mybir.dt.float32r
I32 = mybir.dt.int32

P = 128
D = 1024
KD = D // P
SEQ = 1024
NB = 8
TS = 8
NS = NB * TS
T = SEQ + NS
TT = (T + P - 1) // P
TPAD = TT * P
NPAGE = 32
PAGE = 128
NPOOL = 320
H = 6
HD = 64
AW = H * HD
A_COLS = 3 * AW + 256
A_TILES = A_COLS // P
RANK = 256
ROPE = 32
CW = 256
PRE = 15
IN_COLS = 2528
DFF = 2816
FT = DFF // P
EPS = 1e-6
GN_EPS = HD * 1e-5
SCALE = float(HD + ROPE) ** -0.5
CHUNK = 64
DECAY = -float(np.exp(-0.5))
CH = [(0, 384), (384, 384), (768, 320)]
NEG = -1e30

OUT_SHAPES = [(1, SEQ, D), (NB, TS, D), (1, 1, SEQ, RANK), (1, 1, SEQ, ROPE), (1, 1, H, HD, HD), (1, 1, A_COLS),
              (1, 1, PRE, CW), (1, 1, 2, DFF), (1, NB, TS, RANK), (1, NB, TS, ROPE), (1, NB, H, HD, HD),
              (1, NB, A_COLS), (1, NB, PRE, CW), (1, NB, 2, DFF)]

VEC = {}
for _name, _n in (("mu_shift", 11), ("decay_w0", 3), ("iclr_a0", 3), ("k_k", 3), ("k_a", 3), ("r_k", 3),
                  ("kv_norm_g", 2), ("pool_scale", 2), ("norm_ffn_g", 8), ("conv_b", 22), ("conv_w", 66)):
    VEC[_name] = (sum(n for _, n in VEC.values()), _n)
NVEC = sum(n for _, n in VEC.values())

CONST = {}
for _name, _n in (("ident", P), ("ones", P), ("head_ones", P), ("rot", P), ("keep_p", 2 * P), ("keep_s", 2 * P),
                  ("diag_p", P), ("diag_s", P), ("diag_pT", P), ("diag_sT", P), ("off_p", P), ("off_s", P),
                  ("causal", P), ("inv_w", 2), ("inv_cnt", 32), ("seq_of", 8), ("head_sel", 2)):
    CONST[_name] = (sum(n for _, n in CONST.values()), _n)
NCONST = sum(n for _, n in CONST.values())


def constants():
    f = np.float32
    c = np.zeros((P, NCONST), f)

    def put(name, a):
        c[:, CONST[name][0]:CONST[name][0] + CONST[name][1]] = a

    i = np.arange(P)
    s, t = i[:, None], i[None, :]
    put("ident", s == t)
    put("ones", 1.0)
    put("head_ones", s // HD == t // HD)
    rot = np.zeros((P, P), f)
    for m in range(P):
        if m % ROPE < ROPE // 2:
            rot[m + ROPE // 2, m] = -1.0
        else:
            rot[m - ROPE // 2, m] = 1.0
    put("rot", rot)
    for tag, chunk, block in (("p", CHUNK, 16), ("s", TS, TS)):
        same = s // chunk == t // chunk
        put("keep_" + tag, np.concatenate([same & (s < t), same & (s <= t)], 1))
        put("diag_" + tag, s // block == t // block)
        put("diag_" + tag + "T", s // block == t // block)
        put("off_" + tag, s // block != t // block)
    put("causal", np.where(t <= s, 0.0, NEG))
    win = np.array([[2, 8], [4, 16]], f)[i // HD]
    put("inv_w", 1.0 / win)
    pos = np.arange(16)
    put("inv_cnt", (win[:, :, None] / np.minimum(pos[None, None] + 1, win[:, :, None])).reshape(P, 32))
    put("seq_of", (i[:, None] // TS == np.arange(NB)[None]) & (i[:, None] < NS))
    put("head_sel", (i[:, None] // HD == np.arange(2)[None]))
    pos = np.concatenate([np.arange(SEQ), NPAGE * PAGE + np.tile(np.arange(TS), NB)]).astype(f)
    inv = (f(10000.0) ** (-np.arange(0, ROPE, 2, dtype=f) / f(ROPE))).astype(f)
    ang = (pos[:, None] * inv[None]).astype(f)
    rope = np.stack([np.tile(np.cos(ang).T, (8, 1)), np.tile(np.sin(ang).T, (8, 1))], 1).astype(f)
    fresh = np.ones((P, TPAD), f)
    fresh[:, 0:SEQ:CHUNK] = 0.0
    fresh[:, SEQ::TS] = 0.0
    b = np.arange(NB)
    key = np.arange(NS)
    q = np.arange(H * TS)
    new = (key[None, None] // TS == b[None, :, None]) & (key[None, None] % TS <= q[:, None, None] % TS)
    newmask = np.where(new, 0.0, NEG).astype(f).reshape(H * TS, NB * NS)
    return {"c_const": c, "c_rope": rope, "c_fresh": fresh, "c_newmask": newmask}


def build(nc, I, outs, upto="all"):
    (y_prompt, y_sample, kv_p, kr_p, wkv_p, shift_p, pool_p, conv_p, kv_s, kr_s, wkv_s, shift_s, pool_s,
     conv_s) = outs
    ctx = ExitStack()
    with ctx:
        def sb(name, words, dt=F32, parts=P):
            return ctx.enter_context(nc.sbuf_tensor(name, [parts, words], dt))

        stage_sems = []

        def sem(name):
            stage_sems.append(nc.alloc_semaphore(name))
            return stage_sems[-1]

        s_po, s_wo, s_co = (nc.alloc_semaphore(n) for n in ("pool_shift_out", "states_out", "history_out"))
        s_nat = [nc.alloc_semaphore(f"rows_out{i}") for i in range(2)]
        s_y = [nc.alloc_semaphore(f"final_out{i}") for i in range(3)]

        def new_stage():
            nc.clear_and_free_semaphores(list(stage_sems))
            stage_sems.clear()
            nc.all_engine_barrier()

        PS = [ctx.enter_context(nc.psum_tensor(f"bank{i}", [P, 512], F32)) for i in range(8)]

        R0 = 0
        RA = R0 + KD * T
        RS = RA + KD * T
        RC = RS + A_TILES * TPAD
        RW = RC + (NCONST + 7) // 8 * 8
        RM = RW + 4 * KD * P
        RK_ = RM + 1632
        WORK = 15296
        arena = sb("arena", RK_ + WORK)
        base = 16512

        def lay(name, word, words, dt=F32):
            assert word % 8 == 0 and word + words <= RK_ + WORK, (name, word, words)
            return nc.alloc_sbuf_tensor_at(name, [P, words], dt, offset=base + 4 * word)

        res = lay("residualT", R0, KD * T)
        actA = lay("mixedT", RA, KD * T)
        sT_ = lay("rwkv_streamsT", RS, A_TILES * TPAD)
        con = lay("constants", RC, NCONST)
        wring = lay("weight_ring", RW, 4 * KD * P)
        small = lay("small", RM, 1632)
        work = lay("work", RK_, WORK)

        xT = res[:, :].rearrange("p (k t) -> p k t", k=KD)
        mixT = actA[:, :].rearrange("p (k t) -> p k t", k=KD)
        sT = sT_[:, :].rearrange("p (m t) -> p m t", m=A_TILES)
        spill = nc.dram_tensor("residual_spill", (P, KD, T), F32, kind="Internal").ap()

        def tiled(ap, k=KD):
            return ap.rearrange("p (k t) -> p k t", k=k)

        def split_pair(name, word_hi, word_lo, words, k):
            hi, lo = lay(name + "_hi", word_hi, words, F32R), lay(name + "_lo", word_lo, words, F32R)
            return tiled(hi[:, :], k), tiled(lo[:, :], k)

        def product(pe, out, w, x, first, last):
            pe.matmul(out, w[0], x[0], start=first, stop=False)
            pe.matmul(out, w[1], x[0], start=False, stop=False)
            return pe.matmul(out, w[0], x[1], start=False, stop=last)

        def C(name):
            return con[:, CONST[name][0]:CONST[name][0] + CONST[name][1]]

        ident, ones = C("ident"), C("ones")
        at = [0]

        def piece(n):
            at[0] += n
            assert at[0] <= 1632, at
            return small[:, at[0] - n:at[0]]

        vecs = piece(NVEC + 2)[:, 0:NVEC]
        shiftT = piece(A_TILES * NB).rearrange("p (m b) -> p m b", m=A_TILES)
        lnx = piece(6)
        poolT = piece(2 * 120).rearrange("p (m q) -> p m q", m=2)
        convT = piece(FT * 16).rearrange("p (m q) -> p m q", m=FT)
        stat = piece(32)
        epsc = piece(4)
        ckv_new = piece(RANK)[0:NS, :]
        ckvT_new = piece(2 * NS).rearrange("p (k t) -> p k t", k=2)
        krT_new = piece(NS)
        halves = piece(9)
        shift_out = piece(9 * A_TILES).rearrange("p (j m) -> p j m", m=A_TILES)

        def vec(name, k):
            return vecs[:, VEC[name][0] + k:VEC[name][0] + k + 1]

        def chain(eng, signal):
            count = [0]

            def link(ins):
                count[0] += 1
                ins.then_inc(signal, 1)
                eng.wait_ge(signal, count[0])
            return link

        class Carve:
            def __init__(self, base=0):
                self.at = base

            def take(self, n):
                self.at += n
                assert self.at <= WORK, self.at
                return work[:, self.at - n:self.at]

        xn = split_pair("normedT", R0, RA, KD * T, KD)
        xraw = [sT_[:, i * D:(i + 1) * D].rearrange("p (k t) -> p k t", k=KD) for i in range(2)]
        s_xo = [sem(f"x_spilled{i}") for i in range(2)]
        c_hi = sem("norm_hi")
        cw = Carve()
        xin = [cw.take(D) for _ in range(3)]
        xsc = [cw.take(D) for _ in range(2)]
        sq_junk = cw.take(D)
        g_rows = cw.take(D)
        vrows = cw.take(P)
        shrows = cw.take(A_COLS)
        cvrows = cw.take(DFF)
        plrows = cw.take(CW)
        s_const, s_vec, s_st, s_g = sem("consts_in"), sem("vectors_in"), sem("states_in"), sem("gain_in")
        s_x = [sem(f"x_in{i}") for i in range(3)]
        x_sq, x_rt, x_rs, x_sc = sem("x_squared"), sem("x_root"), sem("x_recip"), sem("x_scaled")
        t_raw, t_nrm, c_raw, c_nrm = sem("raw_turned"), sem("norm_turned"), sem("raw_copied"), sem("norm_copied")
        t_vec, c_vec, t_st, c_st = sem("vec_turned"), sem("vec_copied"), sem("state_turned"), sem("state_copied")
        s_eps = sem("eps_set")

        def rows_of(i):
            return P if i < TT - 1 else NS

        with nc.Block() as block:
            def copy_raw(act, i):
                n = rows_of(i)
                act.wait_ge(t_raw, i + 1)
                if i >= 2:
                    act.wait_ge(s_xo[i % 2], 16 * (i // 2))
                for j in range(2):
                    nc.scalar.copy(xraw[i % 2][:, 4 * j:4 * j + 4, 0:n],
                                   tiled(PS[4 * (i % 2) + j][:, :], 4)[:, :, 0:n]).then_inc(c_raw, 1)

            def spill_x(sp, i):
                n = rows_of(i)
                sp.wait_ge(c_raw, 2 * i + 2)
                sp.dma_start(spill[:, :, i * P:i * P + n], xraw[i % 2][:, :, 0:n]).then_inc(s_xo[i % 2], 16)

            def norm_hi(act, i):
                n = rows_of(i)
                act.wait_ge(t_nrm, i + 1)
                for j in range(2):
                    nc.scalar.copy(xn[0][:, 4 * j:4 * j + 4, i * P:i * P + n],
                                   tiled(PS[4 * (i % 2) + 2 + j][:, :], 4)[:, :, 0:n]).then_inc(c_hi, 1)

            def norm_lo(dve, i):
                n = rows_of(i)
                for j in range(2):
                    dve.wait_ge(c_hi, 2 * i + j + 1)
                    at_ = (slice(None), slice(4 * j, 4 * j + 4), slice(i * P, i * P + n))
                    dve.tensor_tensor(xn[1][at_], tiled(PS[4 * (i % 2) + 2 + j][:, :], 4)[:, :, 0:n],
                                      xn[0][at_].bitcast(F32), ALU.subtract).then_inc(c_nrm, 1)

            @block.sync
            def _(sp):
                for i in range(TT):
                    n = rows_of(i)
                    if i >= 3:
                        sp.wait_ge(t_raw, i - 2)
                        sp.wait_ge(x_sc, i - 2)
                    src = I["x_prompt"][0, i * P:(i + 1) * P, :] if i < TT - 1 else \
                        I["x_sample"].rearrange("b t d -> (b t) d")
                    sp.dma_start(xin[i % 3][0:n, :], src).then_inc(s_x[i % 3], 16)
                    if i == 0:
                        sp.dma_start(con[:, :], I["c_const"]).then_inc(s_const, 16)
                    if i >= 2:
                        spill_x(sp, i - 2)
                for i in (TT - 2, TT - 1):
                    spill_x(sp, i)
                sp.wait_ge(s_xo[0], 16 * 5)
                sp.wait_ge(s_xo[1], 16 * 4)

            @block.scalar
            def _(act):
                act.dma_start(g_rows, I["norm_mix_g"][0, :].partition_broadcast(P)).then_inc(s_g, 16)
                for name, (a, n) in VEC.items():
                    src = I[name]
                    src = src.rearrange({2: "l d -> (l d)", 3: "l a d -> (l a d)"}[len(src.shape)])
                    act.dma_start(vrows[a:a + n, :], src.rearrange("(a p) -> a p", p=P)).then_inc(s_vec, 16)
                act.dma_start(shrows[0:NB, :], I["state_shift"][0]).then_inc(s_st, 16)
                act.dma_start(plrows[0:120, :], I["state_pool"][0].rearrange("b t c -> (b t) c")).then_inc(s_st, 16)
                for j, name in enumerate(("lnx_w", "lnx_b")):
                    act.dma_start(plrows[120 + 3 * j:123 + 3 * j, 0:P],
                                  I[name][0].rearrange("(a p) -> a p", p=P)).then_inc(s_st, 16)
                act.dma_start(cvrows[0:16, :], I["state_conv"][0].rearrange("b t c -> (b t) c")).then_inc(s_st, 16)
                act.wait_ge(s_eps, 1)
                for i in range(TT):
                    n = rows_of(i)
                    act.wait_ge(s_x[i % 3], 16 * (i // 3 + 1))
                    if i >= 1:
                        act.wait_ge(x_sq, i)
                    nc.scalar.activation(sq_junk[0:n, :], xin[i % 3][0:n, :], ACT.Square,
                                         accum_out=stat[0:n, i:i + 1]).then_inc(x_sq, 1)
                    act.wait_ge(x_sq, i + 1)
                    nc.scalar.activation(stat[0:n, 10 + i:11 + i], stat[0:n, i:i + 1], ACT.Sqrt,
                                         bias=epsc[0:n, 0:1], scale=1.0 / D).then_inc(x_rt, 1)
                    if i >= 1:
                        copy_raw(act, i - 1)
                        norm_hi(act, i - 1)
                copy_raw(act, TT - 1)
                norm_hi(act, TT - 1)

            @block.vector
            def _(dve):
                dve.memset(epsc[:, 0:1], EPS)
                dve.memset(epsc[:, 1:2], GN_EPS)
                dve.memset(epsc[:, 2:3], 1e-24).then_inc(s_eps, 1)
                dve.wait_ge(t_vec, 1)
                dve.tensor_copy(vecs, PS[6][:, 0:NVEC]).then_inc(c_vec, 1)
                dve.wait_ge(t_st, 1)
                dve.tensor_copy(shiftT, PS[6][:, 128:216].rearrange("p (m b) -> p m b", b=NB)).then_inc(c_st, 1)
                dve.tensor_copy(poolT[:, 0], PS[6][:, 216:336])
                dve.tensor_copy(lnx, PS[6][:, 336:342])
                dve.tensor_copy(poolT[:, 1], PS[6][:, 342:462]).then_inc(c_st, 1)
                dve.tensor_copy(convT, PS[7][:, 0:352].rearrange("p (m q) -> p m q", m=FT)).then_inc(c_st, 1)
                dve.wait_ge(s_g, 16)
                for i in range(TT):
                    n = rows_of(i)
                    dve.wait_ge(x_rt, i + 1)
                    dve.reciprocal(stat[0:n, 20 + i:21 + i], stat[0:n, 10 + i:11 + i]).then_inc(x_rs, 1)
                    dve.wait_ge(x_rs, i + 1)
                    if i >= 2:
                        dve.wait_ge(t_nrm, i - 1)
                    dve.scalar_tensor_tensor(out=xsc[i % 2][0:n, :], in0=xin[i % 3][0:n, :],
                                             scalar=stat[0:n, 20 + i:21 + i], in1=g_rows[0:n, :],
                                             op0=ALU.mult, op1=ALU.mult).then_inc(x_sc, 1)
                    if i >= 1:
                        norm_lo(dve, i - 1)
                norm_lo(dve, TT - 1)

            @block.tensor
            def _(pe):
                pe.wait_ge(s_const, 16)
                pe.wait_ge(s_vec, 16 * len(VEC))
                pe.transpose(PS[6][:, 0:NVEC], vrows[0:NVEC, :], ident[0:NVEC, 0:NVEC]).then_inc(t_vec, 1)
                pe.wait_ge(s_st, 80)
                pe.wait_ge(c_vec, 1)
                for m in range(A_TILES):
                    pe.transpose(PS[6][:, 128 + NB * m:128 + NB * m + NB], shrows[0:NB, m * P:(m + 1) * P],
                                 ident[0:NB, 0:NB])
                for m, n in enumerate((126, 120)):
                    pe.transpose(PS[6][:, 216 + 126 * m:216 + 126 * m + n], plrows[0:n, m * P:(m + 1) * P],
                                 ident[0:n, 0:n])
                for m in range(FT):
                    last = pe.transpose(PS[7][:, 16 * m:16 * m + 16], cvrows[0:16, m * P:(m + 1) * P],
                                        ident[0:16, 0:16])
                last.then_inc(t_st, 1)
                for i in range(TT):
                    n = rows_of(i)
                    for which, (src, b0) in enumerate(((xin[i % 3], 0), (xsc[i % 2], 2))):
                        if which == 0:
                            pe.wait_ge(s_x[i % 3], 16 * (i // 3 + 1))
                        else:
                            pe.wait_ge(x_sc, i + 1)
                            if i == 1:
                                pe.wait_ge(c_st, 3)
                        if i >= 2:
                            pe.wait_ge(c_raw if which == 0 else c_nrm, 2 * (i - 1))
                        for k in range(KD):
                            bank = PS[4 * (i % 2) + b0 + k // 4]
                            last = pe.transpose(bank[:, (k % 4) * P:(k % 4) * P + n], src[0:n, k * P:(k + 1) * P],
                                                ident[0:n, 0:n])
                        last.then_inc(t_raw if which == 0 else t_nrm, 1)
        if upto == "load":
            return

        new_stage()
        A, B = A_COLS, A_COLS + 864
        tiles = [([(m * P, P)], ("rwkv", m)) for m in range(A_TILES)]
        tiles += [([(B + m * P, P)], ("pool", m)) for m in range(2)]
        tiles += [([(A + m * P, P)], ("qn", m)) for m in range(3)]
        tiles += [([(A + 384, P)], ("rope", 0)), ([(A + 512, 64), (A + 832, 32)], ("rope", 1)),
                  ([(A + 576, P)], ("ckv", 0)), ([(A + 704, P)], ("ckv", 1))]
        cw = Carve()
        ckv = cw.take(2 * T).rearrange("p (k t) -> p k t", k=2)
        rp = cw.take(2 * T).rearrange("p (k t) -> p k t", k=2)
        qn = cw.take(3 * T).rearrange("p (k t) -> p k t", k=3)
        mla_end = cw.at
        LW = PRE + SEQ + NB * (PRE + TS)
        pl = cw.take(2 * LW).rearrange("p (m w) -> p m w", m=2)
        pool_end = cw.at
        PW = 1 + SEQ + NB * (TS + 1)
        pring = [cw.take(PW) for _ in range(2)]
        w_in = I["w_in"][0].rearrange("(k p) c -> p k c", p=P)
        assert cw.at <= WORK - 2 * KD * P
        wraw = [tiled(work[:, WORK - (2 - i) * KD * P:][:, 0:KD * P]) for i in range(2)]
        w_in_sem = [sem(f"w_in{i}") for i in range(2)]
        w_hi, w_lo = sem("w_in_hi"), sem("w_in_lo")
        widths = [sum(n for _, n in c) for c, _ in tiles]
        proj_mm, proj_cp, mixed, prep, diffed = (sem("proj_ready"), sem("proj_copied"), sem("shift_mixed"),
                                                 sem("prefix_set"), sem("shift_diff"))
        pieces = [len(c) for c, _ in tiles]

        def seg(ap, pre):
            return (ap[:, pre:pre + SEQ],
                    ap[:, pre + SEQ:pre + SEQ + NB * (pre + TS)].rearrange("p (b w) -> p b w", b=NB))

        wsp = [split_pair(f"w{i}", RW + i * 2 * KD * P, RW + (i * 2 + 1) * KD * P, KD * P, KD) for i in range(2)]

        def split_hi(i, m, raw, done, free, per):
            act = nc.scalar
            if i >= 2:
                act.wait_ge(free, per * (i - 1))
            act.copy(wsp[i % 2][0][:, 0:m[0], 0:m[1]], raw[:, 0:m[0], 0:m[1]]).then_inc(done, 1)

        def split_lo(i, m, raw, hi_done, done):
            dve = nc.vector
            dve.wait_ge(hi_done, i + 1)
            dve.tensor_tensor(wsp[i % 2][1][:, 0:m[0], 0:m[1]], raw[:, 0:m[0], 0:m[1]],
                              wsp[i % 2][0][:, 0:m[0], 0:m[1]].bitcast(F32), ALU.subtract).then_inc(done, 1)

        with nc.Block() as block:
            def in_hi(act, i):
                act.wait_ge(w_in_sem[i % 2], 16 * sum(pieces[i % 2:i + 1:2]))
                split_hi(i, (KD, widths[i]), wraw[i % 2], w_hi, proj_mm, 3)

            def in_lo(dve, i):
                split_lo(i, (KD, widths[i]), wraw[i % 2], w_hi, w_lo)

            @block.sync
            def _(sp):
                for i, (cols, _) in enumerate(tiles):
                    if i >= 2:
                        sp.wait_ge(w_lo, i - 1)
                    o = 0
                    for c, n in cols:
                        sp.dma_start(wraw[i % 2][:, :, o:o + n], w_in[:, :, c:c + n]).then_inc(w_in_sem[i % 2], 16)
                        o += n

            @block.tensor
            def _(pe):
                for i, (cols, _) in enumerate(tiles):
                    m = sum(n for _, n in cols)
                    pe.wait_ge(w_lo, i + 1)
                    for c, (t0, n) in enumerate(CH):
                        g = 3 * i + c
                        if g >= 8:
                            pe.wait_ge(proj_cp, g - 7)
                        for k in range(KD):
                            last = product(pe, PS[g % 8][0:m, 0:n], [w[:, k, 0:m] for w in wsp[i % 2]],
                                           [x[:, k, t0:t0 + n] for x in xn], k == 0, k == KD - 1)
                        last.then_inc(proj_mm, 1)

            @block.scalar
            def _(act):
                in_hi(act, 0)
                for i, (cols, (kind, j)) in enumerate(tiles):
                    if i + 1 < len(tiles):
                        in_hi(act, i + 1)
                    m = sum(n for _, n in cols)
                    if kind == "rwkv":
                        act.wait_ge(prep, 1)
                        if j >= 2:
                            act.wait_ge(mixed, j - 1)
                        p_seq, s_seq = seg(pring[j % 2], 1)
                        s_seq = s_seq[:, :, 1:]
                    elif kind == "pool":
                        p_seq, s_seq = seg(pl[:, j], PRE)
                        s_seq = s_seq[:, :, PRE:]
                    else:
                        dst = {"qn": qn, "rope": rp, "ckv": ckv}[kind][:, j]
                        p_seq, s_seq = dst[0:m, 0:SEQ], dst[0:m, SEQ:T]
                    for c, (t0, n) in enumerate(CH):
                        g = 3 * i + c
                        act.wait_ge(proj_mm, g + 1)
                        bank = PS[g % 8]
                        k = min(n, SEQ - t0)
                        ins = nc.scalar.copy(p_seq[0:m, t0:t0 + k], bank[0:m, 0:k])
                        if c == 2:
                            src = bank[0:m, k:k + NS]
                            if kind in ("rwkv", "pool"):
                                src = src.rearrange("p (b t) -> p b t", b=NB)
                            ins = nc.scalar.copy(s_seq, src)
                        ins.then_inc(proj_cp, 1)

            @block.gpsimd
            def _(pool):
                for j in range(2):
                    nc.gpsimd.memset(pring[j][:, 0:1], 0.0)
                    nc.gpsimd.memset(pl[:, j, 0:PRE], 0.0)
                nc.gpsimd.memset(sT[:, :, T:TPAD], 0.0).then_inc(prep, 1)
                for j in range(2):
                    nc.gpsimd.tensor_copy(seg(pl[:, j], PRE)[1][:, :, 0:PRE],
                                          poolT[:, j].rearrange("p (b t) -> p b t", b=NB)).then_inc(prep, 1)

            @block.vector
            def _(dve):
                in_lo(dve, 0)
                in_lo(dve, 1)
                for m in range(A_TILES):
                    buf = pring[m % 2]
                    p_cur, s_all = seg(buf, 1)
                    dve.tensor_copy(s_all[:, :, 0], shiftT[:, m, :]).then_inc(diffed, 1)
                    dve.wait_ge(diffed, 3 * m + 1)
                    dve.wait_ge(proj_cp, 3 * (m + 1))
                    dve.wait_ge(prep, 1)
                    s_new = sT[:, m, SEQ:T].rearrange("p (b t) -> p b t", b=NB)
                    dve.tensor_tensor(sT[:, m, 0:SEQ], buf[:, 0:SEQ], p_cur, ALU.subtract).then_inc(diffed, 1)
                    dve.tensor_tensor(s_new, s_all[:, :, 0:TS], s_all[:, :, 1:], ALU.subtract).then_inc(diffed, 1)
                    dve.tensor_copy(shift_out[:, 0:1, m], p_cur[:, SEQ - 1:SEQ])
                    dve.tensor_copy(shift_out[:, 1:9, m], s_all[:, :, TS])
                    dve.wait_ge(diffed, 3 * m + 3)
                    dve.scalar_tensor_tensor(out=sT[:, m, 0:SEQ], in0=sT[:, m, 0:SEQ], scalar=vec("mu_shift", m),
                                             in1=p_cur, op0=ALU.mult, op1=ALU.add)
                    dve.scalar_tensor_tensor(out=s_new, in0=s_new, scalar=vec("mu_shift", m), in1=s_all[:, :, 1:],
                                             op0=ALU.mult, op1=ALU.add).then_inc(mixed, 1)
                    in_lo(dve, m + 2)
                for i in range(A_TILES + 2, len(tiles)):
                    in_lo(dve, i)
        if upto == "proj":
            return

        new_stage()
        cw = Carve(pool_end)
        sumA, sumB = cw.take(LW), cw.take(LW)
        dT = wring[:, 0:2 * T].rearrange("p (m t) -> p m t", m=2)
        pool_w = wring[:, 2 * T:2 * T + 256].rearrange("p (m c) -> p m c", m=2)
        po = wring[:, 2 * T + 256:2 * T + 256 + 270]
        po_p, po_s = po[:, 0:30], po[:, 30:270]
        po_nat = wring[:, 2 * T + 526:2 * T + 526 + 3 * P].rearrange("p (q c) -> p q c", q=3)
        ends, sh_nat = sem("pool_steps"), wring[:, 2 * T + 910:2 * T + 910 + P]
        s_pw0, s_pw, pool_mm, pool_cp, po_ready, po_t, po_cp = (
            sem("pool_w_cleared"), sem("pool_w_in"), sem("pool_product"),
            sem("pool_scaled"), sem("pool_tail_ready"), sem("pool_tail_turned"), sem("pool_tail_copied"))
        with nc.Block() as block:
            @block.gpsimd
            def _(pool):
                nc.gpsimd.memset(pool_w, 0.0).then_inc(s_pw0, 1)

            @block.sync
            def _(sp):
                sp.wait_ge(s_pw0, 1)
                for g in range(4):
                    r = HD * (g % 2)
                    sp.dma_start(pool_w[r:r + HD, g // 2, r:r + HD], I["pool_w"][0, g]).then_inc(s_pw, 16)
                sp.wait_ge(po_cp, 4)
                sp.dma_start(pool_p[0, 0].rearrange("t (m c) -> (t m) c", m=2), po_nat[0:30, 0]).then_inc(s_po, 16)
                flat = pool_s[0].rearrange("b t (m c) -> (b t m) c", m=2)
                for q in range(2):
                    sp.dma_start(flat[120 * q:120 * q + 120, :], po_nat[0:120, 1 + q]).then_inc(s_po, 16)
                sp.dma_start(shift_p[0].rearrange("a (m c) -> (a m) c", c=P), sh_nat[0:A_TILES, :]).then_inc(s_po, 16)
                sp.dma_start(shift_s[0].rearrange("b (m c) -> (b m) c", c=P),
                             sh_nat[A_TILES:9 * A_TILES, :]).then_inc(s_po, 16)
                sp.wait_ge(s_po, 80)

            @block.vector
            def _(dve):
                link = chain(dve, ends)
                for m in range(2):
                    u = pl[:, m]
                    dve.tensor_copy(po_p.rearrange("p (t m) -> p t m", m=2)[:, :, m], u[:, SEQ:PRE + SEQ])
                    dve.tensor_copy(po_s.rearrange("p (b t m) -> p b t m", b=NB, m=2)[:, :, :, m],
                                    seg(u, PRE)[1][:, :, TS:]).then_inc(po_ready, 1)
                    link(dve.tensor_tensor(sumA[:, 1:], u[:, 1:], u[:, :LW - 1], ALU.add))
                    if m == 0:
                        link(dve.tensor_tensor(sumB[:, 3:], sumA[:, 3:], sumA[:, 1:LW - 2], ALU.add))
                    else:
                        link(dve.tensor_tensor(sumB[:, 3:], sumA[:, 3:], sumA[:, 1:LW - 2], ALU.add))
                        link(dve.tensor_tensor(sumA[:, 7:], sumB[:, 7:], sumB[:, 3:LW - 4], ALU.add))
                        link(dve.tensor_tensor(sumB[HD:, 15:], sumA[HD:, 15:], sumA[HD:, 7:LW - 8], ALU.add))
                    for r, src in ((0, sumA), (HD, sumB)):
                        rows = slice(r, r + HD)
                        link(dve.tensor_tensor(src[rows, PRE:PRE + 16], src[rows, PRE:PRE + 16],
                                               C("inv_cnt")[rows, 16 * m:16 * m + 16], ALU.mult))
                        dve.scalar_tensor_tensor(out=dT[rows, m, 0:SEQ], in0=seg(src, PRE)[0][rows],
                                                 scalar=C("inv_w")[rows, m:m + 1], in1=seg(u, PRE)[0][rows],
                                                 op0=ALU.mult, op1=ALU.subtract)
                        link(dve.scalar_tensor_tensor(
                            out=dT[rows, m, SEQ:T].rearrange("p (b t) -> p b t", b=NB),
                            in0=seg(src, PRE)[1][rows, :, PRE:], scalar=C("inv_w")[rows, m:m + 1],
                            in1=seg(u, PRE)[1][rows, :, PRE:], op0=ALU.mult, op1=ALU.subtract))

            @block.tensor
            def _(pe):
                pe.wait_ge(s_pw, 64)
                pe.wait_ge(po_ready, 2)
                for q, src in enumerate((po_p, po_s[:, 0:120], po_s[:, 120:240], shift_out)):
                    if q == 3:
                        src = src.rearrange("p j m -> p (j m)")
                    n = src.shape[1]
                    pe.transpose(PS[6][0:n, q * P:q * P + P], src, ident).then_inc(po_t, 1)
                for m in range(2):
                    pe.wait_ge(ends, (6, 14)[m])
                    for c, (t0, n) in enumerate(CH):
                        pe.matmul(PS[3 * m + c][:, 0:n], pool_w[:, m], dT[:, m, t0:t0 + n], start=True,
                                  stop=True).then_inc(pool_mm, 1)

            @block.scalar
            def _(act):
                for q, n in enumerate((30, 120, 120, 99)):
                    act.wait_ge(po_t, 4)
                    dst = po_nat[0:n, q] if q < 3 else sh_nat[0:n, :]
                    nc.scalar.copy(dst, PS[6][0:n, q * P:q * P + P]).then_inc(po_cp, 1)
                for m in range(2):
                    for c, (t0, n) in enumerate(CH):
                        act.wait_ge(pool_mm, 3 * m + c + 1)
                        nc.scalar.activation(mixT[:, 6 + m, t0:t0 + n], PS[3 * m + c][:, 0:n], ACT.Copy,
                                             scale=vec("pool_scale", m)).then_inc(pool_cp, 1)
        if upto == "pool":
            return

        new_stage()
        cw = Carve(mla_end)
        vnat = cw.take(8 * AW).rearrange("p (i c) -> p i c", i=8)
        sqc = cw.take(2 * T).rearrange("p (k t) -> p k t", k=2)
        rinv = cw.take(T)
        nat = cw.take(2 * 288).rearrange("p (s c) -> p s c", s=2)
        cs = wring[:, 0:2 * T].rearrange("p (a t) -> p a t", a=2)
        rot_sin = wring[:, 2 * T:3 * T]
        w_uv = wring[:, 3 * T:3 * T + 768].rearrange("p (k c) -> p k c", k=2)
        spare = actA[:, 0:3 * T]
        w_uk = spare[:, 2048:2816].rearrange("p (k c) -> p k c", k=2)
        s_cs, s_wk, c_sq, c_sum, c_rt, c_ri, c_n, r_mm, r_sin, r_cos, r_done = (
            sem("angles_in"), sem("w_latent_in"), sem("latent_squared"), sem("latent_summed"),
            sem("latent_root"), sem("latent_recip"), sem("latent_normed"), sem("rotated"), sem("sin_part"),
            sem("cos_part"), sem("rope_done"))
        v_mm, v_cp, n_t, n_cp = (sem("values_ready"), sem("values_copied"), sem("rows_turned"),
                                 sem("rows_copied"))
        s_xr = sem("residual_back")
        s_kn = sem("new_keys_cleared")
        rope_jobs = [(a, c) for a in range(2) for c in range(3)]
        with nc.Block() as block:
            @block.sync
            def _(sp):
                sp.dma_start(cs, I["c_rope"]).then_inc(s_cs, 16)
                sp.dma_start(xT, spill).then_inc(s_xr, 16)
                sp.dma_start(w_uk, I["w_uk"][0].rearrange("(k p) h d -> p k (h d)", p=P)).then_inc(s_wk, 16)
                sp.dma_start(w_uv, I["w_uv"][0].rearrange("(k p) h d -> p k (h d)", p=P)).then_inc(s_wk, 16)
                for i in range(TT):
                    n = rows_of(i)
                    sp.wait_ge(n_cp, i + 1)
                    if i < TT - 1:
                        sp.dma_start(kv_p[0, 0, i * P:(i + 1) * P, :], nat[:, i % 2, 0:256]).then_inc(s_nat[i % 2], 16)
                        sp.dma_start(kr_p[0, 0, i * P:(i + 1) * P, :], nat[:, i % 2, 256:]).then_inc(s_nat[i % 2], 16)
                    else:
                        sp.dma_start(kv_s[0].rearrange("b t c -> (b t) c"), nat[0:n, i % 2, 0:256]).then_inc(s_nat[i % 2], 16)
                        sp.dma_start(kr_s[0].rearrange("b t c -> (b t) c"), nat[0:n, i % 2, 256:]).then_inc(s_nat[i % 2], 16)
                sp.wait_ge(s_xr, 16)
                sp.wait_ge(s_nat[0], 160)
                sp.wait_ge(s_nat[1], 128)

            @block.scalar
            def _(act):
                nc.scalar.activation(sqc, ckv, ACT.Square).then_inc(c_sq, 1)
                for c, (t0, n) in enumerate(CH):
                    act.wait_ge(c_sum, c + 1)
                    nc.scalar.activation(rinv[:, t0:t0 + n], PS[c][:, 0:n], ACT.Sqrt, bias=epsc[:, 0:1],
                                         scale=1.0 / RANK).then_inc(c_rt, 1)
                for i in range(8):
                    act.wait_ge(v_mm, i + 1)
                    nc.scalar.copy(vnat[:, i], PS[i % 2][:, 0:AW]).then_inc(v_cp, 1)

            @block.gpsimd
            def _(pool):
                pool.wait_ge(s_cs, 16)
                nc.gpsimd.memset(krT_new, 0.0).then_inc(s_kn, 1)
                for j, (a, c) in enumerate(rope_jobs):
                    t0, n = CH[c]
                    m = P if a == 0 else 96
                    pool.wait_ge(r_mm, j + 1)
                    nc.gpsimd.tensor_tensor(rp[0:m, a, t0:t0 + n], rp[0:m, a, t0:t0 + n], cs[0:m, 0, t0:t0 + n],
                                            ALU.mult).then_inc(r_cos, 1)
                    pool.wait_ge(r_sin, j + 1)
                    pool.wait_ge(r_cos, j + 1)
                    nc.gpsimd.tensor_tensor(rp[0:m, a, t0:t0 + n], rp[0:m, a, t0:t0 + n], rot_sin[0:m, t0:t0 + n],
                                            ALU.add).then_inc(r_done, 1)
                pool.wait_ge(r_done, 6)
                pool.wait_ge(s_kn, 1)
                nc.gpsimd.tensor_copy(krT_new[64:96, :], rp[64:96, 1, SEQ:T])

            @block.vector
            def _(dve):
                dve.wait_ge(s_cs, 16)
                for c, (t0, n) in enumerate(CH):
                    dve.wait_ge(c_rt, c + 1)
                    dve.reciprocal(rinv[:, t0:t0 + n], rinv[:, t0:t0 + n]).then_inc(c_ri, 1)
                    dve.wait_ge(c_ri, c + 1)
                    for k in range(2):
                        dve.scalar_tensor_tensor(out=ckv[:, k, t0:t0 + n], in0=ckv[:, k, t0:t0 + n],
                                                 scalar=vec("kv_norm_g", k), in1=rinv[:, t0:t0 + n],
                                                 op0=ALU.mult, op1=ALU.mult).then_inc(c_n, 1)
                for j, (a, c) in enumerate(rope_jobs):
                    t0, n = CH[c]
                    m = P if a == 0 else 96
                    dve.wait_ge(r_mm, j + 1)
                    if j >= 3:
                        dve.wait_ge(r_done, j - 2)
                    dve.tensor_tensor(rot_sin[0:m, t0:t0 + n], PS[3 + j % 3][0:m, 0:n], cs[0:m, 1, t0:t0 + n],
                                      ALU.mult).then_inc(r_sin, 1)
                dve.wait_ge(c_n, 6)
                dve.tensor_copy(ckvT_new, ckv[:, :, SEQ:T])
                for i in range(TT):
                    n = rows_of(i)
                    dve.wait_ge(n_t, i + 1)
                    if i >= 2:
                        dve.wait_ge(s_nat[i % 2], 32 * (i // 2))
                    dve.tensor_copy(nat[0:n, i % 2, :], PS[6 + i % 2][0:n, 0:288]).then_inc(n_cp, 1)
                    if i == TT - 1:
                        dve.tensor_copy(ckv_new, PS[6 + i % 2][0:n, 0:RANK]).then_inc(n_cp, 1)

            @block.tensor
            def _(pe):
                pe.wait_ge(c_sq, 1)
                for c, (t0, n) in enumerate(CH):
                    for k in range(2):
                        last = pe.matmul(PS[c][:, 0:n], ones, sqc[:, k, t0:t0 + n], start=(k == 0), stop=(k == 1))
                    last.then_inc(c_sum, 1)
                for j, (a, c) in enumerate(rope_jobs):
                    t0, n = CH[c]
                    m = P if a == 0 else 96
                    if j >= 3:
                        pe.wait_ge(r_sin, j - 2)
                    pe.matmul(PS[3 + j % 3][0:m, 0:n], C("rot")[0:m, 0:m], rp[0:m, a, t0:t0 + n], start=True,
                              stop=True).then_inc(r_mm, 1)
                pe.wait_ge(s_wk, 32)
                pe.wait_ge(c_n, 6)
                for i in range(8):
                    if i >= 2:
                        pe.wait_ge(v_cp, i - 1)
                    for k in range(2):
                        last = pe.matmul(PS[i % 2][:, 0:AW], ckv[:, k, i * P:(i + 1) * P], w_uv[:, k],
                                         start=(k == 0), stop=(k == 1))
                    last.then_inc(v_mm, 1)
                pe.wait_ge(r_done, 6)
                for i in range(TT):
                    n = rows_of(i)
                    if i >= 2:
                        pe.wait_ge(n_cp, i - 1)
                    for k in range(2):
                        pe.transpose(PS[6 + i % 2][0:n, k * P:(k + 1) * P], ckv[:, k, i * P:i * P + n], ident)
                    pe.transpose(PS[6 + i % 2][0:n, 256:288], rp[64:96, 1, i * P:i * P + n],
                                 ident[64:96, 64:96]).then_inc(n_t, 1)
        if upto == "latent":
            return

        new_stage()
        cw = Carve(mla_end + 8 * AW)
        qcat = [cw.take(SEQ) for _ in range(2)]
        stat_a = cw.take(4 * 48).rearrange("p (a i) -> p a i", a=4)
        kcat = [spare[:, j * SEQ:(j + 1) * SEQ] for j in range(2)]
        prob = [wring[:, j * SEQ:(j + 1) * SEQ] for j in range(2)]
        probT = [wring[:, (4 + j) * 512:(5 + j) * 512] for j in range(2)]
        items = [(h, i) for h in range(H) for i in range(8)]
        uses = [("keys", 0)]
        for h, i in items:
            uses.append(("item", 8 * h + i))
            if i == 5 and h + 1 < H:
                uses.append(("keys", h + 1))
        use_of = {u: n for n, u in enumerate(uses)}
        units = [(it, b0, min(4, items[it][1] + 1 - b0)) for it in range(48) for b0 in range(0, items[it][1] + 1, 4)]
        last_unit = {it: max(u for u, x in enumerate(units) if x[0] == it) for it in range(48)}
        s_q, keys_mm, keys_cp, s_kr, sc_mm, sc_masked, sc_max, sc_bias, p_exp, p_rec, p_div, p_t, p_cp, o_mm, o_cp = (
            [sem("queries_in0"), sem("queries_in1")], sem("keys_ready"), sem("keys_copied"), sem("rope_keys_set"),
            sem("scores_ready"), sem("scores_masked"), sem("scores_max"), sem("scores_bias"), sem("weights_ready"),
            sem("weight_sums_recip"), sem("weights_normed"), sem("weights_turned"), sem("weightsT_copied"),
            sem("attn_out_ready"), sem("attn_out_copied"))

        def score_bank(use):
            return PS[2 * (use % 2)], PS[2 * (use % 2) + 1]

        def copy_weights(dve, it):
            for u in range(last_unit[it - 1] + 1 if it else 0, last_unit[it] + 1):
                n = units[u][2] * P
                dve.wait_ge(p_t, u + 1)
                if u >= 2:
                    dve.wait_ge(o_mm, u - 1)
                dve.tensor_copy(probT[u % 2][:, 0:n], PS[4 + u % 2][:, 0:n]).then_inc(p_cp, 1)

        def copy_out(act, it):
            h, i = items[it]
            r = HD * (h % 2)
            act.wait_ge(o_mm, last_unit[it] + 1)
            nc.scalar.copy(mixT[r:r + HD, 3 + h // 2, i * P:(i + 1) * P],
                           PS[6 + it % 2][r:r + HD, 0:P]).then_inc(o_cp, 1)

        def free_use(pe, n):
            if n < 2:
                return
            kind, x = uses[n - 2]
            if kind == "keys":
                pe.wait_ge(keys_cp, 2 * (x + 1))
            else:
                pe.wait_ge(p_exp, x + 1)

        sc_max2 = sem("weight_sums_joined")

        with nc.Block() as block:
            @block.sync
            def _(sp):
                for h in range(H):
                    if h >= 2:
                        sp.wait_ge(sc_mm, 8 * (h - 1))
                    r = HD * (h % 2)
                    sp.dma_start(qcat[h % 2][0:HD, :], qn[r:r + HD, h // 2, 0:SEQ]).then_inc(s_q[h % 2], 16)
                    r = ROPE * (h % 4)
                    sp.dma_start(qcat[h % 2][HD:96, :], rp[r:r + ROPE, h // 4, 0:SEQ]).then_inc(s_q[h % 2], 16)

            @block.gpsimd
            def _(pool):
                for j in range(2):
                    nc.gpsimd.tensor_copy(kcat[j][64:96, :], rp[64:96, 1, 0:SEQ]).then_inc(s_kr, 1)
                for it, (h, i) in enumerate(items):
                    n = (i + 1) * P
                    pool.wait_ge(p_rec, it + 1)
                    nc.gpsimd.tensor_scalar(prob[it % 2][:, 0:n], prob[it % 2][:, 0:n], stat_a[:, 3, it:it + 1],
                                            None, ALU.mult).then_inc(p_div, 1)

            @block.tensor
            def _(pe):
                def keys(h):
                    n = use_of["keys", h]
                    free_use(pe, n)
                    for half in range(2):
                        for k in range(2):
                            last = pe.matmul(score_bank(n)[half][0:HD, :], w_uk[:, k, h * HD:(h + 1) * HD],
                                             ckv[:, k, 512 * half:512 * half + 512], start=(k == 0), stop=(k == 1))
                        last.then_inc(keys_mm, 1)

                def scores(it):
                    h, i = items[it]
                    n = use_of["item", it]
                    free_use(pe, n)
                    if i == 0:
                        pe.wait_ge(keys_cp, 2 * (h + 1))
                        pe.wait_ge(s_kr, 2)
                        pe.wait_ge(s_q[h % 2], 32 * (h // 2 + 1))
                    w = (i + 1) * P
                    for half in range(0, w, 512):
                        m = min(512, w - half)
                        last = pe.matmul(score_bank(n)[half // 512][:, 0:m], qcat[h % 2][0:96, i * P:(i + 1) * P],
                                         kcat[h % 2][0:96, half:half + m], start=True, stop=True)
                    last.then_inc(sc_mm, 1)

                def turn(u):
                    it, b0, nb = units[u]
                    pe.wait_ge(p_div, it + 1)
                    if u >= 2:
                        pe.wait_ge(p_cp, u - 1)
                    for b in range(nb):
                        last = pe.transpose(PS[4 + u % 2][:, b * P:(b + 1) * P],
                                            prob[it % 2][:, (b0 + b) * P:(b0 + b + 1) * P], ident)
                    last.then_inc(p_t, 1)

                def values(u):
                    it, b0, nb = units[u]
                    h, i = items[it]
                    r = HD * (h % 2)
                    pe.wait_ge(p_cp, u + 1)
                    if b0 == 0 and it >= 2:
                        pe.wait_ge(o_cp, it - 1)
                    for b in range(nb):
                        last = pe.matmul(PS[6 + it % 2][r:r + HD, 0:P], vnat[:, b0 + b, h * HD:(h + 1) * HD],
                                         probT[u % 2][:, b * P:(b + 1) * P], start=(b0 + b == 0),
                                         stop=(b0 + b == i))
                    last.then_inc(o_mm, 1)

                keys(0)
                scores(0)
                for it in range(48):
                    if it + 1 < 48:
                        if use_of["item", it + 1] == use_of["item", it] + 2:
                            keys(items[it][0] + 1)
                        scores(it + 1)
                    for u in range(last_unit[it - 1] + 1 if it else 0, last_unit[it] + 1):
                        turn(u)
                        if u >= 1:
                            values(u - 1)
                values(len(units) - 1)

            @block.vector
            def _(dve):
                for it, (h, i) in enumerate(items):
                    w = (i + 1) * P
                    bank = score_bank(use_of["item", it])
                    dve.wait_ge(sc_mm, it + 1)
                    diag = bank[i // 4][:, (i % 4) * P:(i % 4) * P + P]
                    dve.tensor_tensor(diag, diag, C("causal"), ALU.add).then_inc(sc_masked, 1)
                    dve.wait_ge(sc_masked, it + 1)
                    if w > 512:
                        dve.tensor_reduce(stat_a[:, 0, it:it + 1], bank[0][:, :], AX_X, ALU.max).then_inc(sc_max, 1)
                        dve.tensor_reduce(stat_a[:, 1, it:it + 1], bank[1][:, 0:w - 512], AX_X,
                                          ALU.max).then_inc(sc_max, 1)
                    else:
                        for a in range(2):
                            dve.tensor_reduce(stat_a[:, a, it:it + 1], bank[0][:, 0:w] if a == 0 else bank[0][:, 0:P],
                                              AX_X, ALU.max).then_inc(sc_max, 1)
                    dve.wait_ge(sc_max, 2 * (it + 1))
                    dve.tensor_scalar(stat_a[:, 0, it:it + 1], stat_a[:, 0, it:it + 1], stat_a[:, 1, it:it + 1],
                                      -SCALE, ALU.max, ALU.mult).then_inc(sc_bias, 1)
                    if it >= 1:
                        copy_weights(dve, it - 1)
                    dve.wait_ge(p_exp, it + 1)
                    if w > 512:
                        dve.tensor_scalar(stat_a[:, 1, it:it + 1], stat_a[:, 1, it:it + 1], stat_a[:, 2, it:it + 1],
                                          None, ALU.add).then_inc(sc_max2, 1)
                        dve.wait_ge(sc_max2, sum(1 for _, j in items[:it + 1] if j >= 4))
                    dve.reciprocal(stat_a[:, 3, it:it + 1], stat_a[:, 1 if w > 512 else 2, it:it + 1]).then_inc(p_rec, 1)
                copy_weights(dve, 47)

            @block.scalar
            def _(act):
                def copy_keys(h):
                    n = use_of["keys", h]
                    if h >= 2:
                        act.wait_ge(sc_mm, 8 * (h - 1))
                    for half in range(2):
                        act.wait_ge(keys_mm, 2 * h + half + 1)
                        nc.scalar.copy(kcat[h % 2][0:HD, 512 * half:512 * half + 512],
                                       score_bank(n)[half][0:HD, :]).then_inc(keys_cp, 1)

                copy_keys(0)
                for it, (h, i) in enumerate(items):
                    n = use_of["item", it]
                    if n >= 1 and uses[n - 1][0] == "keys" and it > 0:
                        copy_keys(uses[n - 1][1])
                    w = (i + 1) * P
                    bank = score_bank(n)
                    act.wait_ge(sc_bias, it + 1)
                    if it >= 2:
                        act.wait_ge(p_t, last_unit[it - 2] + 1)
                    parts = [(0, w)] if w <= 512 else [(0, 512), (512, w)]
                    for j, (a, b) in enumerate(parts):
                        ins = nc.scalar.activation(prob[it % 2][:, a:b], bank[j][:, 0:b - a], ACT.Exp,
                                                   bias=stat_a[:, 0, it:it + 1], scale=SCALE,
                                                   accum_out=stat_a[:, 2 - j, it:it + 1])
                    ins.then_inc(p_exp, 1)
                    if it >= 1:
                        copy_out(act, it - 1)
                copy_out(act, 47)
        if upto == "attn":
            return

        new_stage()
        QN = NB * H * TS
        HT = H * TS
        cw = Carve(WORK - 6 * QN)
        q_lat = cw.take(2 * QN).rearrange("p (k q) -> p k q", k=2)
        q_rope = cw.take(4 * QN).rearrange("p (r q) -> p r q", r=4)
        w_ukT = wring[:, 0:3 * RANK].rearrange("p (m c) -> p m c", m=3)
        s_qr0 = sem("rope_q_cleared")
        s_qr, s_qr4, wu_t, wu_cp, ql_mm, ql_cp = (sem("rope_q_in"), sem("rope_q_spread"), sem("w_uk_turned"),
                                                  sem("w_ukT_copied"), sem("q_lat_ready"), sem("q_lat_copied"))
        with nc.Block() as block:
            @block.sync
            def _(sp):
                sp.wait_ge(s_qr0, 1)
                for h in range(H):
                    r = ROPE * (h % 4)
                    for b in range(NB):
                        q0 = b * HT + h * TS
                        sp.dma_start(q_rope[0:ROPE, 0, q0:q0 + TS],
                                     rp[r:r + ROPE, h // 4, SEQ + b * TS:SEQ + (b + 1) * TS]).then_inc(s_qr, 16)
                sp.wait_ge(s_qr, 16 * H * NB)
                for r in range(1, 4):
                    sp.dma_start(q_rope[ROPE * r:ROPE * (r + 1), r], q_rope[0:ROPE, 0]).then_inc(s_qr4, 16)
                sp.wait_ge(s_qr4, 48)

            @block.gpsimd
            def _(pool):
                nc.gpsimd.memset(q_rope, 0.0).then_inc(s_qr0, 1)

            @block.tensor
            def _(pe):
                for m in range(3):
                    for k in range(2):
                        last = pe.transpose(PS[m][:, k * P:(k + 1) * P], w_uk[:, k, m * P:(m + 1) * P], ident)
                last.then_inc(wu_t, 1)
                pe.wait_ge(wu_cp, 3)
                for h in range(H):
                    r = HD * (h % 2)
                    for k in range(2):
                        last = pe.matmul(PS[4 + k + r // 32][:, (h // 2) * NS:(h // 2 + 1) * NS], w_ukT[r:r + HD, h // 2, k * P:(k + 1) * P],
                                         qn[r:r + HD, h // 2, SEQ:T], start=True, stop=True)
                last.then_inc(ql_mm, 1)

            @block.vector
            def _(dve):
                dve.wait_ge(wu_t, 1)
                for m in range(3):
                    dve.tensor_copy(w_ukT[:, m], PS[m][:, 0:RANK]).then_inc(wu_cp, 1)
                dve.wait_ge(ql_mm, 1)
                for k in range(2):
                    for odd in range(2):
                        dst = q_lat[:, k].rearrange("p (b h o t) -> p o b h t", b=NB, h=H // 2, o=2)[:, odd]
                        src = PS[4 + k + 2 * odd][:, 0:QN // 2].rearrange("p (h b t) -> p b h t", b=NB, h=H // 2)
                        dve.tensor_copy(dst, src).then_inc(ql_cp, 1)
        if upto == "queries":
            return

        new_stage()
        NG = NPAGE // 4
        NPT = NG + 1
        RK = 4
        cw = Carve()
        krr = cw.take(RK * P).rearrange("p (s c) -> p s c", s=RK)
        keyT = cw.take(2 * 2 * 512).rearrange("p (s k c) -> p s k c", s=2, k=2)
        krT = cw.take(2 * P).rearrange("p (s c) -> p s c", s=2)
        pr = cw.take(2 * 512).rearrange("p (s c) -> p s c", s=2)
        prT = cw.take(2 * 4 * HT).rearrange("p (s c) -> p s c", s=2)
        part = cw.take(2 * NPT * RANK).rearrange("p (s g c) -> p s g c", s=2, g=NPT)
        newmask = cw.take(NB * NS).rearrange("p (b c) -> p b c", b=NB)
        o_nat = cw.take(2 * RANK).rearrange("p (s c) -> p s c", s=2)
        w_uv2 = cw.take(768).rearrange("p (k c) -> p k c", k=2)
        mx = cw.take(NB * NPT).rearrange("p (b g) -> p b g", b=NB)
        bias = cw.take(NB * NPT).rearrange("p (b g) -> p b g", b=NB)
        sums = cw.take(NB * NPT).rearrange("p (b g) -> p b g", b=NB)
        wts = cw.take(NB * NPT).rearrange("p (b g) -> p b g", b=NB)
        tot = cw.take(NB * 4).rearrange("p (b a) -> p b a", b=NB)
        pages = cw.take(NB * NPAGE).bitcast(I32)
        assert cw.at <= WORK - 6 * QN, cw.at
        kslot = [wring[:, i * 1024:(i + 1) * 1024].rearrange("p (r c) -> p r c", r=4) for i in range(RK)]
        steps = [(b, g) for b in range(NB) for g in range(NPT)]

        def tile_no(b, g):
            return b * NG + g

        def scores_before(s):
            return s

        (s_pg, s_nm, k_t, k_cpa, k_cpb, ds_mm, ds_mask, ds_max, ds_bias, dp_exp, dp_t, dp_cp, do_mm, do_cp) = (
            sem("page_table_in"), sem("tables_in"), sem("rows_turned2"), sem("keysT_copied_a"),
            sem("keysT_copied_b"), sem("dscores_ready"), sem("dscores_masked"), sem("dscores_max"),
            sem("dscores_bias"), sem("dweights_ready"), sem("dweights_turned"), sem("dweightsT_copied"),
            sem("dparts_ready"), sem("dparts_copied"))
        s_k = [sem(f"rows_in{i}") for i in range(RK)]
        j_max, j_w, j_sum, j_acc, j_t, j_cp, j_ready = (sem("join_max"), sem("join_weights"), sem("join_sum"),
                                                        sem("join_steps"), sem("joined_turned"),
                                                        sem("joined_copied"), sem("joined"))
        y_mm, y_cp = sem("decode_values_ready"), sem("decode_values_copied")
        kv_pages = I["cache_kv_latent"][0].rearrange("n (p r) c -> n p (r c)", r=4)
        kr_pages = I["cache_k_rope"][0].rearrange("n (p r) c -> n p (r c)", r=4)
        with nc.Block() as block:
            @block.sync
            def _(sp):
                sp.dma_start(pages[0:1, :], I["page_table"].rearrange("b n -> (b n)").unsqueeze(0)).then_inc(s_pg, 16)
                sp.dma_start(newmask[0:HT], I["c_newmask"].rearrange("q (b c) -> q b c", b=NB)).then_inc(s_nm, 16)
                sp.dma_start(w_uv2, I["w_uv"][0].rearrange("(k p) h d -> p k (h d)", p=P)).then_inc(s_nm, 16)
                sp.wait_ge(s_pg, 16)
                for b in range(NB):
                    for g in range(NG):
                        n = tile_no(b, g)
                        if n >= RK:
                            pb, pg = divmod(n - RK, NG)
                            sp.wait_ge(do_mm, pb * NPT + pg + 1)
                        for q in range(4):
                            page = sp.value_load(pages[0:1, 4 * n + q:4 * n + q + 1], min_val=0, max_val=NPOOL - 1)
                            rows = slice(32 * q, 32 * q + 32)
                            sp.dma_start(wring[rows, (n % RK) * 1024:(n % RK + 1) * 1024],
                                         kv_pages[bass.ds(page, 1)].rearrange("a p c -> (a p) c")
                                         ).then_inc(s_k[n % RK], 16)
                            sp.dma_start(krr[rows, n % RK, :],
                                         kr_pages[bass.ds(page, 1)].rearrange("a p c -> (a p) c")
                                         ).then_inc(s_k[n % RK], 16)

            @block.tensor
            def _(pe):
                def turn_keys(s):
                    b, g = steps[s]
                    if g == NG:
                        return
                    n = tile_no(b, g)
                    pe.wait_ge(s_k[n % RK], 128 * (n // RK + 1))
                    if n >= 1:
                        pe.wait_ge(k_cpa, n)
                        pe.wait_ge(k_cpb, 2 * n)
                    for k in range(2):
                        for r in range(4):
                            pe.transpose(PS[k][:, r * P:(r + 1) * P], kslot[n % RK][:, r, k * P:(k + 1) * P], ident)
                    pe.transpose(PS[2][:, 0:P], krr[:, n % RK, :], ident).then_inc(k_t, 1)

                def dscores(s):
                    b, g = steps[s]
                    q0 = b * HT
                    bank = PS[3 + s % 2]
                    if s >= 2:
                        pe.wait_ge(dp_exp, s - 1)
                    if g < NG:
                        n = tile_no(b, g)
                        pe.wait_ge(k_cpa, n + 1)
                        pe.wait_ge(k_cpb, 2 * n + 2)
                        for r in range(4):
                            pe.matmul(bank[0:HT, r * P:(r + 1) * P], q_rope[:, r, q0:q0 + HT], krT[:, n % 2, :],
                                      start=(r == 0), stop=False, skip_group_check=True)
                        for k in range(2):
                            last = pe.matmul(bank[0:HT, :], q_lat[:, k, q0:q0 + HT], keyT[:, n % 2, k, :],
                                             start=False, stop=(k == 1), skip_group_check=True)
                    else:
                        for k in range(2):
                            pe.matmul(bank[0:HT, 0:NS], q_lat[:, k, q0:q0 + HT], ckvT_new[:, k], start=(k == 0),
                                      stop=False)
                        last = pe.matmul(bank[0:HT, 0:NS], q_rope[:, 2, q0:q0 + HT], krT_new,
                                         start=False, stop=True)
                    last.then_inc(ds_mm, 1)

                def turn_weights(s):
                    b, g = steps[s]
                    pe.wait_ge(dp_exp, s + 1)
                    if s >= 1:
                        pe.wait_ge(dp_cp, s)
                    if g < NG:
                        for r in range(4):
                            last = pe.transpose(PS[5][:, r * HT:(r + 1) * HT], pr[0:HT, s % 2, r * P:(r + 1) * P],
                                                ident[0:HT, 0:HT])
                    else:
                        last = pe.transpose(PS[5][0:NS, 0:HT], pr[0:HT, s % 2, 0:NS], ident[0:HT, 0:HT])
                    last.then_inc(dp_t, 1)

                def dvalues(s):
                    b, g = steps[s]
                    pe.wait_ge(dp_cp, s + 1)
                    if s >= 2:
                        pe.wait_ge(do_cp, s - 1)
                    bank = PS[6 + s % 2]
                    if g < NG:
                        n = tile_no(b, g)
                        for r in range(4):
                            last = pe.matmul(bank[0:HT, 0:RANK], prT[:, s % 2, r * HT:(r + 1) * HT],
                                             kslot[n % RK][:, r, :], start=(r == 0), stop=(r == 3))
                    else:
                        last = pe.matmul(bank[0:HT, 0:RANK], prT[0:NS, s % 2, 0:HT], ckv_new, start=True, stop=True)
                    last.then_inc(do_mm, 1)

                def turn_joined(b):
                    pe.wait_ge(j_ready, b + 1)
                    if b >= 1:
                        pe.wait_ge(j_cp, b)
                    for k in range(2):
                        last = pe.transpose(PS[2][:, P + k * HT:P + (k + 1) * HT],
                                            o_nat[0:HT, b % 2, k * P:(k + 1) * P], ident[0:HT, 0:HT])
                    last.then_inc(j_t, 1)

                pe.wait_ge(s_nm, 32)
                for s in range(len(steps)):
                    turn_keys(s)
                    if s >= 1:
                        turn_weights(s - 1)
                    dscores(s)
                    if s >= 1:
                        dvalues(s - 1)
                    b, g = steps[s]
                    if g == 6 and b >= 1:
                        pe.wait_ge(k_cpb, 2 * tile_no(b, g) + 2)
                        turn_joined(b - 1)
                turn_weights(len(steps) - 1)
                dvalues(len(steps) - 1)
                turn_joined(NB - 1)
                pe.wait_ge(j_cp, NB)
                for h in range(H):
                    r = HD * (h % 2)
                    for k in range(2):
                        rhs = q_lat[:, k].rearrange("p (b h t) -> p h b t", b=NB, h=H)[:, h]
                        last = pe.matmul(PS[h % 2][r:r + HD, (h // 2) * NS:(h // 2 + 1) * NS],
                                         w_uv2[:, k, h * HD:(h + 1) * HD], rhs, start=(k == 0), stop=(k == 1))
                last.then_inc(y_mm, 1)

            @block.vector
            def _(dve):
                def copy_keys(s):
                    b, g = steps[s]
                    if g == NG:
                        return
                    n = tile_no(b, g)
                    dve.wait_ge(k_t, n + 1)
                    if n >= 2:
                        dve.wait_ge(ds_mm, ((n - 2) // NG) * NPT + (n - 2) % NG + 1)
                    dve.tensor_copy(keyT[:, n % 2, 0, :], PS[0][:, :]).then_inc(k_cpa, 1)

                def softmax_max(s):
                    b, g = steps[s]
                    w = 512 if g < NG else NS
                    bank = PS[3 + s % 2]
                    dve.wait_ge(ds_mm, s + 1)
                    if g == NG:
                        dve.tensor_tensor(bank[0:HT, 0:NS], bank[0:HT, 0:NS], newmask[0:HT, b], ALU.add
                                          ).then_inc(ds_mask, 1)
                        dve.wait_ge(ds_mask, b + 1)
                    dve.tensor_reduce(mx[0:HT, b, g:g + 1], bank[0:HT, 0:w], AX_X, ALU.max).then_inc(ds_max, 1)
                    dve.wait_ge(ds_max, s + 1)
                    dve.tensor_scalar(bias[0:HT, b, g:g + 1], mx[0:HT, b, g:g + 1], -SCALE, None, ALU.mult
                                      ).then_inc(ds_bias, 1)

                def copy_part(s):
                    b, g = steps[s]
                    dve.wait_ge(do_mm, s + 1)
                    if g == 0 and b >= 2:
                        dve.wait_ge(j_ready, b - 1)
                    dve.tensor_copy(part[0:HT, b % 2, g, :], PS[6 + s % 2][0:HT, 0:RANK]).then_inc(do_cp, 1)

                def join_max(b):
                    dve.wait_ge(ds_max, NPT * (b + 1))
                    dve.tensor_reduce(tot[0:HT, b, 0:1], mx[0:HT, b, :], AX_X, ALU.max).then_inc(j_max, 1)
                    dve.wait_ge(j_max, 2 * b + 1)
                    dve.tensor_scalar(tot[0:HT, b, 1:2], tot[0:HT, b, 0:1], -SCALE, None, ALU.mult).then_inc(j_max, 1)

                def join_sum(b):
                    dve.wait_ge(j_w, b + 1)
                    dve.wait_ge(dp_exp, NPT * (b + 1))
                    dve.tensor_tensor(sums[0:HT, b, :], sums[0:HT, b, :], wts[0:HT, b, :], ALU.mult).then_inc(j_sum, 1)
                    dve.wait_ge(j_sum, 3 * b + 1)
                    dve.tensor_reduce(tot[0:HT, b, 2:3], sums[0:HT, b, :], AX_X, ALU.add).then_inc(j_sum, 1)
                    dve.wait_ge(j_sum, 3 * b + 2)
                    dve.reciprocal(tot[0:HT, b, 3:4], tot[0:HT, b, 2:3]).then_inc(j_sum, 1)

                def join(b):
                    o = o_nat[0:HT, b % 2, :]
                    dve.wait_ge(do_cp, NPT * (b + 1))
                    if b >= 2:
                        dve.wait_ge(j_t, b - 1)
                    for g in range(NPT):
                        w = wts[0:HT, b, g:g + 1]
                        if g == 0:
                            dve.tensor_scalar(o, part[0:HT, b % 2, g, :], w, None, ALU.mult).then_inc(j_acc, 1)
                        else:
                            dve.wait_ge(j_acc, NPT * b + g)
                            dve.scalar_tensor_tensor(out=o, in0=part[0:HT, b % 2, g, :], scalar=w, in1=o,
                                                     op0=ALU.mult, op1=ALU.add).then_inc(j_acc, 1)
                    dve.wait_ge(j_acc, NPT * (b + 1))
                    dve.wait_ge(j_sum, 3 * b + 3)
                    dve.tensor_scalar(o, o, tot[0:HT, b, 3:4], None, ALU.mult).then_inc(j_ready, 1)

                for s in range(len(steps)):
                    b, g = steps[s]
                    copy_keys(s)
                    if s >= 1:
                        dve.wait_ge(dp_t, s)
                        if s >= 3:
                            dve.wait_ge(do_mm, s - 2)
                        n, w = (P, 4 * HT) if steps[s - 1][1] < NG else (NS, HT)
                        dve.tensor_copy(prT[0:n, (s - 1) % 2, 0:w], PS[5][0:n, 0:w]).then_inc(dp_cp, 1)
                    softmax_max(s)
                    if s >= 1:
                        copy_part(s - 1)
                    if g == 1 and b >= 1:
                        join_max(b - 1)
                    if g == 3 and b >= 1:
                        join_sum(b - 1)
                        join(b - 1)
                s = len(steps)
                dve.wait_ge(dp_t, s)
                dve.tensor_copy(prT[0:NS, (s - 1) % 2, 0:HT], PS[5][0:NS, 0:HT]).then_inc(dp_cp, 1)
                copy_part(s - 1)
                join_max(NB - 1)
                join_sum(NB - 1)
                join(NB - 1)
                dve.wait_ge(y_mm, 1)
                for h in range(H):
                    r = HD * (h % 2)
                    dve.tensor_copy(mixT[r:r + HD, 3 + h // 2, SEQ:T],
                                    PS[h % 2][r:r + HD, (h // 2) * NS:(h // 2 + 1) * NS])

            @block.scalar
            def _(act):
                def copy_keys(s):
                    b, g = steps[s]
                    if g == NG:
                        return
                    n = tile_no(b, g)
                    act.wait_ge(k_t, n + 1)
                    if n >= 2:
                        act.wait_ge(ds_mm, ((n - 2) // NG) * NPT + (n - 2) % NG + 1)
                    nc.scalar.copy(keyT[:, n % 2, 1, :], PS[1][:, :]).then_inc(k_cpb, 1)
                    nc.scalar.copy(krT[:, n % 2, :], PS[2][:, 0:P]).then_inc(k_cpb, 1)

                def exps(s):
                    b, g = steps[s]
                    w = 512 if g < NG else NS
                    act.wait_ge(ds_bias, s + 1)
                    if s >= 2:
                        act.wait_ge(dp_t, s - 1)
                    nc.scalar.activation(pr[0:HT, s % 2, 0:w], PS[3 + s % 2][0:HT, 0:w], ACT.Exp,
                                         bias=bias[0:HT, b, g:g + 1], scale=SCALE,
                                         accum_out=sums[0:HT, b, g:g + 1]).then_inc(dp_exp, 1)

                def join_weights(b):
                    act.wait_ge(j_max, 2 * b + 2)
                    nc.scalar.activation(wts[0:HT, b, :], mx[0:HT, b, :], ACT.Exp, bias=tot[0:HT, b, 1:2],
                                         scale=SCALE).then_inc(j_w, 1)

                def copy_joined(b):
                    act.wait_ge(j_t, b + 1)
                    for k in range(2):
                        ins = nc.scalar.copy(q_lat[:, k, b * HT:(b + 1) * HT], PS[2][:, P + k * HT:P + (k + 1) * HT])
                    ins.then_inc(j_cp, 1)

                for s in range(len(steps)):
                    b, g = steps[s]
                    copy_keys(s)
                    if g == 7 and b >= 1:
                        copy_joined(b - 1)
                    exps(s)
                    if g == 1 and b >= 1:
                        join_weights(b - 1)
                join_weights(NB - 1)
                copy_joined(NB - 1)
        if upto == "decode":
            return

        new_stage()
        cw = Carve()
        AR = cw.take(3 * TT * 2 * P).rearrange("p (m i w t) -> p m i w t", m=3, i=TT, w=2)
        loop_base = cw.at
        fresh, lg, cum, dec, icl, kkn, k2 = (cw.take(TPAD) for _ in range(7))
        w2 = wring[:, 0:AW]
        g2 = wring[:, AW:2 * AW]
        prod, di = wring[:, 768:768 + TPAD], wring[:, 768 + TPAD:768 + 2 * TPAD]
        nch = SEQ // CHUNK
        dc = piece(3 * (nch + NB)).rearrange("p (m c) -> p m c", m=3)
        tch = [(c * 384, 384) for c in range(3)]

        def tiles3(ap):
            return ap.rearrange("p (i t) -> p i t", t=P)

        (s_w2, s_hv, p_th, p_kk, pss_mm, p_rt, z_mm, p_tw, p_dve, p_ex, p_go, b_mm, b_cp) = (
            sem("lora_in"), sem("half_biases"), sem("lora_tanh"), sem("keys_squared"), sem("key_norms_summed"),
            sem("key_norms_root"), sem("lora_products"), sem("gates_tanh"),
            sem("operand_steps"), sem("decays_exp"), sem("operands_done"), sem("bonus_summed"),
            sem("bonus_written"))
        p_rn0, p_rr, p_prod, p_ch = (sem("key_norms_clamped"), sem("key_norms_inverse"), sem("bonus_product"),
                                     sem("operand_chain"))
        sq_tmp = [icl, kkn, k2]
        with nc.Block() as block:
            @block.sync
            def _(sp):
                sp.dma_start(w2[0:64], I["decay_w2"][0]).then_inc(s_w2, 16)
                sp.dma_start(w2[64:128], I["iclr_a2"][0]).then_inc(s_w2, 16)
                sp.dma_start(g2, I["gate_g2"][0]).then_inc(s_w2, 16)
                sp.dma_start(fresh, I["c_fresh"]).then_inc(s_w2, 16)

            @block.scalar
            def _(act):
                for m in range(3):
                    nc.scalar.activation(sq_tmp[m], sT[:, 3 + m], ACT.Square, scale=vec("k_k", m)).then_inc(p_kk, 1)
                for m in range(3):
                    act.wait_ge(p_rn0, 3 * m + 3)
                    nc.scalar.activation(AR[:, m, :, 0], AR[:, m, :, 0], ACT.Sqrt).then_inc(p_rt, 1)
                nc.scalar.activation(sT[0:64, 9], sT[0:64, 9], ACT.Tanh).then_inc(p_th, 1)
                act.wait_ge(s_hv, 1)
                for m in range(3):
                    if m >= 1:
                        act.wait_ge(p_go, m)
                    for w, dst in enumerate((lg, icl)):
                        for c, (t0, n) in enumerate(tch):
                            act.wait_ge(z_mm, 6 * m + 3 * w + c + 1)
                            nc.scalar.activation(dst[:, t0:t0 + n], PS[3 * w + c][:, 0:n], ACT.Tanh, scale=0.5,
                                                 bias=halves[:, 3 * w + m:3 * w + m + 1]).then_inc(p_tw, 1)
                    act.wait_ge(p_dve, 2 * m + 1)
                    nc.scalar.activation(dec, cum, ACT.Exp).then_inc(p_ex, 1)
                    nc.scalar.activation(di, cum, ACT.Exp, scale=-1.0).then_inc(p_ex, 1)
                    act.wait_ge(p_dve, 2 * m + 2)
                    nc.scalar.activation(lg, lg, ACT.Exp).then_inc(p_ex, 1)

            @block.tensor
            def _(pe):
                for m in range(3):
                    pe.wait_ge(p_kk, m + 1)
                    for c, (t0, n) in enumerate(tch):
                        g = 3 * m + c
                        if g >= 8:
                            pe.wait_ge(p_rn0, g - 7)
                        pe.matmul(PS[g % 8][:, 0:n], C("head_ones"), sq_tmp[m][:, t0:t0 + n], start=True,
                                  stop=True).then_inc(pss_mm, 1)
                pe.wait_ge(s_w2, 64)
                pe.wait_ge(p_th, 1)
                pe.wait_ge(p_rn0, 9)
                for m in range(3):
                    for w in range(2):
                        rows = slice(64 * w, 64 * w + 64)
                        for c, (t0, n) in enumerate(tch):
                            if m >= 1:
                                pe.wait_ge(p_tw, 6 * (m - 1) + 3 * w + c + 1)
                            pe.matmul(PS[3 * w + c][:, 0:n], w2[rows, m * P:(m + 1) * P], sT[rows, 9, t0:t0 + n],
                                      start=True, stop=True).then_inc(z_mm, 1)
                    pe.wait_ge(p_prod, m + 1)
                    for c, (t0, n) in enumerate(CH):
                        g = 3 * m + c
                        if g >= 2:
                            pe.wait_ge(b_cp, g - 1)
                        pe.matmul(PS[6 + g % 2][:, 0:n], C("head_ones"), prod[:, t0:t0 + n], start=True,
                                  stop=True).then_inc(b_mm, 1)

            @block.vector
            def _(dve):
                dve.tensor_scalar(halves[:, 0:6], vecs[:, VEC["decay_w0"][0]:VEC["decay_w0"][0] + 6], 0.5, None,
                                  ALU.mult)
                dve.tensor_scalar(halves[:, 6:9], vecs[:, VEC["k_a"][0]:VEC["k_a"][0] + 3], -1.0, 1.0, ALU.mult,
                                  ALU.add).then_inc(s_hv, 1)
                dve.wait_ge(s_hv, 1)
                for m in range(3):
                    for c, (t0, n) in enumerate(tch):
                        g = 3 * m + c
                        dve.wait_ge(pss_mm, g + 1)
                        ins = dve.tensor_scalar(AR[:, m, 3 * c:3 * c + 3, 0], tiles3(PS[g % 8][:, 0:n]), 1e-24,
                                                None, ALU.max).then_inc(p_rn0, 1)
                for m in range(3):
                    dve.wait_ge(p_rt, m + 1)
                    dve.reciprocal(AR[:, m, :, 0], AR[:, m, :, 0]).then_inc(p_rr, 1)
                dve.wait_ge(s_w2, 64)
                link = chain(dve, p_ch)
                for m in range(3):
                    r, k = sT[:, m], sT[:, 3 + m]
                    dve.wait_ge(p_tw, 6 * m + 6)
                    link(dve.tensor_scalar(lg, lg, DECAY / 2, DECAY / 2, ALU.mult, ALU.add))
                    dve.tensor_tensor_scan(cum, fresh, lg, 0.0, ALU.mult, ALU.add).then_inc(p_dve, 1)
                    dve.wait_ge(p_dve, 2 * m + 1)
                    dve.tensor_tensor(lg, cum, lg, ALU.subtract).then_inc(p_dve, 1)
                    dve.wait_ge(p_rr, m + 1)
                    link(dve.scalar_tensor_tensor(out=tiles3(kkn), in0=tiles3(k), scalar=vec("k_k", m),
                                                  in1=AR[:, m, :, 0], op0=ALU.mult, op1=ALU.mult))
                    link(dve.tensor_scalar(icl, icl, 0.5, 0.5, ALU.mult, ALU.add))
                    link(dve.tensor_scalar(k2, icl, vec("k_a", m), halves[:, 6 + m:7 + m], ALU.mult, ALU.add))
                    link(dve.tensor_tensor(k2, k2, k, ALU.mult))
                    if m >= 1:
                        dve.wait_ge(b_mm, 3 * m)
                    dve.scalar_tensor_tensor(out=prod, in0=r, scalar=vec("r_k", m), in1=k2, op0=ALU.mult,
                                             op1=ALU.mult).then_inc(p_prod, 1)
                    link(dve.tensor_tensor(icl, icl, kkn, ALU.mult))
                    dve.wait_ge(p_ex, 3 * m + 1)
                    link(dve.tensor_tensor(AR[:, m, :, 1], tiles3(r), tiles3(dec), ALU.mult))
                    dve.tensor_copy(dc[:, m, 0:nch], dec[:, CHUNK - 1:SEQ:CHUNK])
                    dve.tensor_copy(dc[:, m, nch:], dec[:, SEQ + TS - 1:T:TS])
                    dve.wait_ge(p_ex, 3 * m + 2)
                    dve.tensor_tensor(r, icl, di, ALU.mult)
                    dve.tensor_tensor(k, k2, di, ALU.mult)
                    dve.wait_ge(p_ex, 3 * m + 3)
                    dve.scalar_tensor_tensor(out=AR[:, m, :, 0], in0=tiles3(kkn), scalar=-1.0, in1=tiles3(lg),
                                             op0=ALU.mult, op1=ALU.mult).then_inc(p_go, 1)
                    for c, (t0, n) in enumerate(CH):
                        dve.wait_ge(b_mm, 3 * m + c + 1)
                        dve.tensor_tensor(mixT[:, m, t0:t0 + n], PS[6 + (3 * m + c) % 2][:, 0:n],
                                          sT[:, 6 + m, t0:t0 + n], ALU.mult).then_inc(b_cp, 1)
                    dve.wait_ge(p_go, m + 1)
        if upto == "operands":
            return

        new_stage()
        cw = Carve(loop_base)
        hb = cw.take(5 * 1536).rearrange("p (h b w) -> p h b w", h=5, b=6)
        hb5 = wring[:, 768:768 + 1536].rearrange("p (b w) -> p b w", b=6)
        at2 = [2304]

        def wr(n):
            at2[0] += n
            assert at2[0] <= 4096
            return wring[:, at2[0] - n:at2[0]]

        nat_b, nat_k, nat_v = wr(AW), wr(AW), wr(AW)
        rt_ = wr(AW).rearrange("p (m t) -> p m t", m=3)
        scr = sT[:, 9]
        states = scr[:, 0:768].rearrange("p (s m v) -> p s m v", s=4, m=3)
        gts = scr[:, 768:1152].rearrange("p (m c v) -> p m c v", m=3, c=2)
        hss = cw.take(AW).rearrange("p (m c v) -> p m c v", m=3, c=2)

        def buf(h, b):
            return hb[:, h, b] if h < 5 else hb5[:, b]

        NQ, MP, XX, ND, PA, PB = range(6)
        STG = ["NQ", "MP", "NT", "MV", "P2", "A1", "P4", "A2", "P8", "A4", "A8", "ZT", "Z2", "B2", "B1", "RT"]
        OPS = 4 + 6 * len(STG) + 12 + 2 + 6
        NPT_ = TT - 1
        ON_DVE = {"NQ", "MP", "NT", "A1", "A2", "A4", "A8", "B2", "B1", "RT"}

        def op(i, what, h=0, c=0):
            if what == "nat":
                k = h
            elif what == "GH":
                k = 4 + 6 * len(STG) + 2 * h + c
            elif what == "CH":
                k = 4 + 6 * len(STG) + 12 + c
            elif what == "Y":
                k = 4 + 6 * len(STG) + 14 + h
            else:
                k = 4 + 6 * STG.index(what) + h
            return i * OPS + k

        def decode_op(n):
            i, k = divmod(n, OPS)
            if k < 4:
                return i, "nat", k, 0
            k -= 4
            if k < 6 * len(STG):
                return i, STG[k // 6], k % 6, 0
            k -= 6 * len(STG)
            if k < 12:
                return i, "GH", k // 2, k % 2
            if k < 14:
                return i, "CH", 0, k - 12
            return i, "Y", k - 14, 0

        def by_dve(n):
            i, what, h, c = decode_op(n)
            return what in ON_DVE or what in ("GH", "CH") or (what == "nat" and h == 0)

        NOPS = NPT_ * OPS + 4 + 6 * len(STG)
        dve_before, act_before = [0], [0]
        for n in range(NOPS):
            dve_before.append(dve_before[-1] + by_dve(n))
            act_before.append(act_before[-1] + (not by_dve(n)))
        rw_mm, rw_dve, rw_act, rw_pool, s_s0 = (sem("rw_product"), sem("rw_taken_dve"), sem("rw_taken_act"),
                                                sem("rw_transposed_blocks"), sem("rw_state_zeroed"))

        def taken(eng, n):
            if by_dve(n):
                eng.wait_ge(rw_dve, dve_before[n] + 1)
            else:
                eng.wait_ge(rw_act, act_before[n] + 1)

        def head(h):
            return slice(64 * (h % 2), 64 * (h % 2) + 64), h // 2

        def masks(i):
            return "_p" if i < NPT_ else "_s"

        def solve_ops(pe, i):
            def bank(n):
                if n >= 8:
                    taken(pe, n - 8)
                return PS[n % 8]

            for j, src in enumerate((None, 0, 3, 6)):
                n = op(i, "nat", j)
                b = bank(n)
                for m in range(3):
                    x = AR[:, m, i, 0] if src is None else sT[:, src + m, i * P:(i + 1) * P]
                    last = pe.transpose(b[:, m * P:(m + 1) * P], x, ident)
                last.then_inc(rw_mm, 1)
            for what in STG:
                for h in range(H):
                    n = op(i, what, h)
                    b = bank(n)
                    rows, m = head(h)
                    x = buf(h, XX)
                    if what in ("NQ", "MP"):
                        src = sT[rows, m if what == "NQ" else 3 + m, i * P:(i + 1) * P]
                        last = pe.matmul(b[:, 0:256], src, AR[rows, m, i].rearrange("p w t -> p (w t)"),
                                         start=True, stop=True)
                    elif what == "NT":
                        taken(pe, op(i, "NQ", h))
                        last = pe.transpose(b[:, 0:P], buf(h, NQ)[:, 0:P], ident)
                    elif what == "MV":
                        taken(pe, op(i, "MP", h))
                        taken(pe, op(i, "nat", 3))
                        last = pe.matmul(b[:, 0:HD], buf(h, MP)[:, 0:P], nat_v[:, h * HD:(h + 1) * HD], start=True,
                                         stop=True)
                    elif what in ("P2", "P4"):
                        src = buf(h, ND if what == "P2" else PA)
                        taken(pe, op(i, "NT" if what == "P2" else "P2", h))
                        if what == "P2":
                            pe.wait_ge(rw_pool, 6 * i + h + 1)
                        pe.matmul(b[:, 0:P], src[:, P:], src[:, 0:P], start=True, stop=True)
                        last = pe.matmul(b[:, P:256], src[:, 0:P], src[:, P:], start=True, stop=True)
                    elif what == "P8":
                        taken(pe, op(i, "P4", h))
                        last = pe.matmul(b[:, 0:P], buf(h, PB)[:, 0:P], buf(h, PB)[:, P:], start=True, stop=True)
                    elif what in ("A1", "A2", "A4", "A8"):
                        prev = {"A1": "MV", "A2": "A1", "A4": "A2", "A8": "A4"}[what]
                        taken(pe, op(i, prev, h))
                        if what == "A1":
                            taken(pe, op(i, "nat", 0))
                        else:
                            taken(pe, op(i, {"A2": "P2", "A4": "P4", "A8": "P8"}[what], h))
                        w = {"A1": buf(h, ND)[:, P:], "A2": buf(h, PA)[:, P:], "A4": buf(h, PB)[:, P:],
                             "A8": buf(h, ND)[:, 0:P]}[what]
                        last = pe.matmul(b[:, 0:256], w, x, start=True, stop=True)
                    elif what == "ZT":
                        taken(pe, op(i, "A8", h))
                        last = pe.transpose(b[:, 0:P], x[:, P:], ident)
                    elif what == "Z2":
                        taken(pe, op(i, "ZT", h))
                        last = pe.matmul(b[:, 0:P], x[:, P:], buf(h, PA)[:, 0:P], start=True, stop=True)
                    elif what in ("B2", "B1"):
                        taken(pe, op(i, "Z2" if what == "B2" else "B2", h))
                        w = buf(h, PA)[:, P:] if what == "B2" else buf(h, PA)[:, 0:P]
                        last = pe.matmul(b[:, 0:P], w, x[:, 0:P], start=True, stop=True)
                    else:
                        taken(pe, op(i, "B1", h))
                        last = pe.matmul(b[rows, 0:P], x[:, 0:HD], buf(h, NQ)[:, P:], start=True, stop=True)
                    last.then_inc(rw_mm, 1)

        def solve_dve(dve, i):
            mk = masks(i)
            n = op(i, "nat", 0)
            dve.wait_ge(rw_mm, n + 1)
            b = PS[n % 8]
            for h in range(H):
                ins = dve.tensor_copy(buf(h, XX)[:, 0:HD], b[:, h * HD:(h + 1) * HD])
            ins.then_inc(rw_dve, 1)
            for what in STG:
                for h in range(H):
                    if what not in ON_DVE:
                        continue
                    n = op(i, what, h)
                    b = PS[n % 8]
                    rows, m = head(h)
                    dve.wait_ge(rw_mm, n + 1)
                    if what in ("NQ", "MP"):
                        ins = dve.tensor_tensor(buf(h, NQ if what == "NQ" else MP), b[:, 0:256], C("keep" + mk),
                                                ALU.mult)
                    elif what == "NT":
                        dve.tensor_tensor(buf(h, ND)[:, 0:P], b[:, 0:P], C("diag" + mk), ALU.mult)
                        ins = dve.tensor_tensor(buf(h, XX)[:, P:], b[:, 0:P], C("off" + mk), ALU.mult)
                    elif what in ("A1", "A2", "A4", "A8"):
                        ins = dve.tensor_tensor(buf(h, XX), b[:, 0:256], buf(h, XX), ALU.add)
                    elif what in ("B2", "B1"):
                        ins = dve.tensor_tensor(buf(h, XX)[:, 0:P], b[:, 0:P], buf(h, XX)[:, 0:P], ALU.add)
                    else:
                        ins = dve.tensor_tensor(rt_[rows, m], b[rows, 0:P], AR[rows, m, i, 1], ALU.add)
                    ins.then_inc(rw_dve, 1)

        def solve_act(act, i):
            for j, dst in enumerate((None, nat_b, nat_k, nat_v)):
                if dst is None:
                    continue
                n = op(i, "nat", j)
                act.wait_ge(rw_mm, n + 1)
                nc.scalar.copy(dst, PS[n % 8][:, 0:AW]).then_inc(rw_act, 1)
            for what in STG:
                for h in range(H):
                    if what in ON_DVE:
                        continue
                    n = op(i, what, h)
                    b = PS[n % 8]
                    act.wait_ge(rw_mm, n + 1)
                    dst, w = {"MV": (buf(h, XX)[:, HD:P], HD), "P2": (buf(h, PA), 256), "P4": (buf(h, PB), 256),
                              "P8": (buf(h, ND)[:, 0:P], P), "ZT": (buf(h, PA)[:, 0:P], P),
                              "Z2": (buf(h, PA)[:, P:], P)}[what]
                    nc.scalar.copy(dst, b[:, 0:w]).then_inc(rw_act, 1)

        def solve_pool(pool, i):
            for h in range(H):
                taken(pool, op(i, "NQ", h))
                if i >= 1:
                    pool.wait_ge(rw_mm, op(i - 1, "A8", h) + 1)
                nc.gpsimd.tensor_tensor(buf(h, ND)[:, P:], buf(h, NQ)[:, 0:P], C("diag" + masks(i)), ALU.mult
                                        ).then_inc(rw_pool, 1)

        with nc.Block() as block:
            @block.gpsimd
            def _(pool):
                nc.gpsimd.memset(states[:, 0], 0.0).then_inc(s_s0, 1)
                for i in range(NPT_):
                    solve_pool(pool, i)

            @block.tensor
            def _(pe):
                pe.wait_ge(s_s0, 1)
                for i in range(NPT_):
                    solve_ops(pe, i)
                    for h in range(H):
                        rows, m = head(h)
                        cols = slice(h * HD, (h + 1) * HD)
                        x = buf(h, XX)
                        for c in range(2):
                            n = op(i, "GH", h, c)
                            taken(pe, n - 8)
                            b = PS[n % 8]
                            tr = slice(64 * c, 64 * c + 64)
                            pe.matmul(b[rows, 0:HD], x[tr, 0:HD], nat_b[tr, cols], start=True, stop=False,
                                      skip_group_check=True)
                            pe.matmul(b[rows, HD:P], nat_b[tr, cols], x[tr, HD:P], start=False, stop=False,
                                      skip_group_check=True)
                            pe.matmul(b[rows, HD:P], nat_k[tr, cols], nat_v[tr, cols], start=False, stop=True,
                                      skip_group_check=True).then_inc(rw_mm, 1)
                    for c in range(2):
                        n = op(i, "CH", 0, c)
                        taken(pe, n - 8)
                        taken(pe, op(i, "GH", 5, c))
                        if 2 * i + c >= 1:
                            taken(pe, op(i, "CH", 0, 0) if c else op(i - 1, "CH", 0, 1))
                        for h in range(H):
                            rows, m = head(h)
                            last = pe.matmul(PS[n % 8][rows, m * HD:(m + 1) * HD], gts[rows, m, c],
                                             states[rows, (2 * i + c) % 4, m], start=True, stop=True)
                        last.then_inc(rw_mm, 1)
                    for h in range(H):
                        rows, m = head(h)
                        n = op(i, "Y", h)
                        taken(pe, n - 8)
                        taken(pe, op(i, "RT", h))
                        b = PS[n % 8]
                        pe.matmul(b[rows, 0:P], buf(h, XX)[:, HD:P], buf(h, NQ)[:, P:], start=True, stop=False,
                                  skip_group_check=True)
                        pe.matmul(b[rows, 0:P], nat_v[:, h * HD:(h + 1) * HD], buf(h, MP)[:, P:], start=False,
                                  stop=False, skip_group_check=True)
                        for c in range(2):
                            last = pe.matmul(b[rows, 64 * c:64 * c + 64], states[rows, (2 * i + c) % 4, m],
                                             rt_[rows, m, 64 * c:64 * c + 64], start=False, stop=(c == 1),
                                             skip_group_check=True)
                        last.then_inc(rw_mm, 1)

            @block.vector
            def _(dve):
                for i in range(NPT_):
                    solve_dve(dve, i)
                    for h in range(H):
                        rows, m = head(h)
                        for c in range(2):
                            n = op(i, "GH", h, c)
                            dve.wait_ge(rw_mm, n + 1)
                            b = PS[n % 8]
                            eye = ident[rows, 64 * (h % 2):64 * (h % 2) + 64]
                            dve.tensor_tensor(gts[rows, m, c], b[rows, 0:HD], eye, ALU.add)
                            dve.tensor_scalar(hss[rows, m, c], b[rows, HD:P], dc[rows, m, 2 * i + c:2 * i + c + 1],
                                              None, ALU.mult).then_inc(rw_dve, 1)
                    for c in range(2):
                        n = op(i, "CH", 0, c)
                        q = 2 * i + c
                        dve.wait_ge(rw_mm, n + 1)
                        for m in range(3):
                            ins = dve.scalar_tensor_tensor(out=states[:, (q + 1) % 4, m],
                                                           in0=PS[n % 8][:, m * HD:(m + 1) * HD],
                                                           scalar=dc[:, m, q:q + 1], in1=hss[:, m, c],
                                                           op0=ALU.mult, op1=ALU.add)
                        ins.then_inc(rw_dve, 1)

            @block.scalar
            def _(act):
                for i in range(NPT_):
                    solve_act(act, i)
                    for h in range(H):
                        rows, m = head(h)
                        n = op(i, "Y", h)
                        act.wait_ge(rw_mm, n + 1)
                        nc.scalar.copy(AR[rows, m, i, 0], PS[n % 8][rows, 0:P]).then_inc(rw_act, 1)
        if upto == "recur":
            return

        i8 = TT - 1
        SL = sT[:, 3:5, 0:768].rearrange("p a (q c) -> p a q c", q=2)
        s0 = [sT[:, m, 0:512] for m in range(3)]
        um = [sT[0:64, 5, 0:512], sT[0:64, 6, 0:512]]
        vm = [sT[0:64, 7, 0:512], sT[0:64, 8, 0:512]]
        spread = [sT[:, 5, 512:896], sT[:, 6, 512:896]]
        hss_out = sT[0:64, 7, 512:896]
        wt, ut = (x.rearrange("p (m t) -> p m t", m=3) for x in spread)
        s_sl, st_t, st_cp, sm_mm, sm_act, sm_dve, sm_vm, s_w1 = (
            sem("states_in2"), sem("states_turned"), sem("statesT_copied"), sem("sample_product"),
            sem("sample_taken_act"), sem("sample_taken_dve"), sem("sample_values_spread"),
            sem("sample_steps"))

        def s_taken(eng, q):
            if q < 18:
                eng.wait_ge(sm_act, q + 1)
            elif q < 30:
                eng.wait_ge(sm_dve, q - 17)
            else:
                eng.wait_ge(sm_act, q - 11)

        with nc.Block() as block:
            @block.sync
            def _(sp):
                for b in range(NB):
                    q, half = divmod(b, 2)
                    sp.dma_start(SL[64 * half:64 * half + 64, q // 2, q % 2].rearrange("p (h j) -> p h j", h=H),
                                 I["state_wkv"][0, b].rearrange("h i j -> i h j")).then_inc(s_sl, 16)
                sp.wait_ge(sm_act, 22)
                for b in range(NB):
                    q, half = divmod(b, 2)
                    sp.dma_start(wkv_s[0, b].rearrange("h i j -> i h j"),
                                 SL[64 * half:64 * half + 64, q // 2, q % 2].rearrange("p (h j) -> p h j", h=H)
                                 ).then_inc(s_wo, 16)
                sp.dma_start(wkv_p[0, 0].rearrange("h i j -> i h j"),
                             hss_out.rearrange("p (h j) -> p h j", h=H)).then_inc(s_wo, 16)
                sp.wait_ge(s_wo, 16 * 9)

            @block.gpsimd
            def _(pool):
                solve_pool(pool, i8)

            @block.tensor
            def _(pe):
                solve_ops(pe, i8)
                taken(pe, op(i8, "RT", 5))
                taken(pe, op(i8, "Z2", 5))
                pe.wait_ge(s_sl, 128)
                for m in range(3):
                    for q in range(4):
                        last = pe.transpose(PS[m][:, q * P:(q + 1) * P], SL[:, q // 2, q % 2, m * P:(m + 1) * P], ident)
                last.then_inc(st_t, 1)
                pe.wait_ge(st_cp, 3)
                for q in range(34):
                    b = PS[q % 8]
                    if q >= 8:
                        s_taken(pe, q - 8)
                    what, h = divmod(q, 6)
                    if q < 30:
                        rows, m = head(h)
                        x = buf(h, XX)
                        cols = slice(h * HD, (h + 1) * HD)
                    if what == 0:
                        last = pe.matmul(b[rows, 0:NS], x[:, 0:HD], ident[:, 0:NS], start=True, stop=True)
                    elif what == 1:
                        s_taken(pe, h)
                        pe.matmul(b[rows, 0:NS], x[:, HD:P], ident[:, 0:NS], start=True, stop=False,
                                  skip_group_check=True)
                        for s in range(NB):
                            last = pe.matmul(b[rows, TS * s:TS * s + TS], s0[m][rows, s * HD:(s + 1) * HD],
                                             wt[rows, m, TS * s:TS * s + TS], start=False, stop=(s == NB - 1),
                                             skip_group_check=True)
                    elif what == 2:
                        pe.matmul(b[rows, 0:P], x[:, HD:P], buf(h, NQ)[:, P:], start=True, stop=False,
                                  skip_group_check=True)
                        pe.matmul(b[rows, 0:P], nat_v[:, cols], buf(h, MP)[:, P:], start=False, stop=False,
                                  skip_group_check=True)
                        for s in range(NB):
                            last = pe.matmul(b[rows, TS * s:TS * s + TS], s0[m][rows, s * HD:(s + 1) * HD],
                                             rt_[rows, m, TS * s:TS * s + TS], start=False, stop=(s == NB - 1),
                                             skip_group_check=True)
                    elif what == 3:
                        s_taken(pe, 6 + h)
                        last = pe.matmul(b[0:NS, 0:HD], ut[rows, m, 0:NS], ident[rows, 64 * (h % 2):64 * (h % 2) + 64],
                                         start=True, stop=True)
                    elif what == 4:
                        s_taken(pe, 18 + h)
                        pe.wait_ge(sm_vm, h + 1)
                        pe.matmul(b[rows, :], nat_b[0:NS, cols], um[h % 2], start=True, stop=False)
                        last = pe.matmul(b[rows, :], nat_k[0:NS, cols], vm[h % 2], start=False, stop=True)
                    elif q < 33:
                        m = q - 30
                        s_taken(pe, 29)
                        for k in range(4):
                            last = pe.transpose(b[:, k * P:(k + 1) * P], s0[m][:, k * P:(k + 1) * P], ident)
                    else:
                        for m in range(3):
                            last = pe.transpose(b[0:HD, m * P:(m + 1) * P], states[:, nch % 4, m], ident)
                    last.then_inc(sm_mm, 1)

            @block.vector
            def _(dve):
                solve_dve(dve, i8)
                dve.wait_ge(st_t, 1)
                for m in range(3):
                    dve.tensor_copy(s0[m], PS[m][:, :]).then_inc(st_cp, 1)

                def expand(h):
                    sel = C("seq_of")[0:NS, :].unsqueeze(2).broadcast_to([NS, NB, HD])
                    cols = slice(h * HD, (h + 1) * HD)
                    if h >= 2:
                        dve.wait_ge(sm_mm, 24 + h - 1)
                    dve.tensor_tensor(vm[h % 2].rearrange("p (b v) -> p b v", b=NB),
                                      nat_v[0:NS, cols].unsqueeze(1).broadcast_to([NS, NB, HD]), sel, ALU.mult
                                      ).then_inc(sm_vm, 1)
                    dve.wait_ge(sm_mm, 18 + h + 1)
                    dve.tensor_tensor(um[h % 2].rearrange("p (b v) -> p b v", b=NB),
                                      PS[(18 + h) % 8][0:NS, 0:HD].unsqueeze(1).broadcast_to([NS, NB, HD]), sel,
                                      ALU.mult).then_inc(sm_dve, 1)

                def new_state(h):
                    rows, m = head(h)
                    dve.wait_ge(sm_mm, 24 + h + 1)
                    st = s0[m][rows]
                    dve.tensor_tensor(st, PS[(24 + h) % 8][rows, :], st, ALU.add).then_inc(s_w1, 1)
                    dve.wait_ge(s_w1, h + 1)
                    st = st.rearrange("p (b v) -> p b v", b=NB)
                    dve.tensor_tensor(st, st, dc[rows, m, nch:].unsqueeze(2).broadcast_to([HD, NB, HD]), ALU.mult
                                      ).then_inc(sm_dve, 1)

                for h in range(H):
                    expand(h)
                for h in range(H):
                    new_state(h)

            @block.scalar
            def _(act):
                solve_act(act, i8)
                for q in range(18):
                    what, h = divmod(q, 6)
                    rows, m = head(h)
                    act.wait_ge(sm_mm, q + 1)
                    b = PS[q % 8]
                    dst = (wt[rows, m], ut[rows, m], AR[rows, m, i8, 0])[what]
                    w = NS if what < 2 else P
                    nc.scalar.copy(dst[:, 0:w], b[rows, 0:w]).then_inc(sm_act, 1)
                for q in range(30, 34):
                    act.wait_ge(sm_mm, q + 1)
                    b = PS[q % 8]
                    if q < 33:
                        m = q - 30
                        nc.scalar.copy(SL[:, :, :, m * P:(m + 1) * P],
                                       b[:, :].rearrange("p (a q c) -> p a q c", a=2, q=2)).then_inc(sm_act, 1)
                    else:
                        nc.scalar.copy(hss_out, b[0:HD, 0:AW]).then_inc(sm_act, 1)
        if upto == "recur_s":
            return

        new_stage()
        cw = Carve(loop_base)
        ysq = [cw.take(384) for _ in range(2)]
        yrt = [cw.take(384) for _ in range(2)]
        yout = [cw.take(384) for _ in range(2)]
        jobs = [(m, c) for m in range(3) for c in range(3)]
        g_sig, y_mean, y_cen, y_sqd, y_var, y_root, y_ri, y_st, g_mm, y_done = (
            sem("gate_sigmoid"), sem("y_mean"), sem("y_centred"), sem("y_squared"), sem("y_variance"),
            sem("y_root"), sem("y_recip"), sem("y_steps"), sem("gate_product"), sem("mixed_written"))
        with nc.Block() as block:
            @block.tensor
            def _(pe):
                def mean(j):
                    m, c = jobs[j]
                    if j >= 2:
                        pe.wait_ge(y_cen, j - 1)
                    pe.matmul(PS[j % 2][:, 0:384], C("head_ones"), AR[:, m, 3 * c:3 * c + 3, 0], start=True,
                              stop=True).then_inc(y_mean, 1)

                mean(0)
                for j, (m, c) in enumerate(jobs):
                    if j + 1 < len(jobs):
                        mean(j + 1)
                    pe.wait_ge(y_sqd, j + 1)
                    if j >= 2:
                        pe.wait_ge(y_root, j - 1)
                        pe.wait_ge(y_done, j - 1)
                    pe.matmul(PS[2 + j % 2][:, 0:384], C("head_ones"), ysq[j % 2], start=True,
                              stop=True).then_inc(y_var, 1)
                    pe.wait_ge(g_sig, 2)
                    pe.matmul(PS[4 + j % 2][:, 0:384], g2[:, m * P:(m + 1) * P], sT[:, 10, 384 * c:384 * (c + 1)],
                              start=True, stop=True).then_inc(g_mm, 1)

            @block.scalar
            def _(act):
                nc.scalar.activation(sT[:, 10], sT[:, 10], ACT.Tanh, scale=0.5).then_inc(g_sig, 1)
                for j in range(len(jobs)):
                    m, c = jobs[j]
                    act.wait_ge(y_cen, j + 1)
                    if j >= 2:
                        act.wait_ge(y_var, j - 1)
                    nc.scalar.activation(tiles3(ysq[j % 2]), AR[:, m, 3 * c:3 * c + 3, 0], ACT.Square
                                         ).then_inc(y_sqd, 1)
                    act.wait_ge(y_var, j + 1)
                    if j >= 2:
                        act.wait_ge(y_done, j - 1)
                    nc.scalar.activation(yrt[j % 2], PS[2 + j % 2][:, 0:384], ACT.Sqrt, scale=1.0 / HD,
                                         bias=epsc[:, 1:2]).then_inc(y_root, 1)

            @block.vector
            def _(dve):
                dve.wait_ge(g_sig, 1)
                dve.tensor_scalar(sT[:, 10], sT[:, 10], 0.5, 0.5, ALU.mult, ALU.add).then_inc(g_sig, 1)

                def centre(j):
                    m, c = jobs[j]
                    y = AR[:, m, 3 * c:3 * c + 3, 0]
                    dve.wait_ge(y_mean, j + 1)
                    dve.scalar_tensor_tensor(out=y, in0=tiles3(PS[j % 2][:, 0:384]), scalar=-1.0 / HD, in1=y,
                                             op0=ALU.mult, op1=ALU.add).then_inc(y_cen, 1)

                link = chain(dve, y_st)
                centre(0)
                for j, (m, c) in enumerate(jobs):
                    if j + 1 < len(jobs):
                        centre(j + 1)
                    y, o = AR[:, m, 3 * c:3 * c + 3, 0], yout[j % 2]
                    t0, n = CH[c]
                    dve.wait_ge(y_root, j + 1)
                    link(dve.reciprocal(yrt[j % 2], yrt[j % 2]))
                    link(dve.tensor_tensor(tiles3(o), y, tiles3(yrt[j % 2]), ALU.mult))
                    link(dve.tensor_scalar(o, o, lnx[:, m:m + 1], lnx[:, 3 + m:4 + m], ALU.mult, ALU.add))
                    link(dve.tensor_tensor(o[:, 0:n], o[:, 0:n], mixT[:, m, t0:t0 + n], ALU.add))
                    dve.wait_ge(g_mm, j + 1)
                    dve.tensor_tensor(mixT[:, m, t0:t0 + n], PS[4 + j % 2][:, 0:n], o[:, 0:n], ALU.mult
                                      ).then_inc(y_done, 1)
        if upto == "mixed":
            return

        new_stage()
        w_out = I["w_out"][0].rearrange("(k p) c -> p k c", p=P)
        mx2 = split_pair("mixed", RS, RK_, KD * T, KD)
        cw = Carve(KD * T)
        wraw = [tiled(cw.take(KD * P)) for _ in range(2)]
        sqa, sqb, rstd = cw.take(T), cw.take(T), cw.take(T)
        xn2 = split_pair("normed2T", RA, RS, KD * T, KD)
        s_w = [sem(f"w_out_in{i}") for i in range(2)]
        w_hi, w_lo, x_hi, x_lo = sem("w_out_hi"), sem("w_out_lo"), sem("mixed_hi"), sem("mixed_lo")
        op_mm, op_cp, n_sq, n_acc, n_mm, n_rt, n_ri, n_t, n_hi, n_lo = (
            sem("out_product"), sem("residual_added"), sem("res_squared"), sem("res_squares_added"),
            sem("res_summed"), sem("res_root"), sem("res_recip"), sem("res_normed"), sem("res_normed_hi"),
            sem("res_normed_lo"))
        parts = [(c, k) for c in range(3) for k in range(KD)]
        with nc.Block() as block:
            def out_hi(act, m):
                act.wait_ge(s_w[m % 2], 16 * (m // 2 + 1))
                split_hi(m, (KD, P), wraw[m % 2], w_hi, op_mm, 3)

            @block.sync
            def _(sp):
                for m in range(KD):
                    if m >= 2:
                        sp.wait_ge(w_lo, m - 1)
                    sp.dma_start(wraw[m % 2], w_out[:, :, m * P:(m + 1) * P]).then_inc(s_w[m % 2], 16)

            @block.tensor
            def _(pe):
                for m in range(KD):
                    pe.wait_ge(w_lo, m + 1)
                    for c, (t0, n) in enumerate(CH):
                        g = 3 * m + c
                        if g >= 5:
                            pe.wait_ge(op_cp, g - 4)
                        for k in range(KD):
                            if m == 0:
                                pe.wait_ge(x_lo, KD * c + k + 1)
                            last = product(pe, PS[g % 5][:, 0:n], [w[:, k] for w in wsp[m % 2]],
                                           [x[:, k, t0:t0 + n] for x in mx2], k == 0, k == KD - 1)
                        last.then_inc(op_mm, 1)
                for c, (t0, n) in enumerate(CH):
                    pe.wait_ge(n_acc, 3 * (KD - 1) + c + 1)
                    pe.matmul(PS[5 + c][:, 0:n], ones, sqa[:, t0:t0 + n], start=True, stop=True).then_inc(n_mm, 1)

            @block.scalar
            def _(act):
                out_hi(act, 0)
                for c, k in parts:
                    t0, n = CH[c]
                    nc.scalar.copy(mx2[0][:, k, t0:t0 + n], mixT[:, k, t0:t0 + n]).then_inc(x_hi, 1)
                out_hi(act, 1)
                for m in range(KD):
                    for c, (t0, n) in enumerate(CH):
                        act.wait_ge(op_cp, 3 * m + c + 1)
                        if m >= 2:
                            act.wait_ge(n_acc, 3 * (m - 1) + c + 1)
                        dst = sqa if m == 0 else sqb
                        nc.scalar.activation(dst[:, t0:t0 + n], xT[:, m, t0:t0 + n], ACT.Square).then_inc(n_sq, 1)
                    if m + 2 < KD:
                        out_hi(act, m + 2)
                for c, (t0, n) in enumerate(CH):
                    act.wait_ge(n_mm, c + 1)
                    nc.scalar.activation(rstd[:, t0:t0 + n], PS[5 + c][:, 0:n], ACT.Sqrt, scale=1.0 / D,
                                         bias=epsc[:, 0:1]).then_inc(n_rt, 1)
                for j, (c, k) in enumerate(parts):
                    t0, n = CH[c]
                    act.wait_ge(n_t, j + 1)
                    nc.scalar.copy(xn2[0][:, k, t0:t0 + n], (sqa, sqb)[j % 2][:, t0:t0 + n]).then_inc(n_hi, 1)

            @block.vector
            def _(dve):
                split_lo(0, (KD, P), wraw[0], w_hi, w_lo)
                for j, (c, k) in enumerate(parts):
                    t0, n = CH[c]
                    dve.wait_ge(x_hi, j + 1)
                    dve.tensor_tensor(mx2[1][:, k, t0:t0 + n], mixT[:, k, t0:t0 + n],
                                      mx2[0][:, k, t0:t0 + n].bitcast(F32), ALU.subtract).then_inc(x_lo, 1)
                split_lo(1, (KD, P), wraw[1], w_hi, w_lo)
                for m in range(KD):
                    for c, (t0, n) in enumerate(CH):
                        g = 3 * m + c
                        dve.wait_ge(op_mm, g + 1)
                        dve.tensor_tensor(xT[:, m, t0:t0 + n], PS[g % 5][:, 0:n], xT[:, m, t0:t0 + n], ALU.add
                                          ).then_inc(op_cp, 1)
                    if m + 2 < KD:
                        split_lo(m + 2, (KD, P), wraw[m % 2], w_hi, w_lo)
                for c, (t0, n) in enumerate(CH):
                    dve.wait_ge(n_rt, c + 1)
                    dve.reciprocal(rstd[:, t0:t0 + n], rstd[:, t0:t0 + n]).then_inc(n_ri, 1)
                for j in range(len(parts) + 1):
                    if j < len(parts):
                        c, k = parts[j]
                        t0, n = CH[c]
                        dve.wait_ge(n_ri, c + 1)
                        if j >= 2:
                            dve.wait_ge(n_lo, j - 1)
                        else:
                            dve.wait_ge(n_mm, 3)
                        dve.scalar_tensor_tensor(out=(sqa, sqb)[j % 2][:, t0:t0 + n], in0=xT[:, k, t0:t0 + n],
                                                 scalar=vec("norm_ffn_g", k), in1=rstd[:, t0:t0 + n],
                                                 op0=ALU.mult, op1=ALU.mult).then_inc(n_t, 1)
                    if j >= 1:
                        c, k = parts[j - 1]
                        t0, n = CH[c]
                        dve.wait_ge(n_hi, j)
                        dve.tensor_tensor(xn2[1][:, k, t0:t0 + n], (sqa, sqb)[(j - 1) % 2][:, t0:t0 + n],
                                          xn2[0][:, k, t0:t0 + n].bitcast(F32), ALU.subtract).then_inc(n_lo, 1)

            @block.gpsimd
            def _(pool):
                for c in range(3):
                    pool.wait_ge(n_sq, c + 1)
                    pool.sem_inc(n_acc, 1)
                for m in range(1, KD):
                    for c, (t0, n) in enumerate(CH):
                        pool.wait_ge(n_sq, 3 * m + c + 1)
                        nc.gpsimd.tensor_tensor(sqa[:, t0:t0 + n], sqa[:, t0:t0 + n], sqb[:, t0:t0 + n], ALU.add
                                                ).then_inc(n_acc, 1)
        if upto == "outproj":
            return

        new_stage()
        GROUPS = [5, 5, 4, 4, 4]
        G = max(GROUPS)
        first_of = [sum(GROUPS[:i]) for i in range(len(GROUPS) + 1)]
        stream = []
        for gi, n in enumerate(GROUPS):
            for f in range(first_of[gi], first_of[gi] + n):
                stream.append(("gate", f))
                if f == first_of[gi] and gi:
                    stream += [("down", gi - 1, m) for m in range(KD)]
                stream.append(("up", f))
        stream += [("down", len(GROUPS) - 1, m) for m in range(KD)]
        NW = len(stream)
        nth = {"gate": 0, "up": 0, "down": 0}
        order = []
        for item in stream:
            order.append(nth[item[0]])
            nth[item[0]] += 1
        S2 = KD * T
        gend = sT_[:, S2:S2 + 18 * FT].rearrange("p (j f) -> p j f", f=FT)
        S2 += (18 * FT + 7) // 8 * 8
        cv, hraw = sT_[:, S2:S2 + T], sT_[:, S2 + T:S2 + 2 * T]
        S2 += 2 * T
        h2 = split_pair("inner", RK_, RK_ + G * T, G * T, G)
        cw = Carve(2 * G * T)
        GW = 2 + SEQ + NB * (2 + TS)
        gring = [cw.take(GW) for _ in range(2)]
        wraw = [tiled(sT_[:, S2:S2 + KD * P]), tiled(cw.take(KD * P)), tiled(cw.take(KD * P))]
        assert S2 + KD * P <= A_TILES * TPAD
        w_up = I["w_up"][0].rearrange("(k p) c -> p k c", p=P)
        w_down = I["w_down"][0].rearrange("(f p) c -> p f c", p=P)
        s_wu = [sem(f"w_ffn_in{i}") for i in range(3)]
        w_hi, w_lo = sem("w_ffn_hi"), sem("w_ffn_lo")
        f_mm, f_gate, f_conv, f_steps, f_tanh, f_pre, f_st, f_up, f_hh, f_hl, f_dn = (
            sem("ffn_product"), sem("gate_copied"), sem("conv_done"), sem("conv_steps"), sem("silu_tanh"),
            sem("gate_prefix"), sem("gate_history"), sem("up_taken"), sem("inner_hi"), sem("inner_lo"),
            sem("down_added"))

        def rows_w(j):
            return KD if stream[j][0] != "down" else GROUPS[stream[j][1]]

        def slot_of(f):
            gi = max(i for i in range(len(GROUPS)) if first_of[i] <= f)
            return f - first_of[gi]

        def down_after(f):
            gi = max(i for i in range(len(GROUPS)) if first_of[i] <= f)
            return KD * gi

        with nc.Block() as block:
            def ffn_hi(act, j):
                act.wait_ge(s_wu[j % 3], 16 * (j // 3 + 1))
                split_hi(j, (rows_w(j), P), wraw[j % 3], w_hi, f_mm, 3)

            def ffn_lo(dve, j):
                split_lo(j, (rows_w(j), P), wraw[j % 3], w_hi, w_lo)

            @block.sync
            def _(sp):
                for j, item in enumerate(stream):
                    if j >= 3:
                        sp.wait_ge(w_lo, j - 2)
                    if item[0] == "down":
                        f0 = first_of[item[1]]
                        src = w_down[:, f0:f0 + rows_w(j), item[2] * P:(item[2] + 1) * P]
                    else:
                        c0 = item[1] * P + (0 if item[0] == "up" else DFF)
                        src = w_up[:, :, c0:c0 + P]
                    sp.dma_start(wraw[j % 3][:, 0:rows_w(j)], src).then_inc(s_wu[j % 3], 16)

            @block.tensor
            def _(pe):
                for j, item in enumerate(stream):
                    pe.wait_ge(w_lo, j + 1)
                    if item[0] == "down":
                        pe.wait_ge(f_hl, first_of[item[1] + 1])
                    x = h2 if item[0] == "down" else xn2
                    for c, (t0, n) in enumerate(CH):
                        g = 3 * j + c
                        if g >= 8:
                            pj, pc = divmod(g - 8, 3)
                            done = {"gate": f_gate, "up": f_up, "down": f_dn}[stream[pj][0]]
                            pe.wait_ge(done, 3 * order[pj] + pc + 1)
                        for k in range(rows_w(j)):
                            last = product(pe, PS[g % 8][:, 0:n], [w[:, k] for w in wsp[j % 2]],
                                           [v[:, k, t0:t0 + n] for v in x], k == 0, k == rows_w(j) - 1)
                        last.then_inc(f_mm, 1)

            @block.gpsimd
            def _(pool):
                for j in range(2):
                    ins = nc.gpsimd.memset(gring[j][:, 0:2], 0.0)
                ins.then_inc(f_pre, 1)
                for f in range(FT):
                    if f >= 2:
                        pool.wait_ge(f_conv, f - 1)
                    nc.gpsimd.tensor_copy(seg(gring[f % 2], 2)[1][:, :, 0:2],
                                          convT[:, f].rearrange("p (b t) -> p b t", b=NB)).then_inc(f_pre, 1)
                    pool.wait_ge(f_gate, 3 * f + 3)
                    p_seq, s_seq = seg(gring[f % 2], 2)
                    nc.gpsimd.tensor_copy(gend[:, 0:2, f], p_seq[:, SEQ - 2:SEQ])
                    nc.gpsimd.tensor_copy(gend[:, 2:18, f].rearrange("p (b t) -> p b t", b=NB),
                                          s_seq[:, :, TS:TS + 2]).then_inc(f_st, 1)

            @block.scalar
            def _(act):
                def gate(j, f):
                    if f >= 2:
                        act.wait_ge(f_conv, f - 1)
                        act.wait_ge(f_st, f - 1)
                    p_seq, s_seq = seg(gring[f % 2], 2)
                    for c, (t0, n) in enumerate(CH):
                        g = 3 * j + c
                        act.wait_ge(f_mm, g + 1)
                        k = min(n, SEQ - t0)
                        ins = nc.scalar.copy(p_seq[:, t0:t0 + k], PS[g % 8][:, 0:k])
                        if c == 2:
                            ins = nc.scalar.copy(s_seq[:, :, 2:], PS[g % 8][:, k:k + NS].rearrange(
                                "p (b t) -> p b t", b=NB))
                        ins.then_inc(f_gate, 1)
                    act.wait_ge(f_conv, f + 1)
                    if f >= 1:
                        act.wait_ge(f_hl, f)
                    nc.scalar.activation(hraw, cv, ACT.Tanh, scale=0.5).then_inc(f_tanh, 1)

                ffn_hi(act, 0)
                ffn_hi(act, 1)
                for j, item in enumerate(stream):
                    if item[0] == "gate":
                        gate(j, item[1])
                    elif item[0] == "up":
                        f = item[1]
                        act.wait_ge(f_up, 3 * f + 3)
                        if down_after(f):
                            act.wait_ge(f_dn, 3 * down_after(f))
                        nc.scalar.copy(h2[0][:, slot_of(f)], hraw).then_inc(f_hh, 1)
                    if j + 2 < NW:
                        ffn_hi(act, j + 2)

            @block.vector
            def _(dve):
                link = chain(dve, f_steps)

                def conv(f):
                    p_all = gring[f % 2][:, 0:2 + SEQ]
                    s_all = seg(gring[f % 2], 2)[1]
                    cv_s = cv[:, SEQ:T].rearrange("p (b t) -> p b t", b=NB)
                    dve.wait_ge(f_gate, 3 * f + 3)
                    dve.wait_ge(f_pre, f + 2)
                    for t in range(3):
                        w = vec("conv_w", t * FT + f)
                        if t == 0:
                            dve.tensor_scalar(cv[:, 0:SEQ], p_all[:, 0:SEQ], w, vec("conv_b", f), ALU.mult, ALU.add)
                            link(dve.tensor_scalar(cv_s, s_all[:, :, 0:TS], w, vec("conv_b", f), ALU.mult, ALU.add))
                        else:
                            dve.scalar_tensor_tensor(out=cv[:, 0:SEQ], in0=p_all[:, t:t + SEQ], scalar=w,
                                                     in1=cv[:, 0:SEQ], op0=ALU.mult, op1=ALU.add)
                            ins = dve.scalar_tensor_tensor(out=cv_s, in0=s_all[:, :, t:t + TS], scalar=w, in1=cv_s,
                                                           op0=ALU.mult, op1=ALU.add)
                            if t == 1:
                                link(ins)
                            else:
                                ins.then_inc(f_conv, 1)

                def inner(j, f):
                    dve.wait_ge(f_tanh, f + 1)
                    link(dve.scalar_tensor_tensor(out=hraw, in0=hraw, scalar=1.0, in1=cv, op0=ALU.add,
                                                  op1=ALU.mult))
                    for c, (t0, n) in enumerate(CH):
                        g = 3 * j + c
                        dve.wait_ge(f_mm, g + 1)
                        dve.scalar_tensor_tensor(out=hraw[:, t0:t0 + n], in0=PS[g % 8][:, 0:n], scalar=0.5,
                                                 in1=hraw[:, t0:t0 + n], op0=ALU.mult, op1=ALU.mult
                                                 ).then_inc(f_up, 1)
                    dve.wait_ge(f_hh, f + 1)
                    dve.tensor_tensor(h2[1][:, slot_of(f)], hraw, h2[0][:, slot_of(f)].bitcast(F32), ALU.subtract
                                      ).then_inc(f_hl, 1)

                ffn_lo(dve, 0)
                ffn_lo(dve, 1)
                for j, item in enumerate(stream):
                    if item[0] == "gate":
                        conv(item[1])
                    elif item[0] == "up":
                        inner(j, item[1])
                    else:
                        m = item[2]
                        for c, (t0, n) in enumerate(CH):
                            dve.wait_ge(f_mm, 3 * j + c + 1)
                            dve.tensor_tensor(xT[:, m, t0:t0 + n], PS[(3 * j + c) % 8][:, 0:n], xT[:, m, t0:t0 + n],
                                              ALU.add).then_inc(f_dn, 1)
                    if j + 2 < NW:
                        ffn_lo(dve, j + 2)
        if upto == "down":
            return

        cnat = wring[:, 0:4 * P].rearrange("p (q c) -> p q c", q=4)
        g_t, g_cp = sem("history_turned"), sem("history_copied")
        with nc.Block() as block:
            @block.sync
            def _(sp):
                sp.wait_ge(g_cp, 1)
                sp.dma_start(conv_p[0, 0].rearrange("t (f c) -> (t f) c", c=P), cnat[0:44, 0]).then_inc(s_co, 16)
                flat = conv_s[0].rearrange("b t (f c) -> (b t f) c", c=P)
                for q in range(3):
                    n = min(P, 352 - q * P)
                    sp.dma_start(flat[q * P:q * P + n, :], cnat[0:n, q + 1]).then_inc(s_co, 16)
                sp.wait_ge(s_co, 64)

            @block.tensor
            def _(pe):
                flat = gend.rearrange("p j f -> p (j f)")
                for q, (a, n) in enumerate(((0, 44), (44, P), (44 + P, P), (44 + 2 * P, 96))):
                    last = pe.transpose(PS[7][0:n, q * P:(q + 1) * P], flat[:, a:a + n], ident)
                last.then_inc(g_t, 1)

            @block.scalar
            def _(act):
                act.wait_ge(g_t, 1)
                for q, n in enumerate((44, P, P, 96)):
                    ins = nc.scalar.copy(cnat[0:n, q], PS[7][0:n, q * P:(q + 1) * P])
                ins.then_inc(g_cp, 1)

        new_stage()
        g_last = work[:, 0:D]
        yrow = [work[:, D * (1 + i):D * (2 + i)] for i in range(3)]
        junk = work[:, 4 * D:4 * D + 512]
        fs = small[:, 0:5 * TT].rearrange("p (i a) -> p i a", i=TT)
        s_gl, e_t, e_sq, e_sum, e_rt, e_ri, e_y = (sem("final_gain_in"), sem("final_turned"), sem("final_squared"),
                                                   sem("final_sum"), sem("final_root"), sem("final_recip"),
                                                   sem("final_scaled"))
        with nc.Block() as block:
            @block.sync
            def _(sp):
                sp.dma_start(g_last, I["norm_final_g"].partition_broadcast(P)).then_inc(s_gl, 16)
                for i in range(TT):
                    n = rows_of(i)
                    sp.wait_ge(e_y, 2 * i + 2)
                    dst = y_prompt[0, i * P:(i + 1) * P, :] if i < TT - 1 else y_sample.rearrange("b t d -> (b t) d")
                    sp.dma_start(dst, yrow[i % 3][0:n, :]).then_inc(s_y[i % 3], 16)
                for j in range(3):
                    sp.wait_ge(s_y[j], 48)

            @block.tensor
            def _(pe):
                for i in range(TT):
                    n = rows_of(i)
                    if i >= 4:
                        pe.wait_ge(e_y, 2 * (i - 3))
                    for k in range(KD):
                        last = pe.transpose(PS[2 * (i % 4) + k // 4][0:n, (k % 4) * P:(k % 4 + 1) * P],
                                            xT[:, k, i * P:i * P + n], ident)
                    last.then_inc(e_t, 1)

            @block.scalar
            def _(act):
                for i in range(TT):
                    n = rows_of(i)
                    act.wait_ge(e_t, i + 1)
                    for j in range(2):
                        k = 2 * i + j
                        if k >= 1:
                            act.wait_ge(e_sq, k)
                        nc.scalar.activation(junk[0:n, :], PS[2 * (i % 4) + j][0:n, :], ACT.Square,
                                             accum_out=fs[0:n, i, j:j + 1]).then_inc(e_sq, 1)
                    act.wait_ge(e_sum, i + 1)
                    nc.scalar.activation(fs[0:n, i, 3:4], fs[0:n, i, 2:3], ACT.Sqrt, scale=1.0 / D,
                                         bias=epsc[0:n, 0:1]).then_inc(e_rt, 1)

            @block.vector
            def _(dve):
                dve.wait_ge(s_gl, 16)
                for i in range(TT):
                    n = rows_of(i)
                    dve.wait_ge(e_sq, 2 * i + 2)
                    dve.tensor_tensor(fs[0:n, i, 2:3], fs[0:n, i, 0:1], fs[0:n, i, 1:2], ALU.add).then_inc(e_sum, 1)
                    dve.wait_ge(e_rt, i + 1)
                    dve.reciprocal(fs[0:n, i, 4:5], fs[0:n, i, 3:4]).then_inc(e_ri, 1)
                    dve.wait_ge(e_ri, i + 1)
                    if i >= 3:
                        dve.wait_ge(s_y[i % 3], 16 * (i // 3))
                    for j in range(2):
                        dve.scalar_tensor_tensor(out=yrow[i % 3][0:n, 512 * j:512 * j + 512],
                                                 in0=PS[2 * (i % 4) + j][0:n, :], scalar=fs[0:n, i, 4:5],
                                                 in1=g_last[0:n, 512 * j:512 * j + 512], op0=ALU.mult,
                                                 op1=ALU.mult).then_inc(e_y, 1)


def kernel(**inputs):
    import numpy as _np
    import concourse.bacc as _bacc
    from concourse import mybir as _mybir
    from concourse.bass_utils import run_bass_kernel_spmd as _run

    nc = _bacc.Bacc("TRN2", target_bir_lowering=False, num_devices=1)
    arrays, args = {}, {}
    for name, a in {**inputs, **constants()}.items():
        a = _np.ascontiguousarray(a)
        arrays[f"in_{name}_dram"] = a
        args[name] = nc.dram_tensor(f"in_{name}_dram", a.shape, _mybir.dt.from_np(a.dtype), kind="ExternalInput").ap()
    outs = [nc.dram_tensor(f"out_{i}_dram", shape, _mybir.dt.float32, kind="ExternalOutput").ap()
            for i, shape in enumerate(OUT_SHAPES)]
    build(nc, args, outs)
    r = _run(nc, [arrays], core_ids=[0])
    return tuple(r.results[0][f"out_{i}_dram"] for i in range(len(OUT_SHAPES)))
```

```python
from contextlib import ExitStack

import numpy as np
import concourse.bass as bass
from concourse import mybir

ALU = mybir.AluOpType
ACT = mybir.ActivationFunctionType
AX_X = mybir.AxisListType.X
F32 = mybir.dt.float32
F32R = mybir.dt.float32r
I32 = mybir.dt.int32

P = 128
D = 1024
KD = D // P
SEQ = 1024
NB = 8
TS = 8
NS = NB * TS
T = SEQ + NS
TT = (T + P - 1) // P
TPAD = TT * P
NPAGE = 32
PAGE = 128
NPOOL = 320
H = 6
HD = 64
AW = H * HD
A_COLS = 3 * AW + 256
A_TILES = A_COLS // P
RANK = 256
ROPE = 32
CW = 256
PRE = 15
IN_COLS = 2528
DFF = 2816
FT = DFF // P
EPS = 1e-6
GN_EPS = HD * 1e-5
SCALE = float(HD + ROPE) ** -0.5
CHUNK = 64
DECAY = -float(np.exp(-0.5))
CH = [(0, 384), (384, 384), (768, 320)]
NEG = -1e30

OUT_SHAPES = [(1, SEQ, D), (NB, TS, D), (1, 1, SEQ, RANK), (1, 1, SEQ, ROPE), (1, 1, H, HD, HD), (1, 1, A_COLS),
              (1, 1, PRE, CW), (1, 1, 2, DFF), (1, NB, TS, RANK), (1, NB, TS, ROPE), (1, NB, H, HD, HD),
              (1, NB, A_COLS), (1, NB, PRE, CW), (1, NB, 2, DFF)]

VEC = {}
for _name, _n in (("mu_shift", 11), ("decay_w0", 3), ("iclr_a0", 3), ("k_k", 3), ("k_a", 3), ("r_k", 3),
                  ("kv_norm_g", 2), ("pool_scale", 2), ("norm_ffn_g", 8), ("conv_b", 22), ("conv_w", 66)):
    VEC[_name] = (sum(n for _, n in VEC.values()), _n)
NVEC = sum(n for _, n in VEC.values())

CONST = {}
for _name, _n in (("ident", P), ("ones", P), ("head_ones", P), ("rot", P), ("keep_p", 2 * P), ("keep_s", 2 * P),
                  ("diag_p", P), ("diag_s", P), ("diag_pT", P), ("diag_sT", P), ("off_p", P), ("off_s", P),
                  ("causal", P), ("inv_w", 2), ("inv_cnt", 32), ("seq_of", 8), ("head_sel", 2)):
    CONST[_name] = (sum(n for _, n in CONST.values()), _n)
NCONST = sum(n for _, n in CONST.values())


def constants():
    f = np.float32
    c = np.zeros((P, NCONST), f)

    def put(name, a):
        c[:, CONST[name][0]:CONST[name][0] + CONST[name][1]] = a

    i = np.arange(P)
    s, t = i[:, None], i[None, :]
    put("ident", s == t)
    put("ones", 1.0)
    put("head_ones", s // HD == t // HD)
    rot = np.zeros((P, P), f)
    for m in range(P):
        if m % ROPE < ROPE // 2:
            rot[m + ROPE // 2, m] = -1.0
        else:
            rot[m - ROPE // 2, m] = 1.0
    put("rot", rot)
    for tag, chunk, block in (("p", CHUNK, 16), ("s", TS, TS)):
        same = s // chunk == t // chunk
        put("keep_" + tag, np.concatenate([same & (s < t), same & (s <= t)], 1))
        put("diag_" + tag, s // block == t // block)
        put("diag_" + tag + "T", s // block == t // block)
        put("off_" + tag, s // block != t // block)
    put("causal", np.where(t <= s, 0.0, NEG))
    win = np.array([[2, 8], [4, 16]], f)[i // HD]
    put("inv_w", 1.0 / win)
    pos = np.arange(16)
    put("inv_cnt", (win[:, :, None] / np.minimum(pos[None, None] + 1, win[:, :, None])).reshape(P, 32))
    put("seq_of", (i[:, None] // TS == np.arange(NB)[None]) & (i[:, None] < NS))
    put("head_sel", (i[:, None] // HD == np.arange(2)[None]))
    pos = np.concatenate([np.arange(SEQ), NPAGE * PAGE + np.tile(np.arange(TS), NB)]).astype(f)
    inv = (f(10000.0) ** (-np.arange(0, ROPE, 2, dtype=f) / f(ROPE))).astype(f)
    ang = (pos[:, None] * inv[None]).astype(f)
    rope = np.stack([np.tile(np.cos(ang).T, (8, 1)), np.tile(np.sin(ang).T, (8, 1))], 1).astype(f)
    fresh = np.ones((P, TPAD), f)
    fresh[:, 0:SEQ:CHUNK] = 0.0
    fresh[:, SEQ::TS] = 0.0
    key = np.arange(NS)
    row = np.arange(P)
    seq = np.arange(NB // 2)[None, :] + NB // 2 * (row[:, None] // HD)
    new = (key // TS == seq[:, :, None]) & (key % TS <= row[:, None, None] % TS)
    newmask = np.where(new, 0.0, NEG).astype(f).reshape(P, NB // 2 * NS)
    return {"c_const": c, "c_rope": rope, "c_fresh": fresh, "c_newmask": newmask}


def build(nc, I, outs, upto="all"):
    (y_prompt, y_sample, kv_p, kr_p, wkv_p, shift_p, pool_p, conv_p, kv_s, kr_s, wkv_s, shift_s, pool_s,
     conv_s) = outs
    ctx = ExitStack()
    with ctx:
        def sb(name, words, dt=F32, parts=P):
            return ctx.enter_context(nc.sbuf_tensor(name, [parts, words], dt))

        stage_sems = []

        def sem(name):
            stage_sems.append(nc.alloc_semaphore(name))
            return stage_sems[-1]

        s_po, s_wo, s_co = (nc.alloc_semaphore(n) for n in ("pool_shift_out", "states_out", "history_out"))
        s_nat = [nc.alloc_semaphore(f"rows_out{i}") for i in range(2)]
        s_y = [nc.alloc_semaphore(f"final_out{i}") for i in range(3)]

        def new_stage():
            nc.clear_and_free_semaphores(list(stage_sems))
            stage_sems.clear()
            nc.all_engine_barrier()

        PS = [ctx.enter_context(nc.psum_tensor(f"bank{i}", [P, 512], F32)) for i in range(8)]

        R0 = 0
        RA = R0 + KD * T
        RS = RA + KD * T
        RC = RS + A_TILES * TPAD
        RW = RC + (NCONST + 7) // 8 * 8
        RM = RW + 4 * KD * P
        RK_ = RM + 1632
        WORK = 15296
        arena = sb("arena", RK_ + WORK)
        base = 16512

        def lay(name, word, words, dt=F32):
            assert word % 8 == 0 and word + words <= RK_ + WORK, (name, word, words)
            return nc.alloc_sbuf_tensor_at(name, [P, words], dt, offset=base + 4 * word)

        res = lay("residualT", R0, KD * T)
        actA = lay("mixedT", RA, KD * T)
        sT_ = lay("rwkv_streamsT", RS, A_TILES * TPAD)
        con = lay("constants", RC, NCONST)
        wring = lay("weight_ring", RW, 4 * KD * P)
        small = lay("small", RM, 1632)
        work = lay("work", RK_, WORK)

        xT = res[:, :].rearrange("p (k t) -> p k t", k=KD)
        mixT = actA[:, :].rearrange("p (k t) -> p k t", k=KD)
        sT = sT_[:, :].rearrange("p (m t) -> p m t", m=A_TILES)
        spill = nc.dram_tensor("residual_spill", (P, KD, T), F32, kind="Internal").ap()

        def tiled(ap, k=KD):
            return ap.rearrange("p (k t) -> p k t", k=k)

        def split_pair(name, word_hi, word_lo, words, k):
            hi, lo = lay(name + "_hi", word_hi, words, F32R), lay(name + "_lo", word_lo, words, F32R)
            return tiled(hi[:, :], k), tiled(lo[:, :], k)

        def product(pe, out, w, x, first, last):
            pe.matmul(out, w[0], x[0], start=first, stop=False)
            pe.matmul(out, w[1], x[0], start=False, stop=False)
            return pe.matmul(out, w[0], x[1], start=False, stop=last)

        def C(name):
            return con[:, CONST[name][0]:CONST[name][0] + CONST[name][1]]

        ident, ones = C("ident"), C("ones")
        at = [0]

        def piece(n):
            at[0] += n
            assert at[0] <= 1632, at
            return small[:, at[0] - n:at[0]]

        vecs = piece(NVEC + 2)[:, 0:NVEC]
        shiftT = piece(A_TILES * NB).rearrange("p (m b) -> p m b", m=A_TILES)
        lnx = piece(6)
        poolT = piece(2 * 120).rearrange("p (m q) -> p m q", m=2)
        convT = piece(FT * 16).rearrange("p (m q) -> p m q", m=FT)
        stat = piece(32)
        epsc = piece(4)
        ckv_new = piece(RANK)[0:NS, :]
        ckvT_new = piece(2 * NS).rearrange("p (k t) -> p k t", k=2)
        krT_new = piece(NS)
        halves = piece(9)
        shift_out = piece(9 * A_TILES).rearrange("p (j m) -> p j m", m=A_TILES)

        def vec(name, k):
            return vecs[:, VEC[name][0] + k:VEC[name][0] + k + 1]

        def chain(eng, signal):
            count = [0]

            def link(ins):
                count[0] += 1
                ins.then_inc(signal, 1)
                eng.wait_ge(signal, count[0])
            return link

        class Carve:
            def __init__(self, base=0):
                self.at = base

            def take(self, n):
                self.at += n
                assert self.at <= WORK, self.at
                return work[:, self.at - n:self.at]

        xn = split_pair("normedT", R0, RA, KD * T, KD)
        xraw = [sT_[:, i * D:(i + 1) * D].rearrange("p (k t) -> p k t", k=KD) for i in range(2)]
        s_xo = [sem(f"x_spilled{i}") for i in range(2)]
        c_hi = sem("norm_hi")
        cw = Carve()
        xin = [cw.take(D) for _ in range(3)]
        xsc = [cw.take(D) for _ in range(2)]
        sq_junk = cw.take(D)
        g_rows = cw.take(D)
        vrows = cw.take(P)
        shrows = cw.take(A_COLS)
        cvrows = cw.take(DFF)
        plrows = cw.take(CW)
        s_const, s_vec, s_st, s_g = sem("consts_in"), sem("vectors_in"), sem("states_in"), sem("gain_in")
        s_x = [sem(f"x_in{i}") for i in range(3)]
        x_sq, x_rt, x_rs, x_sc = sem("x_squared"), sem("x_root"), sem("x_recip"), sem("x_scaled")
        t_raw, t_nrm, c_raw, c_nrm = sem("raw_turned"), sem("norm_turned"), sem("raw_copied"), sem("norm_copied")
        t_vec, c_vec, t_st, c_st = sem("vec_turned"), sem("vec_copied"), sem("state_turned"), sem("state_copied")
        s_eps = sem("eps_set")

        def rows_of(i):
            return P if i < TT - 1 else NS

        with nc.Block() as block:
            def copy_raw(act, i):
                n = rows_of(i)
                act.wait_ge(t_raw, i + 1)
                if i >= 2:
                    act.wait_ge(s_xo[i % 2], 16 * (i // 2))
                for j in range(2):
                    nc.scalar.copy(xraw[i % 2][:, 4 * j:4 * j + 4, 0:n],
                                   tiled(PS[4 * (i % 2) + j][:, :], 4)[:, :, 0:n]).then_inc(c_raw, 1)

            def spill_x(sp, i):
                n = rows_of(i)
                sp.wait_ge(c_raw, 2 * i + 2)
                sp.dma_start(spill[:, :, i * P:i * P + n], xraw[i % 2][:, :, 0:n]).then_inc(s_xo[i % 2], 16)

            def norm_hi(act, i):
                n = rows_of(i)
                act.wait_ge(t_nrm, i + 1)
                for j in range(2):
                    nc.scalar.copy(xn[0][:, 4 * j:4 * j + 4, i * P:i * P + n],
                                   tiled(PS[4 * (i % 2) + 2 + j][:, :], 4)[:, :, 0:n]).then_inc(c_hi, 1)

            def norm_lo(dve, i):
                n = rows_of(i)
                for j in range(2):
                    dve.wait_ge(c_hi, 2 * i + j + 1)
                    at_ = (slice(None), slice(4 * j, 4 * j + 4), slice(i * P, i * P + n))
                    dve.tensor_tensor(xn[1][at_], tiled(PS[4 * (i % 2) + 2 + j][:, :], 4)[:, :, 0:n],
                                      xn[0][at_].bitcast(F32), ALU.subtract).then_inc(c_nrm, 1)

            @block.sync
            def _(sp):
                for i in range(TT):
                    n = rows_of(i)
                    if i >= 3:
                        sp.wait_ge(t_raw, i - 2)
                        sp.wait_ge(x_sc, i - 2)
                    src = I["x_prompt"][0, i * P:(i + 1) * P, :] if i < TT - 1 else \
                        I["x_sample"].rearrange("b t d -> (b t) d")
                    sp.dma_start(xin[i % 3][0:n, :], src).then_inc(s_x[i % 3], 16)
                    if i == 0:
                        sp.dma_start(con[:, :], I["c_const"]).then_inc(s_const, 16)
                    if i >= 2:
                        spill_x(sp, i - 2)
                for i in (TT - 2, TT - 1):
                    spill_x(sp, i)
                sp.wait_ge(s_xo[0], 16 * 5)
                sp.wait_ge(s_xo[1], 16 * 4)

            @block.scalar
            def _(act):
                act.dma_start(g_rows, I["norm_mix_g"][0, :].partition_broadcast(P)).then_inc(s_g, 16)
                for name, (a, n) in VEC.items():
                    src = I[name]
                    src = src.rearrange({2: "l d -> (l d)", 3: "l a d -> (l a d)"}[len(src.shape)])
                    act.dma_start(vrows[a:a + n, :], src.rearrange("(a p) -> a p", p=P)).then_inc(s_vec, 16)
                act.dma_start(shrows[0:NB, :], I["state_shift"][0]).then_inc(s_st, 16)
                act.dma_start(plrows[0:120, :], I["state_pool"][0].rearrange("b t c -> (b t) c")).then_inc(s_st, 16)
                for j, name in enumerate(("lnx_w", "lnx_b")):
                    act.dma_start(plrows[120 + 3 * j:123 + 3 * j, 0:P],
                                  I[name][0].rearrange("(a p) -> a p", p=P)).then_inc(s_st, 16)
                act.dma_start(cvrows[0:16, :], I["state_conv"][0].rearrange("b t c -> (b t) c")).then_inc(s_st, 16)
                act.wait_ge(s_eps, 1)
                for i in range(TT):
                    n = rows_of(i)
                    act.wait_ge(s_x[i % 3], 16 * (i // 3 + 1))
                    if i >= 1:
                        act.wait_ge(x_sq, i)
                    nc.scalar.activation(sq_junk[0:n, :], xin[i % 3][0:n, :], ACT.Square,
                                         accum_out=stat[0:n, i:i + 1]).then_inc(x_sq, 1)
                    act.wait_ge(x_sq, i + 1)
                    nc.scalar.activation(stat[0:n, 10 + i:11 + i], stat[0:n, i:i + 1], ACT.Sqrt,
                                         bias=epsc[0:n, 0:1], scale=1.0 / D).then_inc(x_rt, 1)
                    if i >= 1:
                        copy_raw(act, i - 1)
                        norm_hi(act, i - 1)
                copy_raw(act, TT - 1)
                norm_hi(act, TT - 1)

            @block.vector
            def _(dve):
                dve.memset(epsc[:, 0:1], EPS)
                dve.memset(epsc[:, 1:2], GN_EPS)
                dve.memset(epsc[:, 2:3], 1e-24).then_inc(s_eps, 1)
                dve.wait_ge(t_vec, 1)
                dve.tensor_copy(vecs, PS[6][:, 0:NVEC]).then_inc(c_vec, 1)
                dve.wait_ge(t_st, 1)
                dve.tensor_copy(shiftT, PS[6][:, 128:216].rearrange("p (m b) -> p m b", b=NB)).then_inc(c_st, 1)
                dve.tensor_copy(poolT[:, 0], PS[6][:, 216:336])
                dve.tensor_copy(lnx, PS[6][:, 336:342])
                dve.tensor_copy(poolT[:, 1], PS[6][:, 342:462]).then_inc(c_st, 1)
                dve.tensor_copy(convT, PS[7][:, 0:352].rearrange("p (m q) -> p m q", m=FT)).then_inc(c_st, 1)
                dve.wait_ge(s_g, 16)
                for i in range(TT):
                    n = rows_of(i)
                    dve.wait_ge(x_rt, i + 1)
                    dve.reciprocal(stat[0:n, 20 + i:21 + i], stat[0:n, 10 + i:11 + i]).then_inc(x_rs, 1)
                    dve.wait_ge(x_rs, i + 1)
                    if i >= 2:
                        dve.wait_ge(t_nrm, i - 1)
                    dve.scalar_tensor_tensor(out=xsc[i % 2][0:n, :], in0=xin[i % 3][0:n, :],
                                             scalar=stat[0:n, 20 + i:21 + i], in1=g_rows[0:n, :],
                                             op0=ALU.mult, op1=ALU.mult).then_inc(x_sc, 1)
                    if i >= 1:
                        norm_lo(dve, i - 1)
                norm_lo(dve, TT - 1)

            @block.tensor
            def _(pe):
                pe.wait_ge(s_const, 16)
                pe.wait_ge(s_vec, 16 * len(VEC))
                pe.transpose(PS[6][:, 0:NVEC], vrows[0:NVEC, :], ident[0:NVEC, 0:NVEC]).then_inc(t_vec, 1)
                pe.wait_ge(s_st, 80)
                pe.wait_ge(c_vec, 1)
                for m in range(A_TILES):
                    pe.transpose(PS[6][:, 128 + NB * m:128 + NB * m + NB], shrows[0:NB, m * P:(m + 1) * P],
                                 ident[0:NB, 0:NB])
                for m, n in enumerate((126, 120)):
                    pe.transpose(PS[6][:, 216 + 126 * m:216 + 126 * m + n], plrows[0:n, m * P:(m + 1) * P],
                                 ident[0:n, 0:n])
                for m in range(FT):
                    last = pe.transpose(PS[7][:, 16 * m:16 * m + 16], cvrows[0:16, m * P:(m + 1) * P],
                                        ident[0:16, 0:16])
                last.then_inc(t_st, 1)
                for i in range(TT):
                    n = rows_of(i)
                    for which, (src, b0) in enumerate(((xin[i % 3], 0), (xsc[i % 2], 2))):
                        if which == 0:
                            pe.wait_ge(s_x[i % 3], 16 * (i // 3 + 1))
                        else:
                            pe.wait_ge(x_sc, i + 1)
                            if i == 1:
                                pe.wait_ge(c_st, 3)
                        if i >= 2:
                            pe.wait_ge(c_raw if which == 0 else c_nrm, 2 * (i - 1))
                        for k in range(KD):
                            bank = PS[4 * (i % 2) + b0 + k // 4]
                            last = pe.transpose(bank[:, (k % 4) * P:(k % 4) * P + n], src[0:n, k * P:(k + 1) * P],
                                                ident[0:n, 0:n])
                        last.then_inc(t_raw if which == 0 else t_nrm, 1)
        if upto == "load":
            return

        new_stage()
        A, B = A_COLS, A_COLS + 864
        tiles = [([(m * P, P)], ("rwkv", m)) for m in range(A_TILES)]
        tiles += [([(B + m * P, P)], ("pool", m)) for m in range(2)]
        tiles += [([(A + m * P, P)], ("qn", m)) for m in range(3)]
        tiles += [([(A + 384, P)], ("rope", 0)), ([(A + 512, 64), (A + 832, 32)], ("rope", 1)),
                  ([(A + 576, P)], ("ckv", 0)), ([(A + 704, P)], ("ckv", 1))]
        cw = Carve()
        ckv = cw.take(2 * T).rearrange("p (k t) -> p k t", k=2)
        rp = cw.take(2 * T).rearrange("p (k t) -> p k t", k=2)
        qn = cw.take(3 * T).rearrange("p (k t) -> p k t", k=3)
        mla_end = cw.at
        LW = PRE + SEQ + NB * (PRE + TS)
        pl = cw.take(2 * LW).rearrange("p (m w) -> p m w", m=2)
        pool_end = cw.at
        PW = 1 + SEQ + NB * (TS + 1)
        pring = [cw.take(PW) for _ in range(2)]
        w_in = I["w_in"][0].rearrange("(k p) c -> p k c", p=P)
        assert cw.at <= WORK - 2 * KD * P
        wraw = [tiled(work[:, WORK - (2 - i) * KD * P:][:, 0:KD * P]) for i in range(2)]
        w_in_sem = [sem(f"w_in{i}") for i in range(2)]
        w_hi, w_lo = sem("w_in_hi"), sem("w_in_lo")
        widths = [sum(n for _, n in c) for c, _ in tiles]
        proj_mm, proj_cp, mixed, prep, diffed = (sem("proj_ready"), sem("proj_copied"), sem("shift_mixed"),
                                                 sem("prefix_set"), sem("shift_diff"))
        pieces = [len(c) for c, _ in tiles]

        def seg(ap, pre):
            return (ap[:, pre:pre + SEQ],
                    ap[:, pre + SEQ:pre + SEQ + NB * (pre + TS)].rearrange("p (b w) -> p b w", b=NB))

        wsp = [split_pair(f"w{i}", RW + i * 2 * KD * P, RW + (i * 2 + 1) * KD * P, KD * P, KD) for i in range(2)]

        def split_hi(i, m, raw, done, free, per):
            act = nc.scalar
            if i >= 2:
                act.wait_ge(free, per * (i - 1))
            act.copy(wsp[i % 2][0][:, 0:m[0], 0:m[1]], raw[:, 0:m[0], 0:m[1]]).then_inc(done, 1)

        def split_lo(i, m, raw, hi_done, done):
            dve = nc.vector
            dve.wait_ge(hi_done, i + 1)
            dve.tensor_tensor(wsp[i % 2][1][:, 0:m[0], 0:m[1]], raw[:, 0:m[0], 0:m[1]],
                              wsp[i % 2][0][:, 0:m[0], 0:m[1]].bitcast(F32), ALU.subtract).then_inc(done, 1)

        with nc.Block() as block:
            def in_hi(act, i):
                act.wait_ge(w_in_sem[i % 2], 16 * sum(pieces[i % 2:i + 1:2]))
                split_hi(i, (KD, widths[i]), wraw[i % 2], w_hi, proj_mm, 3)

            def in_lo(dve, i):
                split_lo(i, (KD, widths[i]), wraw[i % 2], w_hi, w_lo)

            @block.sync
            def _(sp):
                for i, (cols, _) in enumerate(tiles):
                    if i >= 2:
                        sp.wait_ge(w_lo, i - 1)
                    o = 0
                    for c, n in cols:
                        sp.dma_start(wraw[i % 2][:, :, o:o + n], w_in[:, :, c:c + n]).then_inc(w_in_sem[i % 2], 16)
                        o += n

            @block.tensor
            def _(pe):
                for i, (cols, _) in enumerate(tiles):
                    m = sum(n for _, n in cols)
                    pe.wait_ge(w_lo, i + 1)
                    for c, (t0, n) in enumerate(CH):
                        g = 3 * i + c
                        if g >= 8:
                            pe.wait_ge(proj_cp, g - 7)
                        for k in range(KD):
                            last = product(pe, PS[g % 8][0:m, 0:n], [w[:, k, 0:m] for w in wsp[i % 2]],
                                           [x[:, k, t0:t0 + n] for x in xn], k == 0, k == KD - 1)
                        last.then_inc(proj_mm, 1)

            @block.scalar
            def _(act):
                in_hi(act, 0)
                for i, (cols, (kind, j)) in enumerate(tiles):
                    if i + 1 < len(tiles):
                        in_hi(act, i + 1)
                    m = sum(n for _, n in cols)
                    if kind == "rwkv":
                        act.wait_ge(prep, 1)
                        if j >= 2:
                            act.wait_ge(mixed, j - 1)
                        p_seq, s_seq = seg(pring[j % 2], 1)
                        s_seq = s_seq[:, :, 1:]
                    elif kind == "pool":
                        p_seq, s_seq = seg(pl[:, j], PRE)
                        s_seq = s_seq[:, :, PRE:]
                    else:
                        dst = {"qn": qn, "rope": rp, "ckv": ckv}[kind][:, j]
                        p_seq, s_seq = dst[0:m, 0:SEQ], dst[0:m, SEQ:T]
                    for c, (t0, n) in enumerate(CH):
                        g = 3 * i + c
                        act.wait_ge(proj_mm, g + 1)
                        bank = PS[g % 8]
                        k = min(n, SEQ - t0)
                        ins = nc.scalar.copy(p_seq[0:m, t0:t0 + k], bank[0:m, 0:k])
                        if c == 2:
                            src = bank[0:m, k:k + NS]
                            if kind in ("rwkv", "pool"):
                                src = src.rearrange("p (b t) -> p b t", b=NB)
                            ins = nc.scalar.copy(s_seq, src)
                        ins.then_inc(proj_cp, 1)

            @block.gpsimd
            def _(pool):
                for j in range(2):
                    nc.gpsimd.memset(pring[j][:, 0:1], 0.0)
                    nc.gpsimd.memset(pl[:, j, 0:PRE], 0.0)
                nc.gpsimd.memset(sT[:, :, T:TPAD], 0.0).then_inc(prep, 1)
                for j in range(2):
                    nc.gpsimd.tensor_copy(seg(pl[:, j], PRE)[1][:, :, 0:PRE],
                                          poolT[:, j].rearrange("p (b t) -> p b t", b=NB)).then_inc(prep, 1)

            @block.vector
            def _(dve):
                in_lo(dve, 0)
                in_lo(dve, 1)
                for m in range(A_TILES):
                    buf = pring[m % 2]
                    p_cur, s_all = seg(buf, 1)
                    dve.tensor_copy(s_all[:, :, 0], shiftT[:, m, :]).then_inc(diffed, 1)
                    dve.wait_ge(diffed, 3 * m + 1)
                    dve.wait_ge(proj_cp, 3 * (m + 1))
                    dve.wait_ge(prep, 1)
                    s_new = sT[:, m, SEQ:T].rearrange("p (b t) -> p b t", b=NB)
                    dve.tensor_tensor(sT[:, m, 0:SEQ], buf[:, 0:SEQ], p_cur, ALU.subtract).then_inc(diffed, 1)
                    dve.tensor_tensor(s_new, s_all[:, :, 0:TS], s_all[:, :, 1:], ALU.subtract).then_inc(diffed, 1)
                    dve.tensor_copy(shift_out[:, 0:1, m], p_cur[:, SEQ - 1:SEQ])
                    dve.tensor_copy(shift_out[:, 1:9, m], s_all[:, :, TS])
                    dve.wait_ge(diffed, 3 * m + 3)
                    dve.scalar_tensor_tensor(out=sT[:, m, 0:SEQ], in0=sT[:, m, 0:SEQ], scalar=vec("mu_shift", m),
                                             in1=p_cur, op0=ALU.mult, op1=ALU.add)
                    dve.scalar_tensor_tensor(out=s_new, in0=s_new, scalar=vec("mu_shift", m), in1=s_all[:, :, 1:],
                                             op0=ALU.mult, op1=ALU.add).then_inc(mixed, 1)
                    in_lo(dve, m + 2)
                for i in range(A_TILES + 2, len(tiles)):
                    in_lo(dve, i)
        if upto == "proj":
            return

        new_stage()
        cw = Carve(pool_end)
        sumA, sumB = cw.take(LW), cw.take(LW)
        dT = wring[:, 0:2 * T].rearrange("p (m t) -> p m t", m=2)
        pool_w = wring[:, 2 * T:2 * T + 256].rearrange("p (m c) -> p m c", m=2)
        po = wring[:, 2 * T + 256:2 * T + 256 + 270]
        po_p, po_s = po[:, 0:30], po[:, 30:270]
        po_nat = wring[:, 2 * T + 526:2 * T + 526 + 3 * P].rearrange("p (q c) -> p q c", q=3)
        ends, sh_nat = sem("pool_steps"), wring[:, 2 * T + 910:2 * T + 910 + P]
        s_pw0, s_pw, pool_mm, pool_cp, po_ready, po_t, po_cp = (
            sem("pool_w_cleared"), sem("pool_w_in"), sem("pool_product"),
            sem("pool_scaled"), sem("pool_tail_ready"), sem("pool_tail_turned"), sem("pool_tail_copied"))
        with nc.Block() as block:
            @block.gpsimd
            def _(pool):
                nc.gpsimd.memset(pool_w, 0.0).then_inc(s_pw0, 1)

            @block.sync
            def _(sp):
                sp.wait_ge(s_pw0, 1)
                for g in range(4):
                    r = HD * (g % 2)
                    sp.dma_start(pool_w[r:r + HD, g // 2, r:r + HD], I["pool_w"][0, g]).then_inc(s_pw, 16)
                sp.wait_ge(po_cp, 4)
                sp.dma_start(pool_p[0, 0].rearrange("t (m c) -> (t m) c", m=2), po_nat[0:30, 0]).then_inc(s_po, 16)
                flat = pool_s[0].rearrange("b t (m c) -> (b t m) c", m=2)
                for q in range(2):
                    sp.dma_start(flat[120 * q:120 * q + 120, :], po_nat[0:120, 1 + q]).then_inc(s_po, 16)
                sp.dma_start(shift_p[0].rearrange("a (m c) -> (a m) c", c=P), sh_nat[0:A_TILES, :]).then_inc(s_po, 16)
                sp.dma_start(shift_s[0].rearrange("b (m c) -> (b m) c", c=P),
                             sh_nat[A_TILES:9 * A_TILES, :]).then_inc(s_po, 16)
                sp.wait_ge(s_po, 80)

            @block.vector
            def _(dve):
                link = chain(dve, ends)
                for m in range(2):
                    u = pl[:, m]
                    dve.tensor_copy(po_p.rearrange("p (t m) -> p t m", m=2)[:, :, m], u[:, SEQ:PRE + SEQ])
                    dve.tensor_copy(po_s.rearrange("p (b t m) -> p b t m", b=NB, m=2)[:, :, :, m],
                                    seg(u, PRE)[1][:, :, TS:]).then_inc(po_ready, 1)
                    link(dve.tensor_tensor(sumA[:, 1:], u[:, 1:], u[:, :LW - 1], ALU.add))
                    if m == 0:
                        link(dve.tensor_tensor(sumB[:, 3:], sumA[:, 3:], sumA[:, 1:LW - 2], ALU.add))
                    else:
                        link(dve.tensor_tensor(sumB[:, 3:], sumA[:, 3:], sumA[:, 1:LW - 2], ALU.add))
                        link(dve.tensor_tensor(sumA[:, 7:], sumB[:, 7:], sumB[:, 3:LW - 4], ALU.add))
                        link(dve.tensor_tensor(sumB[HD:, 15:], sumA[HD:, 15:], sumA[HD:, 7:LW - 8], ALU.add))
                    for r, src in ((0, sumA), (HD, sumB)):
                        rows = slice(r, r + HD)
                        link(dve.tensor_tensor(src[rows, PRE:PRE + 16], src[rows, PRE:PRE + 16],
                                               C("inv_cnt")[rows, 16 * m:16 * m + 16], ALU.mult))
                        dve.scalar_tensor_tensor(out=dT[rows, m, 0:SEQ], in0=seg(src, PRE)[0][rows],
                                                 scalar=C("inv_w")[rows, m:m + 1], in1=seg(u, PRE)[0][rows],
                                                 op0=ALU.mult, op1=ALU.subtract)
                        link(dve.scalar_tensor_tensor(
                            out=dT[rows, m, SEQ:T].rearrange("p (b t) -> p b t", b=NB),
                            in0=seg(src, PRE)[1][rows, :, PRE:], scalar=C("inv_w")[rows, m:m + 1],
                            in1=seg(u, PRE)[1][rows, :, PRE:], op0=ALU.mult, op1=ALU.subtract))

            @block.tensor
            def _(pe):
                pe.wait_ge(s_pw, 64)
                pe.wait_ge(po_ready, 2)
                for q, src in enumerate((po_p, po_s[:, 0:120], po_s[:, 120:240], shift_out)):
                    if q == 3:
                        src = src.rearrange("p j m -> p (j m)")
                    n = src.shape[1]
                    pe.transpose(PS[6][0:n, q * P:q * P + P], src, ident).then_inc(po_t, 1)
                for m in range(2):
                    pe.wait_ge(ends, (6, 14)[m])
                    for c, (t0, n) in enumerate(CH):
                        pe.matmul(PS[3 * m + c][:, 0:n], pool_w[:, m], dT[:, m, t0:t0 + n], start=True,
                                  stop=True).then_inc(pool_mm, 1)

            @block.scalar
            def _(act):
                for q, n in enumerate((30, 120, 120, 99)):
                    act.wait_ge(po_t, 4)
                    dst = po_nat[0:n, q] if q < 3 else sh_nat[0:n, :]
                    nc.scalar.copy(dst, PS[6][0:n, q * P:q * P + P]).then_inc(po_cp, 1)
                for m in range(2):
                    for c, (t0, n) in enumerate(CH):
                        act.wait_ge(pool_mm, 3 * m + c + 1)
                        nc.scalar.activation(mixT[:, 6 + m, t0:t0 + n], PS[3 * m + c][:, 0:n], ACT.Copy,
                                             scale=vec("pool_scale", m)).then_inc(pool_cp, 1)
        if upto == "pool":
            return

        new_stage()
        cw = Carve(mla_end)
        vnat = cw.take(8 * AW).rearrange("p (i c) -> p i c", i=8)
        sqc = cw.take(2 * T).rearrange("p (k t) -> p k t", k=2)
        rinv = cw.take(T)
        nat = cw.take(2 * 288).rearrange("p (s c) -> p s c", s=2)
        cs = wring[:, 0:2 * T].rearrange("p (a t) -> p a t", a=2)
        rot_sin = wring[:, 2 * T:3 * T]
        w_uv = wring[:, 3 * T:3 * T + 768].rearrange("p (k c) -> p k c", k=2)
        spare = actA[:, 0:3 * T]
        w_uk = res[:, 7936:8704].rearrange("p (k c) -> p k c", k=2)
        s_cs, s_wk, c_sq, c_sum, c_rt, c_ri, c_n, r_mm, r_sin, r_cos, r_done = (
            sem("angles_in"), sem("w_latent_in"), sem("latent_squared"), sem("latent_summed"),
            sem("latent_root"), sem("latent_recip"), sem("latent_normed"), sem("rotated"), sem("sin_part"),
            sem("cos_part"), sem("rope_done"))
        v_mm, v_cp, n_t, n_cp = (sem("values_ready"), sem("values_copied"), sem("rows_turned"),
                                 sem("rows_copied"))
        s_kn = sem("new_keys_cleared")
        rope_jobs = [(a, c) for a in range(2) for c in range(3)]
        with nc.Block() as block:
            @block.sync
            def _(sp):
                sp.dma_start(cs, I["c_rope"]).then_inc(s_cs, 16)
                sp.dma_start(w_uk, I["w_uk"][0].rearrange("(k p) h d -> p k (h d)", p=P)).then_inc(s_wk, 16)
                sp.dma_start(w_uv, I["w_uv"][0].rearrange("(k p) h d -> p k (h d)", p=P)).then_inc(s_wk, 16)
                for i in range(TT):
                    n = rows_of(i)
                    sp.wait_ge(n_cp, i + 1)
                    if i < TT - 1:
                        sp.dma_start(kv_p[0, 0, i * P:(i + 1) * P, :], nat[:, i % 2, 0:256]).then_inc(s_nat[i % 2], 16)
                        sp.dma_start(kr_p[0, 0, i * P:(i + 1) * P, :], nat[:, i % 2, 256:]).then_inc(s_nat[i % 2], 16)
                    else:
                        sp.dma_start(kv_s[0].rearrange("b t c -> (b t) c"), nat[0:n, i % 2, 0:256]).then_inc(s_nat[i % 2], 16)
                        sp.dma_start(kr_s[0].rearrange("b t c -> (b t) c"), nat[0:n, i % 2, 256:]).then_inc(s_nat[i % 2], 16)
                sp.wait_ge(s_nat[0], 160)
                sp.wait_ge(s_nat[1], 128)

            @block.scalar
            def _(act):
                nc.scalar.activation(sqc, ckv, ACT.Square).then_inc(c_sq, 1)
                for c, (t0, n) in enumerate(CH):
                    act.wait_ge(c_sum, c + 1)
                    nc.scalar.activation(rinv[:, t0:t0 + n], PS[c][:, 0:n], ACT.Sqrt, bias=epsc[:, 0:1],
                                         scale=1.0 / RANK).then_inc(c_rt, 1)
                for i in range(8):
                    act.wait_ge(v_mm, i + 1)
                    nc.scalar.copy(vnat[:, i], PS[i % 2][:, 0:AW]).then_inc(v_cp, 1)

            @block.gpsimd
            def _(pool):
                pool.wait_ge(s_cs, 16)
                nc.gpsimd.memset(krT_new, 0.0).then_inc(s_kn, 1)
                for j, (a, c) in enumerate(rope_jobs):
                    t0, n = CH[c]
                    m = P if a == 0 else 96
                    pool.wait_ge(r_mm, j + 1)
                    nc.gpsimd.tensor_tensor(rp[0:m, a, t0:t0 + n], rp[0:m, a, t0:t0 + n], cs[0:m, 0, t0:t0 + n],
                                            ALU.mult).then_inc(r_cos, 1)
                    pool.wait_ge(r_sin, j + 1)
                    pool.wait_ge(r_cos, j + 1)
                    nc.gpsimd.tensor_tensor(rp[0:m, a, t0:t0 + n], rp[0:m, a, t0:t0 + n], rot_sin[0:m, t0:t0 + n],
                                            ALU.add).then_inc(r_done, 1)
                pool.wait_ge(r_done, 6)
                pool.wait_ge(s_kn, 1)
                nc.gpsimd.tensor_copy(krT_new[64:96, :], rp[64:96, 1, SEQ:T])

            @block.vector
            def _(dve):
                dve.wait_ge(s_cs, 16)
                for c, (t0, n) in enumerate(CH):
                    dve.wait_ge(c_rt, c + 1)
                    dve.reciprocal(rinv[:, t0:t0 + n], rinv[:, t0:t0 + n]).then_inc(c_ri, 1)
                    dve.wait_ge(c_ri, c + 1)
                    for k in range(2):
                        dve.scalar_tensor_tensor(out=ckv[:, k, t0:t0 + n], in0=ckv[:, k, t0:t0 + n],
                                                 scalar=vec("kv_norm_g", k), in1=rinv[:, t0:t0 + n],
                                                 op0=ALU.mult, op1=ALU.mult).then_inc(c_n, 1)
                for j, (a, c) in enumerate(rope_jobs):
                    t0, n = CH[c]
                    m = P if a == 0 else 96
                    dve.wait_ge(r_mm, j + 1)
                    if j >= 3:
                        dve.wait_ge(r_done, j - 2)
                    dve.tensor_tensor(rot_sin[0:m, t0:t0 + n], PS[3 + j % 3][0:m, 0:n], cs[0:m, 1, t0:t0 + n],
                                      ALU.mult).then_inc(r_sin, 1)
                dve.wait_ge(c_n, 6)
                dve.tensor_copy(ckvT_new, ckv[:, :, SEQ:T])
                for i in range(TT):
                    n = rows_of(i)
                    dve.wait_ge(n_t, i + 1)
                    if i >= 2:
                        dve.wait_ge(s_nat[i % 2], 32 * (i // 2))
                    dve.tensor_copy(nat[0:n, i % 2, :], PS[6 + i % 2][0:n, 0:288]).then_inc(n_cp, 1)
                    if i == TT - 1:
                        dve.tensor_copy(ckv_new, PS[6 + i % 2][0:n, 0:RANK]).then_inc(n_cp, 1)

            @block.tensor
            def _(pe):
                pe.wait_ge(c_sq, 1)
                for c, (t0, n) in enumerate(CH):
                    for k in range(2):
                        last = pe.matmul(PS[c][:, 0:n], ones, sqc[:, k, t0:t0 + n], start=(k == 0), stop=(k == 1))
                    last.then_inc(c_sum, 1)
                for j, (a, c) in enumerate(rope_jobs):
                    t0, n = CH[c]
                    m = P if a == 0 else 96
                    if j >= 3:
                        pe.wait_ge(r_sin, j - 2)
                    pe.matmul(PS[3 + j % 3][0:m, 0:n], C("rot")[0:m, 0:m], rp[0:m, a, t0:t0 + n], start=True,
                              stop=True).then_inc(r_mm, 1)
                pe.wait_ge(s_wk, 32)
                pe.wait_ge(c_n, 6)
                for i in range(8):
                    if i >= 2:
                        pe.wait_ge(v_cp, i - 1)
                    for k in range(2):
                        last = pe.matmul(PS[i % 2][:, 0:AW], ckv[:, k, i * P:(i + 1) * P], w_uv[:, k],
                                         start=(k == 0), stop=(k == 1))
                    last.then_inc(v_mm, 1)
                pe.wait_ge(r_done, 6)
                for i in range(TT):
                    n = rows_of(i)
                    if i >= 2:
                        pe.wait_ge(n_cp, i - 1)
                    for k in range(2):
                        pe.transpose(PS[6 + i % 2][0:n, k * P:(k + 1) * P], ckv[:, k, i * P:i * P + n], ident)
                    pe.transpose(PS[6 + i % 2][0:n, 256:288], rp[64:96, 1, i * P:i * P + n],
                                 ident[64:96, 64:96]).then_inc(n_t, 1)
        if upto == "latent":
            return

        NX = NB // 2
        HT = H * TS
        NG = NPAGE // 4
        NPT = NG + 1
        NL = 5
        EARLY = 2
        loads = [(x, g) for x in range(NX) for g in range(NG)]
        kslot = [res[:, i * 1024:(i + 1) * 1024] for i in range(6)]
        kslot += [wring[:, i * 1024:(i + 1) * 1024] for i in range(4)]
        krr = res[:, 6144:6144 + 2 * NL * P].rearrange("p (s c) -> p s c", s=2 * NL)
        pages = res[:, 7424:7680].bitcast(I32)
        newmask = res[:, 7680:7936].rearrange("p (x c) -> p x c", x=NX)
        kv_pages = I["cache_kv_latent"][0].rearrange("n (p r) c -> n p (r c)", r=4)
        kr_pages = I["cache_k_rope"][0].rearrange("n (p r) c -> n p (r c)", r=4)
        s_pg, s_nm = nc.alloc_semaphore("page_table_in"), nc.alloc_semaphore("tables_in")
        s_k = [[nc.alloc_semaphore(f"rows_in{f}{i}") for i in range(NL)] for f in range(2)]
        s_kx = [nc.alloc_semaphore(f"rope_rows_in{i}") for i in range(NL)]

        def step_of(j):
            return j // NG * NPT + j % NG

        def load_page(eng, f, j, q):
            x, g = loads[j]
            at_ = (x + NX * f) * NPAGE + 4 * g + q
            return eng.value_load(pages[0:1, at_:at_ + 1], min_val=0, max_val=NPOOL - 1)

        def load_rows(eng, j, f):
            slot = 2 * (j % NL) + f
            for q in range(4):
                page = load_page(eng, f, j, q)
                rows = slice(32 * q, 32 * q + 32)
                eng.dma_start(kslot[slot][rows], kv_pages[bass.ds(page, 1)].rearrange("a p c -> (a p) c")
                              ).then_inc(s_k[f][j % NL], 16)
                if f == 0 or q < 3:
                    eng.dma_start(krr[rows, slot, :], kr_pages[bass.ds(page, 1)].rearrange("a p c -> (a p) c")
                                  ).then_inc(s_k[f][j % NL], 16)
            if f == 0:
                page = load_page(eng, 1, j, 3)
                eng.dma_start(krr[96:P, slot + 1, :], kr_pages[bass.ds(page, 1)].rearrange("a p c -> (a p) c")
                              ).then_inc(s_kx[j % NL], 16)

        new_stage()
        cw = Carve(mla_end + 8 * AW)
        qcat = [cw.take(SEQ) for _ in range(4)]
        stat_a = cw.take(4 * 48).rearrange("p (a i) -> p a i", a=4)
        diag = [cw.take(P) for _ in range(2)]
        kcat = [spare[:, j * SEQ:(j + 1) * SEQ] for j in range(3)] + [kslot[4]]
        prob = [wring[:, j * SEQ:(j + 1) * SEQ] for j in range(2)] + [kslot[5]]
        probT = [wring[:, (4 + j) * 512:(5 + j) * 512] for j in range(4)]
        pairs = [(m, i) for m in range(3) for i in range(8)]
        NQ = len(pairs)
        units = [(q, b0) for q in range(NQ) for b0 in range(0, pairs[q][1] + 1, 4)]
        units_of = {q: [u for u, x in enumerate(units) if x[0] == q] for q in range(NQ)}

        ring, holder, banks_of, freed_by = [0], {}, {}, {}

        def take_banks(use, n):
            banks_of[use] = [(ring[0] + i) % 4 for i in range(n)]
            ring[0] += n
            freed_by[use] = [holder[b] for b in banks_of[use] if b in holder]
            for b in banks_of[use]:
                holder[b] = use

        def keys_before(q):
            if q == 0:
                return 0
            m, i = pairs[q]
            return m + 1 if i == 6 and m < 2 else None

        for q in range(NQ):
            if keys_before(q) is not None:
                take_banks(("keys", keys_before(q)), 2)
            for f in range(2):
                take_banks(("item", 2 * q + f), 1 + pairs[q][1] // 4)

        s_q, keys_mm, keys_cp, s_kr, sc_mm, sc_masked, sc_max, sc_bias, p_exp, p_sum, p_rec, p_diag, o_cp = (
            [sem("queries_in0"), sem("queries_in1")], sem("keys_ready"), sem("keys_copied"), sem("rope_keys_set"),
            sem("scores_ready"), sem("scores_masked"), sem("scores_max"), sem("scores_bias"), sem("weights_ready"),
            sem("weight_sums_joined"), sem("weight_sums_recip"), sem("weight_sums_diagonal"),
            sem("attn_out_written"))
        p_t = [sem(f"weights_turned{f}") for f in range(2)]
        p_cp = [sem(f"weightsT_copied{f}") for f in range(2)]
        o_mm = sem("attn_out_ready")
        s_z, o_sp = sem("odd_rows_cleared"), sem("sums_spread")
        spread = spare[:, 3 * SEQ:3 * SEQ + P]

        def head_rows(f):
            return slice(0, 96) if f == 0 else slice(0, P)

        def copy_weights(eng_copy, eng, u, f):
            q, b0 = units[u]
            n = min(4, pairs[q][1] + 1 - b0) * P
            eng.wait_ge(p_t[f], u + 1)
            if u >= 2:
                eng.wait_ge(o_mm, u - 1)
            eng_copy(probT[2 * (u % 2) + f][:, 0:n], PS[4 + f][:, 0:n]).then_inc(p_cp[f], 1)

        with nc.Block() as block:
            @block.sync
            def _(sp):
                sp.dma_start(pages[0:1, :], I["page_table"].rearrange("b n -> (b n)").unsqueeze(0)).then_inc(s_pg, 16)
                sp.wait_ge(s_z, 1)
                for m in range(3):
                    if m >= 2:
                        sp.wait_ge(sc_mm, 16 * (m - 1))
                    for f in range(2):
                        h = 2 * m + f
                        dst = qcat[2 * (m % 2) + f]
                        r = HD * f
                        sp.dma_start(dst[r:r + HD, :], qn[r:r + HD, m, 0:SEQ]).then_inc(s_q[m % 2], 16)
                        r = ROPE * (h % 4)
                        o = (64, 32)[f]
                        sp.dma_start(dst[o:o + ROPE, :], rp[r:r + ROPE, h // 4, 0:SEQ]).then_inc(s_q[m % 2], 16)
                    if m == 1:
                        sp.dma_start(newmask, I["c_newmask"].rearrange("q (x c) -> q x c", x=NX)).then_inc(s_nm, 16)
                        sp.wait_ge(s_pg, 16)
                        for j in range(EARLY):
                            load_rows(sp, j, 0)

            @block.gpsimd
            def _(pool):
                for j in (1, 3):
                    nc.gpsimd.memset(qcat[j][0:ROPE, :], 0.0)
                    ins = nc.gpsimd.memset(kcat[j][0:ROPE, :], 0.0)
                ins.then_inc(s_z, 1)
                for j in range(4):
                    o = (64, 32)[j % 2]
                    nc.gpsimd.tensor_copy(kcat[j][o:o + ROPE, :], rp[64:96, 1, 0:SEQ]).then_inc(s_kr, 1)
                for q in range(NQ):
                    for f in range(2):
                        it = 2 * q + f
                        pool.wait_ge(p_rec, it + 1)
                        if q >= 1:
                            pool.wait_ge(o_mm, units_of[q - 1][-1] + 1)
                        nc.gpsimd.tensor_scalar(diag[f], ident, stat_a[:, 3, it:it + 1], None, ALU.mult
                                                ).then_inc(p_diag, 1)
                    if q == 8:
                        pool.wait_ge(s_pg, 16)
                        for j in range(EARLY):
                            load_rows(pool, j, 1)

            @block.tensor
            def _(pe):
                def take(use):
                    for kind, x in freed_by[use]:
                        if kind == "keys":
                            pe.wait_ge(keys_cp, 4 * (x + 1))
                        else:
                            pe.wait_ge(p_exp, x + 1)

                def keys(m):
                    take(("keys", m))
                    for half, b in enumerate(banks_of["keys", m]):
                        for k in range(2):
                            for f in range(2):
                                h = 2 * m + f
                                last = pe.matmul(PS[b][HD * f:HD * f + HD, :], w_uk[:, k, h * HD:(h + 1) * HD],
                                                 ckv[:, k, 512 * half:512 * half + 512], start=(k == 0),
                                                 stop=(k == 1), skip_group_check=True)
                        last.then_inc(keys_mm, 1)

                def scores(it):
                    (m, i), f = pairs[it // 2], it % 2
                    take(("item", it))
                    if i == 0 and f == 0:
                        pe.wait_ge(keys_cp, 4 * (m + 1))
                        pe.wait_ge(s_kr, 4)
                        pe.wait_ge(s_q[m % 2], 64 * (m // 2 + 1))
                    w = (i + 1) * P
                    j = 2 * (m % 2) + f
                    for half, b in enumerate(banks_of["item", it]):
                        n = min(512, w - 512 * half)
                        last = pe.matmul(PS[b][:, 0:n], qcat[j][head_rows(f), i * P:(i + 1) * P],
                                         kcat[j][head_rows(f), 512 * half:512 * half + n], start=True, stop=True)
                    last.then_inc(sc_mm, 1)

                def turn(u):
                    q, b0 = units[u]
                    for f in range(2):
                        it = 2 * q + f
                        pe.wait_ge(p_exp, it + 1)
                        if u >= 1:
                            pe.wait_ge(p_cp[f], u)
                        for b in range(min(4, pairs[q][1] + 1 - b0)):
                            last = pe.transpose(PS[4 + f][:, b * P:(b + 1) * P],
                                                prob[it % 3][:, (b0 + b) * P:(b0 + b + 1) * P], ident)
                        last.then_inc(p_t[f], 1)

                def values(u):
                    q, b0 = units[u]
                    m, i = pairs[q]
                    out = PS[6 + q % 2]
                    for f in range(2):
                        pe.wait_ge(p_cp[f], u + 1)
                    if b0 == 0 and q >= 2:
                        pe.wait_ge(o_cp, q - 1)
                    for b in range(b0, min(b0 + 4, i + 1)):
                        for f in range(2):
                            h = 2 * m + f
                            last = pe.matmul(out[HD * f:HD * f + HD, 0:P], vnat[:, b, h * HD:(h + 1) * HD],
                                             probT[2 * (u % 2) + f][:, (b - b0) * P:(b - b0 + 1) * P],
                                             start=(b == 0), stop=(b == i), skip_group_check=True)
                    if u == units_of[q][-1]:
                        pe.wait_ge(p_diag, 2 * q + 2)
                        for f in range(2):
                            last = pe.matmul(out[HD * f:HD * f + HD, P:2 * P], ones[:, 0:HD], diag[f], start=True,
                                             stop=True, skip_group_check=True)
                    last.then_inc(o_mm, 1)

                keys(0)
                scores(0)
                scores(1)
                for q in range(NQ):
                    if q + 1 < NQ:
                        if keys_before(q + 1) is not None:
                            keys(keys_before(q + 1))
                        scores(2 * q + 2)
                    for n, u in enumerate(units_of[q]):
                        turn(u)
                        if n == 0 and q + 1 < NQ:
                            scores(2 * q + 3)
                        if u >= 1:
                            values(u - 1)
                values(len(units) - 1)

            @block.vector
            def _(dve):
                def softmax_max(it):
                    (m, i), f = pairs[it // 2], it % 2
                    w = (i + 1) * P
                    bank = [PS[b] for b in banks_of["item", it]]
                    dve.wait_ge(sc_mm, it + 1)
                    own = bank[-1][:, (i % 4) * P:(i % 4) * P + P]
                    dve.tensor_tensor(own, own, C("causal"), ALU.add).then_inc(sc_masked, 1)
                    n_max = sum(1 + pairs[j // 2][1] // 4 for j in range(it))
                    if w > 512:
                        dve.tensor_reduce(stat_a[:, 0, it:it + 1], bank[0][:, :], AX_X, ALU.max).then_inc(sc_max, 1)
                    dve.wait_ge(sc_masked, it + 1)
                    a = 1 if w > 512 else 0
                    dve.tensor_reduce(stat_a[:, a, it:it + 1], bank[a][:, 0:w - 512 * a], AX_X,
                                      ALU.max).then_inc(sc_max, 1)
                    dve.wait_ge(sc_max, n_max + 1 + a)
                    if a:
                        ins = dve.tensor_scalar(stat_a[:, 0, it:it + 1], stat_a[:, 0, it:it + 1],
                                                stat_a[:, 1, it:it + 1], -SCALE, ALU.max, ALU.mult)
                    else:
                        ins = dve.tensor_scalar(stat_a[:, 0, it:it + 1], stat_a[:, 0, it:it + 1], -SCALE, None,
                                                ALU.mult)
                    ins.then_inc(sc_bias, 1)

                def recips(q):
                    two = slice(2 * q, 2 * q + 2)
                    dve.wait_ge(p_exp, 2 * q + 2)
                    src = stat_a[:, 2, two]
                    if pairs[q][1] >= 4:
                        dve.tensor_tensor(stat_a[:, 1, two], stat_a[:, 1, two], src, ALU.add).then_inc(p_sum, 1)
                        dve.wait_ge(p_sum, sum(1 for _, i in pairs[:q + 1] if i >= 4))
                        src = stat_a[:, 1, two]
                    dve.reciprocal(stat_a[:, 3, two], src).then_inc(p_rec, 2)

                def write_out(q):
                    m, i = pairs[q]
                    out = PS[6 + q % 2]
                    dve.wait_ge(o_mm, units_of[q][-1] + 1)
                    if q >= 1:
                        dve.wait_ge(o_cp, q)
                    dve.tensor_copy(spread, out[:, P:2 * P]).then_inc(o_sp, 1)
                    dve.wait_ge(o_sp, q + 1)
                    dve.tensor_tensor(mixT[:, 3 + m, i * P:(i + 1) * P], out[:, 0:P], spread, ALU.mult
                                      ).then_inc(o_cp, 1)

                softmax_max(0)
                softmax_max(1)
                for q in range(NQ):
                    if q + 1 < NQ:
                        softmax_max(2 * q + 2)
                    recips(q)
                    for n, u in enumerate(units_of[q]):
                        copy_weights(dve.tensor_copy, dve, u, 0)
                        if n == 0 and q + 1 < NQ:
                            softmax_max(2 * q + 3)
                    if q >= 1:
                        write_out(q - 1)
                write_out(NQ - 1)

            @block.scalar
            def _(act):
                def copy_keys(m):
                    for half, b in enumerate(banks_of["keys", m]):
                        act.wait_ge(keys_mm, 2 * m + half + 1)
                        for f in range(2):
                            rows = slice(HD * f, HD * f + HD)
                            nc.scalar.copy(kcat[2 * (m % 2) + f][rows, 512 * half:512 * half + 512],
                                           PS[b][rows, :]).then_inc(keys_cp, 1)

                def weights(it):
                    q = it // 2
                    w = (pairs[q][1] + 1) * P
                    act.wait_ge(sc_bias, it + 1)
                    if it >= 3:
                        act.wait_ge(p_t[(it - 3) % 2], units_of[(it - 3) // 2][-1] + 1)
                    for j, b in enumerate(banks_of["item", it]):
                        n = min(512, w - 512 * j)
                        ins = nc.scalar.activation(prob[it % 3][:, 512 * j:512 * j + n], PS[b][:, 0:n], ACT.Exp,
                                                   bias=stat_a[:, 0, it:it + 1], scale=SCALE,
                                                   accum_out=stat_a[:, 2 - j, it:it + 1])
                    ins.then_inc(p_exp, 1)

                copy_keys(0)
                weights(0)
                weights(1)
                for q in range(NQ):
                    if q + 1 < NQ:
                        if keys_before(q + 1) is not None:
                            copy_keys(keys_before(q + 1))
                        weights(2 * q + 2)
                    for n, u in enumerate(units_of[q]):
                        copy_weights(nc.scalar.copy, act, u, 1)
                        if n == 0 and q + 1 < NQ:
                            weights(2 * q + 3)
        if upto == "attn":
            return

        new_stage()
        QN = NX * P
        cw = Carve(WORK - 6 * QN)
        q_lat = cw.take(2 * QN).rearrange("p (k q) -> p k q", k=2)
        q_rope = cw.take(4 * QN).rearrange("p (r q) -> p r q", r=4)
        w_ukT = wring[:, 0:3 * RANK].rearrange("p (m c) -> p m c", m=3)
        s_q0, s_qr, wu_t, wu_cp, ql_mm = (sem("queries_cleared"), sem("rope_q_set"), sem("w_uk_turned"),
                                          sem("w_ukT_copied"), sem("q_lat_ready"))

        def by_half(ap, h):
            return ap.rearrange("p (x f c) -> p f x c", x=NX, f=2)[:, :, :, h * TS:(h + 1) * TS]

        def of_sample(ap):
            return ap.rearrange("p (f x t) -> p f x t", f=2, x=NX)

        with nc.Block() as block:
            @block.gpsimd
            def _(pool):
                nc.gpsimd.memset(q_rope[:, 2:4], 0.0).then_inc(s_q0, 1)
                nc.gpsimd.memset(q_lat, 0.0).then_inc(s_q0, 1)

            @block.tensor
            def _(pe):
                for m in range(3):
                    for k in range(2):
                        last = pe.transpose(PS[m][:, k * P:(k + 1) * P], w_uk[:, k, m * P:(m + 1) * P], ident)
                last.then_inc(wu_t, 1)
                pe.wait_ge(wu_cp, 3)
                for h in range(H):
                    r = HD * (h % 2)
                    for k in range(2):
                        last = pe.matmul(PS[4 + k + 2 * (h % 2)][:, (h // 2) * NS:(h // 2 + 1) * NS],
                                         w_ukT[r:r + HD, h // 2, k * P:(k + 1) * P],
                                         qn[r:r + HD, h // 2, SEQ:T], start=True, stop=True)
                last.then_inc(ql_mm, 1)

            def rope_queries(eng_copy, versions):
                for h in range(H):
                    r0 = ROPE * (h % 4)
                    for r in versions:
                        eng_copy(by_half(q_rope[ROPE * r:ROPE * (r + 1), r], h),
                                 of_sample(rp[r0:r0 + ROPE, h // 4, SEQ:T]))

            def latent_queries(eng_copy, k):
                for h in range(H):
                    eng_copy(by_half(q_lat[:, k], h),
                             of_sample(PS[4 + k + 2 * (h % 2)][:, (h // 2) * NS:(h // 2 + 1) * NS]))

            @block.vector
            def _(dve):
                dve.memset(q_rope[:, 0:2], 0.0).then_inc(s_qr, 1)
                dve.wait_ge(wu_t, 1)
                for m in range(3):
                    dve.tensor_copy(w_ukT[:, m], PS[m][:, 0:RANK]).then_inc(wu_cp, 1)
                dve.wait_ge(s_qr, 1)
                rope_queries(dve.tensor_copy, (0, 1))
                dve.wait_ge(ql_mm, 1)
                dve.wait_ge(s_q0, 2)
                latent_queries(dve.tensor_copy, 0)

            @block.scalar
            def _(act):
                act.wait_ge(s_q0, 1)
                rope_queries(nc.scalar.copy, (2, 3))
                act.wait_ge(ql_mm, 1)
                act.wait_ge(s_q0, 2)
                latent_queries(nc.scalar.copy, 1)
        if upto == "queries":
            return

        new_stage()
        cw = Carve()
        keyT = cw.take(2 * 2 * 2 * 512).rearrange("p (s f k c) -> p s f k c", s=2, f=2, k=2)
        krT = cw.take(2 * 2 * P).rearrange("p (s f c) -> p s f c", s=2, f=2)
        pr = cw.take(2 * 512).rearrange("p (s c) -> p s c", s=2)
        prT = cw.take(2 * 4 * P).rearrange("p (s c) -> p s c", s=2)
        part = cw.take(2 * NPT * RANK).rearrange("p (s g c) -> p s g c", s=2, g=NPT)
        o_nat = cw.take(2 * RANK).rearrange("p (s c) -> p s c", s=2)
        mx, bias, sums, wts = (cw.take(NX * NPT).rearrange("p (x g) -> p x g", x=NX) for _ in range(4))
        tot = cw.take(NX * 4).rearrange("p (x a) -> p x a", x=NX)
        assert cw.at <= WORK - 6 * QN, cw.at
        w_uv2 = res[:, 7936:8704].rearrange("p (k c) -> p k c", k=2)
        steps = [(x, g) for x in range(NX) for g in range(NPT)]
        NSTEP = len(steps)

        (k_t, k_cpa, k_cpb, ds_mm, ds_mask, ds_max, ds_bias, dp_exp, dp_t, dp_cp, do_mm, do_cp) = (
            sem("rows_turned2"), sem("keysT_copied_a"),
            sem("keysT_copied_b"), sem("dscores_ready"), sem("dscores_masked"), sem("dscores_max"),
            sem("dscores_bias"), sem("dweights_ready"), sem("dweights_turned"), sem("dweightsT_copied"),
            sem("dparts_ready"), sem("dparts_copied"))
        s_uv = sem("w_uv_in")
        j_max, j_w, j_sum, j_acc, j_t, j_cp, j_ready = (sem("join_max"), sem("join_weights"), sem("join_sum"),
                                                        sem("join_steps"), sem("joined_turned"),
                                                        sem("joined_copied"), sem("joined"))
        y_mm = sem("decode_values_ready")
        with nc.Block() as block:
            def all_loads(eng, f):
                for j in range(EARLY, len(loads)):
                    if j >= NL:
                        eng.wait_ge(do_mm, step_of(j - NL) + 1)
                    load_rows(eng, j, f)

            @block.sync
            def _(sp):
                sp.dma_start(w_uv2, I["w_uv"][0].rearrange("(k p) h d -> p k (h d)", p=P)).then_inc(s_uv, 16)
                all_loads(sp, 0)

            @block.gpsimd
            def _(pool):
                all_loads(pool, 1)

            @block.tensor
            def _(pe):
                def turn_keys(j, f):
                    slot = 2 * (j % NL) + f
                    pe.wait_ge(s_k[f][j % NL], (128, 112)[f] * (j // NL + 1))
                    if f == 1:
                        pe.wait_ge(s_kx[j % NL], 16 * (j // NL + 1))
                    n = 2 * j + f
                    if n >= 1:
                        pe.wait_ge(k_cpa, n)
                        pe.wait_ge(k_cpb, 2 * n)
                    rows = kslot[slot].rearrange("p (r c) -> p r c", r=4)
                    for k in range(2):
                        for r in range(4):
                            pe.transpose(PS[k][:, r * P:(r + 1) * P], rows[:, r, k * P:(k + 1) * P], ident)
                    pe.transpose(PS[2][:, 0:P], krr[:, slot, :], ident).then_inc(k_t, 1)

                def dscores(s):
                    x, g = steps[s]
                    bank = PS[3 + s % 2]
                    if s >= 2:
                        pe.wait_ge(dp_exp, s - 1)
                    q = [(slice(HD * f, HD * f + HD), slice(x * P + HD * f, x * P + HD * f + HD)) for f in range(2)]
                    if g < NG:
                        j = x * NG + g
                        pe.wait_ge(k_cpa, 2 * j + 2)
                        pe.wait_ge(k_cpb, 4 * j + 4)
                        for r in range(4):
                            for f, (out, cols) in enumerate(q):
                                pe.matmul(bank[out, r * P:(r + 1) * P], q_rope[:, r, cols], krT[:, j % 2, f, :],
                                          start=(r == 0), stop=False, skip_group_check=True)
                        for k in range(2):
                            for f, (out, cols) in enumerate(q):
                                last = pe.matmul(bank[out, :], q_lat[:, k, cols], keyT[:, j % 2, f, k, :],
                                                 start=False, stop=(k == 1), skip_group_check=True)
                    else:
                        for k in range(2):
                            for out, cols in q:
                                pe.matmul(bank[out, 0:NS], q_lat[:, k, cols], ckvT_new[:, k], start=(k == 0),
                                          stop=False, skip_group_check=True)
                        for out, cols in q:
                            last = pe.matmul(bank[out, 0:NS], q_rope[:, 2, cols], krT_new, start=False, stop=True,
                                             skip_group_check=True)
                    last.then_inc(ds_mm, 1)

                def turn_weights(s):
                    pe.wait_ge(dp_exp, s + 1)
                    if s >= 1:
                        pe.wait_ge(dp_cp, s)
                    if steps[s][1] < NG:
                        for r in range(4):
                            last = pe.transpose(PS[5][:, r * P:(r + 1) * P], pr[:, s % 2, r * P:(r + 1) * P], ident)
                    else:
                        last = pe.transpose(PS[5][0:NS, 0:P], pr[:, s % 2, 0:NS], ident)
                    last.then_inc(dp_t, 1)

                def dvalues(s, part_of):
                    x, g = steps[s]
                    bank = PS[6 + s % 2]
                    if part_of == 0:
                        pe.wait_ge(dp_cp, s + 1)
                        if s >= 2:
                            pe.wait_ge(do_cp, s - 1)
                    if g < NG:
                        j = x * NG + g
                        for r in (2 * part_of, 2 * part_of + 1):
                            for f in range(2):
                                rows = kslot[2 * (j % NL) + f]
                                last = pe.matmul(bank[HD * f:HD * f + HD, 0:RANK],
                                                 prT[:, s % 2, r * P + HD * f:r * P + HD * f + HD],
                                                 rows[:, r * RANK:(r + 1) * RANK], start=(r == 0), stop=(r == 3),
                                                 skip_group_check=True)
                    elif part_of == 1:
                        last = pe.matmul(bank[:, 0:RANK], prT[0:NS, s % 2, 0:P], ckv_new, start=True, stop=True)
                    if part_of == 1:
                        last.then_inc(do_mm, 1)

                def turn_joined(x):
                    pe.wait_ge(j_ready, x + 1)
                    if x >= 1:
                        pe.wait_ge(j_cp, x)
                    for k in range(2):
                        last = pe.transpose(PS[2][:, P + k * P:P + (k + 1) * P],
                                            o_nat[:, x % 2, k * P:(k + 1) * P], ident)
                    last.then_inc(j_t, 1)

                pe.wait_ge(s_nm, 16)
                turn_keys(0, 0)
                turn_keys(0, 1)
                for s in range(NSTEP):
                    x, g = steps[s]
                    following = s + 1 < NSTEP and steps[s + 1][1] < NG and steps[s + 1]
                    dscores(s)
                    if g == 6 and x >= 1:
                        turn_joined(x - 1)
                        pe.wait_ge(j_cp, x)
                    if following:
                        turn_keys(following[0] * NG + following[1], 0)
                    if s >= 1:
                        dvalues(s - 1, 0)
                    if following:
                        turn_keys(following[0] * NG + following[1], 1)
                    turn_weights(s)
                    if s >= 1:
                        dvalues(s - 1, 1)
                for half in range(2):
                    dvalues(NSTEP - 1, half)
                turn_joined(NX - 1)
                pe.wait_ge(j_cp, NX)
                pe.wait_ge(s_uv, 16)
                for h in range(H):
                    r = HD * (h % 2)
                    for k in range(2):
                        rhs = by_half(q_lat[:, k], h)
                        last = pe.matmul(of_sample(PS[h % 2][r:r + HD, (h // 2) * NS:(h // 2 + 1) * NS]),
                                         w_uv2[:, k, h * HD:(h + 1) * HD], rhs, start=(k == 0), stop=(k == 1))
                last.then_inc(y_mm, 1)

            @block.vector
            def _(dve):
                def copy_keys(j, f):
                    dve.wait_ge(k_t, 2 * j + f + 1)
                    if j >= 2:
                        dve.wait_ge(ds_mm, step_of(j - 2) + 1)
                    dve.tensor_copy(keyT[:, j % 2, f, 0, :], PS[0][:, :]).then_inc(k_cpa, 1)

                def copy_weights(s):
                    dve.wait_ge(dp_t, s + 1)
                    if s >= 2:
                        dve.wait_ge(do_mm, s - 1)
                    n, w = (P, 4 * P) if steps[s][1] < NG else (NS, P)
                    dve.tensor_copy(prT[0:n, s % 2, 0:w], PS[5][0:n, 0:w]).then_inc(dp_cp, 1)

                def softmax_max(s):
                    x, g = steps[s]
                    w = 512 if g < NG else NS
                    bank = PS[3 + s % 2]
                    dve.wait_ge(ds_mm, s + 1)
                    if g == NG:
                        dve.tensor_tensor(bank[:, 0:NS], bank[:, 0:NS], newmask[:, x], ALU.add).then_inc(ds_mask, 1)
                        dve.wait_ge(ds_mask, x + 1)
                    dve.tensor_reduce(mx[:, x, g:g + 1], bank[:, 0:w], AX_X, ALU.max).then_inc(ds_max, 1)
                    dve.wait_ge(ds_max, s + 1)
                    dve.tensor_scalar(bias[:, x, g:g + 1], mx[:, x, g:g + 1], -SCALE, None, ALU.mult
                                      ).then_inc(ds_bias, 1)

                def copy_part(s):
                    x, g = steps[s]
                    dve.wait_ge(do_mm, s + 1)
                    if g == 0 and x >= 2:
                        dve.wait_ge(j_ready, x - 1)
                    dve.tensor_copy(part[:, x % 2, g, :], PS[6 + s % 2][:, 0:RANK]).then_inc(do_cp, 1)

                def join_max(x):
                    dve.wait_ge(ds_max, NPT * (x + 1))
                    dve.tensor_reduce(tot[:, x, 0:1], mx[:, x, :], AX_X, ALU.max).then_inc(j_max, 1)
                    dve.wait_ge(j_max, 2 * x + 1)
                    dve.tensor_scalar(tot[:, x, 1:2], tot[:, x, 0:1], -SCALE, None, ALU.mult).then_inc(j_max, 1)

                def join_sum(x):
                    dve.wait_ge(j_w, x + 1)
                    dve.wait_ge(dp_exp, NPT * (x + 1))
                    dve.tensor_tensor(sums[:, x, :], sums[:, x, :], wts[:, x, :], ALU.mult).then_inc(j_sum, 1)
                    dve.wait_ge(j_sum, 3 * x + 1)
                    dve.tensor_reduce(tot[:, x, 2:3], sums[:, x, :], AX_X, ALU.add).then_inc(j_sum, 1)
                    dve.wait_ge(j_sum, 3 * x + 2)
                    dve.reciprocal(tot[:, x, 3:4], tot[:, x, 2:3]).then_inc(j_sum, 1)

                def join(x):
                    o = o_nat[:, x % 2, :]
                    dve.wait_ge(do_cp, NPT * (x + 1))
                    if x >= 2:
                        dve.wait_ge(j_t, x - 1)
                    for g in range(NPT):
                        w = wts[:, x, g:g + 1]
                        if g == 0:
                            dve.tensor_scalar(o, part[:, x % 2, g, :], w, None, ALU.mult).then_inc(j_acc, 1)
                        else:
                            dve.wait_ge(j_acc, NPT * x + g)
                            dve.scalar_tensor_tensor(out=o, in0=part[:, x % 2, g, :], scalar=w, in1=o,
                                                     op0=ALU.mult, op1=ALU.add).then_inc(j_acc, 1)
                    dve.wait_ge(j_acc, NPT * (x + 1))
                    dve.wait_ge(j_sum, 3 * x + 3)
                    dve.tensor_scalar(o, o, tot[:, x, 3:4], None, ALU.mult).then_inc(j_ready, 1)

                copy_keys(0, 0)
                copy_keys(0, 1)
                for s in range(NSTEP):
                    x, g = steps[s]
                    following = s + 1 < NSTEP and steps[s + 1][1] < NG and steps[s + 1]
                    softmax_max(s)
                    for half in range(2):
                        if following:
                            copy_keys(following[0] * NG + following[1], half)
                    copy_weights(s)
                    if s >= 1:
                        copy_part(s - 1)
                    if g == 1 and x >= 1:
                        join_max(x - 1)
                    if g == 3 and x >= 1:
                        join_sum(x - 1)
                        join(x - 1)
                copy_part(NSTEP - 1)
                join_max(NX - 1)
                join_sum(NX - 1)
                join(NX - 1)
                dve.wait_ge(y_mm, 1)
                for h in range(H):
                    r = HD * (h % 2)
                    dve.tensor_copy(mixT[r:r + HD, 3 + h // 2, SEQ:T],
                                    PS[h % 2][r:r + HD, (h // 2) * NS:(h // 2 + 1) * NS])

            @block.scalar
            def _(act):
                def copy_keys(j, f):
                    act.wait_ge(k_t, 2 * j + f + 1)
                    if j >= 2:
                        act.wait_ge(ds_mm, step_of(j - 2) + 1)
                    nc.scalar.copy(keyT[:, j % 2, f, 1, :], PS[1][:, :]).then_inc(k_cpb, 1)
                    nc.scalar.copy(krT[:, j % 2, f, :], PS[2][:, 0:P]).then_inc(k_cpb, 1)

                def exps(s):
                    x, g = steps[s]
                    w = 512 if g < NG else NS
                    act.wait_ge(ds_bias, s + 1)
                    if s >= 2:
                        act.wait_ge(dp_t, s - 1)
                    nc.scalar.activation(pr[:, s % 2, 0:w], PS[3 + s % 2][:, 0:w], ACT.Exp,
                                         bias=bias[:, x, g:g + 1], scale=SCALE,
                                         accum_out=sums[:, x, g:g + 1]).then_inc(dp_exp, 1)

                def join_weights(x):
                    act.wait_ge(j_max, 2 * x + 2)
                    nc.scalar.activation(wts[:, x, :], mx[:, x, :], ACT.Exp, bias=tot[:, x, 1:2],
                                         scale=SCALE).then_inc(j_w, 1)

                def copy_joined(x):
                    act.wait_ge(j_t, x + 1)
                    for k in range(2):
                        ins = nc.scalar.copy(q_lat[:, k, x * P:(x + 1) * P], PS[2][:, P + k * P:P + (k + 1) * P])
                    ins.then_inc(j_cp, 1)

                copy_keys(0, 0)
                copy_keys(0, 1)
                for s in range(NSTEP):
                    x, g = steps[s]
                    following = s + 1 < NSTEP and steps[s + 1][1] < NG and steps[s + 1]
                    exps(s)
                    if g == 6 and x >= 1:
                        copy_joined(x - 1)
                    for half in range(2):
                        if following:
                            copy_keys(following[0] * NG + following[1], half)
                    if g == 1 and x >= 1:
                        join_weights(x - 1)
                join_weights(NX - 1)
                copy_joined(NX - 1)
        if upto == "decode":
            return

        new_stage()
        cw = Carve()
        AR = cw.take(3 * TT * 2 * P).rearrange("p (m i w t) -> p m i w t", m=3, i=TT, w=2)
        loop_base = cw.at
        fresh, lg, cum, dec, icl, kkn, k2 = (cw.take(TPAD) for _ in range(7))
        w2 = wring[:, 0:AW]
        g2 = wring[:, AW:2 * AW]
        prod, di = wring[:, 768:768 + TPAD], wring[:, 768 + TPAD:768 + 2 * TPAD]
        nch = SEQ // CHUNK
        dc = piece(3 * (nch + NB)).rearrange("p (m c) -> p m c", m=3)
        tch = [(c * 384, 384) for c in range(3)]

        def tiles3(ap):
            return ap.rearrange("p (i t) -> p i t", t=P)

        (s_w2, s_hv, p_th, p_kk, pss_mm, p_rt, z_mm, p_tw, p_dve, p_ex, p_go, b_mm, b_cp) = (
            sem("lora_in"), sem("half_biases"), sem("lora_tanh"), sem("keys_squared"), sem("key_norms_summed"),
            sem("key_norms_root"), sem("lora_products"), sem("gates_tanh"),
            sem("operand_steps"), sem("decays_exp"), sem("operands_done"), sem("bonus_summed"),
            sem("bonus_written"))
        p_rn0, p_rr, p_prod, p_ch = (sem("key_norms_clamped"), sem("key_norms_inverse"), sem("bonus_product"),
                                     sem("operand_chain"))
        sq_tmp = [icl, kkn, k2]
        with nc.Block() as block:
            @block.sync
            def _(sp):
                sp.dma_start(w2[0:64], I["decay_w2"][0]).then_inc(s_w2, 16)
                sp.dma_start(w2[64:128], I["iclr_a2"][0]).then_inc(s_w2, 16)
                sp.dma_start(g2, I["gate_g2"][0]).then_inc(s_w2, 16)
                sp.dma_start(fresh, I["c_fresh"]).then_inc(s_w2, 16)

            @block.scalar
            def _(act):
                for m in range(3):
                    nc.scalar.activation(sq_tmp[m], sT[:, 3 + m], ACT.Square, scale=vec("k_k", m)).then_inc(p_kk, 1)
                for m in range(3):
                    act.wait_ge(p_rn0, 3 * m + 3)
                    nc.scalar.activation(AR[:, m, :, 0], AR[:, m, :, 0], ACT.Sqrt).then_inc(p_rt, 1)
                nc.scalar.activation(sT[0:64, 9], sT[0:64, 9], ACT.Tanh).then_inc(p_th, 1)
                act.wait_ge(s_hv, 1)
                for m in range(3):
                    if m >= 1:
                        act.wait_ge(p_go, m)
                    for w, dst in enumerate((lg, icl)):
                        for c, (t0, n) in enumerate(tch):
                            act.wait_ge(z_mm, 6 * m + 3 * w + c + 1)
                            nc.scalar.activation(dst[:, t0:t0 + n], PS[3 * w + c][:, 0:n], ACT.Tanh, scale=0.5,
                                                 bias=halves[:, 3 * w + m:3 * w + m + 1]).then_inc(p_tw, 1)
                    act.wait_ge(p_dve, 2 * m + 1)
                    nc.scalar.activation(dec, cum, ACT.Exp).then_inc(p_ex, 1)
                    nc.scalar.activation(di, cum, ACT.Exp, scale=-1.0).then_inc(p_ex, 1)
                    act.wait_ge(p_dve, 2 * m + 2)
                    nc.scalar.activation(lg, lg, ACT.Exp).then_inc(p_ex, 1)

            @block.tensor
            def _(pe):
                for m in range(3):
                    pe.wait_ge(p_kk, m + 1)
                    for c, (t0, n) in enumerate(tch):
                        g = 3 * m + c
                        if g >= 8:
                            pe.wait_ge(p_rn0, g - 7)
                        pe.matmul(PS[g % 8][:, 0:n], C("head_ones"), sq_tmp[m][:, t0:t0 + n], start=True,
                                  stop=True).then_inc(pss_mm, 1)
                pe.wait_ge(s_w2, 64)
                pe.wait_ge(p_th, 1)
                pe.wait_ge(p_rn0, 9)
                for m in range(3):
                    for w in range(2):
                        rows = slice(64 * w, 64 * w + 64)
                        for c, (t0, n) in enumerate(tch):
                            if m >= 1:
                                pe.wait_ge(p_tw, 6 * (m - 1) + 3 * w + c + 1)
                            pe.matmul(PS[3 * w + c][:, 0:n], w2[rows, m * P:(m + 1) * P], sT[rows, 9, t0:t0 + n],
                                      start=True, stop=True).then_inc(z_mm, 1)
                    pe.wait_ge(p_prod, m + 1)
                    for c, (t0, n) in enumerate(CH):
                        g = 3 * m + c
                        if g >= 2:
                            pe.wait_ge(b_cp, g - 1)
                        pe.matmul(PS[6 + g % 2][:, 0:n], C("head_ones"), prod[:, t0:t0 + n], start=True,
                                  stop=True).then_inc(b_mm, 1)

            @block.vector
            def _(dve):
                dve.tensor_scalar(halves[:, 0:6], vecs[:, VEC["decay_w0"][0]:VEC["decay_w0"][0] + 6], 0.5, None,
                                  ALU.mult)
                dve.tensor_scalar(halves[:, 6:9], vecs[:, VEC["k_a"][0]:VEC["k_a"][0] + 3], -1.0, 1.0, ALU.mult,
                                  ALU.add).then_inc(s_hv, 1)
                dve.wait_ge(s_hv, 1)
                for m in range(3):
                    for c, (t0, n) in enumerate(tch):
                        g = 3 * m + c
                        dve.wait_ge(pss_mm, g + 1)
                        ins = dve.tensor_scalar(AR[:, m, 3 * c:3 * c + 3, 0], tiles3(PS[g % 8][:, 0:n]), 1e-24,
                                                None, ALU.max).then_inc(p_rn0, 1)
                for m in range(3):
                    dve.wait_ge(p_rt, m + 1)
                    dve.reciprocal(AR[:, m, :, 0], AR[:, m, :, 0]).then_inc(p_rr, 1)
                dve.wait_ge(s_w2, 64)
                link = chain(dve, p_ch)
                for m in range(3):
                    r, k = sT[:, m], sT[:, 3 + m]
                    dve.wait_ge(p_tw, 6 * m + 6)
                    link(dve.tensor_scalar(lg, lg, DECAY / 2, DECAY / 2, ALU.mult, ALU.add))
                    dve.tensor_tensor_scan(cum, fresh, lg, 0.0, ALU.mult, ALU.add).then_inc(p_dve, 1)
                    dve.wait_ge(p_dve, 2 * m + 1)
                    dve.tensor_tensor(lg, cum, lg, ALU.subtract).then_inc(p_dve, 1)
                    dve.wait_ge(p_rr, m + 1)
                    link(dve.scalar_tensor_tensor(out=tiles3(kkn), in0=tiles3(k), scalar=vec("k_k", m),
                                                  in1=AR[:, m, :, 0], op0=ALU.mult, op1=ALU.mult))
                    link(dve.tensor_scalar(icl, icl, 0.5, 0.5, ALU.mult, ALU.add))
                    link(dve.tensor_scalar(k2, icl, vec("k_a", m), halves[:, 6 + m:7 + m], ALU.mult, ALU.add))
                    link(dve.tensor_tensor(k2, k2, k, ALU.mult))
                    if m >= 1:
                        dve.wait_ge(b_mm, 3 * m)
                    dve.scalar_tensor_tensor(out=prod, in0=r, scalar=vec("r_k", m), in1=k2, op0=ALU.mult,
                                             op1=ALU.mult).then_inc(p_prod, 1)
                    link(dve.tensor_tensor(icl, icl, kkn, ALU.mult))
                    dve.wait_ge(p_ex, 3 * m + 1)
                    link(dve.tensor_tensor(AR[:, m, :, 1], tiles3(r), tiles3(dec), ALU.mult))
                    dve.tensor_copy(dc[:, m, 0:nch], dec[:, CHUNK - 1:SEQ:CHUNK])
                    dve.tensor_copy(dc[:, m, nch:], dec[:, SEQ + TS - 1:T:TS])
                    dve.wait_ge(p_ex, 3 * m + 2)
                    dve.tensor_tensor(r, icl, di, ALU.mult)
                    dve.tensor_tensor(k, k2, di, ALU.mult)
                    dve.wait_ge(p_ex, 3 * m + 3)
                    dve.scalar_tensor_tensor(out=AR[:, m, :, 0], in0=tiles3(kkn), scalar=-1.0, in1=tiles3(lg),
                                             op0=ALU.mult, op1=ALU.mult).then_inc(p_go, 1)
                    for c, (t0, n) in enumerate(CH):
                        dve.wait_ge(b_mm, 3 * m + c + 1)
                        dve.tensor_tensor(mixT[:, m, t0:t0 + n], PS[6 + (3 * m + c) % 2][:, 0:n],
                                          sT[:, 6 + m, t0:t0 + n], ALU.mult).then_inc(b_cp, 1)
                    dve.wait_ge(p_go, m + 1)
        if upto == "operands":
            return

        new_stage()
        cw = Carve(loop_base)
        hb = cw.take(5 * 1536).rearrange("p (h b w) -> p h b w", h=5, b=6)
        hb5 = wring[:, 768:768 + 1536].rearrange("p (b w) -> p b w", b=6)
        at2 = [2304]

        def wr(n):
            at2[0] += n
            assert at2[0] <= 4096
            return wring[:, at2[0] - n:at2[0]]

        nat_b, nat_k, nat_v = wr(AW), wr(AW), wr(AW)
        rt_ = wr(AW).rearrange("p (m t) -> p m t", m=3)
        scr = sT[:, 9]
        states = scr[:, 0:768].rearrange("p (s m v) -> p s m v", s=4, m=3)
        gts = scr[:, 768:1152].rearrange("p (m c v) -> p m c v", m=3, c=2)
        hss = cw.take(AW).rearrange("p (m c v) -> p m c v", m=3, c=2)

        def buf(h, b):
            return hb[:, h, b] if h < 5 else hb5[:, b]

        NQ, MP, XX, ND, PA, PB = range(6)
        STG = ["NQ", "MP", "NT", "MV", "P2", "A1", "P4", "A2", "P8", "A4", "A8", "ZT", "Z2", "B2", "B1", "RT"]
        OPS = 4 + 6 * len(STG) + 12 + 2 + 6
        NPT_ = TT - 1
        ON_DVE = {"NQ", "MP", "NT", "A1", "A2", "A4", "A8", "B2", "B1", "RT"}

        def op(i, what, h=0, c=0):
            if what == "nat":
                k = h
            elif what == "GH":
                k = 4 + 6 * len(STG) + 2 * h + c
            elif what == "CH":
                k = 4 + 6 * len(STG) + 12 + c
            elif what == "Y":
                k = 4 + 6 * len(STG) + 14 + h
            else:
                k = 4 + 6 * STG.index(what) + h
            return i * OPS + k

        def decode_op(n):
            i, k = divmod(n, OPS)
            if k < 4:
                return i, "nat", k, 0
            k -= 4
            if k < 6 * len(STG):
                return i, STG[k // 6], k % 6, 0
            k -= 6 * len(STG)
            if k < 12:
                return i, "GH", k // 2, k % 2
            if k < 14:
                return i, "CH", 0, k - 12
            return i, "Y", k - 14, 0

        def by_dve(n):
            i, what, h, c = decode_op(n)
            return what in ON_DVE or what in ("GH", "CH") or (what == "nat" and h == 0)

        NOPS = NPT_ * OPS + 4 + 6 * len(STG)
        dve_before, act_before = [0], [0]
        for n in range(NOPS):
            dve_before.append(dve_before[-1] + by_dve(n))
            act_before.append(act_before[-1] + (not by_dve(n)))
        rw_mm, rw_dve, rw_act, rw_pool, s_s0 = (sem("rw_product"), sem("rw_taken_dve"), sem("rw_taken_act"),
                                                sem("rw_transposed_blocks"), sem("rw_state_zeroed"))

        def taken(eng, n):
            if by_dve(n):
                eng.wait_ge(rw_dve, dve_before[n] + 1)
            else:
                eng.wait_ge(rw_act, act_before[n] + 1)

        def head(h):
            return slice(64 * (h % 2), 64 * (h % 2) + 64), h // 2

        def masks(i):
            return "_p" if i < NPT_ else "_s"

        def solve_ops(pe, i):
            def bank(n):
                if n >= 8:
                    taken(pe, n - 8)
                return PS[n % 8]

            for j, src in enumerate((None, 0, 3, 6)):
                n = op(i, "nat", j)
                b = bank(n)
                for m in range(3):
                    x = AR[:, m, i, 0] if src is None else sT[:, src + m, i * P:(i + 1) * P]
                    last = pe.transpose(b[:, m * P:(m + 1) * P], x, ident)
                last.then_inc(rw_mm, 1)
            for what in STG:
                for h in range(H):
                    n = op(i, what, h)
                    b = bank(n)
                    rows, m = head(h)
                    x = buf(h, XX)
                    if what in ("NQ", "MP"):
                        src = sT[rows, m if what == "NQ" else 3 + m, i * P:(i + 1) * P]
                        last = pe.matmul(b[:, 0:256], src, AR[rows, m, i].rearrange("p w t -> p (w t)"),
                                         start=True, stop=True)
                    elif what == "NT":
                        taken(pe, op(i, "NQ", h))
                        last = pe.transpose(b[:, 0:P], buf(h, NQ)[:, 0:P], ident)
                    elif what == "MV":
                        taken(pe, op(i, "MP", h))
                        taken(pe, op(i, "nat", 3))
                        last = pe.matmul(b[:, 0:HD], buf(h, MP)[:, 0:P], nat_v[:, h * HD:(h + 1) * HD], start=True,
                                         stop=True)
                    elif what in ("P2", "P4"):
                        src = buf(h, ND if what == "P2" else PA)
                        taken(pe, op(i, "NT" if what == "P2" else "P2", h))
                        if what == "P2":
                            pe.wait_ge(rw_pool, 6 * i + h + 1)
                        pe.matmul(b[:, 0:P], src[:, P:], src[:, 0:P], start=True, stop=True)
                        last = pe.matmul(b[:, P:256], src[:, 0:P], src[:, P:], start=True, stop=True)
                    elif what == "P8":
                        taken(pe, op(i, "P4", h))
                        last = pe.matmul(b[:, 0:P], buf(h, PB)[:, 0:P], buf(h, PB)[:, P:], start=True, stop=True)
                    elif what in ("A1", "A2", "A4", "A8"):
                        prev = {"A1": "MV", "A2": "A1", "A4": "A2", "A8": "A4"}[what]
                        taken(pe, op(i, prev, h))
                        if what == "A1":
                            taken(pe, op(i, "nat", 0))
                        else:
                            taken(pe, op(i, {"A2": "P2", "A4": "P4", "A8": "P8"}[what], h))
                        w = {"A1": buf(h, ND)[:, P:], "A2": buf(h, PA)[:, P:], "A4": buf(h, PB)[:, P:],
                             "A8": buf(h, ND)[:, 0:P]}[what]
                        last = pe.matmul(b[:, 0:256], w, x, start=True, stop=True)
                    elif what == "ZT":
                        taken(pe, op(i, "A8", h))
                        last = pe.transpose(b[:, 0:P], x[:, P:], ident)
                    elif what == "Z2":
                        taken(pe, op(i, "ZT", h))
                        last = pe.matmul(b[:, 0:P], x[:, P:], buf(h, PA)[:, 0:P], start=True, stop=True)
                    elif what in ("B2", "B1"):
                        taken(pe, op(i, "Z2" if what == "B2" else "B2", h))
                        w = buf(h, PA)[:, P:] if what == "B2" else buf(h, PA)[:, 0:P]
                        last = pe.matmul(b[:, 0:P], w, x[:, 0:P], start=True, stop=True)
                    else:
                        taken(pe, op(i, "B1", h))
                        last = pe.matmul(b[rows, 0:P], x[:, 0:HD], buf(h, NQ)[:, P:], start=True, stop=True)
                    last.then_inc(rw_mm, 1)

        def solve_dve(dve, i):
            mk = masks(i)
            n = op(i, "nat", 0)
            dve.wait_ge(rw_mm, n + 1)
            b = PS[n % 8]
            for h in range(H):
                ins = dve.tensor_copy(buf(h, XX)[:, 0:HD], b[:, h * HD:(h + 1) * HD])
            ins.then_inc(rw_dve, 1)
            for what in STG:
                for h in range(H):
                    if what not in ON_DVE:
                        continue
                    n = op(i, what, h)
                    b = PS[n % 8]
                    rows, m = head(h)
                    dve.wait_ge(rw_mm, n + 1)
                    if what in ("NQ", "MP"):
                        ins = dve.tensor_tensor(buf(h, NQ if what == "NQ" else MP), b[:, 0:256], C("keep" + mk),
                                                ALU.mult)
                    elif what == "NT":
                        dve.tensor_tensor(buf(h, ND)[:, 0:P], b[:, 0:P], C("diag" + mk), ALU.mult)
                        ins = dve.tensor_tensor(buf(h, XX)[:, P:], b[:, 0:P], C("off" + mk), ALU.mult)
                    elif what in ("A1", "A2", "A4", "A8"):
                        ins = dve.tensor_tensor(buf(h, XX), b[:, 0:256], buf(h, XX), ALU.add)
                    elif what in ("B2", "B1"):
                        ins = dve.tensor_tensor(buf(h, XX)[:, 0:P], b[:, 0:P], buf(h, XX)[:, 0:P], ALU.add)
                    else:
                        ins = dve.tensor_tensor(rt_[rows, m], b[rows, 0:P], AR[rows, m, i, 1], ALU.add)
                    ins.then_inc(rw_dve, 1)

        def solve_act(act, i):
            for j, dst in enumerate((None, nat_b, nat_k, nat_v)):
                if dst is None:
                    continue
                n = op(i, "nat", j)
                act.wait_ge(rw_mm, n + 1)
                nc.scalar.copy(dst, PS[n % 8][:, 0:AW]).then_inc(rw_act, 1)
            for what in STG:
                for h in range(H):
                    if what in ON_DVE:
                        continue
                    n = op(i, what, h)
                    b = PS[n % 8]
                    act.wait_ge(rw_mm, n + 1)
                    dst, w = {"MV": (buf(h, XX)[:, HD:P], HD), "P2": (buf(h, PA), 256), "P4": (buf(h, PB), 256),
                              "P8": (buf(h, ND)[:, 0:P], P), "ZT": (buf(h, PA)[:, 0:P], P),
                              "Z2": (buf(h, PA)[:, P:], P)}[what]
                    nc.scalar.copy(dst, b[:, 0:w]).then_inc(rw_act, 1)

        def solve_pool(pool, i):
            for h in range(H):
                taken(pool, op(i, "NQ", h))
                if i >= 1:
                    pool.wait_ge(rw_mm, op(i - 1, "A8", h) + 1)
                nc.gpsimd.tensor_tensor(buf(h, ND)[:, P:], buf(h, NQ)[:, 0:P], C("diag" + masks(i)), ALU.mult
                                        ).then_inc(rw_pool, 1)

        with nc.Block() as block:
            @block.gpsimd
            def _(pool):
                nc.gpsimd.memset(states[:, 0], 0.0).then_inc(s_s0, 1)
                for i in range(NPT_):
                    solve_pool(pool, i)

            @block.tensor
            def _(pe):
                pe.wait_ge(s_s0, 1)
                for i in range(NPT_):
                    solve_ops(pe, i)
                    for h in range(H):
                        rows, m = head(h)
                        cols = slice(h * HD, (h + 1) * HD)
                        x = buf(h, XX)
                        for c in range(2):
                            n = op(i, "GH", h, c)
                            taken(pe, n - 8)
                            b = PS[n % 8]
                            tr = slice(64 * c, 64 * c + 64)
                            pe.matmul(b[rows, 0:HD], x[tr, 0:HD], nat_b[tr, cols], start=True, stop=False,
                                      skip_group_check=True)
                            pe.matmul(b[rows, HD:P], nat_b[tr, cols], x[tr, HD:P], start=False, stop=False,
                                      skip_group_check=True)
                            pe.matmul(b[rows, HD:P], nat_k[tr, cols], nat_v[tr, cols], start=False, stop=True,
                                      skip_group_check=True).then_inc(rw_mm, 1)
                    for c in range(2):
                        n = op(i, "CH", 0, c)
                        taken(pe, n - 8)
                        taken(pe, op(i, "GH", 5, c))
                        if 2 * i + c >= 1:
                            taken(pe, op(i, "CH", 0, 0) if c else op(i - 1, "CH", 0, 1))
                        for h in range(H):
                            rows, m = head(h)
                            last = pe.matmul(PS[n % 8][rows, m * HD:(m + 1) * HD], gts[rows, m, c],
                                             states[rows, (2 * i + c) % 4, m], start=True, stop=True)
                        last.then_inc(rw_mm, 1)
                    for h in range(H):
                        rows, m = head(h)
                        n = op(i, "Y", h)
                        taken(pe, n - 8)
                        taken(pe, op(i, "RT", h))
                        b = PS[n % 8]
                        pe.matmul(b[rows, 0:P], buf(h, XX)[:, HD:P], buf(h, NQ)[:, P:], start=True, stop=False,
                                  skip_group_check=True)
                        pe.matmul(b[rows, 0:P], nat_v[:, h * HD:(h + 1) * HD], buf(h, MP)[:, P:], start=False,
                                  stop=False, skip_group_check=True)
                        for c in range(2):
                            last = pe.matmul(b[rows, 64 * c:64 * c + 64], states[rows, (2 * i + c) % 4, m],
                                             rt_[rows, m, 64 * c:64 * c + 64], start=False, stop=(c == 1),
                                             skip_group_check=True)
                        last.then_inc(rw_mm, 1)

            @block.vector
            def _(dve):
                for i in range(NPT_):
                    solve_dve(dve, i)
                    for h in range(H):
                        rows, m = head(h)
                        for c in range(2):
                            n = op(i, "GH", h, c)
                            dve.wait_ge(rw_mm, n + 1)
                            b = PS[n % 8]
                            eye = ident[rows, 64 * (h % 2):64 * (h % 2) + 64]
                            dve.tensor_tensor(gts[rows, m, c], b[rows, 0:HD], eye, ALU.add)
                            dve.tensor_scalar(hss[rows, m, c], b[rows, HD:P], dc[rows, m, 2 * i + c:2 * i + c + 1],
                                              None, ALU.mult).then_inc(rw_dve, 1)
                    for c in range(2):
                        n = op(i, "CH", 0, c)
                        q = 2 * i + c
                        dve.wait_ge(rw_mm, n + 1)
                        for m in range(3):
                            ins = dve.scalar_tensor_tensor(out=states[:, (q + 1) % 4, m],
                                                           in0=PS[n % 8][:, m * HD:(m + 1) * HD],
                                                           scalar=dc[:, m, q:q + 1], in1=hss[:, m, c],
                                                           op0=ALU.mult, op1=ALU.add)
                        ins.then_inc(rw_dve, 1)

            @block.scalar
            def _(act):
                for i in range(NPT_):
                    solve_act(act, i)
                    for h in range(H):
                        rows, m = head(h)
                        n = op(i, "Y", h)
                        act.wait_ge(rw_mm, n + 1)
                        nc.scalar.copy(AR[rows, m, i, 0], PS[n % 8][rows, 0:P]).then_inc(rw_act, 1)
        if upto == "recur":
            return

        i8 = TT - 1
        SL = sT[:, 3:5, 0:768].rearrange("p a (q c) -> p a q c", q=2)
        s0 = [sT[:, m, 0:512] for m in range(3)]
        um = [sT[0:64, 5, 0:512], sT[0:64, 6, 0:512]]
        vm = [sT[0:64, 7, 0:512], sT[0:64, 8, 0:512]]
        spread = [sT[:, 5, 512:896], sT[:, 6, 512:896]]
        hss_out = sT[0:64, 7, 512:896]
        wt, ut = (x.rearrange("p (m t) -> p m t", m=3) for x in spread)
        s_sl, st_t, st_cp, sm_mm, sm_act, sm_dve, sm_vm, s_w1 = (
            sem("states_in2"), sem("states_turned"), sem("statesT_copied"), sem("sample_product"),
            sem("sample_taken_act"), sem("sample_taken_dve"), sem("sample_values_spread"),
            sem("sample_steps"))

        def s_taken(eng, q):
            if q < 18:
                eng.wait_ge(sm_act, q + 1)
            elif q < 30:
                eng.wait_ge(sm_dve, q - 17)
            else:
                eng.wait_ge(sm_act, q - 11)

        with nc.Block() as block:
            @block.sync
            def _(sp):
                for b in range(NB):
                    q, half = divmod(b, 2)
                    sp.dma_start(SL[64 * half:64 * half + 64, q // 2, q % 2].rearrange("p (h j) -> p h j", h=H),
                                 I["state_wkv"][0, b].rearrange("h i j -> i h j")).then_inc(s_sl, 16)
                sp.wait_ge(sm_act, 22)
                for b in range(NB):
                    q, half = divmod(b, 2)
                    sp.dma_start(wkv_s[0, b].rearrange("h i j -> i h j"),
                                 SL[64 * half:64 * half + 64, q // 2, q % 2].rearrange("p (h j) -> p h j", h=H)
                                 ).then_inc(s_wo, 16)
                sp.dma_start(wkv_p[0, 0].rearrange("h i j -> i h j"),
                             hss_out.rearrange("p (h j) -> p h j", h=H)).then_inc(s_wo, 16)
                sp.wait_ge(s_wo, 16 * 9)

            @block.gpsimd
            def _(pool):
                solve_pool(pool, i8)

            @block.tensor
            def _(pe):
                solve_ops(pe, i8)
                taken(pe, op(i8, "RT", 5))
                taken(pe, op(i8, "Z2", 5))
                pe.wait_ge(s_sl, 128)
                for m in range(3):
                    for q in range(4):
                        last = pe.transpose(PS[m][:, q * P:(q + 1) * P], SL[:, q // 2, q % 2, m * P:(m + 1) * P], ident)
                last.then_inc(st_t, 1)
                pe.wait_ge(st_cp, 3)
                for q in range(34):
                    b = PS[q % 8]
                    if q >= 8:
                        s_taken(pe, q - 8)
                    what, h = divmod(q, 6)
                    if q < 30:
                        rows, m = head(h)
                        x = buf(h, XX)
                        cols = slice(h * HD, (h + 1) * HD)
                    if what == 0:
                        last = pe.matmul(b[rows, 0:NS], x[:, 0:HD], ident[:, 0:NS], start=True, stop=True)
                    elif what == 1:
                        s_taken(pe, h)
                        pe.matmul(b[rows, 0:NS], x[:, HD:P], ident[:, 0:NS], start=True, stop=False,
                                  skip_group_check=True)
                        for s in range(NB):
                            last = pe.matmul(b[rows, TS * s:TS * s + TS], s0[m][rows, s * HD:(s + 1) * HD],
                                             wt[rows, m, TS * s:TS * s + TS], start=False, stop=(s == NB - 1),
                                             skip_group_check=True)
                    elif what == 2:
                        pe.matmul(b[rows, 0:P], x[:, HD:P], buf(h, NQ)[:, P:], start=True, stop=False,
                                  skip_group_check=True)
                        pe.matmul(b[rows, 0:P], nat_v[:, cols], buf(h, MP)[:, P:], start=False, stop=False,
                                  skip_group_check=True)
                        for s in range(NB):
                            last = pe.matmul(b[rows, TS * s:TS * s + TS], s0[m][rows, s * HD:(s + 1) * HD],
                                             rt_[rows, m, TS * s:TS * s + TS], start=False, stop=(s == NB - 1),
                                             skip_group_check=True)
                    elif what == 3:
                        s_taken(pe, 6 + h)
                        last = pe.matmul(b[0:NS, 0:HD], ut[rows, m, 0:NS], ident[rows, 64 * (h % 2):64 * (h % 2) + 64],
                                         start=True, stop=True)
                    elif what == 4:
                        s_taken(pe, 18 + h)
                        pe.wait_ge(sm_vm, h + 1)
                        pe.matmul(b[rows, :], nat_b[0:NS, cols], um[h % 2], start=True, stop=False)
                        last = pe.matmul(b[rows, :], nat_k[0:NS, cols], vm[h % 2], start=False, stop=True)
                    elif q < 33:
                        m = q - 30
                        s_taken(pe, 29)
                        for k in range(4):
                            last = pe.transpose(b[:, k * P:(k + 1) * P], s0[m][:, k * P:(k + 1) * P], ident)
                    else:
                        for m in range(3):
                            last = pe.transpose(b[0:HD, m * P:(m + 1) * P], states[:, nch % 4, m], ident)
                    last.then_inc(sm_mm, 1)

            @block.vector
            def _(dve):
                solve_dve(dve, i8)
                dve.wait_ge(st_t, 1)
                for m in range(3):
                    dve.tensor_copy(s0[m], PS[m][:, :]).then_inc(st_cp, 1)

                def expand(h):
                    sel = C("seq_of")[0:NS, :].unsqueeze(2).broadcast_to([NS, NB, HD])
                    cols = slice(h * HD, (h + 1) * HD)
                    if h >= 2:
                        dve.wait_ge(sm_mm, 24 + h - 1)
                    dve.tensor_tensor(vm[h % 2].rearrange("p (b v) -> p b v", b=NB),
                                      nat_v[0:NS, cols].unsqueeze(1).broadcast_to([NS, NB, HD]), sel, ALU.mult
                                      ).then_inc(sm_vm, 1)
                    dve.wait_ge(sm_mm, 18 + h + 1)
                    dve.tensor_tensor(um[h % 2].rearrange("p (b v) -> p b v", b=NB),
                                      PS[(18 + h) % 8][0:NS, 0:HD].unsqueeze(1).broadcast_to([NS, NB, HD]), sel,
                                      ALU.mult).then_inc(sm_dve, 1)

                def new_state(h):
                    rows, m = head(h)
                    dve.wait_ge(sm_mm, 24 + h + 1)
                    st = s0[m][rows]
                    dve.tensor_tensor(st, PS[(24 + h) % 8][rows, :], st, ALU.add).then_inc(s_w1, 1)
                    dve.wait_ge(s_w1, h + 1)
                    st = st.rearrange("p (b v) -> p b v", b=NB)
                    dve.tensor_tensor(st, st, dc[rows, m, nch:].unsqueeze(2).broadcast_to([HD, NB, HD]), ALU.mult
                                      ).then_inc(sm_dve, 1)

                for h in range(H):
                    expand(h)
                for h in range(H):
                    new_state(h)

            @block.scalar
            def _(act):
                solve_act(act, i8)
                for q in range(18):
                    what, h = divmod(q, 6)
                    rows, m = head(h)
                    act.wait_ge(sm_mm, q + 1)
                    b = PS[q % 8]
                    dst = (wt[rows, m], ut[rows, m], AR[rows, m, i8, 0])[what]
                    w = NS if what < 2 else P
                    nc.scalar.copy(dst[:, 0:w], b[rows, 0:w]).then_inc(sm_act, 1)
                for q in range(30, 34):
                    act.wait_ge(sm_mm, q + 1)
                    b = PS[q % 8]
                    if q < 33:
                        m = q - 30
                        nc.scalar.copy(SL[:, :, :, m * P:(m + 1) * P],
                                       b[:, :].rearrange("p (a q c) -> p a q c", a=2, q=2)).then_inc(sm_act, 1)
                    else:
                        nc.scalar.copy(hss_out, b[0:HD, 0:AW]).then_inc(sm_act, 1)
        if upto == "recur_s":
            return

        new_stage()
        cw = Carve(loop_base)
        ysq = [cw.take(384) for _ in range(2)]
        yrt = [cw.take(384) for _ in range(2)]
        yout = [cw.take(384) for _ in range(2)]
        jobs = [(m, c) for m in range(3) for c in range(3)]
        g_sig, y_mean, y_cen, y_sqd, y_var, y_root, y_ri, y_st, g_mm, y_done = (
            sem("gate_sigmoid"), sem("y_mean"), sem("y_centred"), sem("y_squared"), sem("y_variance"),
            sem("y_root"), sem("y_recip"), sem("y_steps"), sem("gate_product"), sem("mixed_written"))
        s_xr = sem("residual_back")
        with nc.Block() as block:
            @block.sync
            def _(sp):
                sp.dma_start(xT, spill).then_inc(s_xr, 16)
                sp.wait_ge(s_xr, 16)

            @block.tensor
            def _(pe):
                def mean(j):
                    m, c = jobs[j]
                    if j >= 2:
                        pe.wait_ge(y_cen, j - 1)
                    pe.matmul(PS[j % 2][:, 0:384], C("head_ones"), AR[:, m, 3 * c:3 * c + 3, 0], start=True,
                              stop=True).then_inc(y_mean, 1)

                mean(0)
                for j, (m, c) in enumerate(jobs):
                    if j + 1 < len(jobs):
                        mean(j + 1)
                    pe.wait_ge(y_sqd, j + 1)
                    if j >= 2:
                        pe.wait_ge(y_root, j - 1)
                        pe.wait_ge(y_done, j - 1)
                    pe.matmul(PS[2 + j % 2][:, 0:384], C("head_ones"), ysq[j % 2], start=True,
                              stop=True).then_inc(y_var, 1)
                    pe.wait_ge(g_sig, 2)
                    pe.matmul(PS[4 + j % 2][:, 0:384], g2[:, m * P:(m + 1) * P], sT[:, 10, 384 * c:384 * (c + 1)],
                              start=True, stop=True).then_inc(g_mm, 1)

            @block.scalar
            def _(act):
                nc.scalar.activation(sT[:, 10], sT[:, 10], ACT.Tanh, scale=0.5).then_inc(g_sig, 1)
                for j in range(len(jobs)):
                    m, c = jobs[j]
                    act.wait_ge(y_cen, j + 1)
                    if j >= 2:
                        act.wait_ge(y_var, j - 1)
                    nc.scalar.activation(tiles3(ysq[j % 2]), AR[:, m, 3 * c:3 * c + 3, 0], ACT.Square
                                         ).then_inc(y_sqd, 1)
                    act.wait_ge(y_var, j + 1)
                    if j >= 2:
                        act.wait_ge(y_done, j - 1)
                    nc.scalar.activation(yrt[j % 2], PS[2 + j % 2][:, 0:384], ACT.Sqrt, scale=1.0 / HD,
                                         bias=epsc[:, 1:2]).then_inc(y_root, 1)

            @block.vector
            def _(dve):
                dve.wait_ge(g_sig, 1)
                dve.tensor_scalar(sT[:, 10], sT[:, 10], 0.5, 0.5, ALU.mult, ALU.add).then_inc(g_sig, 1)

                def centre(j):
                    m, c = jobs[j]
                    y = AR[:, m, 3 * c:3 * c + 3, 0]
                    dve.wait_ge(y_mean, j + 1)
                    dve.scalar_tensor_tensor(out=y, in0=tiles3(PS[j % 2][:, 0:384]), scalar=-1.0 / HD, in1=y,
                                             op0=ALU.mult, op1=ALU.add).then_inc(y_cen, 1)

                link = chain(dve, y_st)
                centre(0)
                for j, (m, c) in enumerate(jobs):
                    if j + 1 < len(jobs):
                        centre(j + 1)
                    y, o = AR[:, m, 3 * c:3 * c + 3, 0], yout[j % 2]
                    t0, n = CH[c]
                    dve.wait_ge(y_root, j + 1)
                    link(dve.reciprocal(yrt[j % 2], yrt[j % 2]))
                    link(dve.tensor_tensor(tiles3(o), y, tiles3(yrt[j % 2]), ALU.mult))
                    link(dve.tensor_scalar(o, o, lnx[:, m:m + 1], lnx[:, 3 + m:4 + m], ALU.mult, ALU.add))
                    link(dve.tensor_tensor(o[:, 0:n], o[:, 0:n], mixT[:, m, t0:t0 + n], ALU.add))
                    dve.wait_ge(g_mm, j + 1)
                    dve.tensor_tensor(mixT[:, m, t0:t0 + n], PS[4 + j % 2][:, 0:n], o[:, 0:n], ALU.mult
                                      ).then_inc(y_done, 1)
        if upto == "mixed":
            return

        new_stage()
        w_out = I["w_out"][0].rearrange("(k p) c -> p k c", p=P)
        mx2 = split_pair("mixed", RS, RK_, KD * T, KD)
        cw = Carve(KD * T)
        wraw = [tiled(cw.take(KD * P)) for _ in range(2)]
        sqa, sqb, rstd = cw.take(T), cw.take(T), cw.take(T)
        xn2 = split_pair("normed2T", RA, RS, KD * T, KD)
        s_w = [sem(f"w_out_in{i}") for i in range(2)]
        w_hi, w_lo, x_hi, x_lo = sem("w_out_hi"), sem("w_out_lo"), sem("mixed_hi"), sem("mixed_lo")
        op_mm, op_cp, n_sq, n_acc, n_mm, n_rt, n_ri, n_t, n_hi, n_lo = (
            sem("out_product"), sem("residual_added"), sem("res_squared"), sem("res_squares_added"),
            sem("res_summed"), sem("res_root"), sem("res_recip"), sem("res_normed"), sem("res_normed_hi"),
            sem("res_normed_lo"))
        parts = [(c, k) for c in range(3) for k in range(KD)]
        with nc.Block() as block:
            def out_hi(act, m):
                act.wait_ge(s_w[m % 2], 16 * (m // 2 + 1))
                split_hi(m, (KD, P), wraw[m % 2], w_hi, op_mm, 3)

            @block.sync
            def _(sp):
                for m in range(KD):
                    if m >= 2:
                        sp.wait_ge(w_lo, m - 1)
                    sp.dma_start(wraw[m % 2], w_out[:, :, m * P:(m + 1) * P]).then_inc(s_w[m % 2], 16)

            @block.tensor
            def _(pe):
                for m in range(KD):
                    pe.wait_ge(w_lo, m + 1)
                    for c, (t0, n) in enumerate(CH):
                        g = 3 * m + c
                        if g >= 5:
                            pe.wait_ge(op_cp, g - 4)
                        for k in range(KD):
                            if m == 0:
                                pe.wait_ge(x_lo, KD * c + k + 1)
                            last = product(pe, PS[g % 5][:, 0:n], [w[:, k] for w in wsp[m % 2]],
                                           [x[:, k, t0:t0 + n] for x in mx2], k == 0, k == KD - 1)
                        last.then_inc(op_mm, 1)
                for c, (t0, n) in enumerate(CH):
                    pe.wait_ge(n_acc, 3 * (KD - 1) + c + 1)
                    pe.matmul(PS[5 + c][:, 0:n], ones, sqa[:, t0:t0 + n], start=True, stop=True).then_inc(n_mm, 1)

            @block.scalar
            def _(act):
                out_hi(act, 0)
                for c, k in parts:
                    t0, n = CH[c]
                    nc.scalar.copy(mx2[0][:, k, t0:t0 + n], mixT[:, k, t0:t0 + n]).then_inc(x_hi, 1)
                out_hi(act, 1)
                for m in range(KD):
                    for c, (t0, n) in enumerate(CH):
                        act.wait_ge(op_cp, 3 * m + c + 1)
                        if m >= 2:
                            act.wait_ge(n_acc, 3 * (m - 1) + c + 1)
                        dst = sqa if m == 0 else sqb
                        nc.scalar.activation(dst[:, t0:t0 + n], xT[:, m, t0:t0 + n], ACT.Square).then_inc(n_sq, 1)
                    if m + 2 < KD:
                        out_hi(act, m + 2)
                for c, (t0, n) in enumerate(CH):
                    act.wait_ge(n_mm, c + 1)
                    nc.scalar.activation(rstd[:, t0:t0 + n], PS[5 + c][:, 0:n], ACT.Sqrt, scale=1.0 / D,
                                         bias=epsc[:, 0:1]).then_inc(n_rt, 1)
                for j, (c, k) in enumerate(parts):
                    t0, n = CH[c]
                    act.wait_ge(n_t, j + 1)
                    nc.scalar.copy(xn2[0][:, k, t0:t0 + n], (sqa, sqb)[j % 2][:, t0:t0 + n]).then_inc(n_hi, 1)

            @block.vector
            def _(dve):
                split_lo(0, (KD, P), wraw[0], w_hi, w_lo)
                for j, (c, k) in enumerate(parts):
                    t0, n = CH[c]
                    dve.wait_ge(x_hi, j + 1)
                    dve.tensor_tensor(mx2[1][:, k, t0:t0 + n], mixT[:, k, t0:t0 + n],
                                      mx2[0][:, k, t0:t0 + n].bitcast(F32), ALU.subtract).then_inc(x_lo, 1)
                split_lo(1, (KD, P), wraw[1], w_hi, w_lo)
                for m in range(KD):
                    for c, (t0, n) in enumerate(CH):
                        g = 3 * m + c
                        dve.wait_ge(op_mm, g + 1)
                        dve.tensor_tensor(xT[:, m, t0:t0 + n], PS[g % 5][:, 0:n], xT[:, m, t0:t0 + n], ALU.add
                                          ).then_inc(op_cp, 1)
                    if m + 2 < KD:
                        split_lo(m + 2, (KD, P), wraw[m % 2], w_hi, w_lo)
                for c, (t0, n) in enumerate(CH):
                    dve.wait_ge(n_rt, c + 1)
                    dve.reciprocal(rstd[:, t0:t0 + n], rstd[:, t0:t0 + n]).then_inc(n_ri, 1)
                for j in range(len(parts) + 1):
                    if j < len(parts):
                        c, k = parts[j]
                        t0, n = CH[c]
                        dve.wait_ge(n_ri, c + 1)
                        if j >= 2:
                            dve.wait_ge(n_lo, j - 1)
                        else:
                            dve.wait_ge(n_mm, 3)
                        dve.scalar_tensor_tensor(out=(sqa, sqb)[j % 2][:, t0:t0 + n], in0=xT[:, k, t0:t0 + n],
                                                 scalar=vec("norm_ffn_g", k), in1=rstd[:, t0:t0 + n],
                                                 op0=ALU.mult, op1=ALU.mult).then_inc(n_t, 1)
                    if j >= 1:
                        c, k = parts[j - 1]
                        t0, n = CH[c]
                        dve.wait_ge(n_hi, j)
                        dve.tensor_tensor(xn2[1][:, k, t0:t0 + n], (sqa, sqb)[(j - 1) % 2][:, t0:t0 + n],
                                          xn2[0][:, k, t0:t0 + n].bitcast(F32), ALU.subtract).then_inc(n_lo, 1)

            @block.gpsimd
            def _(pool):
                for c in range(3):
                    pool.wait_ge(n_sq, c + 1)
                    pool.sem_inc(n_acc, 1)
                for m in range(1, KD):
                    for c, (t0, n) in enumerate(CH):
                        pool.wait_ge(n_sq, 3 * m + c + 1)
                        nc.gpsimd.tensor_tensor(sqa[:, t0:t0 + n], sqa[:, t0:t0 + n], sqb[:, t0:t0 + n], ALU.add
                                                ).then_inc(n_acc, 1)
        if upto == "outproj":
            return

        new_stage()
        GROUPS = [5, 5, 4, 4, 4]
        G = max(GROUPS)
        first_of = [sum(GROUPS[:i]) for i in range(len(GROUPS) + 1)]
        stream = []
        for gi, n in enumerate(GROUPS):
            for f in range(first_of[gi], first_of[gi] + n):
                stream.append(("gate", f))
                if f == first_of[gi] and gi:
                    stream += [("down", gi - 1, m) for m in range(KD)]
                stream.append(("up", f))
        stream += [("down", len(GROUPS) - 1, m) for m in range(KD)]
        NW = len(stream)
        nth = {"gate": 0, "up": 0, "down": 0}
        order = []
        for item in stream:
            order.append(nth[item[0]])
            nth[item[0]] += 1
        S2 = KD * T
        gend = sT_[:, S2:S2 + 18 * FT].rearrange("p (j f) -> p j f", f=FT)
        S2 += (18 * FT + 7) // 8 * 8
        cv, hraw = sT_[:, S2:S2 + T], sT_[:, S2 + T:S2 + 2 * T]
        S2 += 2 * T
        h2 = split_pair("inner", RK_, RK_ + G * T, G * T, G)
        cw = Carve(2 * G * T)
        GW = 2 + SEQ + NB * (2 + TS)
        gring = [cw.take(GW) for _ in range(2)]
        wraw = [tiled(sT_[:, S2:S2 + KD * P]), tiled(cw.take(KD * P)), tiled(cw.take(KD * P))]
        assert S2 + KD * P <= A_TILES * TPAD
        w_up = I["w_up"][0].rearrange("(k p) c -> p k c", p=P)
        w_down = I["w_down"][0].rearrange("(f p) c -> p f c", p=P)
        s_wu = [sem(f"w_ffn_in{i}") for i in range(3)]
        w_hi, w_lo = sem("w_ffn_hi"), sem("w_ffn_lo")
        f_mm, f_gate, f_conv, f_steps, f_tanh, f_pre, f_st, f_up, f_hh, f_hl, f_dn = (
            sem("ffn_product"), sem("gate_copied"), sem("conv_done"), sem("conv_steps"), sem("silu_tanh"),
            sem("gate_prefix"), sem("gate_history"), sem("up_taken"), sem("inner_hi"), sem("inner_lo"),
            sem("down_added"))

        def rows_w(j):
            return KD if stream[j][0] != "down" else GROUPS[stream[j][1]]

        def slot_of(f):
            gi = max(i for i in range(len(GROUPS)) if first_of[i] <= f)
            return f - first_of[gi]

        def down_after(f):
            gi = max(i for i in range(len(GROUPS)) if first_of[i] <= f)
            return KD * gi

        with nc.Block() as block:
            def ffn_hi(act, j):
                act.wait_ge(s_wu[j % 3], 16 * (j // 3 + 1))
                split_hi(j, (rows_w(j), P), wraw[j % 3], w_hi, f_mm, 3)

            def ffn_lo(dve, j):
                split_lo(j, (rows_w(j), P), wraw[j % 3], w_hi, w_lo)

            @block.sync
            def _(sp):
                for j, item in enumerate(stream):
                    if j >= 3:
                        sp.wait_ge(w_lo, j - 2)
                    if item[0] == "down":
                        f0 = first_of[item[1]]
                        src = w_down[:, f0:f0 + rows_w(j), item[2] * P:(item[2] + 1) * P]
                    else:
                        c0 = item[1] * P + (0 if item[0] == "up" else DFF)
                        src = w_up[:, :, c0:c0 + P]
                    sp.dma_start(wraw[j % 3][:, 0:rows_w(j)], src).then_inc(s_wu[j % 3], 16)

            @block.tensor
            def _(pe):
                for j, item in enumerate(stream):
                    pe.wait_ge(w_lo, j + 1)
                    if item[0] == "down":
                        pe.wait_ge(f_hl, first_of[item[1] + 1])
                    x = h2 if item[0] == "down" else xn2
                    for c, (t0, n) in enumerate(CH):
                        g = 3 * j + c
                        if g >= 8:
                            pj, pc = divmod(g - 8, 3)
                            done = {"gate": f_gate, "up": f_up, "down": f_dn}[stream[pj][0]]
                            pe.wait_ge(done, 3 * order[pj] + pc + 1)
                        for k in range(rows_w(j)):
                            last = product(pe, PS[g % 8][:, 0:n], [w[:, k] for w in wsp[j % 2]],
                                           [v[:, k, t0:t0 + n] for v in x], k == 0, k == rows_w(j) - 1)
                        last.then_inc(f_mm, 1)

            @block.gpsimd
            def _(pool):
                for j in range(2):
                    ins = nc.gpsimd.memset(gring[j][:, 0:2], 0.0)
                ins.then_inc(f_pre, 1)
                for f in range(FT):
                    if f >= 2:
                        pool.wait_ge(f_conv, f - 1)
                    nc.gpsimd.tensor_copy(seg(gring[f % 2], 2)[1][:, :, 0:2],
                                          convT[:, f].rearrange("p (b t) -> p b t", b=NB)).then_inc(f_pre, 1)
                    pool.wait_ge(f_gate, 3 * f + 3)
                    p_seq, s_seq = seg(gring[f % 2], 2)
                    nc.gpsimd.tensor_copy(gend[:, 0:2, f], p_seq[:, SEQ - 2:SEQ])
                    nc.gpsimd.tensor_copy(gend[:, 2:18, f].rearrange("p (b t) -> p b t", b=NB),
                                          s_seq[:, :, TS:TS + 2]).then_inc(f_st, 1)

            @block.scalar
            def _(act):
                def gate(j, f):
                    if f >= 2:
                        act.wait_ge(f_conv, f - 1)
                        act.wait_ge(f_st, f - 1)
                    p_seq, s_seq = seg(gring[f % 2], 2)
                    for c, (t0, n) in enumerate(CH):
                        g = 3 * j + c
                        act.wait_ge(f_mm, g + 1)
                        k = min(n, SEQ - t0)
                        ins = nc.scalar.copy(p_seq[:, t0:t0 + k], PS[g % 8][:, 0:k])
                        if c == 2:
                            ins = nc.scalar.copy(s_seq[:, :, 2:], PS[g % 8][:, k:k + NS].rearrange(
                                "p (b t) -> p b t", b=NB))
                        ins.then_inc(f_gate, 1)
                    act.wait_ge(f_conv, f + 1)
                    if f >= 1:
                        act.wait_ge(f_hl, f)
                    nc.scalar.activation(hraw, cv, ACT.Tanh, scale=0.5).then_inc(f_tanh, 1)

                ffn_hi(act, 0)
                ffn_hi(act, 1)
                for j, item in enumerate(stream):
                    if item[0] == "gate":
                        gate(j, item[1])
                    elif item[0] == "up":
                        f = item[1]
                        act.wait_ge(f_up, 3 * f + 3)
                        if down_after(f):
                            act.wait_ge(f_dn, 3 * down_after(f))
                        nc.scalar.copy(h2[0][:, slot_of(f)], hraw).then_inc(f_hh, 1)
                    if j + 2 < NW:
                        ffn_hi(act, j + 2)

            @block.vector
            def _(dve):
                link = chain(dve, f_steps)

                def conv(f):
                    p_all = gring[f % 2][:, 0:2 + SEQ]
                    s_all = seg(gring[f % 2], 2)[1]
                    cv_s = cv[:, SEQ:T].rearrange("p (b t) -> p b t", b=NB)
                    dve.wait_ge(f_gate, 3 * f + 3)
                    dve.wait_ge(f_pre, f + 2)
                    for t in range(3):
                        w = vec("conv_w", t * FT + f)
                        if t == 0:
                            dve.tensor_scalar(cv[:, 0:SEQ], p_all[:, 0:SEQ], w, vec("conv_b", f), ALU.mult, ALU.add)
                            link(dve.tensor_scalar(cv_s, s_all[:, :, 0:TS], w, vec("conv_b", f), ALU.mult, ALU.add))
                        else:
                            dve.scalar_tensor_tensor(out=cv[:, 0:SEQ], in0=p_all[:, t:t + SEQ], scalar=w,
                                                     in1=cv[:, 0:SEQ], op0=ALU.mult, op1=ALU.add)
                            ins = dve.scalar_tensor_tensor(out=cv_s, in0=s_all[:, :, t:t + TS], scalar=w, in1=cv_s,
                                                           op0=ALU.mult, op1=ALU.add)
                            if t == 1:
                                link(ins)
                            else:
                                ins.then_inc(f_conv, 1)

                def inner(j, f):
                    dve.wait_ge(f_tanh, f + 1)
                    link(dve.scalar_tensor_tensor(out=hraw, in0=hraw, scalar=1.0, in1=cv, op0=ALU.add,
                                                  op1=ALU.mult))
                    for c, (t0, n) in enumerate(CH):
                        g = 3 * j + c
                        dve.wait_ge(f_mm, g + 1)
                        dve.scalar_tensor_tensor(out=hraw[:, t0:t0 + n], in0=PS[g % 8][:, 0:n], scalar=0.5,
                                                 in1=hraw[:, t0:t0 + n], op0=ALU.mult, op1=ALU.mult
                                                 ).then_inc(f_up, 1)
                    dve.wait_ge(f_hh, f + 1)
                    dve.tensor_tensor(h2[1][:, slot_of(f)], hraw, h2[0][:, slot_of(f)].bitcast(F32), ALU.subtract
                                      ).then_inc(f_hl, 1)

                ffn_lo(dve, 0)
                ffn_lo(dve, 1)
                for j, item in enumerate(stream):
                    if item[0] == "gate":
                        conv(item[1])
                    elif item[0] == "up":
                        inner(j, item[1])
                    else:
                        m = item[2]
                        for c, (t0, n) in enumerate(CH):
                            dve.wait_ge(f_mm, 3 * j + c + 1)
                            dve.tensor_tensor(xT[:, m, t0:t0 + n], PS[(3 * j + c) % 8][:, 0:n], xT[:, m, t0:t0 + n],
                                              ALU.add).then_inc(f_dn, 1)
                    if j + 2 < NW:
                        ffn_lo(dve, j + 2)
        if upto == "down":
            return

        cnat = wring[:, 0:4 * P].rearrange("p (q c) -> p q c", q=4)
        g_t, g_cp = sem("history_turned"), sem("history_copied")
        with nc.Block() as block:
            @block.sync
            def _(sp):
                sp.wait_ge(g_cp, 1)
                sp.dma_start(conv_p[0, 0].rearrange("t (f c) -> (t f) c", c=P), cnat[0:44, 0]).then_inc(s_co, 16)
                flat = conv_s[0].rearrange("b t (f c) -> (b t f) c", c=P)
                for q in range(3):
                    n = min(P, 352 - q * P)
                    sp.dma_start(flat[q * P:q * P + n, :], cnat[0:n, q + 1]).then_inc(s_co, 16)
                sp.wait_ge(s_co, 64)

            @block.tensor
            def _(pe):
                flat = gend.rearrange("p j f -> p (j f)")
                for q, (a, n) in enumerate(((0, 44), (44, P), (44 + P, P), (44 + 2 * P, 96))):
                    last = pe.transpose(PS[7][0:n, q * P:(q + 1) * P], flat[:, a:a + n], ident)
                last.then_inc(g_t, 1)

            @block.scalar
            def _(act):
                act.wait_ge(g_t, 1)
                for q, n in enumerate((44, P, P, 96)):
                    ins = nc.scalar.copy(cnat[0:n, q], PS[7][0:n, q * P:(q + 1) * P])
                ins.then_inc(g_cp, 1)

        new_stage()
        g_last = work[:, 0:D]
        yrow = [work[:, D * (1 + i):D * (2 + i)] for i in range(3)]
        junk = work[:, 4 * D:4 * D + 512]
        fs = small[:, 0:5 * TT].rearrange("p (i a) -> p i a", i=TT)
        s_gl, e_t, e_sq, e_sum, e_rt, e_ri, e_y = (sem("final_gain_in"), sem("final_turned"), sem("final_squared"),
                                                   sem("final_sum"), sem("final_root"), sem("final_recip"),
                                                   sem("final_scaled"))
        with nc.Block() as block:
            @block.sync
            def _(sp):
                sp.dma_start(g_last, I["norm_final_g"].partition_broadcast(P)).then_inc(s_gl, 16)
                for i in range(TT):
                    n = rows_of(i)
                    sp.wait_ge(e_y, 2 * i + 2)
                    dst = y_prompt[0, i * P:(i + 1) * P, :] if i < TT - 1 else y_sample.rearrange("b t d -> (b t) d")
                    sp.dma_start(dst, yrow[i % 3][0:n, :]).then_inc(s_y[i % 3], 16)
                for j in range(3):
                    sp.wait_ge(s_y[j], 48)

            @block.tensor
            def _(pe):
                for i in range(TT):
                    n = rows_of(i)
                    if i >= 4:
                        pe.wait_ge(e_y, 2 * (i - 3))
                    for k in range(KD):
                        last = pe.transpose(PS[2 * (i % 4) + k // 4][0:n, (k % 4) * P:(k % 4 + 1) * P],
                                            xT[:, k, i * P:i * P + n], ident)
                    last.then_inc(e_t, 1)

            @block.scalar
            def _(act):
                for i in range(TT):
                    n = rows_of(i)
                    act.wait_ge(e_t, i + 1)
                    for j in range(2):
                        k = 2 * i + j
                        if k >= 1:
                            act.wait_ge(e_sq, k)
                        nc.scalar.activation(junk[0:n, :], PS[2 * (i % 4) + j][0:n, :], ACT.Square,
                                             accum_out=fs[0:n, i, j:j + 1]).then_inc(e_sq, 1)
                    act.wait_ge(e_sum, i + 1)
                    nc.scalar.activation(fs[0:n, i, 3:4], fs[0:n, i, 2:3], ACT.Sqrt, scale=1.0 / D,
                                         bias=epsc[0:n, 0:1]).then_inc(e_rt, 1)

            @block.vector
            def _(dve):
                dve.wait_ge(s_gl, 16)
                for i in range(TT):
                    n = rows_of(i)
                    dve.wait_ge(e_sq, 2 * i + 2)
                    dve.tensor_tensor(fs[0:n, i, 2:3], fs[0:n, i, 0:1], fs[0:n, i, 1:2], ALU.add).then_inc(e_sum, 1)
                    dve.wait_ge(e_rt, i + 1)
                    dve.reciprocal(fs[0:n, i, 4:5], fs[0:n, i, 3:4]).then_inc(e_ri, 1)
                    dve.wait_ge(e_ri, i + 1)
                    if i >= 3:
                        dve.wait_ge(s_y[i % 3], 16 * (i // 3))
                    for j in range(2):
                        dve.scalar_tensor_tensor(out=yrow[i % 3][0:n, 512 * j:512 * j + 512],
                                                 in0=PS[2 * (i % 4) + j][0:n, :], scalar=fs[0:n, i, 4:5],
                                                 in1=g_last[0:n, 512 * j:512 * j + 512], op0=ALU.mult,
                                                 op1=ALU.mult).then_inc(e_y, 1)


def kernel(**inputs):
    import numpy as _np
    import concourse.bacc as _bacc
    from concourse import mybir as _mybir
    from concourse.bass_utils import run_bass_kernel_spmd as _run

    nc = _bacc.Bacc("TRN2", target_bir_lowering=False, num_devices=1)
    arrays, args = {}, {}
    for name, a in {**inputs, **constants()}.items():
        a = _np.ascontiguousarray(a)
        arrays[f"in_{name}_dram"] = a
        args[name] = nc.dram_tensor(f"in_{name}_dram", a.shape, _mybir.dt.from_np(a.dtype), kind="ExternalInput").ap()
    outs = [nc.dram_tensor(f"out_{i}_dram", shape, _mybir.dt.float32, kind="ExternalOutput").ap()
            for i, shape in enumerate(OUT_SHAPES)]
    build(nc, args, outs)
    r = _run(nc, [arrays], core_ids=[0])
    return tuple(r.results[0][f"out_{i}_dram"] for i in range(len(OUT_SHAPES)))
```

```python
from contextlib import ExitStack

import numpy as np
import concourse.bass as bass
from concourse import mybir

ALU = mybir.AluOpType
ACT = mybir.ActivationFunctionType
AX_X = mybir.AxisListType.X
F32 = mybir.dt.float32
F32R = mybir.dt.float32r
I32 = mybir.dt.int32

P = 128
D = 1024
KD = D // P
SEQ = 1024
NB = 8
TS = 8
NS = NB * TS
T = SEQ + NS
TT = (T + P - 1) // P
TPAD = TT * P
NPAGE = 32
PAGE = 128
NPOOL = 320
H = 6
HD = 64
AW = H * HD
A_COLS = 3 * AW + 256
A_TILES = A_COLS // P
RANK = 256
ROPE = 32
CW = 256
PRE = 15
DFF = 2816
FT = DFF // P
EPS = 1e-6
GN_EPS = HD * 1e-5
SCALE = float(HD + ROPE) ** -0.5
CHUNK = 64
DECAY = -float(np.exp(-0.5))
CH = [(0, 384), (384, 384), (768, 320)]
NEG = -1e30

OUT_SHAPES = [(1, SEQ, D), (NB, TS, D), (1, 1, SEQ, RANK), (1, 1, SEQ, ROPE), (1, 1, H, HD, HD), (1, 1, A_COLS),
              (1, 1, PRE, CW), (1, 1, 2, DFF), (1, NB, TS, RANK), (1, NB, TS, ROPE), (1, NB, H, HD, HD),
              (1, NB, A_COLS), (1, NB, PRE, CW), (1, NB, 2, DFF)]

VEC = {}
for _name, _n in (("mu_shift", 11), ("decay_w0", 3), ("iclr_a0", 3), ("k_k", 3), ("k_a", 3), ("r_k", 3),
                  ("kv_norm_g", 2), ("pool_scale", 2), ("norm_ffn_g", 8), ("conv_b", 22), ("conv_w", 66)):
    VEC[_name] = (sum(n for _, n in VEC.values()), _n)
NVEC = sum(n for _, n in VEC.values())

CONST = {}
for _name, _n in (("ident", P), ("ones", P), ("head_ones", P), ("rot", P), ("keep_p", 2 * P), ("keep_s", 2 * P),
                  ("diag_p", P), ("diag_s", P), ("eye_pair", P), ("off_p", P),
                  ("causal", P), ("inv_w", 2), ("inv_cnt", 32), ("seq_of", 8), ("head_sel", 2)):
    CONST[_name] = (sum(n for _, n in CONST.values()), _n)
NCONST = sum(n for _, n in CONST.values())


def constants():
    f = np.float32
    c = np.zeros((P, NCONST), f)

    def put(name, a):
        c[:, CONST[name][0]:CONST[name][0] + CONST[name][1]] = a

    i = np.arange(P)
    s, t = i[:, None], i[None, :]
    put("ident", s == t)
    put("ones", 1.0)
    put("head_ones", s // HD == t // HD)
    rot = np.zeros((P, P), f)
    for m in range(P):
        if m % ROPE < ROPE // 2:
            rot[m + ROPE // 2, m] = -1.0
        else:
            rot[m - ROPE // 2, m] = 1.0
    put("rot", rot)
    for tag, chunk, block in (("p", CHUNK, 16), ("s", TS, TS)):
        same = s // chunk == t // chunk
        put("keep_" + tag, np.concatenate([same & (s < t), same & (s <= t)], 1))
        put("diag_" + tag, s // block == t // block)
    put("off_p", s // 16 != t // 16)
    put("eye_pair", s % HD == t % HD)
    put("causal", np.where(t <= s, 0.0, NEG))
    win = np.array([[2, 8], [4, 16]], f)[i // HD]
    put("inv_w", 1.0 / win)
    pos = np.arange(16)
    put("inv_cnt", (win[:, :, None] / np.minimum(pos[None, None] + 1, win[:, :, None])).reshape(P, 32))
    put("seq_of", (i[:, None] // TS == np.arange(NB)[None]) & (i[:, None] < NS))
    put("head_sel", (i[:, None] // HD == np.arange(2)[None]))
    pos = np.concatenate([np.arange(SEQ), NPAGE * PAGE + np.tile(np.arange(TS), NB)]).astype(f)
    inv = (f(10000.0) ** (-np.arange(0, ROPE, 2, dtype=f) / f(ROPE))).astype(f)
    ang = (pos[:, None] * inv[None]).astype(f)
    rope = np.stack([np.tile(np.cos(ang).T, (8, 1)), np.tile(np.sin(ang).T, (8, 1))], 1).astype(f)
    fresh = np.ones((P, TPAD), f)
    fresh[:, 0:SEQ:CHUNK] = 0.0
    fresh[:, SEQ::TS] = 0.0
    key = np.arange(NS)
    row = np.arange(P)
    seq = np.arange(NB // 2)[None, :] + NB // 2 * (row[:, None] // HD)
    new = (key // TS == seq[:, :, None]) & (key % TS <= row[:, None, None] % TS)
    newmask = np.where(new, 0.0, NEG).astype(f).reshape(P, NB // 2 * NS)
    heads = np.zeros((P, 3, 32 + P), f)
    for m in range(3):
        for half in range(2):
            heads[HD * half:HD * half + HD, m, 2 * m + half] = 1.0
            heads[2 * m + half:96:32, m, 32 + HD * half:32 + HD * half + HD] = 1.0
    return {"c_heads": heads, "c_const": c, "c_rope": rope, "c_fresh": fresh, "c_newmask": newmask}


def build(nc, I, outs, upto="all"):
    (y_prompt, y_sample, kv_p, kr_p, wkv_p, shift_p, pool_p, conv_p, kv_s, kr_s, wkv_s, shift_s, pool_s,
     conv_s) = outs
    ctx = ExitStack()
    with ctx:
        def sb(name, words, dt=F32, parts=P):
            return ctx.enter_context(nc.sbuf_tensor(name, [parts, words], dt))

        stage_sems = []

        def sem(name):
            stage_sems.append(nc.alloc_semaphore(name))
            return stage_sems[-1]

        YR = 6
        s_po, s_wo, s_co = (nc.alloc_semaphore(n) for n in ("pool_shift_out", "states_out", "history_out"))
        s_nat = nc.alloc_semaphore("rows_out")
        s_y = [nc.alloc_semaphore(f"final_out{i}") for i in range(YR)]

        s_xo = [nc.alloc_semaphore(f"x_spilled{i}") for i in range(3)]
        w_in_sem, s_w, s_wu = ([nc.alloc_semaphore(f"{n}{i}") for i in range(k)]
                               for n, k in (("w_in_in", 2), ("w_out_in", 2), ("w_ffn_in", 3)))

        def new_stage():
            nc.clear_and_free_semaphores(list(stage_sems))
            stage_sems.clear()
            nc.all_engine_barrier()

        PS = [ctx.enter_context(nc.psum_tensor(f"bank{i}", [P, 512], F32)) for i in range(8)]

        R0 = 0
        RA = R0 + KD * T
        RS = RA + KD * T
        RC = RS + A_TILES * TPAD
        RW = RC + (NCONST + 7) // 8 * 8
        RM = RW + 4 * KD * P
        RK_ = RM + 1632
        WORK = 15296
        arena = sb("arena", RK_ + WORK)
        base = 16512

        def lay(name, word, words, dt=F32):
            assert word % 8 == 0 and word + words <= RK_ + WORK, (name, word, words)
            return nc.alloc_sbuf_tensor_at(name, [P, words], dt, offset=base + 4 * word)

        res = lay("residualT", R0, KD * T)
        actA = lay("mixedT", RA, KD * T)
        sT_ = lay("rwkv_streamsT", RS, A_TILES * TPAD)
        con = lay("constants", RC, NCONST)
        wring = lay("weight_ring", RW, 4 * KD * P)
        small = lay("small", RM, 1632)
        work = lay("work", RK_, WORK)

        xT = res[:, :].rearrange("p (k t) -> p k t", k=KD)
        mixT = actA[:, :].rearrange("p (k t) -> p k t", k=KD)
        sT = sT_[:, :].rearrange("p (m t) -> p m t", m=A_TILES)
        spill = nc.dram_tensor("residual_spill", (P, KD, T), F32, kind="Internal").ap()

        def tiled(ap, k=KD):
            return ap.rearrange("p (k t) -> p k t", k=k)

        def split_pair(name, word_hi, word_lo, words, k):
            hi, lo = lay(name + "_hi", word_hi, words, F32R), lay(name + "_lo", word_lo, words, F32R)
            return tiled(hi[:, :], k), tiled(lo[:, :], k)

        def product(pe, out, w, x, first, last):
            pe.matmul(out, w[0], x[0], start=first, stop=False)
            pe.matmul(out, w[1], x[0], start=False, stop=False)
            return pe.matmul(out, w[0], x[1], start=False, stop=last)

        def C(name):
            return con[:, CONST[name][0]:CONST[name][0] + CONST[name][1]]

        ident, ones = C("ident"), C("ones")
        at = [0]

        def piece(n):
            at[0] += n
            assert at[0] <= 1632, at
            return small[:, at[0] - n:at[0]]

        vecs = piece(NVEC + 2)[:, 0:NVEC]
        shiftT = piece(A_TILES * NB).rearrange("p (m b) -> p m b", m=A_TILES)
        lnx = piece(6)
        poolT = piece(2 * 120).rearrange("p (m q) -> p m q", m=2)
        convT = piece(FT * 16).rearrange("p (m q) -> p m q", m=FT)
        stat = piece(32)
        epsc = piece(4)
        ckv_new = piece(RANK)[0:NS, :]
        ckvT_new = piece(2 * NS).rearrange("p (k t) -> p k t", k=2)
        krT_new = piece(NS)
        halves = piece(12)
        shift_out = piece(9 * A_TILES).rearrange("p (j m) -> p j m", m=A_TILES)

        def vec(name, k):
            return vecs[:, VEC[name][0] + k:VEC[name][0] + k + 1]

        def chain(eng, signal):
            count = [0]

            def link(ins):
                count[0] += 1
                ins.then_inc(signal, 1)
                eng.wait_ge(signal, count[0])
            return link

        class Carve:
            def __init__(self, base=0):
                self.at = base

            def take(self, n):
                self.at += n
                assert self.at <= WORK, self.at
                return work[:, self.at - n:self.at]

        xn = split_pair("normedT", R0, RA, KD * T, KD)
        XR = A_TILES * TPAD - 3 * D
        xraw = [sT_[:, XR + i * D:XR + (i + 1) * D].rearrange("p (k t) -> p k t", k=KD) for i in range(3)]
        w_in_raw = [tiled(work[:, WORK - (2 - i) * KD * P:][:, 0:KD * P]) for i in range(2)]
        c_hi = sem("norm_hi")
        STATES_AT = 4
        cw = Carve()
        XS = 4
        xin = [cw.take(D) for _ in range(XS)]
        xsc = [cw.take(D) for _ in range(2)]
        sq_junk = cw.take(D)
        g_rows = cw.take(D)
        vrows = cw.take(P)
        shrows = cw.take(A_COLS)
        cvrows = cw.take(DFF)
        plrows = cw.take(CW)
        s_const, s_vec, s_st, s_g = sem("consts_in"), sem("vectors_in"), sem("states_in"), sem("gain_in")
        s_x = [sem(f"x_in{i}") for i in range(XS)]
        x_sq, x_rt, x_rs, x_sc = sem("x_squared"), sem("x_root"), sem("x_recip"), sem("x_scaled")
        t_raw, t_nrm, c_nrm = sem("raw_turned"), sem("norm_turned"), sem("norm_copied")
        c_raw = [sem(f"raw_copied{j}") for j in range(2)]
        t_vec, c_vec, t_st, c_st = sem("vec_turned"), sem("vec_copied"), sem("state_turned"), sem("state_copied")
        s_eps = sem("eps_set")

        def rows_of(i):
            return P if i < TT - 1 else NS

        with nc.Block() as block:
            def copy_raw(eng_copy, eng, i, j):
                n = rows_of(i)
                eng.wait_ge(t_raw, i + 1)
                if i >= 3:
                    eng.wait_ge(s_xo[i % 3], 16 * (i // 3))
                eng_copy(xraw[i % 3][:, 4 * j:4 * j + 4, 0:n],
                         tiled(PS[4 * (i % 2) + j][:, :], 4)[:, :, 0:n]).then_inc(c_raw[j], 1)

            def spill_x(sp, i):
                n = rows_of(i)
                for j in range(2):
                    sp.wait_ge(c_raw[j], i + 1)
                sp.dma_start(spill[:, :, i * P:i * P + n], xraw[i % 3][:, :, 0:n]).then_inc(s_xo[i % 3], 16)

            def norm_hi(act, i):
                n = rows_of(i)
                act.wait_ge(t_nrm, i + 1)
                for j in range(2):
                    nc.scalar.copy(xn[0][:, 4 * j:4 * j + 4, i * P:i * P + n],
                                   tiled(PS[4 * (i % 2) + 2 + j][:, :], 4)[:, :, 0:n]).then_inc(c_hi, 1)

            def norm_lo(dve, i):
                n = rows_of(i)
                for j in range(2):
                    dve.wait_ge(c_hi, 2 * i + j + 1)
                    at_ = (slice(None), slice(4 * j, 4 * j + 4), slice(i * P, i * P + n))
                    dve.tensor_tensor(xn[1][at_], tiled(PS[4 * (i % 2) + 2 + j][:, :], 4)[:, :, 0:n],
                                      xn[0][at_].bitcast(F32), ALU.subtract).then_inc(c_nrm, 1)

            @block.sync
            def _(sp):
                for i in range(TT):
                    n = rows_of(i)
                    if i >= XS:
                        sp.wait_ge(t_raw, i - XS + 1)
                        sp.wait_ge(x_sc, i - XS + 1)
                    src = I["x_prompt"][0, i * P:(i + 1) * P, :] if i < TT - 1 else \
                        I["x_sample"].rearrange("b t d -> (b t) d")
                    sp.dma_start(xin[i % XS][0:n, :], src).then_inc(s_x[i % XS], 16)
                    if i == 0:
                        sp.dma_start(con[:, :], I["c_const"]).then_inc(s_const, 16)
                    if i >= 3:
                        spill_x(sp, i - 3)
                for i in range(2):
                    sp.dma_start(w_in_raw[i], I["w_in"][0].rearrange("(k p) c -> p k c", p=P)[:, :, i * P:(i + 1) * P]
                                 ).then_inc(w_in_sem[i], 16)
                for i in range(TT - 3, TT):
                    spill_x(sp, i)

            @block.scalar
            def _(act):
                act.dma_start(g_rows, I["norm_mix_g"][0, :].partition_broadcast(P)).then_inc(s_g, 16)
                act.wait_ge(s_eps, 1)
                for i in range(TT):
                    n = rows_of(i)
                    act.wait_ge(s_x[i % XS], 16 * (i // XS + 1))
                    if i >= 1:
                        act.wait_ge(x_sq, i)
                    nc.scalar.activation(sq_junk[0:n, :], xin[i % XS][0:n, :], ACT.Square,
                                         accum_out=stat[0:n, i:i + 1]).then_inc(x_sq, 1)
                    act.wait_ge(x_sq, i + 1)
                    nc.scalar.activation(stat[0:n, 10 + i:11 + i], stat[0:n, i:i + 1], ACT.Sqrt,
                                         bias=epsc[0:n, 0:1], scale=1.0 / D).then_inc(x_rt, 1)
                    if i >= 1:
                        copy_raw(nc.scalar.copy, act, i - 1, 0)
                        norm_hi(act, i - 1)
                copy_raw(nc.scalar.copy, act, TT - 1, 0)
                norm_hi(act, TT - 1)

            @block.gpsimd
            def _(pool):
                for name, (a, n) in VEC.items():
                    src = I[name]
                    src = src.rearrange({2: "l d -> (l d)", 3: "l a d -> (l a d)"}[len(src.shape)])
                    pool.dma_start(vrows[a:a + n, :], src.rearrange("(a p) -> a p", p=P)).then_inc(s_vec, 16)
                pool.dma_start(shrows[0:NB, :], I["state_shift"][0]).then_inc(s_st, 16)
                pool.dma_start(plrows[0:120, :], I["state_pool"][0].rearrange("b t c -> (b t) c")).then_inc(s_st, 16)
                for j, name in enumerate(("lnx_w", "lnx_b")):
                    pool.dma_start(plrows[120 + 3 * j:123 + 3 * j, 0:P],
                                  I[name][0].rearrange("(a p) -> a p", p=P)).then_inc(s_st, 16)
                pool.dma_start(cvrows[0:16, :], I["state_conv"][0].rearrange("b t c -> (b t) c")).then_inc(s_st, 16)

            @block.vector
            def _(dve):
                def copy_states():
                    dve.wait_ge(t_vec, 1)
                    dve.tensor_copy(vecs, PS[6][:, 0:NVEC]).then_inc(c_vec, 1)
                    dve.wait_ge(t_st, 1)
                    dve.tensor_copy(shiftT, PS[6][:, 128:216].rearrange("p (m b) -> p m b", b=NB)).then_inc(c_st, 1)
                    dve.tensor_copy(poolT[:, 0], PS[6][:, 216:336])
                    dve.tensor_copy(lnx, PS[6][:, 336:342])
                    dve.tensor_copy(poolT[:, 1], PS[6][:, 342:462]).then_inc(c_st, 1)
                    dve.tensor_copy(convT, PS[7][:, 0:352].rearrange("p (m q) -> p m q", m=FT)).then_inc(c_st, 1)

                dve.memset(epsc[:, 0:1], EPS)
                dve.memset(epsc[:, 1:2], GN_EPS)
                dve.memset(epsc[:, 2:3], 1e-24).then_inc(s_eps, 1)
                dve.wait_ge(s_g, 16)
                for i in range(TT):
                    n = rows_of(i)
                    dve.wait_ge(x_rt, i + 1)
                    dve.reciprocal(stat[0:n, 20 + i:21 + i], stat[0:n, 10 + i:11 + i]).then_inc(x_rs, 1)
                    dve.wait_ge(x_rs, i + 1)
                    if i >= 2:
                        dve.wait_ge(t_nrm, i - 1)
                    dve.scalar_tensor_tensor(out=xsc[i % 2][0:n, :], in0=xin[i % XS][0:n, :],
                                             scalar=stat[0:n, 20 + i:21 + i], in1=g_rows[0:n, :],
                                             op0=ALU.mult, op1=ALU.mult).then_inc(x_sc, 1)
                    if i >= 1:
                        copy_raw(dve.tensor_copy, dve, i - 1, 1)
                        norm_lo(dve, i - 1)
                    if i == STATES_AT:
                        copy_states()
                copy_raw(dve.tensor_copy, dve, TT - 1, 1)
                norm_lo(dve, TT - 1)

            @block.tensor
            def _(pe):
                def turn_states():
                    pe.wait_ge(c_nrm, 2 * STATES_AT)
                    pe.wait_ge(s_vec, 16 * len(VEC))
                    pe.transpose(PS[6][:, 0:NVEC], vrows[0:NVEC, :], ident[0:NVEC, 0:NVEC]).then_inc(t_vec, 1)
                    pe.wait_ge(s_st, 80)
                    pe.wait_ge(c_vec, 1)
                    for m in range(A_TILES):
                        pe.transpose(PS[6][:, 128 + NB * m:128 + NB * m + NB], shrows[0:NB, m * P:(m + 1) * P],
                                     ident[0:NB, 0:NB])
                    for m, n in enumerate((126, 120)):
                        pe.transpose(PS[6][:, 216 + 126 * m:216 + 126 * m + n], plrows[0:n, m * P:(m + 1) * P],
                                     ident[0:n, 0:n])
                    for m in range(FT):
                        last = pe.transpose(PS[7][:, 16 * m:16 * m + 16], cvrows[0:16, m * P:(m + 1) * P],
                                            ident[0:16, 0:16])
                    last.then_inc(t_st, 1)

                pe.wait_ge(s_const, 16)
                for i in range(TT):
                    n = rows_of(i)
                    for which, (src, b0) in enumerate(((xin[i % XS], 0), (xsc[i % 2], 2))):
                        if which == 0:
                            pe.wait_ge(s_x[i % XS], 16 * (i // XS + 1))
                        else:
                            pe.wait_ge(x_sc, i + 1)
                            if i == STATES_AT + 1:
                                pe.wait_ge(c_st, 3)
                        if i >= 2 and which == 0:
                            for j in range(2):
                                pe.wait_ge(c_raw[j], i - 1)
                        elif i >= 2:
                            pe.wait_ge(c_nrm, 2 * (i - 1))
                        for k in range(KD):
                            bank = PS[4 * (i % 2) + b0 + k // 4]
                            last = pe.transpose(bank[:, (k % 4) * P:(k % 4) * P + n], src[0:n, k * P:(k + 1) * P],
                                                ident[0:n, 0:n])
                        last.then_inc(t_raw if which == 0 else t_nrm, 1)
                    if i == STATES_AT:
                        turn_states()
        if upto == "load":
            return

        new_stage()
        A, B = A_COLS, A_COLS + 864
        tiles = [([(m * P, P)], ("rwkv", m)) for m in range(A_TILES)]
        tiles += [([(B + m * P, P)], ("pool", m)) for m in range(2)]
        tiles += [([(A + m * P, P)], ("qn", m)) for m in range(3)]
        tiles += [([(A + 384, P)], ("rope", 0)), ([(A + 512, 64), (A + 832, 32)], ("rope", 1)),
                  ([(A + 576, P)], ("ckv", 0)), ([(A + 704, P)], ("ckv", 1))]
        cw = Carve()
        ckv = cw.take(2 * T).rearrange("p (k t) -> p k t", k=2)
        rp = cw.take(2 * T).rearrange("p (k t) -> p k t", k=2)
        qn = cw.take(3 * T).rearrange("p (k t) -> p k t", k=3)
        mla_end = cw.at
        LW = PRE + SEQ + NB * (PRE + TS)
        PW = 1 + SEQ + NB * (TS + 1)
        sumA, sumB = cw.take(LW), cw.take(LW)
        pring = [work[:, mla_end + i * PW:mla_end + (i + 1) * PW] for i in range(2)]
        assert PW <= LW
        pl = cw.take(2 * LW).rearrange("p (m w) -> p m w", m=2)
        po = cw.take(270)
        po_p, po_s = po[:, 0:30], po[:, 30:270]
        ends = sem("pool_steps")
        w_in = I["w_in"][0].rearrange("(k p) c -> p k c", p=P)
        assert cw.at <= WORK - 2 * KD * P
        wraw = w_in_raw
        w_hi, w_lo = sem("w_in_hi"), sem("w_in_lo")
        widths = [sum(n for _, n in c) for c, _ in tiles]
        proj_mm, proj_cp, mixed, prep, diffed = (sem("proj_ready"), sem("proj_copied"), sem("shift_mixed"),
                                                 sem("prefix_set"), sem("shift_diff"))
        pieces = [len(c) for c, _ in tiles]

        def seg(ap, pre):
            return (ap[:, pre:pre + SEQ],
                    ap[:, pre + SEQ:pre + SEQ + NB * (pre + TS)].rearrange("p (b w) -> p b w", b=NB))

        wsp = [split_pair(f"w{i}", RW + i * 2 * KD * P, RW + (i * 2 + 1) * KD * P, KD * P, KD) for i in range(2)]

        def split_hi(i, m, raw, done, free, per):
            act = nc.scalar
            if i >= 2:
                act.wait_ge(free, per * (i - 1))
            act.copy(wsp[i % 2][0][:, 0:m[0], 0:m[1]], raw[:, 0:m[0], 0:m[1]]).then_inc(done, 1)

        def split_lo(i, m, raw, hi_done, done):
            dve = nc.vector
            dve.wait_ge(hi_done, i + 1)
            dve.tensor_tensor(wsp[i % 2][1][:, 0:m[0], 0:m[1]], raw[:, 0:m[0], 0:m[1]],
                              wsp[i % 2][0][:, 0:m[0], 0:m[1]].bitcast(F32), ALU.subtract).then_inc(done, 1)

        with nc.Block() as block:
            def in_hi(act, i):
                act.wait_ge(w_in_sem[i % 2], 16 * sum(pieces[i % 2:i + 1:2]))
                split_hi(i, (KD, widths[i]), wraw[i % 2], w_hi, proj_mm, 3)

            def in_lo(dve, i):
                split_lo(i, (KD, widths[i]), wraw[i % 2], w_hi, w_lo)

            @block.sync
            def _(sp):
                for i, (cols, _) in enumerate(tiles):
                    if i < 2:
                        continue
                    sp.wait_ge(w_lo, i - 1)
                    o = 0
                    for c, n in cols:
                        sp.dma_start(wraw[i % 2][:, :, o:o + n], w_in[:, :, c:c + n]).then_inc(w_in_sem[i % 2], 16)
                        o += n

            @block.tensor
            def _(pe):
                for i, (cols, _) in enumerate(tiles):
                    m = sum(n for _, n in cols)
                    pe.wait_ge(w_lo, i + 1)
                    for c, (t0, n) in enumerate(CH):
                        g = 3 * i + c
                        if g >= 8:
                            pe.wait_ge(proj_cp, g - 7)
                        for k in range(KD):
                            last = product(pe, PS[g % 8][0:m, 0:n], [w[:, k, 0:m] for w in wsp[i % 2]],
                                           [x[:, k, t0:t0 + n] for x in xn], k == 0, k == KD - 1)
                        last.then_inc(proj_mm, 1)

            @block.scalar
            def _(act):
                in_hi(act, 0)
                for i, (cols, (kind, j)) in enumerate(tiles):
                    if i + 1 < len(tiles):
                        in_hi(act, i + 1)
                    m = sum(n for _, n in cols)
                    if kind == "rwkv":
                        act.wait_ge(prep, 1)
                        if j >= 2:
                            act.wait_ge(mixed, j - 1)
                        p_seq, s_seq = seg(pring[j % 2], 1)
                        s_seq = s_seq[:, :, 1:]
                    elif kind == "pool":
                        p_seq, s_seq = seg(pl[:, j], PRE)
                        s_seq = s_seq[:, :, PRE:]
                    else:
                        dst = {"qn": qn, "rope": rp, "ckv": ckv}[kind][:, j]
                        p_seq, s_seq = dst[0:m, 0:SEQ], dst[0:m, SEQ:T]
                    for c, (t0, n) in enumerate(CH):
                        g = 3 * i + c
                        act.wait_ge(proj_mm, g + 1)
                        bank = PS[g % 8]
                        k = min(n, SEQ - t0)
                        ins = nc.scalar.copy(p_seq[0:m, t0:t0 + k], bank[0:m, 0:k])
                        if c == 2:
                            src = bank[0:m, k:k + NS]
                            if kind in ("rwkv", "pool"):
                                src = src.rearrange("p (b t) -> p b t", b=NB)
                            ins = nc.scalar.copy(s_seq, src)
                        ins.then_inc(proj_cp, 1)

            @block.gpsimd
            def _(pool):
                for j in range(2):
                    nc.gpsimd.memset(pring[j][:, 0:1], 0.0)
                    nc.gpsimd.memset(pl[:, j, 0:PRE], 0.0)
                for j in range(3):
                    pool.wait_ge(s_xo[j], 48)
                nc.gpsimd.memset(sT[:, :, T:TPAD], 0.0).then_inc(prep, 1)
                for j in range(2):
                    nc.gpsimd.tensor_copy(seg(pl[:, j], PRE)[1][:, :, 0:PRE],
                                          poolT[:, j].rearrange("p (b t) -> p b t", b=NB)).then_inc(prep, 1)

            @block.vector
            def _(dve):
                in_lo(dve, 0)
                in_lo(dve, 1)
                for m in range(A_TILES):
                    buf = pring[m % 2]
                    p_cur, s_all = seg(buf, 1)
                    dve.tensor_copy(s_all[:, :, 0], shiftT[:, m, :]).then_inc(diffed, 1)
                    dve.wait_ge(diffed, 3 * m + 1)
                    dve.wait_ge(proj_cp, 3 * (m + 1))
                    dve.wait_ge(prep, 1)
                    s_new = sT[:, m, SEQ:T].rearrange("p (b t) -> p b t", b=NB)
                    dve.tensor_tensor(sT[:, m, 0:SEQ], buf[:, 0:SEQ], p_cur, ALU.subtract).then_inc(diffed, 1)
                    dve.tensor_tensor(s_new, s_all[:, :, 0:TS], s_all[:, :, 1:], ALU.subtract).then_inc(diffed, 1)
                    dve.tensor_copy(shift_out[:, 0:1, m], p_cur[:, SEQ - 1:SEQ])
                    dve.tensor_copy(shift_out[:, 1:9, m], s_all[:, :, TS])
                    dve.wait_ge(diffed, 3 * m + 3)
                    dve.scalar_tensor_tensor(out=sT[:, m, 0:SEQ], in0=sT[:, m, 0:SEQ], scalar=vec("mu_shift", m),
                                             in1=p_cur, op0=ALU.mult, op1=ALU.add)
                    dve.scalar_tensor_tensor(out=s_new, in0=s_new, scalar=vec("mu_shift", m), in1=s_all[:, :, 1:],
                                             op0=ALU.mult, op1=ALU.add).then_inc(mixed, 1)
                    in_lo(dve, m + 2)
                link = chain(dve, ends)

                def tails(m):
                    u = pl[:, m]
                    dve.wait_ge(prep, 3)
                    dve.wait_ge(proj_cp, 3 * (A_TILES + m + 1))
                    dve.tensor_copy(po_p.rearrange("p (t m) -> p t m", m=2)[:, :, m], u[:, SEQ:PRE + SEQ])
                    link(dve.tensor_copy(po_s.rearrange("p (b t m) -> p b t m", b=NB, m=2)[:, :, :, m],
                                         seg(u, PRE)[1][:, :, TS:]))

                def window_sums(m):
                    u = pl[:, m]
                    link(dve.tensor_tensor(sumA[:, 1:], u[:, 1:], u[:, :LW - 1], ALU.add))
                    link(dve.tensor_tensor(sumB[:, 3:], sumA[:, 3:], sumA[:, 1:LW - 2], ALU.add))
                    if m == 1:
                        link(dve.tensor_tensor(sumA[:, 7:], sumB[:, 7:], sumB[:, 3:LW - 4], ALU.add))
                        link(dve.tensor_tensor(sumB[HD:, 15:], sumA[HD:, 15:], sumA[HD:, 7:LW - 8], ALU.add))

                def differences(m):
                    u = pl[:, m]
                    for r, src in ((0, sumA), (HD, sumB)):
                        rows = slice(r, r + HD)
                        link(dve.tensor_tensor(src[rows, PRE:PRE + 16], src[rows, PRE:PRE + 16],
                                               C("inv_cnt")[rows, 16 * m:16 * m + 16], ALU.mult))
                        for part in range(2):
                            x, w = seg(u, PRE)[part][rows], seg(src, PRE)[part][rows]
                            if part == 1:
                                x, w = x[:, :, PRE:], w[:, :, PRE:]
                            link(dve.scalar_tensor_tensor(out=x, in0=w, scalar=C("inv_w")[rows, m:m + 1], in1=x,
                                                          op0=ALU.mult, op1=ALU.subtract))

                for i in range(A_TILES + 2, len(tiles)):
                    in_lo(dve, i)
                    if i in (A_TILES + 3, A_TILES + 5):
                        m = (i - A_TILES - 3) // 2
                        tails(m)
                        window_sums(m)
                    elif i in (A_TILES + 4, A_TILES + 6):
                        differences((i - A_TILES - 4) // 2)
        if upto == "proj":
            return

        new_stage()
        cw = Carve(mla_end)
        vnat = cw.take(8 * AW).rearrange("p (i c) -> p i c", i=8)
        at4 = [0]

        def free(n):
            at4[0] += n
            assert at4[0] <= 7936
            return res[:, at4[0] - n:at4[0]]

        nat = free(TT * 288).rearrange("p (i c) -> p i c", i=TT)
        sqc = free(2 * T).rearrange("p (k t) -> p k t", k=2)
        rinv = free(T)
        pool_w = free(256).rearrange("p (m c) -> p m c", m=2)
        po_nat = free(3 * P).rearrange("p (q c) -> p q c", q=3)
        sh_nat = free(P)
        s_pw0, s_pw, pool_mm, pool_cp, po_t, po_cp = (
            sem("pool_w_cleared"), sem("pool_w_in"), sem("pool_product"), sem("pool_scaled"),
            sem("pool_tail_turned"), sem("pool_tail_copied"))
        cs = wring[:, 0:2 * T].rearrange("p (a t) -> p a t", a=2)
        rot_sin = wring[:, 2 * T:3 * T]
        w_uv = wring[:, 3 * T:3 * T + 768].rearrange("p (k c) -> p k c", k=2)
        spare = actA[:, 0:3 * T]
        w_uk = res[:, 7936:8704].rearrange("p (k c) -> p k c", k=2)
        s_cs, s_wk, c_sq, c_sum, c_rt, c_ri, c_n, r_mm, r_sin, r_cos, r_done = (
            sem("angles_in"), sem("w_latent_in"), sem("latent_squared"), sem("latent_summed"),
            sem("latent_root"), sem("latent_recip"), sem("latent_normed"), sem("rotated"), sem("sin_part"),
            sem("cos_part"), sem("rope_done"))
        v_mm, v_cp, n_t, n_cp = (sem("values_ready"), sem("values_copied"), sem("rows_turned"),
                                 sem("rows_copied"))
        s_kn = sem("new_keys_cleared")
        rope_jobs = [(a, c) for a in (1, 0) for c in range(3)]
        with nc.Block() as block:
            @block.sync
            def _(sp):
                sp.dma_start(cs, I["c_rope"]).then_inc(s_cs, 16)
                sp.wait_ge(s_pw0, 1)
                for g in range(4):
                    r = HD * (g % 2)
                    sp.dma_start(pool_w[r:r + HD, g // 2, r:r + HD], I["pool_w"][0, g]).then_inc(s_pw, 16)
                sp.dma_start(w_uk, I["w_uk"][0].rearrange("(k p) h d -> p k (h d)", p=P)).then_inc(s_wk, 16)
                sp.dma_start(w_uv, I["w_uv"][0].rearrange("(k p) h d -> p k (h d)", p=P)).then_inc(s_wk, 16)
                sp.wait_ge(po_cp, 4)
                sp.dma_start(pool_p[0, 0].rearrange("t (m c) -> (t m) c", m=2), po_nat[0:30, 0]).then_inc(s_po, 16)
                flat = pool_s[0].rearrange("b t (m c) -> (b t m) c", m=2)
                for q in range(2):
                    sp.dma_start(flat[120 * q:120 * q + 120, :], po_nat[0:120, 1 + q]).then_inc(s_po, 16)
                sp.dma_start(shift_p[0].rearrange("a (m c) -> (a m) c", c=P), sh_nat[0:A_TILES, :]).then_inc(s_po, 16)
                sp.dma_start(shift_s[0].rearrange("b (m c) -> (b m) c", c=P),
                             sh_nat[A_TILES:9 * A_TILES, :]).then_inc(s_po, 16)
                for i in range(0, TT - 1, 4):
                    sp.wait_ge(n_cp, i + 4)
                    rows = slice(i * P, (i + 4) * P)
                    for dst, cols in ((kv_p, slice(0, RANK)), (kr_p, slice(RANK, RANK + ROPE))):
                        sp.dma_start(dst[0, 0, rows, :].rearrange("(i p) c -> p i c", p=P),
                                     nat[:, i:i + 4, cols]).then_inc(s_nat, 16)
                sp.wait_ge(n_cp, TT)
                sp.dma_start(kv_s[0].rearrange("b t c -> (b t) c"), nat[0:NS, TT - 1, 0:RANK]).then_inc(s_nat, 16)
                sp.dma_start(kr_s[0].rearrange("b t c -> (b t) c"), nat[0:NS, TT - 1, RANK:]).then_inc(s_nat, 16)
                sp.wait_ge(s_po, 80)

            @block.scalar
            def _(act):
                nc.scalar.activation(sqc, ckv, ACT.Square).then_inc(c_sq, 1)
                for c, (t0, n) in enumerate(CH):
                    act.wait_ge(c_sum, c + 1)
                    nc.scalar.activation(rinv[:, t0:t0 + n], PS[c][:, 0:n], ACT.Sqrt, bias=epsc[:, 0:1],
                                         scale=1.0 / RANK).then_inc(c_rt, 1)
                act.wait_ge(po_t, 4)
                for q, n in enumerate((30, 120, 120, 99)):
                    dst = po_nat[0:n, q] if q < 3 else sh_nat[0:n, :]
                    nc.scalar.copy(dst, PS[6][0:n, q * P:q * P + P]).then_inc(po_cp, 1)
                for m in range(2):
                    for c, (t0, n) in enumerate(CH):
                        act.wait_ge(pool_mm, 3 * m + c + 1)
                        nc.scalar.activation(mixT[:, 6 + m, t0:t0 + n], PS[(3, 0)[m] + c][:, 0:n], ACT.Copy,
                                             scale=vec("pool_scale", m)).then_inc(pool_cp, 1)
                for i in range(8):
                    act.wait_ge(v_mm, i + 1)
                    nc.scalar.copy(vnat[:, i], PS[i % 2][:, 0:AW]).then_inc(v_cp, 1)

            @block.gpsimd
            def _(pool):
                nc.gpsimd.memset(pool_w, 0.0).then_inc(s_pw0, 1)
                nc.gpsimd.memset(krT_new, 0.0).then_inc(s_kn, 1)
                pool.wait_ge(s_cs, 16)
                for j, (a, c) in enumerate(rope_jobs):
                    t0, n = CH[c]
                    m = P if a == 0 else 96
                    pool.wait_ge(r_mm, j + 1)
                    nc.gpsimd.tensor_tensor(rp[0:m, a, t0:t0 + n], rp[0:m, a, t0:t0 + n], cs[0:m, 0, t0:t0 + n],
                                            ALU.mult).then_inc(r_cos, 1)
                    pool.wait_ge(r_sin, j + 1)
                    pool.wait_ge(r_cos, j + 1)
                    nc.gpsimd.tensor_tensor(rp[0:m, a, t0:t0 + n], rp[0:m, a, t0:t0 + n], rot_sin[0:m, t0:t0 + n],
                                            ALU.add).then_inc(r_done, 1)
                pool.wait_ge(r_done, 6)
                pool.wait_ge(s_kn, 1)
                nc.gpsimd.tensor_copy(krT_new[64:96, :], rp[64:96, 1, SEQ:T])

            @block.vector
            def _(dve):
                dve.wait_ge(s_cs, 16)
                for c, (t0, n) in enumerate(CH):
                    dve.wait_ge(c_rt, c + 1)
                    dve.reciprocal(rinv[:, t0:t0 + n], rinv[:, t0:t0 + n]).then_inc(c_ri, 1)
                    dve.wait_ge(c_ri, c + 1)
                    for k in range(2):
                        dve.scalar_tensor_tensor(out=ckv[:, k, t0:t0 + n], in0=ckv[:, k, t0:t0 + n],
                                                 scalar=vec("kv_norm_g", k), in1=rinv[:, t0:t0 + n],
                                                 op0=ALU.mult, op1=ALU.mult).then_inc(c_n, 1)
                for j, (a, c) in enumerate(rope_jobs):
                    t0, n = CH[c]
                    m = P if a == 0 else 96
                    dve.wait_ge(r_mm, j + 1)
                    if j >= 3:
                        dve.wait_ge(r_done, j - 2)
                    dve.tensor_tensor(rot_sin[0:m, t0:t0 + n], PS[3 + j % 3][0:m, 0:n], cs[0:m, 1, t0:t0 + n],
                                      ALU.mult).then_inc(r_sin, 1)
                dve.wait_ge(c_n, 6)
                dve.tensor_copy(ckvT_new, ckv[:, :, SEQ:T])
                for i in range(TT):
                    n = rows_of(i)
                    dve.wait_ge(n_t, i + 1)
                    dve.tensor_copy(nat[0:n, i, :], PS[6 + i % 2][0:n, 0:288]).then_inc(n_cp, 1)
                    if i == TT - 1:
                        dve.tensor_copy(ckv_new, PS[6 + i % 2][0:n, 0:RANK]).then_inc(n_cp, 1)

            @block.tensor
            def _(pe):
                pe.wait_ge(c_sq, 1)
                for c, (t0, n) in enumerate(CH):
                    for k in range(2):
                        last = pe.matmul(PS[c][:, 0:n], ones, sqc[:, k, t0:t0 + n], start=(k == 0), stop=(k == 1))
                    last.then_inc(c_sum, 1)
                for q, src in enumerate((po_p, po_s[:, 0:120], po_s[:, 120:240], shift_out)):
                    if q == 3:
                        src = src.rearrange("p j m -> p (j m)")
                    n = src.shape[1]
                    pe.transpose(PS[6][0:n, q * P:q * P + P], src, ident).then_inc(po_t, 1)
                pe.wait_ge(s_pw, 64)
                for m in range(2):
                    for c, (t0, n) in enumerate(CH):
                        if m == 1:
                            pe.wait_ge(c_rt, c + 1)
                        k = min(n, SEQ - t0)
                        b = PS[(3, 0)[m] + c]
                        last = pe.matmul(b[:, 0:k], pool_w[:, m], pl[:, m, PRE + t0:PRE + t0 + k], start=True,
                                         stop=True)
                        if k < n:
                            last = pe.matmul(b[:, k:n].rearrange("p (b t) -> p b t", b=NB), pool_w[:, m],
                                             seg(pl[:, m], PRE)[1][:, :, PRE:], start=True, stop=True)
                        last.then_inc(pool_mm, 1)
                def turn_halves(jobs):
                    for j in jobs:
                        a, c = rope_jobs[j]
                        t0, n = CH[c]
                        m = P if a == 0 else 96
                        if j >= 3:
                            pe.wait_ge(r_sin, j - 2)
                        else:
                            pe.wait_ge(pool_cp, j + 1)
                        pe.matmul(PS[3 + j % 3][0:m, 0:n], C("rot")[0:m, 0:m], rp[0:m, a, t0:t0 + n], start=True,
                                  stop=True).then_inc(r_mm, 1)

                def values(tiles):
                    for i in tiles:
                        pe.wait_ge(c_n, 2 * (i * P // CH[0][1]) + 2)
                        if i >= 2:
                            pe.wait_ge(v_cp, i - 1)
                        for k in range(2):
                            last = pe.matmul(PS[i % 2][:, 0:AW], ckv[:, k, i * P:(i + 1) * P], w_uv[:, k],
                                             start=(k == 0), stop=(k == 1))
                        last.then_inc(v_mm, 1)

                turn_halves(range(3))
                pe.wait_ge(s_wk, 32)
                pe.wait_ge(pool_cp, 6)
                pe.wait_ge(po_cp, 4)
                values(range(6))
                turn_halves(range(3, 6))
                values(range(6, 8))
                for i in range(TT):
                    n = rows_of(i)
                    pe.wait_ge(r_done, i * P // CH[0][1] + 1)
                    if i >= 2:
                        pe.wait_ge(n_cp, i - 1)
                    for k in range(2):
                        pe.transpose(PS[6 + i % 2][0:n, k * P:(k + 1) * P], ckv[:, k, i * P:i * P + n], ident)
                    pe.transpose(PS[6 + i % 2][0:n, 256:288], rp[64:96, 1, i * P:i * P + n],
                                 ident[64:96, 64:96]).then_inc(n_t, 1)
        if upto == "latent":
            return

        NX = NB // 2
        NG = NPAGE // 4
        NPT = NG + 1
        NL = 5
        EARLY = 2
        loads = [(x, g) for x in range(NX) for g in range(NG)]
        kslot = [res[:, i * 1024:(i + 1) * 1024] for i in range(6)]
        kslot += [wring[:, i * 1024:(i + 1) * 1024] for i in range(4)]
        krr = res[:, 6144:6144 + 2 * NL * P].rearrange("p (s c) -> p s c", s=2 * NL)
        pages = res[:, 7424:7680].bitcast(I32)
        newmask = res[:, 7680:7936].rearrange("p (x c) -> p x c", x=NX)
        kv_pages = I["cache_kv_latent"][0].rearrange("n (p r) c -> n p (r c)", r=4)
        kr_pages = I["cache_k_rope"][0].rearrange("n (p r) c -> n p (r c)", r=4)
        s_pg, s_nm = nc.alloc_semaphore("page_table_in"), nc.alloc_semaphore("tables_in")
        s_k = [[nc.alloc_semaphore(f"rows_in{f}{i}") for i in range(NL)] for f in range(2)]
        s_kx = [nc.alloc_semaphore(f"rope_rows_in{i}") for i in range(NL)]

        def step_of(j):
            return j // NG * NPT + j % NG

        def load_page(eng, f, j, q):
            x, g = loads[j]
            at_ = (x + NX * f) * NPAGE + 4 * g + q
            return eng.value_load(pages[0:1, at_:at_ + 1], min_val=0, max_val=NPOOL - 1)

        def load_rows(eng, j, f, pages_of=range(4)):
            slot = 2 * (j % NL) + f
            for q in pages_of:
                page = load_page(eng, f, j, q)
                rows = slice(32 * q, 32 * q + 32)
                eng.dma_start(kslot[slot][rows], kv_pages[bass.ds(page, 1)].rearrange("a p c -> (a p) c")
                              ).then_inc(s_k[f][j % NL], 16)
                if f == 0 or q < 3:
                    eng.dma_start(krr[rows, slot, :], kr_pages[bass.ds(page, 1)].rearrange("a p c -> (a p) c")
                                  ).then_inc(s_k[f][j % NL], 16)
            if f == 0:
                page = load_page(eng, 1, j, 3)
                eng.dma_start(krr[96:P, slot + 1, :], kr_pages[bass.ds(page, 1)].rearrange("a p c -> (a p) c")
                              ).then_inc(s_kx[j % NL], 16)

        new_stage()
        cw = Carve(mla_end + 8 * AW)
        qcat = [cw.take(SEQ) for _ in range(4)]
        stat_a = cw.take(4 * 48).rearrange("p (a i) -> p a i", a=4)
        diag = [cw.take(P) for _ in range(2)]
        kcat = [spare[:, j * SEQ:(j + 1) * SEQ] for j in range(3)] + [kslot[4]]
        prob = [wring[:, j * SEQ:(j + 1) * SEQ] for j in range(2)] + [kslot[5]]
        probT = [wring[:, (4 + j) * 512:(5 + j) * 512] for j in range(4)]
        pairs = [(m, i) for m in range(3) for i in range(8)]
        NQ = len(pairs)
        units = [(q, b0) for q in range(NQ) for b0 in range(0, pairs[q][1] + 1, 4)]
        units_of = {q: [u for u, x in enumerate(units) if x[0] == q] for q in range(NQ)}

        ring, holder, banks_of, freed_by = [0], {}, {}, {}

        def take_banks(use, n):
            banks_of[use] = [(ring[0] + i) % 4 for i in range(n)]
            ring[0] += n
            freed_by[use] = [holder[b] for b in banks_of[use] if b in holder]
            for b in banks_of[use]:
                holder[b] = use

        def keys_before(q):
            if q == 0:
                return 0
            m, i = pairs[q]
            return m + 1 if i == 6 and m < 2 else None

        for q in range(NQ):
            if keys_before(q) is not None:
                take_banks(("keys", keys_before(q)), 2)
            for f in range(2):
                take_banks(("item", 2 * q + f), 1 + pairs[q][1] // 4)

        s_q, keys_mm, keys_cp, s_kr, sc_mm, sc_masked, sc_max, sc_bias, p_exp, p_sum, p_rec, p_diag, o_cp = (
            [sem("queries_in0"), sem("queries_in1")], sem("keys_ready"), sem("keys_copied"),
            [sem("rope_keys_set0"), sem("rope_keys_set1")],
            sem("scores_ready"), sem("scores_masked"), sem("scores_max"), sem("scores_bias"), sem("weights_ready"),
            sem("weight_sums_joined"), sem("weight_sums_recip"), sem("weight_sums_diagonal"),
            sem("attn_out_written"))
        p_t = [sem(f"weights_turned{f}") for f in range(2)]
        p_cp = [sem(f"weightsT_copied{f}") for f in range(2)]
        o_mm = sem("attn_out_ready")
        o_sp = sem("sums_spread")
        spread = spare[:, 3 * SEQ:3 * SEQ + P]

        def head_rows(f):
            return slice(0, 96) if f == 0 else slice(0, P)

        def copy_weights(eng_copy, eng, u, f):
            q, b0 = units[u]
            n = min(4, pairs[q][1] + 1 - b0) * P
            eng.wait_ge(p_t[f], u + 1)
            if u >= 2:
                eng.wait_ge(o_mm, u - 1)
            eng_copy(probT[2 * (u % 2) + f][:, 0:n], PS[4 + f][:, 0:n]).then_inc(p_cp[f], 1)

        def rows_are_out(eng):
            eng.wait_ge(s_nat, 16 * 6)

        def rope_keys(eng, pair):
            eng.memset(qcat[2 * pair + 1][0:ROPE, :], 0.0)
            eng.memset(kcat[2 * pair + 1][0:ROPE, :], 0.0)
            for f in range(2):
                o = (64, 32)[f]
                ins = eng.tensor_copy(kcat[2 * pair + f][o:o + ROPE, :], rp[64:96, 1, 0:SEQ])
            ins.then_inc(s_kr[pair], 1)

        with nc.Block() as block:
            @block.sync
            def _(sp):
                sp.dma_start(pages[0:1, :], I["page_table"].rearrange("b n -> (b n)").unsqueeze(0)).then_inc(s_pg, 16)
                for m in range(3):
                    if m >= 2:
                        sp.wait_ge(sc_mm, 16 * (m - 1))
                    for f in range(2):
                        h = 2 * m + f
                        dst = qcat[2 * (m % 2) + f]
                        r = HD * f
                        sp.dma_start(dst[r:r + HD, :], qn[r:r + HD, m, 0:SEQ]).then_inc(s_q[m % 2], 16)
                        r = ROPE * (h % 4)
                        o = (64, 32)[f]
                        sp.dma_start(dst[o:o + ROPE, :], rp[r:r + ROPE, h // 4, 0:SEQ]).then_inc(s_q[m % 2], 16)
                    if m == 1:
                        rows_are_out(sp)
                        sp.dma_start(newmask, I["c_newmask"].rearrange("q (x c) -> q x c", x=NX)).then_inc(s_nm, 16)
                        sp.wait_ge(s_pg, 16)
                        for j in range(EARLY):
                            load_rows(sp, j, 0)

            @block.gpsimd
            def _(pool):
                rope_keys(nc.gpsimd, 1)
                pool.wait_ge(s_kr[1], 1)
                for q in range(NQ):
                    for f in range(2):
                        it = 2 * q + f
                        pool.wait_ge(p_rec, it + 1)
                        if q >= 1:
                            pool.wait_ge(o_mm, units_of[q - 1][-1] + 1)
                        nc.gpsimd.tensor_scalar(diag[f], ident, stat_a[:, 3, it:it + 1], None, ALU.mult
                                                ).then_inc(p_diag, 1)
                    if 8 <= q < 8 + 4 * EARLY:
                        rows_are_out(pool)
                        pool.wait_ge(s_pg, 16)
                        load_rows(pool, (q - 8) // 4, 1, [q % 4])

            @block.tensor
            def _(pe):
                def take(use):
                    for kind, x in freed_by[use]:
                        if kind == "keys":
                            pe.wait_ge(keys_cp, 4 * (x + 1))
                        else:
                            pe.wait_ge(p_exp, x + 1)

                def keys(m):
                    take(("keys", m))
                    for half, b in enumerate(banks_of["keys", m]):
                        for k in range(2):
                            for f in range(2):
                                h = 2 * m + f
                                last = pe.matmul(PS[b][HD * f:HD * f + HD, :], w_uk[:, k, h * HD:(h + 1) * HD],
                                                 ckv[:, k, 512 * half:512 * half + 512], start=(k == 0),
                                                 stop=(k == 1), skip_group_check=True)
                        last.then_inc(keys_mm, 1)

                def scores(it):
                    (m, i), f = pairs[it // 2], it % 2
                    take(("item", it))
                    if i == 0 and f == 0:
                        pe.wait_ge(keys_cp, 4 * (m + 1))
                        if m < 2:
                            pe.wait_ge(s_kr[m], 1)
                        pe.wait_ge(s_q[m % 2], 64 * (m // 2 + 1))
                    w = (i + 1) * P
                    j = 2 * (m % 2) + f
                    for half, b in enumerate(banks_of["item", it]):
                        n = min(512, w - 512 * half)
                        last = pe.matmul(PS[b][:, 0:n], qcat[j][head_rows(f), i * P:(i + 1) * P],
                                         kcat[j][head_rows(f), 512 * half:512 * half + n], start=True, stop=True)
                    last.then_inc(sc_mm, 1)

                def turn(u):
                    q, b0 = units[u]
                    for f in range(2):
                        it = 2 * q + f
                        pe.wait_ge(p_exp, it + 1)
                        if u >= 1:
                            pe.wait_ge(p_cp[f], u)
                        for b in range(min(4, pairs[q][1] + 1 - b0)):
                            last = pe.transpose(PS[4 + f][:, b * P:(b + 1) * P],
                                                prob[it % 3][:, (b0 + b) * P:(b0 + b + 1) * P], ident)
                        last.then_inc(p_t[f], 1)

                def values(u):
                    q, b0 = units[u]
                    m, i = pairs[q]
                    out = PS[6 + q % 2]
                    for f in range(2):
                        pe.wait_ge(p_cp[f], u + 1)
                    if b0 == 0 and q >= 2:
                        pe.wait_ge(o_cp, q - 1)
                    for b in range(b0, min(b0 + 4, i + 1)):
                        for f in range(2):
                            h = 2 * m + f
                            last = pe.matmul(out[HD * f:HD * f + HD, 0:P], vnat[:, b, h * HD:(h + 1) * HD],
                                             probT[2 * (u % 2) + f][:, (b - b0) * P:(b - b0 + 1) * P],
                                             start=(b == 0), stop=(b == i), skip_group_check=True)
                    if u == units_of[q][-1]:
                        pe.wait_ge(p_diag, 2 * q + 2)
                        for f in range(2):
                            last = pe.matmul(out[HD * f:HD * f + HD, P:2 * P], ones[:, 0:HD], diag[f], start=True,
                                             stop=True, skip_group_check=True)
                    last.then_inc(o_mm, 1)

                keys(0)
                scores(0)
                scores(1)
                for q in range(NQ):
                    if q + 1 < NQ:
                        if keys_before(q + 1) is not None:
                            keys(keys_before(q + 1))
                        scores(2 * q + 2)
                    for n, u in enumerate(units_of[q]):
                        turn(u)
                        if n == 0 and q + 1 < NQ:
                            scores(2 * q + 3)
                        if u >= 1:
                            values(u - 1)
                values(len(units) - 1)

            @block.vector
            def _(dve):
                def softmax_max(it):
                    (m, i), f = pairs[it // 2], it % 2
                    w = (i + 1) * P
                    bank = [PS[b] for b in banks_of["item", it]]
                    dve.wait_ge(sc_mm, it + 1)
                    own = bank[-1][:, (i % 4) * P:(i % 4) * P + P]
                    dve.tensor_tensor(own, own, C("causal"), ALU.add).then_inc(sc_masked, 1)
                    n_max = sum(1 + pairs[j // 2][1] // 4 for j in range(it))
                    if w > 512:
                        dve.tensor_reduce(stat_a[:, 0, it:it + 1], bank[0][:, :], AX_X, ALU.max).then_inc(sc_max, 1)
                    dve.wait_ge(sc_masked, it + 1)
                    a = 1 if w > 512 else 0
                    dve.tensor_reduce(stat_a[:, a, it:it + 1], bank[a][:, 0:w - 512 * a], AX_X,
                                      ALU.max).then_inc(sc_max, 1)
                    dve.wait_ge(sc_max, n_max + 1 + a)
                    if a:
                        ins = dve.tensor_scalar(stat_a[:, 0, it:it + 1], stat_a[:, 0, it:it + 1],
                                                stat_a[:, 1, it:it + 1], -SCALE, ALU.max, ALU.mult)
                    else:
                        ins = dve.tensor_scalar(stat_a[:, 0, it:it + 1], stat_a[:, 0, it:it + 1], -SCALE, None,
                                                ALU.mult)
                    ins.then_inc(sc_bias, 1)

                def recips(q):
                    two = slice(2 * q, 2 * q + 2)
                    dve.wait_ge(p_exp, 2 * q + 2)
                    src = stat_a[:, 2, two]
                    if pairs[q][1] >= 4:
                        dve.tensor_tensor(stat_a[:, 1, two], stat_a[:, 1, two], src, ALU.add).then_inc(p_sum, 1)
                        dve.wait_ge(p_sum, sum(1 for _, i in pairs[:q + 1] if i >= 4))
                        src = stat_a[:, 1, two]
                    dve.reciprocal(stat_a[:, 3, two], src).then_inc(p_rec, 2)

                def write_out(q):
                    m, i = pairs[q]
                    out = PS[6 + q % 2]
                    dve.wait_ge(o_mm, units_of[q][-1] + 1)
                    if q >= 1:
                        dve.wait_ge(o_cp, q)
                    dve.tensor_copy(spread, out[:, P:2 * P]).then_inc(o_sp, 1)
                    dve.wait_ge(o_sp, q + 1)
                    dve.tensor_tensor(mixT[:, 3 + m, i * P:(i + 1) * P], out[:, 0:P], spread, ALU.mult
                                      ).then_inc(o_cp, 1)

                rope_keys(dve, 0)
                softmax_max(0)
                softmax_max(1)
                for q in range(NQ):
                    if q + 1 < NQ:
                        softmax_max(2 * q + 2)
                    recips(q)
                    for n, u in enumerate(units_of[q]):
                        copy_weights(dve.tensor_copy, dve, u, 0)
                        if n == 0 and q + 1 < NQ:
                            softmax_max(2 * q + 3)
                    if q >= 1:
                        write_out(q - 1)
                write_out(NQ - 1)

            @block.scalar
            def _(act):
                def copy_keys(m):
                    for half, b in enumerate(banks_of["keys", m]):
                        act.wait_ge(keys_mm, 2 * m + half + 1)
                        for f in range(2):
                            rows = slice(HD * f, HD * f + HD)
                            nc.scalar.copy(kcat[2 * (m % 2) + f][rows, 512 * half:512 * half + 512],
                                           PS[b][rows, :]).then_inc(keys_cp, 1)

                def weights(it):
                    q = it // 2
                    w = (pairs[q][1] + 1) * P
                    act.wait_ge(sc_bias, it + 1)
                    if it >= 3:
                        act.wait_ge(p_t[(it - 3) % 2], units_of[(it - 3) // 2][-1] + 1)
                    for j, b in enumerate(banks_of["item", it]):
                        n = min(512, w - 512 * j)
                        ins = nc.scalar.activation(prob[it % 3][:, 512 * j:512 * j + n], PS[b][:, 0:n], ACT.Exp,
                                                   bias=stat_a[:, 0, it:it + 1], scale=SCALE,
                                                   accum_out=stat_a[:, 2 - j, it:it + 1])
                    ins.then_inc(p_exp, 1)

                copy_keys(0)
                weights(0)
                weights(1)
                for q in range(NQ):
                    if q + 1 < NQ:
                        if keys_before(q + 1) is not None:
                            copy_keys(keys_before(q + 1))
                        weights(2 * q + 2)
                    for n, u in enumerate(units_of[q]):
                        copy_weights(nc.scalar.copy, act, u, 1)
                        if n == 0 and q + 1 < NQ:
                            weights(2 * q + 3)
        if upto == "attn":
            return

        new_stage()
        QN = NX * P
        cw = Carve(WORK - 6 * QN)
        q_lat = cw.take(2 * QN).rearrange("p (k q) -> p k q", k=2)
        q_rope = cw.take(4 * QN).rearrange("p (r q) -> p r q", r=4)
        w_ukT = wring[:, 0:3 * RANK].rearrange("p (m c) -> p m c", m=3)
        s_q0, s_qr, wu_t, wu_cp, ql_mm = (sem("queries_cleared"), sem("rope_q_set"), sem("w_uk_turned"),
                                          sem("w_ukT_copied"), sem("q_lat_ready"))

        def by_half(ap, h):
            return ap.rearrange("p (x f c) -> p f x c", x=NX, f=2)[:, :, :, h * TS:(h + 1) * TS]

        def of_sample(ap):
            return ap.rearrange("p (f x t) -> p f x t", f=2, x=NX)

        with nc.Block() as block:
            @block.gpsimd
            def _(pool):
                nc.gpsimd.memset(q_rope[:, 2:4], 0.0).then_inc(s_q0, 1)
                nc.gpsimd.memset(q_lat, 0.0).then_inc(s_q0, 1)

            @block.tensor
            def _(pe):
                for m in range(3):
                    for k in range(2):
                        last = pe.transpose(PS[m][:, k * P:(k + 1) * P], w_uk[:, k, m * P:(m + 1) * P], ident)
                last.then_inc(wu_t, 1)
                pe.wait_ge(wu_cp, 3)
                for h in range(H):
                    r = HD * (h % 2)
                    for k in range(2):
                        last = pe.matmul(PS[4 + k + 2 * (h % 2)][:, (h // 2) * NS:(h // 2 + 1) * NS],
                                         w_ukT[r:r + HD, h // 2, k * P:(k + 1) * P],
                                         qn[r:r + HD, h // 2, SEQ:T], start=True, stop=True)
                last.then_inc(ql_mm, 1)

            def rope_queries(eng_copy, versions):
                for h in range(H):
                    r0 = ROPE * (h % 4)
                    for r in versions:
                        eng_copy(by_half(q_rope[ROPE * r:ROPE * (r + 1), r], h),
                                 of_sample(rp[r0:r0 + ROPE, h // 4, SEQ:T]))

            def latent_queries(eng_copy, k):
                for h in range(H):
                    eng_copy(by_half(q_lat[:, k], h),
                             of_sample(PS[4 + k + 2 * (h % 2)][:, (h // 2) * NS:(h // 2 + 1) * NS]))

            @block.vector
            def _(dve):
                dve.memset(q_rope[:, 0:2], 0.0).then_inc(s_qr, 1)
                dve.wait_ge(wu_t, 1)
                for m in range(3):
                    dve.tensor_copy(w_ukT[:, m], PS[m][:, 0:RANK]).then_inc(wu_cp, 1)
                dve.wait_ge(s_qr, 1)
                rope_queries(dve.tensor_copy, (0, 1))
                dve.wait_ge(ql_mm, 1)
                dve.wait_ge(s_q0, 2)
                latent_queries(dve.tensor_copy, 0)

            @block.scalar
            def _(act):
                act.wait_ge(s_q0, 1)
                rope_queries(nc.scalar.copy, (2, 3))
                act.wait_ge(ql_mm, 1)
                act.wait_ge(s_q0, 2)
                latent_queries(nc.scalar.copy, 1)
        if upto == "queries":
            return

        new_stage()
        cw = Carve()
        keyT = cw.take(2 * 2 * 2 * 512).rearrange("p (s f k c) -> p s f k c", s=2, f=2, k=2)
        krT = cw.take(2 * 2 * P).rearrange("p (s f c) -> p s f c", s=2, f=2)
        pr = cw.take(2 * 512).rearrange("p (s c) -> p s c", s=2)
        prT = cw.take(2 * 4 * P).rearrange("p (s c) -> p s c", s=2)
        part = cw.take(2 * NPT * RANK).rearrange("p (s g c) -> p s g c", s=2, g=NPT)
        o_nat = cw.take(2 * RANK).rearrange("p (s c) -> p s c", s=2)
        mx, bias, sums, wts = (cw.take(NX * NPT).rearrange("p (x g) -> p x g", x=NX) for _ in range(4))
        tot = cw.take(NX * 4).rearrange("p (x a) -> p x a", x=NX)
        assert cw.at <= WORK - 6 * QN, cw.at
        w_uv2 = res[:, 7936:8704].rearrange("p (k c) -> p k c", k=2)
        steps = [(x, g) for x in range(NX) for g in range(NPT)]
        NSTEP = len(steps)
        JOINED = 2 + (NPT + 1) // 2
        assert JOINED < NG

        (k_t, k_cpa, k_cpb, ds_mm, ds_mask, ds_max, ds_bias, dp_exp, dp_t, dp_cp, do_mm, do_cp) = (
            sem("rows_turned2"), sem("keysT_copied_a"),
            sem("keysT_copied_b"), sem("dscores_ready"), sem("dscores_masked"), sem("dscores_max"),
            sem("dscores_bias"), sem("dweights_ready"), sem("dweights_turned"), sem("dweightsT_copied"),
            sem("dparts_ready"), sem("dparts_copied"))
        s_uv = sem("w_uv_in")
        j_max, j_w, j_sum, j_acc, j_t, j_cp, j_ready = (sem("join_max"), sem("join_weights"), sem("join_sum"),
                                                        sem("join_steps"), sem("joined_turned"),
                                                        sem("joined_copied"), sem("joined"))
        y_mm = sem("decode_values_ready")
        with nc.Block() as block:
            def all_loads(eng, f):
                for j in range(EARLY, len(loads)):
                    if j >= NL:
                        eng.wait_ge(do_mm, step_of(j - NL) + 1)
                    load_rows(eng, j, f)

            @block.sync
            def _(sp):
                sp.dma_start(w_uv2, I["w_uv"][0].rearrange("(k p) h d -> p k (h d)", p=P)).then_inc(s_uv, 16)
                all_loads(sp, 0)

            @block.gpsimd
            def _(pool):
                all_loads(pool, 1)

            @block.tensor
            def _(pe):
                def turn_keys(j, f):
                    slot = 2 * (j % NL) + f
                    pe.wait_ge(s_k[f][j % NL], (128, 112)[f] * (j // NL + 1))
                    if f == 1:
                        pe.wait_ge(s_kx[j % NL], 16 * (j // NL + 1))
                    n = 2 * j + f
                    if n >= 1:
                        pe.wait_ge(k_cpa, n)
                        pe.wait_ge(k_cpb, 2 * n)
                    rows = kslot[slot].rearrange("p (r c) -> p r c", r=4)
                    for k in range(2):
                        for r in range(4):
                            pe.transpose(PS[k][:, r * P:(r + 1) * P], rows[:, r, k * P:(k + 1) * P], ident)
                    pe.transpose(PS[2][:, 0:P], krr[:, slot, :], ident).then_inc(k_t, 1)

                def dscores(s):
                    x, g = steps[s]
                    bank = PS[3 + s % 2]
                    if s >= 2:
                        pe.wait_ge(dp_exp, s - 1)
                    q = [(slice(HD * f, HD * f + HD), slice(x * P + HD * f, x * P + HD * f + HD)) for f in range(2)]
                    if g < NG:
                        j = x * NG + g
                        pe.wait_ge(k_cpa, 2 * j + 2)
                        pe.wait_ge(k_cpb, 4 * j + 4)
                        for r in range(4):
                            for f, (out, cols) in enumerate(q):
                                pe.matmul(bank[out, r * P:(r + 1) * P], q_rope[:, r, cols], krT[:, j % 2, f, :],
                                          start=(r == 0), stop=False, skip_group_check=True)
                        for k in range(2):
                            for f, (out, cols) in enumerate(q):
                                last = pe.matmul(bank[out, :], q_lat[:, k, cols], keyT[:, j % 2, f, k, :],
                                                 start=False, stop=(k == 1), skip_group_check=True)
                    else:
                        for k in range(2):
                            for out, cols in q:
                                pe.matmul(bank[out, 0:NS], q_lat[:, k, cols], ckvT_new[:, k], start=(k == 0),
                                          stop=False, skip_group_check=True)
                        for out, cols in q:
                            last = pe.matmul(bank[out, 0:NS], q_rope[:, 2, cols], krT_new, start=False, stop=True,
                                             skip_group_check=True)
                    last.then_inc(ds_mm, 1)

                def turn_weights(s):
                    pe.wait_ge(dp_exp, s + 1)
                    if s >= 1:
                        pe.wait_ge(dp_cp, s)
                    if steps[s][1] < NG:
                        for r in range(4):
                            last = pe.transpose(PS[5][:, r * P:(r + 1) * P], pr[:, s % 2, r * P:(r + 1) * P], ident)
                    else:
                        last = pe.transpose(PS[5][0:NS, 0:P], pr[:, s % 2, 0:NS], ident)
                    last.then_inc(dp_t, 1)

                def dvalues(s, part_of):
                    x, g = steps[s]
                    bank = PS[6 + s % 2]
                    if part_of == 0:
                        pe.wait_ge(dp_cp, s + 1)
                        if s >= 2:
                            pe.wait_ge(do_cp, s - 1)
                    if g < NG:
                        j = x * NG + g
                        for r in (2 * part_of, 2 * part_of + 1):
                            for f in range(2):
                                rows = kslot[2 * (j % NL) + f]
                                last = pe.matmul(bank[HD * f:HD * f + HD, 0:RANK],
                                                 prT[:, s % 2, r * P + HD * f:r * P + HD * f + HD],
                                                 rows[:, r * RANK:(r + 1) * RANK], start=(r == 0), stop=(r == 3),
                                                 skip_group_check=True)
                    elif part_of == 1:
                        last = pe.matmul(bank[:, 0:RANK], prT[0:NS, s % 2, 0:P], ckv_new, start=True, stop=True)
                    if part_of == 1:
                        last.then_inc(do_mm, 1)

                def turn_joined(x):
                    pe.wait_ge(j_ready, x + 1)
                    if x >= 1:
                        pe.wait_ge(j_cp, x)
                    for k in range(2):
                        last = pe.transpose(PS[2][:, P + k * P:P + (k + 1) * P],
                                            o_nat[:, x % 2, k * P:(k + 1) * P], ident)
                    last.then_inc(j_t, 1)

                pe.wait_ge(s_nm, 16)
                turn_keys(0, 0)
                turn_keys(0, 1)
                for s in range(NSTEP):
                    x, g = steps[s]
                    following = s + 1 < NSTEP and steps[s + 1][1] < NG and steps[s + 1]
                    dscores(s)
                    if g == JOINED and x >= 1:
                        turn_joined(x - 1)
                        pe.wait_ge(j_cp, x)
                    if following:
                        turn_keys(following[0] * NG + following[1], 0)
                    if s >= 1:
                        dvalues(s - 1, 0)
                    if following:
                        turn_keys(following[0] * NG + following[1], 1)
                    turn_weights(s)
                    if s >= 1:
                        dvalues(s - 1, 1)
                for half in range(2):
                    dvalues(NSTEP - 1, half)
                turn_joined(NX - 1)
                pe.wait_ge(j_cp, NX)
                pe.wait_ge(s_uv, 16)
                for h in range(H):
                    r = HD * (h % 2)
                    for k in range(2):
                        rhs = by_half(q_lat[:, k], h)
                        last = pe.matmul(of_sample(PS[h % 2][r:r + HD, (h // 2) * NS:(h // 2 + 1) * NS]),
                                         w_uv2[:, k, h * HD:(h + 1) * HD], rhs, start=(k == 0), stop=(k == 1))
                last.then_inc(y_mm, 1)

            @block.vector
            def _(dve):
                def copy_keys(j, f):
                    dve.wait_ge(k_t, 2 * j + f + 1)
                    if j >= 2:
                        dve.wait_ge(ds_mm, step_of(j - 2) + 1)
                    dve.tensor_copy(keyT[:, j % 2, f, 0, :], PS[0][:, :]).then_inc(k_cpa, 1)

                def copy_weights(s):
                    dve.wait_ge(dp_t, s + 1)
                    if s >= 2:
                        dve.wait_ge(do_mm, s - 1)
                    n, w = (P, 4 * P) if steps[s][1] < NG else (NS, P)
                    dve.tensor_copy(prT[0:n, s % 2, 0:w], PS[5][0:n, 0:w]).then_inc(dp_cp, 1)

                def softmax_max(s):
                    x, g = steps[s]
                    w = 512 if g < NG else NS
                    bank = PS[3 + s % 2]
                    dve.wait_ge(ds_mm, s + 1)
                    if g == NG:
                        dve.tensor_tensor(bank[:, 0:NS], bank[:, 0:NS], newmask[:, x], ALU.add).then_inc(ds_mask, 1)
                        dve.wait_ge(ds_mask, x + 1)
                    dve.tensor_reduce(mx[:, x, g:g + 1], bank[:, 0:w], AX_X, ALU.max).then_inc(ds_max, 1)
                    dve.wait_ge(ds_max, s + 1)
                    dve.tensor_scalar(bias[:, x, g:g + 1], mx[:, x, g:g + 1], -SCALE, None, ALU.mult
                                      ).then_inc(ds_bias, 1)

                def copy_part(s):
                    x, g = steps[s]
                    dve.wait_ge(do_mm, s + 1)
                    if g == 0 and x >= 2:
                        dve.wait_ge(j_ready, x - 1)
                    dve.tensor_copy(part[:, x % 2, g, :], PS[6 + s % 2][:, 0:RANK]).then_inc(do_cp, 1)

                def join_max(x):
                    dve.wait_ge(ds_max, NPT * (x + 1))
                    dve.tensor_reduce(tot[:, x, 0:1], mx[:, x, :], AX_X, ALU.max).then_inc(j_max, 1)
                    dve.wait_ge(j_max, 2 * x + 1)
                    dve.tensor_scalar(tot[:, x, 1:2], tot[:, x, 0:1], -SCALE, None, ALU.mult).then_inc(j_max, 1)

                def join_sum(x):
                    dve.wait_ge(j_w, x + 1)
                    dve.wait_ge(dp_exp, NPT * (x + 1))
                    dve.tensor_tensor(sums[:, x, :], sums[:, x, :], wts[:, x, :], ALU.mult).then_inc(j_sum, 1)
                    dve.wait_ge(j_sum, 3 * x + 1)
                    dve.tensor_reduce(tot[:, x, 2:3], sums[:, x, :], AX_X, ALU.add).then_inc(j_sum, 1)
                    dve.wait_ge(j_sum, 3 * x + 2)
                    dve.reciprocal(tot[:, x, 3:4], tot[:, x, 2:3]).then_inc(j_sum, 1)

                def join(x, parts):
                    o = o_nat[:, x % 2, :]
                    if x >= 2 and parts[0] == 0:
                        dve.wait_ge(j_t, x - 1)
                    dve.wait_ge(do_cp, NPT * x + parts[-1] + 1)
                    for g in parts:
                        w = wts[:, x, g:g + 1]
                        if g == 0:
                            dve.tensor_scalar(o, part[:, x % 2, g, :], w, None, ALU.mult).then_inc(j_acc, 1)
                        else:
                            dve.wait_ge(j_acc, NPT * x + g)
                            dve.scalar_tensor_tensor(out=o, in0=part[:, x % 2, g, :], scalar=w, in1=o,
                                                     op0=ALU.mult, op1=ALU.add).then_inc(j_acc, 1)
                    if parts[-1] < NPT - 1:
                        return
                    dve.wait_ge(j_acc, NPT * (x + 1))
                    dve.wait_ge(j_sum, 3 * x + 3)
                    dve.tensor_scalar(o, o, tot[:, x, 3:4], None, ALU.mult).then_inc(j_ready, 1)

                copy_keys(0, 0)
                copy_keys(0, 1)
                for s in range(NSTEP):
                    x, g = steps[s]
                    following = s + 1 < NSTEP and steps[s + 1][1] < NG and steps[s + 1]
                    softmax_max(s)
                    for half in range(2):
                        if following:
                            copy_keys(following[0] * NG + following[1], half)
                    copy_weights(s)
                    if s >= 1:
                        copy_part(s - 1)
                    if g == 1 and x >= 1:
                        join_max(x - 1)
                    if g == 2 and x >= 1:
                        join_sum(x - 1)
                    if 2 <= g < JOINED and x >= 1:
                        join(x - 1, range(2 * (g - 2), min(2 * (g - 1), NPT)))
                join_max(NX - 1)
                join_sum(NX - 1)
                join(NX - 1, range(NPT - 1))
                copy_part(NSTEP - 1)
                join(NX - 1, range(NPT - 1, NPT))
                dve.wait_ge(y_mm, 1)
                for h in range(H):
                    r = HD * (h % 2)
                    dve.tensor_copy(mixT[r:r + HD, 3 + h // 2, SEQ:T],
                                    PS[h % 2][r:r + HD, (h // 2) * NS:(h // 2 + 1) * NS])

            @block.scalar
            def _(act):
                def copy_keys(j, f):
                    act.wait_ge(k_t, 2 * j + f + 1)
                    if j >= 2:
                        act.wait_ge(ds_mm, step_of(j - 2) + 1)
                    nc.scalar.copy(keyT[:, j % 2, f, 1, :], PS[1][:, :]).then_inc(k_cpb, 1)
                    nc.scalar.copy(krT[:, j % 2, f, :], PS[2][:, 0:P]).then_inc(k_cpb, 1)

                def exps(s):
                    x, g = steps[s]
                    w = 512 if g < NG else NS
                    act.wait_ge(ds_bias, s + 1)
                    if s >= 2:
                        act.wait_ge(dp_t, s - 1)
                    nc.scalar.activation(pr[:, s % 2, 0:w], PS[3 + s % 2][:, 0:w], ACT.Exp,
                                         bias=bias[:, x, g:g + 1], scale=SCALE,
                                         accum_out=sums[:, x, g:g + 1]).then_inc(dp_exp, 1)

                def join_weights(x):
                    act.wait_ge(j_max, 2 * x + 2)
                    nc.scalar.activation(wts[:, x, :], mx[:, x, :], ACT.Exp, bias=tot[:, x, 1:2],
                                         scale=SCALE).then_inc(j_w, 1)

                def copy_joined(x):
                    act.wait_ge(j_t, x + 1)
                    for k in range(2):
                        ins = nc.scalar.copy(q_lat[:, k, x * P:(x + 1) * P], PS[2][:, P + k * P:P + (k + 1) * P])
                    ins.then_inc(j_cp, 1)

                copy_keys(0, 0)
                copy_keys(0, 1)
                for s in range(NSTEP):
                    x, g = steps[s]
                    following = s + 1 < NSTEP and steps[s + 1][1] < NG and steps[s + 1]
                    if g == JOINED and x >= 1:
                        copy_joined(x - 1)
                    if following:
                        copy_keys(following[0] * NG + following[1], 0)
                    exps(s)
                    if following:
                        copy_keys(following[0] * NG + following[1], 1)
                    if g == 1 and x >= 1:
                        join_weights(x - 1)
                join_weights(NX - 1)
                copy_joined(NX - 1)
        if upto == "decode":
            return

        new_stage()
        cw = Carve()
        AR = cw.take(3 * TT * 2 * P).rearrange("p (m i w t) -> p m i w t", m=3, i=TT, w=2)
        loop_base = cw.at
        fresh, lg, cum, dec, icl, kkn, k2 = (cw.take(TPAD) for _ in range(7))
        w2 = wring[:, 0:AW]
        g2 = wring[:, AW:2 * AW]
        prod, di = wring[:, 768:768 + TPAD], wring[:, 768 + TPAD:768 + 2 * TPAD]
        nch = SEQ // CHUNK
        dc = piece(3 * (nch + NB)).rearrange("p (m c) -> p m c", m=3)
        tch = [(c * 384, 384) for c in range(3)]

        def tiles3(ap):
            return ap.rearrange("p (i t) -> p i t", t=P)

        (s_w2, s_hv, p_th, p_kk, pss_mm, p_rt, z_mm, p_tw, p_dve, p_ex, p_go, b_mm, b_cp) = (
            sem("lora_in"), sem("half_biases"), sem("lora_tanh"), sem("keys_squared"), sem("key_norms_summed"),
            sem("key_norms_root"), sem("lora_products"), sem("gates_tanh"),
            sem("operand_steps"), sem("decays_exp"), sem("operands_done"), sem("bonus_summed"),
            sem("bonus_written"))
        heads_in = wring[:, 768 + 2 * TPAD:768 + 2 * TPAD + 480].rearrange("p (m c) -> p m c", m=3)
        norms = wring[:, 768 + 2 * TPAD + 480:768 + 2 * TPAD + 864]
        s_hd = sem("head_sums_in")
        p_rn0, p_rr, p_prod, p_ch, p_t1, p_k2, p_kk2, p_pool = (
            sem("key_norms_clamped"), sem("key_norms_inverse"), sem("bonus_product"), sem("operand_chain"),
            sem("decay_gates"), sem("key_gates"), sem("keys_gated"), sem("operands_of_gpsimd"))
        sq_tmp = [icl, kkn, k2]
        with nc.Block() as block:
            @block.sync
            def _(sp):
                sp.dma_start(heads_in, I["c_heads"]).then_inc(s_hd, 16)
                sp.dma_start(w2[0:64], I["decay_w2"][0]).then_inc(s_w2, 16)
                sp.dma_start(w2[64:128], I["iclr_a2"][0]).then_inc(s_w2, 16)
                sp.dma_start(g2, I["gate_g2"][0]).then_inc(s_w2, 16)
                sp.dma_start(fresh, I["c_fresh"]).then_inc(s_w2, 16)

            @block.scalar
            def _(act):
                for m in range(3):
                    nc.scalar.activation(sq_tmp[m], sT[:, 3 + m], ACT.Square, scale=vec("k_k", m)).then_inc(p_kk, 1)
                act.wait_ge(p_rn0, 1)
                nc.scalar.activation(norms[0:96], norms[0:96], ACT.Sqrt).then_inc(p_rt, 1)
                nc.scalar.activation(sT[0:64, 9], sT[0:64, 9], ACT.Tanh).then_inc(p_th, 1)
                act.wait_ge(s_hv, 1)
                for m in range(3):
                    if m >= 1:
                        act.wait_ge(p_go, m)
                        act.wait_ge(p_pool, 2 * m)
                    for w, dst in enumerate((lg, icl)):
                        for c, (t0, n) in enumerate(tch):
                            act.wait_ge(z_mm, 6 * m + 3 * w + c + 1)
                            nc.scalar.activation(dst[:, t0:t0 + n], PS[3 * w + c][:, 0:n], ACT.Tanh, scale=0.5,
                                                 bias=halves[:, 3 * w + m:3 * w + m + 1]).then_inc(p_tw, 1)
                        if w == 0:
                            act.wait_ge(p_tw, 6 * m + 3)
                            nc.scalar.activation(lg, lg, ACT.Identity, bias=ones[:, 0:1]).then_inc(p_t1, 1)
                    act.wait_ge(p_tw, 6 * m + 6)
                    nc.scalar.activation(k2, icl, ACT.Identity, scale=halves[:, 6 + m:7 + m],
                                         bias=halves[:, 9 + m:10 + m]).then_inc(p_k2, 1)
                    act.wait_ge(p_dve, 2 * m + 1)
                    nc.scalar.activation(dec, cum, ACT.Exp, scale=DECAY / 2).then_inc(p_ex, 1)
                    nc.scalar.activation(di, cum, ACT.Exp, scale=-DECAY / 2).then_inc(p_ex, 1)
                    act.wait_ge(p_dve, 2 * m + 2)
                    nc.scalar.activation(lg, lg, ACT.Exp, scale=DECAY / 2).then_inc(p_ex, 1)

            @block.gpsimd
            def _(pool):
                for m in range(3):
                    pool.wait_ge(p_ex, 3 * m + 1)
                    nc.gpsimd.tensor_tensor(AR[:, m, :, 1], tiles3(sT[:, m]), tiles3(dec), ALU.mult
                                            ).then_inc(p_pool, 1)
                    pool.wait_ge(p_ex, 3 * m + 2)
                    pool.wait_ge(p_kk2, m + 1)
                    nc.gpsimd.tensor_tensor(sT[:, 3 + m], k2, di, ALU.mult).then_inc(p_pool, 1)

            @block.tensor
            def _(pe):
                pe.wait_ge(s_hd, 16)
                for m in range(3):
                    pe.wait_ge(p_kk, m + 1)
                    for c, (t0, n) in enumerate(tch):
                        last = pe.matmul(PS[7][32 * c:32 * c + 32, 0:n], heads_in[:, m, 0:32],
                                         sq_tmp[m][:, t0:t0 + n], start=(m == 0), stop=(m == 2),
                                         skip_group_check=True)
                last.then_inc(pss_mm, 1)
                pe.wait_ge(s_w2, 64)
                pe.wait_ge(p_th, 1)

                def gates(m):
                    for w in range(2):
                        rows = slice(64 * w, 64 * w + 64)
                        for c, (t0, n) in enumerate(tch):
                            if m >= 1:
                                pe.wait_ge(p_tw, 6 * (m - 1) + 3 * w + c + 1)
                            pe.matmul(PS[3 * w + c][:, 0:n], w2[rows, m * P:(m + 1) * P], sT[rows, 9, t0:t0 + n],
                                      start=True, stop=True).then_inc(z_mm, 1)

                gates(0)
                pe.wait_ge(p_rr, 1)
                for m in range(3):
                    for c, (t0, n) in enumerate(tch):
                        u = 6 * m + c
                        if u >= 2:
                            pe.wait_ge(b_cp, u - 1)
                        rows = slice(32 * c, 32 * c + 32)
                        pe.matmul(PS[6 + u % 2][:, 0:n], heads_in[rows, m, 32:], norms[rows, 0:n], start=True,
                                  stop=True).then_inc(b_mm, 1)
                    if m < 2:
                        gates(m + 1)
                    pe.wait_ge(p_prod, m + 1)
                    for c, (t0, n) in enumerate(CH):
                        u = 6 * m + 3 + c
                        pe.wait_ge(b_cp, u - 1)
                        pe.matmul(PS[6 + u % 2][:, 0:n], C("head_ones"), prod[:, t0:t0 + n], start=True,
                                  stop=True).then_inc(b_mm, 1)

            @block.vector
            def _(dve):
                dve.tensor_scalar(halves[:, 0:6], vecs[:, VEC["decay_w0"][0]:VEC["decay_w0"][0] + 6], 0.5, None,
                                  ALU.mult)
                k_a = vecs[:, VEC["k_a"][0]:VEC["k_a"][0] + 3]
                dve.tensor_scalar(halves[:, 6:9], k_a, 0.5, None, ALU.mult)
                dve.tensor_scalar(halves[:, 9:12], k_a, -0.5, 1.0, ALU.mult, ALU.add).then_inc(s_hv, 1)
                dve.wait_ge(s_hv, 1)
                dve.wait_ge(pss_mm, 1)
                dve.tensor_scalar(norms[0:96], PS[7][0:96, 0:384], 1e-24, None, ALU.max).then_inc(p_rn0, 1)
                dve.wait_ge(p_rt, 1)
                dve.reciprocal(norms[0:96], norms[0:96]).then_inc(p_rr, 1)
                dve.wait_ge(s_w2, 64)
                link = chain(dve, p_ch)
                for m in range(3):
                    r, k = sT[:, m], sT[:, 3 + m]
                    dve.wait_ge(p_t1, m + 1)
                    dve.tensor_tensor_scan(cum, fresh, lg, 0.0, ALU.mult, ALU.add).then_inc(p_dve, 1)
                    dve.wait_ge(p_dve, 2 * m + 1)
                    dve.tensor_tensor(lg, cum, lg, ALU.subtract).then_inc(p_dve, 1)
                    for c, (t0, n) in enumerate(tch):
                        dve.wait_ge(b_mm, 6 * m + c + 1)
                        dve.scalar_tensor_tensor(out=kkn[:, t0:t0 + n], in0=k[:, t0:t0 + n],
                                                 scalar=vec("k_k", m), in1=PS[6 + c % 2][:, 0:n],
                                                 op0=ALU.mult, op1=ALU.mult).then_inc(b_cp, 1)
                    dve.wait_ge(b_cp, 6 * m + 3)
                    dve.wait_ge(p_k2, m + 1)
                    dve.tensor_tensor(k2, k2, k, ALU.mult).then_inc(p_kk2, 1)
                    dve.wait_ge(p_kk2, m + 1)
                    if m >= 1:
                        dve.wait_ge(b_mm, 6 * m)
                    dve.scalar_tensor_tensor(out=prod, in0=r, scalar=vec("r_k", m), in1=k2, op0=ALU.mult,
                                             op1=ALU.mult).then_inc(p_prod, 1)
                    link(dve.scalar_tensor_tensor(out=icl, in0=icl, scalar=1.0, in1=kkn, op0=ALU.add, op1=ALU.mult))
                    dve.wait_ge(p_ex, 3 * m + 1)
                    dve.tensor_copy(dc[:, m, 0:nch], dec[:, CHUNK - 1:SEQ:CHUNK])
                    dve.tensor_copy(dc[:, m, nch:], dec[:, SEQ + TS - 1:T:TS])
                    dve.wait_ge(p_ex, 3 * m + 3)
                    dve.scalar_tensor_tensor(out=AR[:, m, :, 0], in0=tiles3(kkn), scalar=-1.0, in1=tiles3(lg),
                                             op0=ALU.mult, op1=ALU.mult)
                    dve.wait_ge(p_pool, 2 * m + 1)
                    dve.scalar_tensor_tensor(out=r, in0=icl, scalar=0.5, in1=di, op0=ALU.mult, op1=ALU.mult
                                             ).then_inc(p_go, 1)
                    for c, (t0, n) in enumerate(CH):
                        dve.wait_ge(b_mm, 6 * m + 3 + c + 1)
                        dve.tensor_tensor(mixT[:, m, t0:t0 + n], PS[6 + (3 + c) % 2][:, 0:n],
                                          sT[:, 6 + m, t0:t0 + n], ALU.mult).then_inc(b_cp, 1)
                    dve.wait_ge(p_go, m + 1)
        if upto == "operands":
            return

        new_stage()
        cw = Carve(loop_base)
        hb = cw.take(5 * 1536).rearrange("p (h b w) -> p h b w", h=5, b=6)
        hb5 = wring[:, 768:768 + 1536].rearrange("p (b w) -> p b w", b=6)
        at2 = [2304]

        def wr(n):
            at2[0] += n
            assert at2[0] <= 4096
            return wring[:, at2[0] - n:at2[0]]

        rt_ = wr(AW).rearrange("p (m t) -> p m t", m=3)
        scr = sT[:, 9]
        states = scr[:, 0:768].rearrange("p (s m v) -> p s m v", s=4, m=3)
        gts = scr[:, 768:1152].rearrange("p (m c v) -> p m c v", m=3, c=2)
        hss = cw.take(AW).rearrange("p (m c v) -> p m c v", m=3, c=2)
        at3 = [0]

        def rr(n):
            at3[0] += n
            assert at3[0] <= KD * T
            return res[:, at3[0] - n:at3[0]]

        tinv = rr(H * P).rearrange("p (h t) -> p h t", h=H)
        lone = rr(2 * H * P).rearrange("p (w h t) -> p w h t", w=2, h=H)
        b_by, v_by = (rr(2 * AW).rearrange("p (c d) -> p c d", c=2) for _ in range(2))
        u_by = rr(H * P).rearrange("p (h c v) -> p h c v", h=H, c=2)
        odd = rr(2 * H * 256).rearrange("p (h b w) -> p h b w", h=H, b=2)

        def buf(h, b, i=0):
            if i % 2 and b < 2:
                return odd[:, h, b]
            return hb[:, h, b] if h < 5 else hb5[:, b]

        def nat(i, src, cols):
            assert cols.start // P == (cols.stop - 1) // P
            m, o = cols.start // P, cols.start % P
            return sT[:, src + m, i * P + o:i * P + o + cols.stop - cols.start]

        NQ, MP, XX, ND, PA, PB = range(6)
        NPT_ = TT - 1
        SOLVE = ["NQ", "MP", "NT", "MV", "P2", "T2", "P4", "T4", "P8", "T8", "AP", "ZT", "H1", "H2", "H3"]
        SOLVE_S = ["NQ", "MP", "NT", "MV", "P2", "T2", "P4", "T4", "AP"]
        ON_DVE = {"NQ", "MP", "NT", "T2", "T4", "T8", "H1", "H2", "H3", "RT", "GH", "CH"}

        def sequence(i):
            ops = [(i, "nat", j) for j in range(4)]
            late = [(i - 1, "CH", 0), (i - 1, "CH", 1)] + [(i - 1, "Y", m) for m in range(3)]
            if not 0 < i < NPT_:
                late = []
            stages = SOLVE if i < NPT_ else SOLVE_S
            ops += late[:1] + [(i, "NQ", h) for h in range(H)]
            ops += late[1:2] + [(i, "MP", h) for h in range(H)] + late[2:]
            ops += [(i, what, h) for what in stages[2:] for h in range(H)]
            ops += [(i, "RT", m) for m in range(3)]
            if i < NPT_:
                ops += [(i, "GH", m) for m in range(3)]
            if i == NPT_ - 1:
                ops += [(i, "CH", 0), (i, "CH", 1)] + [(i, "Y", m) for m in range(3)]
            return ops

        all_ops = [o for i in range(TT) for o in sequence(i)]
        number = {o: n for n, o in enumerate(all_ops)}

        def op(i, what, h=0):
            return number[i, what, h]

        def by_dve(n):
            _, what, h = all_ops[n]
            return what in ON_DVE or (what == "nat" and h == 0)

        dve_before, act_before = [0], [0]
        for n in range(len(all_ops)):
            dve_before.append(dve_before[-1] + by_dve(n))
            act_before.append(act_before[-1] + (not by_dve(n)))
        rw_mm, rw_dve, rw_act, rw_diag, rw_tinv, rw_lone, rw_uby, s_s0 = (
            sem("rw_product"), sem("rw_taken_dve"), sem("rw_taken_act"), sem("rw_diagonal_blocks"),
            sem("rw_inverse_started"), sem("rw_lone_heads"), sem("rw_u_by_chunk"), sem("rw_zeroed"))

        def taken(eng, n):
            if by_dve(n):
                eng.wait_ge(rw_dve, dve_before[n] + 1)
            else:
                eng.wait_ge(rw_act, act_before[n] + 1)

        def head(h):
            return slice(64 * (h % 2), 64 * (h % 2) + 64), h // 2

        def masks(i):
            return "_p" if i < NPT_ else "_s"

        def products(pe, turn):
            for i, what, h in sequence(turn):
                n = op(i, what, h)
                if n >= 8:
                    taken(pe, n - 8)
                last = product_of(pe, i, what, h, PS[n % 8])
                last.then_inc(rw_mm, 1)

        def product_of(pe, i, what, h, b):
            if what == "nat":
                for m in range(3):
                    x = AR[:, m, i, 0] if h == 0 else sT[:, 3 * (h - 1) + m, i * P:(i + 1) * P]
                    last = pe.transpose(b[:, m * P:(m + 1) * P], x, ident)
                return last
            two = [(slice(HD * f, HD * f + HD), 2 * h + f) for f in range(2)]
            if what == "RT":
                for rows, k in two:
                    taken(pe, op(i, "H3" if i < NPT_ else "AP", k))
                    last = pe.matmul(b[rows, 0:P], buf(k, XX)[:, 0:HD], buf(k, NQ, i)[:, P:], start=True, stop=True,
                                     skip_group_check=True)
                return last
            if what == "GH":
                pe.wait_ge(rw_uby, H * i + 2 * h + 2)
                two = [(rows, slice(k * HD, (k + 1) * HD), k) for rows, k in two]
                for rows, cols, k in two:
                    pe.matmul(b[rows, 0:P].rearrange("p (c v) -> p c v", c=2), buf(k, XX)[:, 0:HD],
                              b_by[:, :, cols], start=True, stop=False, skip_group_check=True)
                for rows, cols, k in two:
                    pe.matmul(b[rows, P:2 * P], nat(i, 0, cols), u_by[:, k].rearrange("p c v -> p (c v)"),
                              start=False, stop=False, skip_group_check=True)
                for rows, cols, k in two:
                    last = pe.matmul(b[rows, P:2 * P].rearrange("p (c v) -> p c v", c=2), nat(i, 3, cols),
                                     v_by[:, :, cols], start=False, stop=True, skip_group_check=True)
                return last
            if what == "CH":
                taken(pe, op(i, "GH", 2))
                if h:
                    taken(pe, op(i, "CH", 0))
                elif i:
                    taken(pe, op(i - 1, "CH", 1))
                else:
                    pe.wait_ge(s_s0, 2)
                for k in range(H):
                    rows, m = head(k)
                    last = pe.matmul(b[rows, m * HD:(m + 1) * HD], gts[rows, m, h],
                                     states[rows, (2 * i + h) % 4, m], start=True, stop=True)
                return last
            if what == "Y":
                taken(pe, op(i, "RT", h))
                taken(pe, op(i, "CH", 0))
                for rows, k in two:
                    pe.matmul(b[rows, 0:P], buf(k, XX)[:, HD:P], buf(k, NQ, i)[:, P:], start=True, stop=False,
                              skip_group_check=True)
                for rows, k in two:
                    pe.matmul(b[rows, 0:P], nat(i, 6, slice(k * HD, (k + 1) * HD)), buf(k, MP, i)[:, P:],
                              start=False, stop=False, skip_group_check=True)
                for c in range(2):
                    for rows, k in two:
                        last = pe.matmul(b[rows, 64 * c:64 * c + 64], states[rows, (2 * i + c) % 4, h],
                                         rt_[rows, h, 64 * c:64 * c + 64], start=False, stop=(c == 1),
                                         skip_group_check=True)
                return last
            m = h // 2
            x = buf(h, XX)
            if what in ("NQ", "MP"):
                pe.wait_ge(rw_lone, 12 * i + 6 * (what == "MP") + h + 1)
                return pe.matmul(b[:, 0:256], lone[:, int(what == "MP"), h],
                                 AR[:, m, i].rearrange("p w t -> p (w t)"), start=True, stop=True)
            if what == "NT":
                taken(pe, op(i, "NQ", h))
                return pe.transpose(b[:, 0:P], buf(h, NQ, i)[:, 0:P], ident)
            if what == "MV":
                taken(pe, op(i, "MP", h))
                taken(pe, op(i, "nat", 3))
                return pe.matmul(b[:, 0:P], buf(h, MP, i)[:, 0:P], nat(i, 6, slice(m * P, (m + 1) * P)), start=True,
                                 stop=True)
            if what in ("P2", "P4"):
                src = buf(h, ND if what == "P2" else PA)
                taken(pe, op(i, "NT" if what == "P2" else "P2", h))
                if what == "P2":
                    pe.wait_ge(rw_diag, H * i + h + 1)
                pe.matmul(b[:, 0:P], src[:, P:], src[:, 0:P], start=True, stop=True)
                return pe.matmul(b[:, P:256], src[:, 0:P], src[:, P:], start=True, stop=True)
            if what == "P8":
                taken(pe, op(i, "P4", h))
                return pe.matmul(b[:, 0:P], buf(h, PB)[:, P:], buf(h, PB)[:, 0:P], start=True, stop=True)
            if what in ("T2", "T4", "T8"):
                taken(pe, op(i, "P" + what[1], h))
                if what == "T2":
                    pe.wait_ge(rw_tinv, H * i + h + 1)
                else:
                    taken(pe, op(i, {"T4": "T2", "T8": "T4"}[what], h))
                w = buf(h, {"T2": PA, "T4": PB, "T8": ND}[what])[:, 0:P]
                return pe.matmul(b[:, 0:P], w, tinv[:, h], start=True, stop=True)
            if what == "AP":
                taken(pe, op(i, "T8" if i < NPT_ else "T4", h))
                taken(pe, op(i, "MV", h))
                taken(pe, op(i, "nat", 0))
                return pe.matmul(b[:, 0:P], tinv[:, h], x[:, 0:P], start=True, stop=True)
            if what == "ZT":
                taken(pe, op(i, "NT", h))
                return pe.matmul(b[:, 0:P], x[:, P:], tinv[:, h], start=True, stop=True)
            taken(pe, op(i, {"H1": "ZT", "H2": "H1", "H3": "H2"}[what], h))
            taken(pe, op(i, "AP", h))
            return pe.matmul(b[:, 0:P], buf(h, ND)[:, P:], x[:, 0:P] if what == "H1" else buf(h, PA)[:, 0:P],
                             start=True, stop=True)

        def take_dve(dve, turn):
            mk = masks(turn)
            for i, what, h in sequence(turn):
                n = op(i, what, h)
                if not by_dve(n):
                    continue
                b = PS[n % 8]
                dve.wait_ge(rw_mm, n + 1)
                if what == "nat":
                    for k in range(H):
                        ins = dve.tensor_copy(buf(k, XX)[:, 0:HD], b[:, k * HD:(k + 1) * HD])
                elif what in ("NQ", "MP"):
                    ins = dve.tensor_tensor(buf(h, NQ if what == "NQ" else MP, i), b[:, 0:256], C("keep" + mk), ALU.mult)
                elif what == "NT":
                    ins = dve.tensor_tensor(buf(h, ND)[:, 0:P], b[:, 0:P], C("diag" + mk), ALU.mult)
                    if i < NPT_:
                        ins = dve.tensor_tensor(buf(h, XX)[:, P:], b[:, 0:P], C("off_p"), ALU.mult)
                elif what in ("T2", "T4", "T8"):
                    ins = dve.tensor_tensor(tinv[:, h], b[:, 0:P], tinv[:, h], ALU.add)
                elif what in ("H1", "H2"):
                    ins = dve.tensor_tensor(buf(h, PA)[:, 0:P], b[:, 0:P], buf(h, XX)[:, 0:P], ALU.add)
                elif what == "H3":
                    ins = dve.tensor_tensor(buf(h, XX)[:, 0:P], b[:, 0:P], buf(h, XX)[:, 0:P], ALU.add)
                elif what == "RT":
                    ins = dve.tensor_tensor(rt_[:, h], b[:, 0:P], AR[:, h, i, 1], ALU.add)
                elif what == "GH":
                    dve.tensor_tensor(gts[:, h], b[:, 0:P].rearrange("p (c v) -> p c v", c=2),
                                      C("eye_pair").rearrange("p (c v) -> p c v", c=2), ALU.add)
                    for c in range(2):
                        ins = dve.tensor_scalar(hss[:, h, c], b[:, P + HD * c:P + HD * c + HD],
                                                dc[:, h, 2 * i + c:2 * i + c + 1], None, ALU.mult)
                else:
                    q = 2 * i + h
                    for m in range(3):
                        ins = dve.scalar_tensor_tensor(out=states[:, (q + 1) % 4, m],
                                                       in0=b[:, m * HD:(m + 1) * HD], scalar=dc[:, m, q:q + 1],
                                                       in1=hss[:, m, h], op0=ALU.mult, op1=ALU.add)
                ins.then_inc(rw_dve, 1)

        def take_act(act, turn):
            def u_by_chunk(i, h):
                taken(act, op(i, "H3", h))
                for c in range(2):
                    tr = slice(HD * c, HD * c + HD)
                    ins = nc.scalar.copy(u_by[tr, h, c], buf(h, XX)[tr, HD:P])
                ins.then_inc(rw_uby, 1)

            for i, what, h in sequence(turn):
                n = op(i, what, h)
                if by_dve(n):
                    continue
                b = PS[n % 8]
                act.wait_ge(rw_mm, n + 1)
                if what == "nat":
                    act.wait_ge(rw_lone, 2 * H * (i + 1))
                    ins = nc.scalar.copy(sT[:, 3 * h - 3:3 * h, i * P:(i + 1) * P],
                                         b[:, 0:AW].rearrange("p (m t) -> p m t", m=3))
                    if i < NPT_ and h != 2:
                        for c in range(2):
                            tr = slice(HD * c, HD * c + HD)
                            ins = nc.scalar.copy((b_by if h == 1 else v_by)[tr, c], b[tr, 0:AW])
                elif what == "MV":
                    ins = nc.scalar.copy(buf(h, XX)[:, HD:P], b[:, HD * (h % 2):HD * (h % 2) + HD])
                elif what == "Y":
                    ins = nc.scalar.copy(AR[:, h, i, 0], b[:, 0:P])
                else:
                    dst, w = {"P2": (buf(h, PA), 256), "P4": (buf(h, PB), 256), "P8": (buf(h, ND)[:, 0:P], P),
                              "AP": (buf(h, XX)[:, 0:P], P), "ZT": (buf(h, ND)[:, P:], P)}[what]
                    ins = nc.scalar.copy(dst, b[:, 0:w])
                ins.then_inc(rw_act, 1)
                if what == "ZT" and h == H - 1:
                    for k in range(H):
                        u_by_chunk(i, k)

        def lone_heads(pool, i):
            for w in range(2):
                for h in range(H):
                    rows, m = head(h)
                    if w + h:
                        pool.wait_ge(rw_lone, 2 * H * i + H * w + h)
                    elif i:
                        pool.wait_ge(rw_tinv, H * i)
                    if i >= 1:
                        pool.wait_ge(rw_mm, op(i - 1, ("NQ", "MP")[w], h) + 1)
                    nc.gpsimd.tensor_copy(lone[rows, w, h], sT[rows, 3 * w + m, i * P:(i + 1) * P]
                                          ).then_inc(rw_lone, 1)

        def diagonals(pool, i):
            pool.wait_ge(rw_lone, 2 * H * (i + 1))
            for h in range(H):
                taken(pool, op(i, "NQ", h))
                if i >= 1:
                    pool.wait_ge(rw_mm, op(i - 1, "H3", h) + 1)
                nc.gpsimd.tensor_tensor(buf(h, ND)[:, P:], buf(h, NQ, i)[:, 0:P], C("diag" + masks(i)), ALU.mult
                                        ).then_inc(rw_diag, 1)
                pool.wait_ge(rw_diag, H * i + h + 1)
                nc.gpsimd.tensor_tensor(tinv[:, h], buf(h, ND)[:, P:], ident, ALU.add).then_inc(rw_tinv, 1)

        with nc.Block() as block:
            @block.gpsimd
            def _(pool):
                nc.gpsimd.memset(lone, 0.0).then_inc(s_s0, 1)
                nc.gpsimd.memset(states[:, 0], 0.0)
                nc.gpsimd.memset(b_by, 0.0)
                nc.gpsimd.memset(v_by, 0.0)
                nc.gpsimd.memset(u_by, 0.0).then_inc(s_s0, 1)
                pool.wait_ge(s_s0, 2)
                lone_heads(pool, 0)
                for i in range(NPT_):
                    diagonals(pool, i)
                    lone_heads(pool, i + 1)

            @block.tensor
            def _(pe):
                for i in range(NPT_):
                    products(pe, i)

            @block.vector
            def _(dve):
                for i in range(NPT_):
                    take_dve(dve, i)

            @block.scalar
            def _(act):
                act.wait_ge(s_s0, 2)
                for i in range(NPT_):
                    take_act(act, i)
        if upto == "recur":
            return

        i8 = TT - 1
        SL = sT[:, 3:5, 0:768].rearrange("p a (q c) -> p a q c", q=2)
        s0 = [sT[:, m, 0:512] for m in range(3)]
        um = [sT[0:64, k, a:a + 512] for k, a in ((5, 0), (6, 0), (0, 512), (1, 512))]
        vm = [sT[0:64, k, a:a + 512] for k, a in ((7, 0), (8, 0), (8, 512), (2, 512))]
        spread = [sT[:, 5, 512:896], sT[:, 6, 512:896]]
        hss_out = sT[0:64, 7, 512:896]
        wt, ut = (x.rearrange("p (m t) -> p m t", m=3) for x in spread)
        s_sl, st_t, st_cp, sm_mm, sm_act, sm_dve, sm_vm, sm_add, sm_new = (
            sem("states_in2"), sem("states_turned"), sem("statesT_copied"), sem("sample_product"),
            sem("sample_taken_act"), sem("sample_taken_dve"), sem("sample_values_spread"),
            sem("sample_states_added"), sem("sample_states_new"))

        of_sequence = C("seq_of")[0:NS, :].unsqueeze(2).broadcast_to([NS, NB, HD])

        def s_taken(eng, q):
            if q < 18:
                eng.wait_ge(sm_act, q + 1)
            elif q < 24:
                eng.wait_ge(sm_dve, q - 17)
            elif q < 30:
                eng.wait_ge(sm_add, q - 23)
            else:
                eng.wait_ge(sm_act, q - 11)

        with nc.Block() as block:
            @block.sync
            def _(sp):
                for b in range(NB):
                    q, half = divmod(b, 2)
                    sp.dma_start(SL[64 * half:64 * half + 64, q // 2, q % 2].rearrange("p (h j) -> p h j", h=H),
                                 I["state_wkv"][0, b].rearrange("h i j -> i h j")).then_inc(s_sl, 16)

            @block.gpsimd
            def _(pool):
                diagonals(pool, i8)
                pool.wait_ge(rw_tinv, H * TT)
                taken(pool, op(i8, "nat", 3))
                for h in range(H):
                    if h >= 4:
                        pool.wait_ge(sm_mm, 24 + h - 3)
                    nc.gpsimd.tensor_tensor(vm[h % 4].rearrange("p (b v) -> p b v", b=NB),
                                            nat(i8, 6, slice(h * HD, (h + 1) * HD))[0:NS].unsqueeze(1)
                                            .broadcast_to([NS, NB, HD]), of_sequence, ALU.mult).then_inc(sm_vm, 1)

            @block.tensor
            def _(pe):
                products(pe, i8)
                taken(pe, op(i8, "RT", 2))
                taken(pe, op(i8, "AP", 5))
                pe.wait_ge(s_sl, 128)
                for m in range(3):
                    for q in range(4):
                        last = pe.transpose(PS[m][:, q * P:(q + 1) * P], SL[:, q // 2, q % 2, m * P:(m + 1) * P], ident)
                last.then_inc(st_t, 1)
                pe.wait_ge(st_cp, 3)
                for q in range(34):
                    b = PS[q % 8]
                    if q >= 8:
                        s_taken(pe, q - 8)
                    what, h = divmod(q, 6)
                    if q < 30:
                        rows, m = head(h)
                        x = buf(h, XX)
                        cols = slice(h * HD, (h + 1) * HD)
                    if what == 0:
                        last = pe.matmul(b[rows, 0:NS], x[:, 0:HD], ident[:, 0:NS], start=True, stop=True)
                    elif what == 1:
                        s_taken(pe, h)
                        pe.matmul(b[rows, 0:NS], x[:, HD:P], ident[:, 0:NS], start=True, stop=False,
                                  skip_group_check=True)
                        for s in range(NB):
                            last = pe.matmul(b[rows, TS * s:TS * s + TS], s0[m][rows, s * HD:(s + 1) * HD],
                                             wt[rows, m, TS * s:TS * s + TS], start=False, stop=(s == NB - 1),
                                             skip_group_check=True)
                    elif what == 2:
                        pe.matmul(b[rows, 0:P], x[:, HD:P], buf(h, NQ, i8)[:, P:], start=True, stop=False,
                                  skip_group_check=True)
                        pe.matmul(b[rows, 0:P], nat(i8, 6, cols), buf(h, MP, i8)[:, P:], start=False, stop=False,
                                  skip_group_check=True)
                        for s in range(NB):
                            last = pe.matmul(b[rows, TS * s:TS * s + TS], s0[m][rows, s * HD:(s + 1) * HD],
                                             rt_[rows, m, TS * s:TS * s + TS], start=False, stop=(s == NB - 1),
                                             skip_group_check=True)
                    elif what == 3:
                        s_taken(pe, 6 + h)
                        last = pe.matmul(b[0:NS, 0:HD], ut[rows, m, 0:NS], ident[rows, 64 * (h % 2):64 * (h % 2) + 64],
                                         start=True, stop=True)
                    elif what == 4:
                        s_taken(pe, 18 + h)
                        pe.wait_ge(sm_vm, h + 1)
                        pe.matmul(b[rows, :], nat(i8, 0, cols)[0:NS], um[h % 4], start=True, stop=False)
                        last = pe.matmul(b[rows, :], nat(i8, 3, cols)[0:NS], vm[h % 4], start=False, stop=True)
                    elif q < 33:
                        m = q - 30
                        pe.wait_ge(sm_new, 2 * (m + 1))
                        for k in range(4):
                            last = pe.transpose(b[:, k * P:(k + 1) * P], s0[m][:, k * P:(k + 1) * P], ident)
                    else:
                        for m in range(3):
                            last = pe.transpose(b[0:HD, m * P:(m + 1) * P], states[:, nch % 4, m], ident)
                    last.then_inc(sm_mm, 1)

            @block.vector
            def _(dve):
                take_dve(dve, i8)
                dve.wait_ge(st_t, 1)
                for m in range(3):
                    dve.tensor_copy(s0[m], PS[m][:, :]).then_inc(st_cp, 1)

                def expand(h):
                    if h >= 4:
                        dve.wait_ge(sm_mm, 24 + h - 3)
                    dve.wait_ge(sm_mm, 18 + h + 1)
                    dve.tensor_tensor(um[h % 4].rearrange("p (b v) -> p b v", b=NB),
                                      PS[(18 + h) % 8][0:NS, 0:HD].unsqueeze(1).broadcast_to([NS, NB, HD]),
                                      of_sequence, ALU.mult).then_inc(sm_dve, 1)

                def new_state(h):
                    rows, m = head(h)
                    dve.wait_ge(sm_mm, 24 + h + 1)
                    st = s0[m][rows]
                    dve.tensor_tensor(st, PS[(24 + h) % 8][rows, :], st, ALU.add).then_inc(sm_add, 1)
                    dve.wait_ge(sm_add, h + 1)
                    st = st.rearrange("p (b v) -> p b v", b=NB)
                    dve.tensor_tensor(st, st, dc[rows, m, nch:].unsqueeze(2).broadcast_to([HD, NB, HD]), ALU.mult
                                      ).then_inc(sm_new, 1)

                for h in range(4):
                    expand(h)
                for h in range(H):
                    new_state(h)
                    if h + 4 < H:
                        expand(h + 4)

            @block.scalar
            def _(act):
                take_act(act, i8)
                for q in range(18):
                    what, h = divmod(q, 6)
                    rows, m = head(h)
                    act.wait_ge(sm_mm, q + 1)
                    b = PS[q % 8]
                    dst = (wt[rows, m], ut[rows, m], AR[rows, m, i8, 0])[what]
                    w = NS if what < 2 else P
                    nc.scalar.copy(dst[:, 0:w], b[rows, 0:w]).then_inc(sm_act, 1)
                for q in range(30, 34):
                    act.wait_ge(sm_mm, q + 1)
                    b = PS[q % 8]
                    if q < 33:
                        m = q - 30
                        nc.scalar.copy(SL[:, :, :, m * P:(m + 1) * P],
                                       b[:, :].rearrange("p (a q c) -> p a q c", a=2, q=2)).then_inc(sm_act, 1)
                    else:
                        nc.scalar.copy(hss_out, b[0:HD, 0:AW]).then_inc(sm_act, 1)
        if upto == "recur_s":
            return

        new_stage()
        cw = Carve(loop_base)
        ysq = [cw.take(384) for _ in range(2)]
        yout = [cw.take(384) for _ in range(3)]
        devs = cw.take(384)
        heads_in = cw.take(480).rearrange("p (m c) -> p m c", m=3)
        jobs = [(m, c) for m in range(3) for c in range(3)]
        NJ = len(jobs)
        g_sig, y_mean, y_cen, y_sqd, y_var, y_root, y_ri, y_bc, g_mm, y_done, y_nrm, y_aff, y_bon = (
            sem("gate_sigmoid"), sem("y_mean"), sem("y_centred"), sem("y_squared"), sem("y_variance"),
            sem("y_root"), sem("y_recip"), sem("y_recip_spread"), sem("gate_product"), sem("mixed_written"),
            sem("y_normed"), sem("y_scaled_shifted"), sem("bonus_added"))
        w_out = I["w_out"][0].rearrange("(k p) c -> p k c", p=P)
        w_out_raw = [tiled(work[:, KD * T + 2 * T + i * KD * P:][:, 0:KD * P]) for i in range(2)]
        assert cw.at <= KD * T + 2 * T
        s_xr, s_hd = sem("residual_back"), sem("head_sums_in2")
        with nc.Block() as block:
            @block.sync
            def _(sp):
                sp.dma_start(heads_in, I["c_heads"]).then_inc(s_hd, 16)
                for b in range(NB):
                    q, half = divmod(b, 2)
                    sp.dma_start(wkv_s[0, b].rearrange("h i j -> i h j"),
                                 SL[64 * half:64 * half + 64, q // 2, q % 2].rearrange("p (h j) -> p h j", h=H)
                                 ).then_inc(s_wo, 16)
                sp.dma_start(wkv_p[0, 0].rearrange("h i j -> i h j"),
                             hss_out.rearrange("p (h j) -> p h j", h=H)).then_inc(s_wo, 16)
                for m in range(2):
                    sp.dma_start(w_out_raw[m], w_out[:, :, m * P:(m + 1) * P]).then_inc(s_w[m], 16)
                sp.dma_start(xT, spill).then_inc(s_xr, 16)
                sp.wait_ge(s_xr, 16)
                sp.wait_ge(s_wo, 16 * 9)

            @block.tensor
            def _(pe):
                def mean(j):
                    m, c = jobs[j]
                    if j >= 2:
                        pe.wait_ge(y_cen, j - 1)
                    pe.matmul(PS[j % 2][:, 0:384], C("head_ones"), AR[:, m, 3 * c:3 * c + 3, 0], start=True,
                              stop=True).then_inc(y_mean, 1)

                def gate_product(j):
                    m, c = jobs[j]
                    if j >= 3:
                        pe.wait_ge(y_done, j - 2)
                    pe.matmul(PS[5 + j % 3][:, 0:384], g2[:, m * P:(m + 1) * P], sT[:, 10, 384 * c:384 * (c + 1)],
                              start=True, stop=True).then_inc(g_mm, 1)

                mean(0)
                mean(1)
                pe.wait_ge(s_hd, 16)
                for j, (m, c) in enumerate(jobs):
                    pe.wait_ge(y_sqd, j + 1)
                    pe.matmul(PS[2][32 * c:32 * c + 32, 0:384], heads_in[:, m, 0:32], ysq[j % 2], start=(m == 0),
                              stop=(m == 2), skip_group_check=True).then_inc(y_var, 1)
                    if j + 2 < NJ:
                        mean(j + 2)
                pe.wait_ge(g_sig, 2)
                for j in range(3):
                    gate_product(j)
                pe.wait_ge(y_ri, 1)
                for j, (m, c) in enumerate(jobs):
                    if j >= 2:
                        pe.wait_ge(y_nrm, j - 1)
                    rows = slice(32 * c, 32 * c + 32)
                    pe.matmul(PS[3 + j % 2][:, 0:384], heads_in[rows, m, 32:], devs[rows], start=True, stop=True
                              ).then_inc(y_bc, 1)
                    if 3 <= j:
                        gate_product(j)

            @block.scalar
            def _(act):
                nc.scalar.activation(sT[:, 10], sT[:, 10], ACT.Tanh, scale=0.5).then_inc(g_sig, 1)
                for j, (m, c) in enumerate(jobs):
                    act.wait_ge(y_cen, j + 1)
                    if j >= 2:
                        act.wait_ge(y_var, j - 1)
                    nc.scalar.activation(tiles3(ysq[j % 2]), AR[:, m, 3 * c:3 * c + 3, 0], ACT.Square
                                         ).then_inc(y_sqd, 1)
                act.wait_ge(y_var, NJ)
                nc.scalar.activation(devs[0:96], PS[2][0:96, 0:384], ACT.Sqrt, scale=1.0 / HD, bias=epsc[0:96, 1:2]
                                     ).then_inc(y_root, 1)
                for j, (m, _) in enumerate(jobs):
                    act.wait_ge(y_nrm, j + 1)
                    nc.scalar.activation(yout[j % 3], yout[j % 3], ACT.Identity, scale=lnx[:, m:m + 1],
                                         bias=lnx[:, 3 + m:4 + m]).then_inc(y_aff, 1)

            @block.vector
            def _(dve):
                dve.wait_ge(g_sig, 1)
                dve.tensor_scalar(sT[:, 10], sT[:, 10], 0.5, 0.5, ALU.mult, ALU.add).then_inc(g_sig, 1)
                for j, (m, c) in enumerate(jobs):
                    y = AR[:, m, 3 * c:3 * c + 3, 0]
                    dve.wait_ge(y_mean, j + 1)
                    dve.scalar_tensor_tensor(out=y, in0=tiles3(PS[j % 2][:, 0:384]), scalar=-1.0 / HD, in1=y,
                                             op0=ALU.mult, op1=ALU.add).then_inc(y_cen, 1)
                dve.wait_ge(y_root, 1)
                dve.reciprocal(devs[0:96], devs[0:96]).then_inc(y_ri, 1)

                def gate(j):
                    m, c = jobs[j]
                    t0, n = CH[c]
                    dve.wait_ge(g_mm, j + 1)
                    dve.wait_ge(y_bon, j + 1)
                    dve.tensor_tensor(mixT[:, m, t0:t0 + n], PS[5 + j % 3][:, 0:n], yout[j % 3][:, 0:n], ALU.mult
                                      ).then_inc(y_done, 1)

                for j, (m, c) in enumerate(jobs):
                    dve.wait_ge(y_bc, j + 1)
                    if j >= 3:
                        dve.wait_ge(y_done, j - 2)
                    dve.tensor_tensor(tiles3(yout[j % 3]), tiles3(PS[3 + j % 2][:, 0:384]),
                                      AR[:, m, 3 * c:3 * c + 3, 0], ALU.mult).then_inc(y_nrm, 1)
                    if j >= 2:
                        gate(j - 2)
                gate(NJ - 2)
                gate(NJ - 1)

            @block.gpsimd
            def _(pool):
                for j, (m, c) in enumerate(jobs):
                    t0, n = CH[c]
                    o = yout[j % 3]
                    pool.wait_ge(y_aff, j + 1)
                    nc.gpsimd.tensor_tensor(o[:, 0:n], o[:, 0:n], mixT[:, m, t0:t0 + n], ALU.add
                                            ).then_inc(y_bon, 1)
        if upto == "mixed":
            return

        new_stage()
        LO_NOW = 3
        mx2 = split_pair("mixed", RS + A_TILES * TPAD - KD * T, RK_, KD * T, KD)
        assert LO_NOW * T <= A_TILES * TPAD - KD * T
        cw = Carve(KD * T)
        sqa, sqb = cw.take(T), cw.take(T)
        wraw = w_out_raw
        R1 = KD * T + (18 * FT + 7) // 8 * 8 + 2 * T
        rstd = sT_[:, R1:R1 + T]
        xn2 = split_pair("normed2T", RA, RS, KD * T, KD)
        w_hi, w_lo, x_hi, x_lo = sem("w_out_hi"), sem("w_out_lo"), sem("mixed_hi"), sem("mixed_lo")
        inv_rms = sqb[:, 0:384]
        rms_parts = [(slice(0, 96), slice(0, CH[2][1])), (slice(0, 64), slice(CH[2][1], CH[0][1]))]
        n_sp = sem("res_recip_spread")
        op_mm, op_cp, n_sq, n_acc, n_mm, n_rt, n_ri, n_hi, n_lo = (
            sem("out_product"), sem("residual_added"), sem("res_squared"), sem("res_squares_added"),
            sem("res_summed"), sem("res_root"), sem("res_recip"), sem("res_scaled_hi"), sem("res_scaled_lo"))
        parts = [(c, k) for c in range(3) for k in range(KD)]
        w_up = I["w_up"][0].rearrange("(k p) c -> p k c", p=P)
        ffn_raw = [tiled(work[:, WORK - (i + 1) * KD * P:][:, 0:KD * P]) for i in range(3)]
        with nc.Block() as block:
            def out_hi(act, m):
                act.wait_ge(s_w[m % 2], 16 * (m // 2 + 1))
                split_hi(m, (KD, P), wraw[m % 2], w_hi, op_mm, 3)

            @block.sync
            def _(sp):
                for j in range(2):
                    c0 = DFF if j == 0 else 0
                    sp.dma_start(ffn_raw[j], w_up[:, :, c0:c0 + P]).then_inc(s_wu[j], 16)
                for m in range(2, KD):
                    sp.wait_ge(w_lo, m - 1)
                    sp.dma_start(wraw[m % 2], w_out[:, :, m * P:(m + 1) * P]).then_inc(s_w[m % 2], 16)

            @block.tensor
            def _(pe):
                for m in range(KD):
                    pe.wait_ge(w_lo, m + 1)
                    for c, (t0, n) in enumerate(CH):
                        g = 3 * m + c
                        if g >= 5:
                            pe.wait_ge(op_cp, g - 4)
                        for k in range(KD):
                            if m == 0:
                                pe.wait_ge(x_lo, KD * c + k + 1)
                            last = product(pe, PS[g % 5][:, 0:n], [w[:, k] for w in wsp[m % 2]],
                                           [x[:, k, t0:t0 + n] for x in mx2], k == 0, k == KD - 1)
                        last.then_inc(op_mm, 1)
                for c, (t0, n) in enumerate(CH):
                    pe.wait_ge(n_acc, 3 * (KD - 1) + c + 1)
                    pe.matmul(PS[5][32 * c:32 * c + 32, 0:n], ones[:, 0:32], sqa[:, t0:t0 + n], start=True,
                              stop=True, skip_group_check=True).then_inc(n_mm, 1)
                for c, (t0, n) in enumerate(CH):
                    pe.wait_ge(n_ri, 2)
                    b = PS[(6, 7, 5)[c]]
                    pe.matmul(b[:, 0:n], ones[32 * c:32 * c + 1, :], inv_rms[32 * c:32 * c + 1, 0:n], start=True,
                              stop=True).then_inc(n_sp, 1)

            @block.scalar
            def _(act):
                out_hi(act, 0)
                for c, k in parts:
                    t0, n = CH[c]
                    nc.scalar.copy(mx2[0][:, k, t0:t0 + n], mixT[:, k, t0:t0 + n]).then_inc(x_hi, 1)
                out_hi(act, 1)
                act.wait_ge(x_lo, KD * 3)
                for m in range(KD):
                    for c, (t0, n) in enumerate(CH):
                        act.wait_ge(op_cp, 3 * m + c + 1)
                        if m >= 2:
                            act.wait_ge(n_acc, 3 * (m - 1) + c + 1)
                        dst = sqa if m == 0 else sqb
                        nc.scalar.activation(dst[:, t0:t0 + n], xT[:, m, t0:t0 + n], ACT.Square).then_inc(n_sq, 1)
                        nc.scalar.activation(xn2[0][:, m, t0:t0 + n], xT[:, m, t0:t0 + n], ACT.Copy,
                                             scale=vec("norm_ffn_g", m)).then_inc(n_hi, 1)
                    if m + 2 < KD:
                        out_hi(act, m + 2)
                act.wait_ge(n_mm, 3)
                for rows, cols in rms_parts:
                    nc.scalar.activation(inv_rms[rows, cols], PS[5][rows, cols], ACT.Sqrt, scale=1.0 / D,
                                         bias=epsc[rows, 0:1]).then_inc(n_rt, 1)
                for c, (t0, n) in enumerate(CH):
                    act.wait_ge(n_sp, c + 1)
                    nc.scalar.copy(rstd[:, t0:t0 + n], PS[(6, 7, 5)[c]][:, 0:n])

            @block.vector
            def _(dve):
                def scaled_lo(m):
                    for c, (t0, n) in enumerate(CH):
                        dve.wait_ge(n_hi, 3 * m + c + 1)
                        dve.scalar_tensor_tensor(out=xn2[1][:, m, t0:t0 + n], in0=xT[:, m, t0:t0 + n],
                                                 scalar=vec("norm_ffn_g", m),
                                                 in1=xn2[0][:, m, t0:t0 + n].bitcast(F32), op0=ALU.mult,
                                                 op1=ALU.subtract).then_inc(n_lo, 1)

                split_lo(0, (KD, P), wraw[0], w_hi, w_lo)
                for j, (c, k) in enumerate(parts):
                    t0, n = CH[c]
                    dve.wait_ge(x_hi, j + 1)
                    dve.tensor_tensor(mx2[1][:, k, t0:t0 + n], mixT[:, k, t0:t0 + n],
                                      mx2[0][:, k, t0:t0 + n].bitcast(F32), ALU.subtract).then_inc(x_lo, 1)
                split_lo(1, (KD, P), wraw[1], w_hi, w_lo)
                for m in range(KD):
                    for c, (t0, n) in enumerate(CH):
                        g = 3 * m + c
                        dve.wait_ge(op_mm, g + 1)
                        dve.tensor_tensor(xT[:, m, t0:t0 + n], PS[g % 5][:, 0:n], xT[:, m, t0:t0 + n], ALU.add
                                          ).then_inc(op_cp, 1)
                    if m + 2 < KD:
                        split_lo(m + 2, (KD, P), wraw[m % 2], w_hi, w_lo)
                    if 1 <= m <= LO_NOW:
                        scaled_lo(m - 1)
                for m in range(LO_NOW, KD - 1):
                    scaled_lo(m)
                for j, (rows, cols) in enumerate(rms_parts):
                    dve.wait_ge(n_rt, j + 1)
                    dve.reciprocal(inv_rms[rows, cols], inv_rms[rows, cols]).then_inc(n_ri, 1)
                scaled_lo(KD - 1)

            @block.gpsimd
            def _(pool):
                for c in range(3):
                    pool.wait_ge(n_sq, c + 1)
                    pool.sem_inc(n_acc, 1)
                for m in range(1, KD):
                    for c, (t0, n) in enumerate(CH):
                        pool.wait_ge(n_sq, 3 * m + c + 1)
                        nc.gpsimd.tensor_tensor(sqa[:, t0:t0 + n], sqa[:, t0:t0 + n], sqb[:, t0:t0 + n], ALU.add
                                                ).then_inc(n_acc, 1)
        if upto == "outproj":
            return

        new_stage()
        GROUPS = [4, 4, 4, 4, 3, 3]
        G = max(GROUPS)
        first_of = [sum(GROUPS[:i]) for i in range(len(GROUPS) + 1)]
        stream = []
        for gi, n in enumerate(GROUPS):
            for f in range(first_of[gi], first_of[gi] + n):
                stream.append(("gate", f))
                if f == first_of[gi] and gi:
                    stream += [("down", gi - 1, m) for m in range(KD)]
                stream.append(("up", f))
        stream += [("down", len(GROUPS) - 1, m) for m in range(KD)]
        NW = len(stream)
        nth = {"gate": 0, "up": 0, "down": 0}
        order = []
        for item in stream:
            order.append(nth[item[0]])
            nth[item[0]] += 1
        S2 = KD * T
        gend = sT_[:, S2:S2 + 18 * FT].rearrange("p (j f) -> p j f", f=FT)
        S2 += (18 * FT + 7) // 8 * 8
        cv, hraw = sT_[:, S2:S2 + T], sT_[:, S2 + T:S2 + 2 * T]
        assert S2 + 2 * T == R1
        h2 = split_pair("inner", RK_, RK_ + G * T, G * T, G)
        cw = Carve(2 * G * T)
        GW = 2 + SEQ + NB * (2 + TS)
        gring = [cw.take(GW) for _ in range(2)]
        wraw = ffn_raw
        assert cw.at <= WORK - 3 * KD * P
        w_down = I["w_down"][0].rearrange("(f p) c -> p f c", p=P)
        w_hi, w_lo = sem("w_ffn_hi"), sem("w_ffn_lo")
        f_mm, f_gate, f_conv, f_steps, f_tanh, f_pre, f_st, f_up, f_hh, f_hl, f_dn = (
            sem("ffn_product"), sem("gate_copied"), sem("conv_done"), sem("conv_steps"), sem("silu_tanh"),
            sem("gate_prefix"), sem("gate_history"), sem("up_taken"), sem("inner_hi"), sem("inner_lo"),
            sem("down_added"))

        def rows_w(j):
            return KD if stream[j][0] != "down" else GROUPS[stream[j][1]]

        def slot_of(f):
            gi = max(i for i in range(len(GROUPS)) if first_of[i] <= f)
            return f - first_of[gi]

        def down_after(f):
            gi = max(i for i in range(len(GROUPS)) if first_of[i] <= f)
            return KD * gi

        with nc.Block() as block:
            def ffn_hi(act, j):
                act.wait_ge(s_wu[j % 3], 16 * (j // 3 + 1))
                split_hi(j, (rows_w(j), P), wraw[j % 3], w_hi, f_mm, 3)

            def ffn_lo(dve, j):
                split_lo(j, (rows_w(j), P), wraw[j % 3], w_hi, w_lo)

            @block.sync
            def _(sp):
                for j, item in enumerate(stream):
                    if j < 2:
                        continue
                    if j >= 3:
                        sp.wait_ge(w_lo, j - 2)
                    if item[0] == "down":
                        f0 = first_of[item[1]]
                        src = w_down[:, f0:f0 + rows_w(j), item[2] * P:(item[2] + 1) * P]
                    else:
                        c0 = item[1] * P + (0 if item[0] == "up" else DFF)
                        src = w_up[:, :, c0:c0 + P]
                    sp.dma_start(wraw[j % 3][:, 0:rows_w(j)], src).then_inc(s_wu[j % 3], 16)

            @block.tensor
            def _(pe):
                for j, item in enumerate(stream):
                    pe.wait_ge(w_lo, j + 1)
                    if item[0] == "down":
                        pe.wait_ge(f_hl, first_of[item[1] + 1])
                    x = h2 if item[0] == "down" else xn2
                    for c, (t0, n) in enumerate(CH):
                        g = 3 * j + c
                        if g >= 8:
                            pj, pc = divmod(g - 8, 3)
                            done = {"gate": f_gate, "up": f_up, "down": f_dn}[stream[pj][0]]
                            pe.wait_ge(done, 3 * order[pj] + pc + 1)
                        for k in range(rows_w(j)):
                            last = product(pe, PS[g % 8][:, 0:n], [w[:, k] for w in wsp[j % 2]],
                                           [v[:, k, t0:t0 + n] for v in x], k == 0, k == rows_w(j) - 1)
                        last.then_inc(f_mm, 1)

            @block.gpsimd
            def _(pool):
                for j in range(2):
                    ins = nc.gpsimd.memset(gring[j][:, 0:2], 0.0)
                ins.then_inc(f_pre, 1)
                for f in range(FT):
                    if f >= 2:
                        pool.wait_ge(f_conv, f - 1)
                    nc.gpsimd.tensor_copy(seg(gring[f % 2], 2)[1][:, :, 0:2],
                                          convT[:, f].rearrange("p (b t) -> p b t", b=NB)).then_inc(f_pre, 1)
                    pool.wait_ge(f_gate, 3 * f + 3)
                    p_seq, s_seq = seg(gring[f % 2], 2)
                    nc.gpsimd.tensor_copy(gend[:, 0:2, f], p_seq[:, SEQ - 2:SEQ])
                    nc.gpsimd.tensor_copy(gend[:, 2:18, f].rearrange("p (b t) -> p b t", b=NB),
                                          s_seq[:, :, TS:TS + 2]).then_inc(f_st, 1)

            @block.scalar
            def _(act):
                def gate(j, f):
                    act.wait_ge(f_conv, f + 1)
                    if f >= 1:
                        act.wait_ge(f_hl, f)
                    nc.scalar.activation(hraw, cv, ACT.Tanh, scale=0.5).then_inc(f_tanh, 1)

                ffn_hi(act, 0)
                ffn_hi(act, 1)
                for j, item in enumerate(stream):
                    if item[0] == "gate":
                        gate(j, item[1])
                    elif item[0] == "up":
                        f = item[1]
                        act.wait_ge(f_up, 3 * f + 3)
                        if down_after(f):
                            act.wait_ge(f_dn, 3 * down_after(f))
                        nc.scalar.copy(h2[0][:, slot_of(f)], hraw).then_inc(f_hh, 1)
                    if j + 2 < NW:
                        ffn_hi(act, j + 2)

            @block.vector
            def _(dve):
                link = chain(dve, f_steps)

                def take_gate(j, f):
                    if f >= 2:
                        dve.wait_ge(f_st, f - 1)
                    p_seq, s_seq = seg(gring[f % 2], 2)
                    for c, (t0, n) in enumerate(CH):
                        g = 3 * j + c
                        dve.wait_ge(f_mm, g + 1)
                        k = min(n, SEQ - t0)
                        ins = dve.tensor_tensor(p_seq[:, t0:t0 + k], PS[g % 8][:, 0:k], rstd[:, t0:t0 + k], ALU.mult)
                        if c == 2:
                            by_seq = [x.rearrange("p (b t) -> p b t", b=NB)
                                      for x in (PS[g % 8][:, k:k + NS], rstd[:, SEQ:T])]
                            ins = dve.tensor_tensor(s_seq[:, :, 2:], by_seq[0], by_seq[1], ALU.mult)
                        ins.then_inc(f_gate, 1)

                def conv(f):
                    p_all = gring[f % 2][:, 0:2 + SEQ]
                    s_all = seg(gring[f % 2], 2)[1]
                    cv_s = cv[:, SEQ:T].rearrange("p (b t) -> p b t", b=NB)
                    dve.wait_ge(f_gate, 3 * f + 3)
                    dve.wait_ge(f_pre, f + 2)
                    for t in range(3):
                        w = vec("conv_w", t * FT + f)
                        if t == 0:
                            dve.tensor_scalar(cv[:, 0:SEQ], p_all[:, 0:SEQ], w, vec("conv_b", f), ALU.mult, ALU.add)
                            link(dve.tensor_scalar(cv_s, s_all[:, :, 0:TS], w, vec("conv_b", f), ALU.mult, ALU.add))
                        else:
                            dve.scalar_tensor_tensor(out=cv[:, 0:SEQ], in0=p_all[:, t:t + SEQ], scalar=w,
                                                     in1=cv[:, 0:SEQ], op0=ALU.mult, op1=ALU.add)
                            ins = dve.scalar_tensor_tensor(out=cv_s, in0=s_all[:, :, t:t + TS], scalar=w, in1=cv_s,
                                                           op0=ALU.mult, op1=ALU.add)
                            if t == 1:
                                link(ins)
                            else:
                                ins.then_inc(f_conv, 1)

                def inner(j, f):
                    dve.wait_ge(f_tanh, f + 1)
                    link(dve.scalar_tensor_tensor(out=hraw, in0=hraw, scalar=1.0, in1=cv, op0=ALU.add,
                                                  op1=ALU.mult))
                    link(dve.tensor_tensor(hraw, hraw, rstd, ALU.mult))
                    for c, (t0, n) in enumerate(CH):
                        g = 3 * j + c
                        dve.wait_ge(f_mm, g + 1)
                        dve.scalar_tensor_tensor(out=hraw[:, t0:t0 + n], in0=PS[g % 8][:, 0:n], scalar=0.5,
                                                 in1=hraw[:, t0:t0 + n], op0=ALU.mult, op1=ALU.mult
                                                 ).then_inc(f_up, 1)
                    dve.wait_ge(f_hh, f + 1)
                    dve.tensor_tensor(h2[1][:, slot_of(f)], hraw, h2[0][:, slot_of(f)].bitcast(F32), ALU.subtract
                                      ).then_inc(f_hl, 1)

                ffn_lo(dve, 0)
                ffn_lo(dve, 1)
                for j, item in enumerate(stream):
                    if item[0] == "gate":
                        take_gate(j, item[1])
                        conv(item[1])
                    elif item[0] == "up":
                        inner(j, item[1])
                    else:
                        m = item[2]
                        for c, (t0, n) in enumerate(CH):
                            dve.wait_ge(f_mm, 3 * j + c + 1)
                            dve.tensor_tensor(xT[:, m, t0:t0 + n], PS[(3 * j + c) % 8][:, 0:n], xT[:, m, t0:t0 + n],
                                              ALU.add).then_inc(f_dn, 1)
                    if j + 2 < NW:
                        ffn_lo(dve, j + 2)
        if upto == "down":
            return

        new_stage()
        cnat = wring[:, 0:4 * P].rearrange("p (q c) -> p q c", q=4)
        g_t, g_cp = sem("history_turned"), sem("history_copied")
        g_last = work[:, 0:D]
        yrow = [work[:, D * (1 + i):D * (2 + i)] for i in range(YR)]
        junk = work[:, (1 + YR) * D:(1 + YR) * D + 512]
        fs = small[:, 0:5 * TT].rearrange("p (i a) -> p i a", i=TT)
        s_gl, e_t, e_sq, e_sum, e_rt, e_ri, e_y = (sem("final_gain_in"), sem("final_turned"), sem("final_squared"),
                                                   sem("final_sum"), sem("final_root"), sem("final_recip"),
                                                   sem("final_scaled"))
        with nc.Block() as block:
            @block.sync
            def _(sp):
                sp.dma_start(g_last, I["norm_final_g"].partition_broadcast(P)).then_inc(s_gl, 16)
                sp.wait_ge(g_cp, 1)
                sp.dma_start(conv_p[0, 0].rearrange("t (f c) -> (t f) c", c=P), cnat[0:44, 0]).then_inc(s_co, 16)
                flat = conv_s[0].rearrange("b t (f c) -> (b t f) c", c=P)
                for q in range(3):
                    n = min(P, 352 - q * P)
                    sp.dma_start(flat[q * P:q * P + n, :], cnat[0:n, q + 1]).then_inc(s_co, 16)
                for i in range(TT):
                    n = rows_of(i)
                    sp.wait_ge(e_y, 2 * i + 2)
                    dst = y_prompt[0, i * P:(i + 1) * P, :] if i < TT - 1 else y_sample.rearrange("b t d -> (b t) d")
                    sp.dma_start(dst, yrow[i % YR][0:n, :]).then_inc(s_y[i % YR], 16)
                for j in range(YR):
                    sp.wait_ge(s_y[j], 16 * len(range(j, TT, YR)))
                sp.wait_ge(s_co, 64)

            @block.tensor
            def _(pe):
                flat = gend.rearrange("p j f -> p (j f)")
                for q, (a, n) in enumerate(((0, 44), (44, P), (44 + P, P), (44 + 2 * P, 96))):
                    last = pe.transpose(PS[7][0:n, q * P:(q + 1) * P], flat[:, a:a + n], ident)
                last.then_inc(g_t, 1)
                for i in range(TT):
                    n = rows_of(i)
                    if i == 3:
                        pe.wait_ge(g_cp, 1)
                    if i >= 4:
                        pe.wait_ge(e_y, 2 * (i - 3))
                    for k in range(KD):
                        last = pe.transpose(PS[2 * (i % 4) + k // 4][0:n, (k % 4) * P:(k % 4 + 1) * P],
                                            xT[:, k, i * P:i * P + n], ident)
                    last.then_inc(e_t, 1)

            @block.scalar
            def _(act):
                def squares(i):
                    n = rows_of(i)
                    act.wait_ge(e_t, i + 1)
                    for j in range(2):
                        k = 2 * i + j
                        if k >= 1:
                            act.wait_ge(e_sq, k)
                        nc.scalar.activation(junk[0:n, :], PS[2 * (i % 4) + j][0:n, :], ACT.Square,
                                             accum_out=fs[0:n, i, j:j + 1]).then_inc(e_sq, 1)

                squares(0)
                for i in range(TT):
                    n = rows_of(i)
                    if i + 1 < TT:
                        squares(i + 1)
                    act.wait_ge(e_sum, i + 1)
                    nc.scalar.activation(fs[0:n, i, 3:4], fs[0:n, i, 2:3], ACT.Sqrt, scale=1.0 / D,
                                         bias=epsc[0:n, 0:1]).then_inc(e_rt, 1)

            @block.vector
            def _(dve):
                def total(i):
                    n = rows_of(i)
                    dve.wait_ge(e_sq, 2 * i + 2)
                    dve.tensor_tensor(fs[0:n, i, 2:3], fs[0:n, i, 0:1], fs[0:n, i, 1:2], ALU.add).then_inc(e_sum, 1)

                def scaled(i, j):
                    n = rows_of(i)
                    dve.scalar_tensor_tensor(out=yrow[i % YR][0:n, 512 * j:512 * j + 512],
                                             in0=PS[2 * (i % 4) + j][0:n, :], scalar=fs[0:n, i, 4:5],
                                             in1=g_last[0:n, 512 * j:512 * j + 512], op0=ALU.mult,
                                             op1=ALU.mult).then_inc(e_y, 1)

                dve.wait_ge(g_t, 1)
                for q, n in enumerate((44, P, P, 96)):
                    ins = dve.tensor_copy(cnat[0:n, q], PS[7][0:n, q * P:(q + 1) * P])
                ins.then_inc(g_cp, 1)
                dve.wait_ge(s_gl, 16)
                total(0)
                for i in range(TT):
                    n = rows_of(i)
                    dve.wait_ge(e_rt, i + 1)
                    dve.reciprocal(fs[0:n, i, 4:5], fs[0:n, i, 3:4]).then_inc(e_ri, 1)
                    dve.wait_ge(e_ri, i + 1)
                    if i >= YR:
                        dve.wait_ge(s_y[i % YR], 16 * (i // YR))
                    scaled(i, 0)
                    if i + 1 < TT:
                        total(i + 1)
                    scaled(i, 1)


def kernel(**inputs):
    import numpy as _np
    import concourse.bacc as _bacc
    from concourse import mybir as _mybir
    from concourse.bass_utils import run_bass_kernel_spmd as _run

    nc = _bacc.Bacc("TRN2", target_bir_lowering=False, num_devices=1)
    arrays, args = {}, {}
    for name, a in {**inputs, **constants()}.items():
        a = _np.ascontiguousarray(a)
        arrays[f"in_{name}_dram"] = a
        args[name] = nc.dram_tensor(f"in_{name}_dram", a.shape, _mybir.dt.from_np(a.dtype), kind="ExternalInput").ap()
    outs = [nc.dram_tensor(f"out_{i}_dram", shape, _mybir.dt.float32, kind="ExternalOutput").ap()
            for i, shape in enumerate(OUT_SHAPES)]
    build(nc, args, outs)
    r = _run(nc, [arrays], core_ids=[0])
    return tuple(r.results[0][f"out_{i}_dram"] for i in range(len(OUT_SHAPES)))
```
